# Optimizing a Trainium2 kernel written in Bass

```python
import math
import jax, jax.numpy as jnp
from jax import lax
import numpy as np

D_MODEL = 1024
BATCH = 1
SEQ = 1024
DEPTH = 1
DEC_BATCH = 8
DEC_SEQ = 8
PAST_LEN = 1024
PAGE_SIZE = 128

HEAD_DIM = 64
ATTN_GROUPS = ((128, 1), (512, 4), (2048, 16))
HEADS_PER_GROUP = 4
N_ATTN_HEADS = HEADS_PER_GROUP * len(ATTN_GROUPS)
ATTN_WIDTH = N_ATTN_HEADS * HEAD_DIM
ATTN_OUT_WIDTH = HEADS_PER_GROUP * HEAD_DIM
ROPE_THETA = 10000.0
SSD_D_INNER = D_MODEL
SSD_HEAD_DIM = 64
SSD_HEADS = SSD_D_INNER // SSD_HEAD_DIM
SSD_GROUPS = 2
SSD_HEADS_PER_GROUP = SSD_HEADS // SSD_GROUPS
SSD_STATE = 128
SSD_CONV = 4
SSD_CHUNK = 128
SSD_CONV_DIM = SSD_D_INNER + 2 * SSD_GROUPS * SSD_STATE
N_EXPERT_GROUPS = 4
EXPERTS_PER_GROUP = 8
N_EXPERTS = N_EXPERT_GROUPS * EXPERTS_PER_GROUP
TOP_K = 2
D_FF_EXPERT = 512
MOE_BLOCK = 128
NORM_EPS = 1e-6
IN_SPLITS = (ATTN_WIDTH, ATTN_WIDTH, ATTN_WIDTH, SSD_D_INNER, SSD_CONV_DIM, SSD_HEADS, D_MODEL, D_MODEL)
D_IN_PROJ = 6928

kernel_name = "hybrid_dilated_attn_ssd_hmoe_step"

def _rms_norm(x, w):
    xf = x.astype(jnp.float32)
    y = xf * lax.rsqrt(jnp.mean(xf * xf, axis=-1, keepdims=True) + NORM_EPS)
    return (y * w.astype(jnp.float32)).astype(x.dtype)

def _rope(x, pos):
    half = HEAD_DIM // 2
    inv_freq = ROPE_THETA ** (-jnp.arange(half, dtype=jnp.float32) * (2.0 / HEAD_DIM))
    ang = pos.astype(jnp.float32)[:, None] * inv_freq[None, :]
    ang = jnp.concatenate([ang, ang], axis=-1)[None, :, None, :]
    xf = x.astype(jnp.float32)
    rot = jnp.concatenate([-xf[..., half:], xf[..., :half]], axis=-1)
    return (xf * jnp.cos(ang) + rot * jnp.sin(ang)).astype(x.dtype)

def _dilated_attn_prompt(q, k, v, dil, span):
    b, S, H, Dh = q.shape
    n = S // dil
    nb = -(-n // span)
    npad = nb * span

    def to_blocks(t):
        t = t.reshape(b, n, dil, H, Dh).transpose(0, 2, 1, 3, 4)
        t = jnp.pad(t, ((0, 0), (0, 0), (0, npad - n), (0, 0), (0, 0)))
        return t.reshape(b, dil, nb, span, H, Dh).astype(jnp.float32)

    def with_prev(t):
        prev = jnp.pad(t[:, :, :-1], ((0, 0), (0, 0), (1, 0), (0, 0), (0, 0), (0, 0)))
        return jnp.concatenate([prev, t], axis=3)

    qb = to_blocks(q)
    kk = with_prev(to_blocks(k))
    vv = with_prev(to_blocks(v))
    s = jnp.einsum("brcqhd,brckhd->brchqk", qb, kk) * (Dh ** -0.5)
    i = jnp.arange(span)[:, None]
    j = jnp.arange(2 * span)[None, :]
    blk = jnp.arange(nb)[:, None, None]
    valid = (j >= i) & (j <= i + span) & ((blk > 0) | (j >= span))
    s = jnp.where(valid[None, None, :, None], s, -jnp.inf)
    m = jnp.max(s, axis=-1, keepdims=True)
    p = jnp.exp(s - m)
    den = jnp.sum(p, axis=-1)
    o = jnp.einsum("brchqk,brckhd->brcqhd", p, vv) / jnp.swapaxes(den, -1, -2)[..., None]
    lse = jnp.swapaxes(m[..., 0] + jnp.log(den), -1, -2)
    o = o.reshape(b, dil, npad, H, Dh)[:, :, :n].transpose(0, 2, 1, 3, 4).reshape(b, S, H, Dh)
    lse = lse.reshape(b, dil, npad, H)[:, :, :n].transpose(0, 2, 1, 3).reshape(b, S, H)
    return o, lse

def _dilated_attn_step(q, k_new, v_new, buf, dil, span, window):
    b, T, H, Dh = q.shape
    Lb = buf.shape[1]
    kk = jnp.concatenate([buf[:, :, 0].astype(k_new.dtype), k_new], axis=1)
    vv = jnp.concatenate([buf[:, :, 1].astype(v_new.dtype), v_new], axis=1)
    idx = Lb + jnp.arange(T)[:, None] - dil * jnp.arange(span + 1)[None, :]
    valid = idx >= 0
    idx = jnp.maximum(idx, 0)
    kg = kk[:, idx].astype(jnp.float32)
    vg = vv[:, idx].astype(jnp.float32)
    s = jnp.einsum("bthd,btkhd->bhtk", q.astype(jnp.float32), kg) * (Dh ** -0.5)
    s = jnp.where(valid[None, None], s, -jnp.inf)
    m = jnp.max(s, axis=-1, keepdims=True)
    p = jnp.exp(s - m)
    den = jnp.sum(p, axis=-1)
    o = jnp.einsum("bhtk,btkhd->bthd", p, vg) / jnp.swapaxes(den, 1, 2)[..., None]
    lse = jnp.swapaxes(m[..., 0] + jnp.log(den), 1, 2)
    new_len = min(window, Lb + T)
    new_buf = jnp.stack([kk, vv], axis=2)[:, Lb + T - new_len:]
    return o, lse, new_buf

def _attn_branch(q, k, v, kv_bufs):
    b, L = q.shape[:2]
    outs, lses, new_kv = [], [], []
    for gi, (window, dil) in enumerate(ATTN_GROUPS):
        hs = slice(gi * HEADS_PER_GROUP, (gi + 1) * HEADS_PER_GROUP)
        span = window // dil
        qg, kg, vg = q[:, :, hs], k[:, :, hs], v[:, :, hs]
        if kv_bufs is None:
            o, lse = _dilated_attn_prompt(qg, kg, vg, dil, span)
            keep = min(window, L)
            nbuf = jnp.stack([kg, vg], axis=2)[:, L - keep:]
        else:
            o, lse, nbuf = _dilated_attn_step(qg, kg, vg, kv_bufs[gi], dil, span, window)
        outs.append(o)
        lses.append(lse)
        new_kv.append(nbuf)
    wts = jax.nn.softmax(jnp.stack(lses), axis=0)
    o = jnp.sum(wts[..., None] * jnp.stack(outs), axis=0)
    return o.reshape(b, L, ATTN_OUT_WIDTH).astype(q.dtype), new_kv

def _ssd_scan(x, dt, A, Bm, Cm, h0, chunk):
    b, L, G, E, P = x.shape
    N = Bm.shape[-1]
    nc = L // chunk
    x = x.reshape(b, nc, chunk, G, E, P)
    dt = dt.reshape(b, nc, chunk, G, E)
    Bm = Bm.reshape(b, nc, chunk, G, N)
    Cm = Cm.reshape(b, nc, chunk, G, N)
    a_cs = jnp.cumsum(dt * A, axis=2)
    xdt = x * dt[..., None]
    seg = a_cs[:, :, :, None] - a_cs[:, :, None, :]
    causal = (jnp.arange(chunk)[:, None] >= jnp.arange(chunk)[None, :])[None, None, :, :, None, None]
    decay_ls = jnp.exp(jnp.where(causal, seg, -jnp.inf))
    cb = jnp.einsum("bclgn,bcsgn->bclsg", Cm, Bm)
    y_diag = jnp.einsum("bclsg,bclsge,bcsgep->bclgep", cb, decay_ls, xdt)
    decay_end = jnp.exp(a_cs[:, :, -1:] - a_cs)
    states = jnp.einsum("bclgn,bclge,bclgep->bcgepn", Bm, decay_end, xdt)
    chunk_decay = jnp.exp(a_cs[:, :, -1])

    def step(h, inp):
        dec, st = inp
        return h * dec[..., None, None] + st, h

    h_final, h_prev = lax.scan(step, h0, (jnp.moveaxis(chunk_decay, 1, 0), jnp.moveaxis(states, 1, 0)))
    h_prev = jnp.moveaxis(h_prev, 0, 1)
    y_off = jnp.einsum("bclgn,bcgepn,bclge->bclgep", Cm, h_prev, jnp.exp(a_cs))
    return (y_diag + y_off).reshape(b, L, G, E, P), h_final

def _ssd_branch(z, xbc, dt_raw, conv_state, ssm_state, conv_w, conv_b, dt_bias, A_log, D_skip, ssd_norm_w):
    b, L, _ = xbc.shape
    if conv_state is None:
        conv_state = jnp.zeros((b, SSD_CONV - 1, SSD_CONV_DIM), xbc.dtype)
    xpad = jnp.concatenate([conv_state.astype(xbc.dtype), xbc], axis=1)
    xc = conv_b + sum(xpad[:, t:t + L] * conv_w[t] for t in range(SSD_CONV))
    xc = jax.nn.silu(xc)
    new_conv = xpad[:, L:]
    xs = xc[..., :SSD_D_INNER].reshape(b, L, SSD_GROUPS, SSD_HEADS_PER_GROUP, SSD_HEAD_DIM).astype(jnp.float32)
    Bm = xc[..., SSD_D_INNER:SSD_D_INNER + SSD_GROUPS * SSD_STATE].reshape(b, L, SSD_GROUPS, SSD_STATE).astype(jnp.float32)
    Cm = xc[..., SSD_D_INNER + SSD_GROUPS * SSD_STATE:].reshape(b, L, SSD_GROUPS, SSD_STATE).astype(jnp.float32)
    dt = jax.nn.softplus(dt_raw.astype(jnp.float32) + dt_bias.astype(jnp.float32))
    dt = dt.reshape(b, L, SSD_GROUPS, SSD_HEADS_PER_GROUP)
    A = -jnp.exp(A_log.astype(jnp.float32)).reshape(SSD_GROUPS, SSD_HEADS_PER_GROUP)
    if ssm_state is None:
        h0 = jnp.zeros((b, SSD_GROUPS, SSD_HEADS_PER_GROUP, SSD_HEAD_DIM, SSD_STATE), jnp.float32)
    else:
        h0 = ssm_state.astype(jnp.float32).reshape(b, SSD_GROUPS, SSD_HEADS_PER_GROUP, SSD_HEAD_DIM, SSD_STATE)
    chunk = SSD_CHUNK if L % SSD_CHUNK == 0 else L
    y, h_final = _ssd_scan(xs, dt, A, Bm, Cm, h0, chunk)
    y = y + xs * D_skip.astype(jnp.float32).reshape(SSD_GROUPS, SSD_HEADS_PER_GROUP)[..., None]
    g = (y.reshape(b, L, SSD_D_INNER) * jax.nn.silu(z.astype(jnp.float32))).reshape(b, L, SSD_GROUPS, -1)
    g = g * lax.rsqrt(jnp.mean(g * g, axis=-1, keepdims=True) + NORM_EPS)
    y_out = (g.reshape(b, L, SSD_D_INNER) * ssd_norm_w.astype(jnp.float32)).astype(z.dtype)
    return y_out, new_conv, h_final.reshape(b, SSD_HEADS, SSD_HEAD_DIM, SSD_STATE)

def _hier_moe(x, w_rc, b_rc, w_rf, b_rf, w_eg, w_eu, w_ed):
    n, d = x.shape
    xf = x.astype(jnp.float32)
    lc = xf @ w_rc.astype(jnp.float32) + b_rc.astype(jnp.float32)
    pc = jax.nn.softmax(lc, axis=-1)
    grp = jnp.argmax(lc, axis=-1)
    p_grp = jnp.take_along_axis(pc, grp[:, None], axis=-1)[:, 0]
    lf = (xf @ w_rf.astype(jnp.float32) + b_rf.astype(jnp.float32)).reshape(n, N_EXPERT_GROUPS, EXPERTS_PER_GROUP)
    lf = jnp.take_along_axis(lf, grp[:, None, None], axis=1)[:, 0]
    top_v, top_i = lax.top_k(lf, TOP_K)
    gate = p_grp[:, None] * jax.nn.softmax(top_v, axis=-1)
    expert = grp[:, None] * EXPERTS_PER_GROUP + top_i
    n_assign = n * TOP_K
    e_flat = expert.reshape(-1)
    w_flat = gate.reshape(-1)
    t_flat = jnp.repeat(jnp.arange(n), TOP_K)
    order = jnp.argsort(e_flat)
    e_s, t_s, w_s = e_flat[order], t_flat[order], w_flat[order]
    counts = jnp.zeros((N_EXPERTS,), jnp.int32).at[e_flat].add(1)
    starts = jnp.cumsum(counts) - counts
    pcounts = ((counts + MOE_BLOCK - 1) // MOE_BLOCK) * MOE_BLOCK
    pends = jnp.cumsum(pcounts)
    pstarts = pends - pcounts
    dest = pstarts[e_s] + (jnp.arange(n_assign) - starts[e_s])
    n_blocks = -(-n_assign // MOE_BLOCK) + N_EXPERTS
    xbuf = jnp.zeros((n_blocks * MOE_BLOCK, d), x.dtype).at[dest].set(x[t_s])
    blk_e = jnp.minimum(jnp.searchsorted(pends, jnp.arange(n_blocks) * MOE_BLOCK, side="right"), N_EXPERTS - 1)

    def run_block(args):
        xb, e = args
        hb = jax.nn.silu(xb @ w_eg[e]) * (xb @ w_eu[e])
        return hb @ w_ed[e]

    out = lax.map(run_block, (xbuf.reshape(n_blocks, MOE_BLOCK, d), blk_e)).reshape(n_blocks * MOE_BLOCK, d)
    y = jnp.zeros((n, d), jnp.float32).at[t_s].add(out[dest].astype(jnp.float32) * w_s[:, None])
    return y.astype(x.dtype)

def _decoder_layer(x, pos, kv_bufs, conv_state, ssm_state, norm1_w, w_in, w_attn_br, w_ssd_br, b_gate, w_out,
                   conv_w, conv_b, dt_bias, A_log, D_skip, ssd_norm_w, norm2_w, w_rc, b_rc, w_rf, b_rf,
                   w_eg, w_eu, w_ed):
    b, L, _ = x.shape
    xn = _rms_norm(x, norm1_w)
    u = xn @ w_in
    offs = [int(o) for o in np.cumsum(IN_SPLITS)[:-1]]
    q, k, v, z, xbc, dt_raw, g_a, g_s = jnp.split(u, offs, axis=-1)
    q = _rope(q.reshape(b, L, N_ATTN_HEADS, HEAD_DIM), pos)
    k = _rope(k.reshape(b, L, N_ATTN_HEADS, HEAD_DIM), pos)
    v = v.reshape(b, L, N_ATTN_HEADS, HEAD_DIM)
    y_attn, new_kv = _attn_branch(q, k, v, kv_bufs)
    y_ssd, new_conv, new_ssm = _ssd_branch(z, xbc, dt_raw, conv_state, ssm_state, conv_w, conv_b, dt_bias,
                                           A_log, D_skip, ssd_norm_w)
    merged = (jax.nn.sigmoid(g_a + b_gate[0]) * (y_attn @ w_attn_br)
              + jax.nn.sigmoid(g_s + b_gate[1]) * (y_ssd @ w_ssd_br))
    h = x + merged @ w_out
    hn = _rms_norm(h, norm2_w).reshape(b * L, D_MODEL)
    h = h + _hier_moe(hn, w_rc, b_rc, w_rf, b_rf, w_eg, w_eu, w_ed).reshape(b, L, D_MODEL)
    return h, new_kv, new_conv, new_ssm

def setup_inputs(seed: int = 0) -> dict:
    key = jax.random.key(seed)
    ks = jax.random.split(key, 32)

    def nrm(k, shape, scale):
        return jax.random.normal(k, shape, jnp.float32) * scale

    kv_shape = lambda w: (DEPTH, DEC_BATCH, min(w, PAST_LEN), 2, HEADS_PER_GROUP, HEAD_DIM)
    dt0 = jnp.exp(jax.random.uniform(ks[12], (DEPTH, SSD_HEADS), jnp.float32, math.log(1e-3), math.log(1e-1)))
    return {
        "x_prompt": nrm(ks[0], (BATCH, SEQ, D_MODEL), 1.0),
        "x_sample": nrm(ks[1], (DEC_BATCH, DEC_SEQ, D_MODEL), 1.0),
        "cache_kv_w128": nrm(ks[2], kv_shape(ATTN_GROUPS[0][0]), 1.0),
        "cache_kv_w512": nrm(ks[3], kv_shape(ATTN_GROUPS[1][0]), 1.0),
        "cache_kv_w2048": nrm(ks[4], kv_shape(ATTN_GROUPS[2][0]), 1.0),
        "state_conv": nrm(ks[5], (DEPTH, DEC_BATCH, SSD_CONV - 1, SSD_CONV_DIM), 1.0),
        "state_ssm": nrm(ks[6], (DEPTH, DEC_BATCH, SSD_HEADS, SSD_HEAD_DIM, SSD_STATE), 0.5),
        "norm1_w": 1.0 + nrm(ks[7], (DEPTH, D_MODEL), 0.02),
        "w_in": nrm(ks[8], (DEPTH, D_MODEL, D_IN_PROJ), D_MODEL ** -0.5),
        "w_attn_br": nrm(ks[9], (DEPTH, ATTN_OUT_WIDTH, D_MODEL), ATTN_OUT_WIDTH ** -0.5),
        "w_ssd_br": nrm(ks[10], (DEPTH, SSD_D_INNER, D_MODEL), SSD_D_INNER ** -0.5),
        "b_gate": nrm(ks[11], (DEPTH, 2, D_MODEL), 0.02),
        "w_out": nrm(ks[13], (DEPTH, D_MODEL, D_MODEL), D_MODEL ** -0.5),
        "conv_w": nrm(ks[14], (DEPTH, SSD_CONV, SSD_CONV_DIM), SSD_CONV ** -0.5),
        "conv_b": nrm(ks[15], (DEPTH, SSD_CONV_DIM), 0.02),
        "dt_bias": dt0 + jnp.log(-jnp.expm1(-dt0)),
        "A_log": jnp.log(jax.random.uniform(ks[16], (DEPTH, SSD_HEADS), jnp.float32, 1.0, 16.0)),
        "D_skip": 1.0 + nrm(ks[17], (DEPTH, SSD_HEADS), 0.1),
        "ssd_norm_w": 1.0 + nrm(ks[18], (DEPTH, SSD_D_INNER), 0.02),
        "norm2_w": 1.0 + nrm(ks[19], (DEPTH, D_MODEL), 0.02),
        "w_router_coarse": nrm(ks[20], (DEPTH, D_MODEL, N_EXPERT_GROUPS), D_MODEL ** -0.5),
        "b_router_coarse": nrm(ks[21], (DEPTH, N_EXPERT_GROUPS), 0.01),
        "w_router_fine": nrm(ks[22], (DEPTH, D_MODEL, N_EXPERTS), D_MODEL ** -0.5),
        "b_router_fine": nrm(ks[23], (DEPTH, N_EXPERTS), 0.01),
        "w_expert_gate": nrm(ks[24], (DEPTH, N_EXPERTS, D_MODEL, D_FF_EXPERT), D_MODEL ** -0.5),
        "w_expert_up": nrm(ks[25], (DEPTH, N_EXPERTS, D_MODEL, D_FF_EXPERT), D_MODEL ** -0.5),
        "w_expert_down": nrm(ks[26], (DEPTH, N_EXPERTS, D_FF_EXPERT, D_MODEL), D_FF_EXPERT ** -0.5),
        "final_norm_w": 1.0 + nrm(ks[27], (D_MODEL,), 0.02),
    }

def reference(x_prompt, x_sample, cache_kv_w128, cache_kv_w512, cache_kv_w2048, state_conv, state_ssm,
              norm1_w, w_in, w_attn_br, w_ssd_br, b_gate, w_out, conv_w, conv_b, dt_bias, A_log, D_skip,
              ssd_norm_w, norm2_w, w_router_coarse, b_router_coarse, w_router_fine, b_router_fine,
              w_expert_gate, w_expert_up, w_expert_down, final_norm_w):
    pos_p = jnp.arange(x_prompt.shape[1], dtype=jnp.int32)
    pos_s = PAST_LEN + jnp.arange(x_sample.shape[1], dtype=jnp.int32)
    h_p, h_s = x_prompt, x_sample
    p_kv = ([], [], [])
    s_kv = ([], [], [])
    p_conv, p_ssm, s_conv, s_ssm = [], [], [], []
    for l in range(DEPTH):
        wl = (norm1_w[l], w_in[l], w_attn_br[l], w_ssd_br[l], b_gate[l], w_out[l], conv_w[l], conv_b[l],
              dt_bias[l], A_log[l], D_skip[l], ssd_norm_w[l], norm2_w[l], w_router_coarse[l], b_router_coarse[l],
              w_router_fine[l], b_router_fine[l], w_expert_gate[l], w_expert_up[l], w_expert_down[l])
        h_p, kv_p, c_p, st_p = _decoder_layer(h_p, pos_p, None, None, None, *wl)
        bufs = (cache_kv_w128[l], cache_kv_w512[l], cache_kv_w2048[l])
        h_s, kv_s, c_s, st_s = _decoder_layer(h_s, pos_s, bufs, state_conv[l], state_ssm[l], *wl)
        for gi in range(len(ATTN_GROUPS)):
            p_kv[gi].append(kv_p[gi])
            s_kv[gi].append(kv_s[gi])
        p_conv.append(c_p)
        p_ssm.append(st_p)
        s_conv.append(c_s)
        s_ssm.append(st_s)
    y_prompt = _rms_norm(h_p, final_norm_w)
    y_sample = _rms_norm(h_s, final_norm_w)
    return (y_prompt, y_sample,
            jnp.stack(p_kv[0]), jnp.stack(p_kv[1]), jnp.stack(p_kv[2]), jnp.stack(p_conv), jnp.stack(p_ssm),
            jnp.stack(s_kv[0]), jnp.stack(s_kv[1]), jnp.stack(s_kv[2]), jnp.stack(s_conv), jnp.stack(s_ssm))


_drawn_inputs = setup_inputs


def setup_inputs(seed=0):
    import zlib

    import numpy as np

    out = dict(_drawn_inputs(seed))
    spreads = {}
    factors = {'b_gate': 4.793,
     'ssd_norm_w': 2.713,
     'b_router_coarse': 38.745,
     'b_router_fine': 15.317,
     'final_norm_w': 9.555,
     'norm2_w': 3.25}
    for name, (base, spread) in spreads.items():
        noise = np.random.default_rng([zlib.crc32(name.encode()), seed]).standard_normal(out[name].shape)
        drawn = base * np.exp(spread * noise) if base else spread * noise
        out[name] = __import__('jax').numpy.asarray(drawn.astype(out[name].dtype))
    for name, factor in factors.items():
        out[name] = (out[name] * factor).astype(out[name].dtype)
    return out
```

```python
import concourse.bass as bass
from concourse import mybir
from contextlib import ExitStack
import numpy as np

f32 = mybir.dt.float32
bf16 = mybir.dt.bfloat16
i32 = mybir.dt.int32
u32 = mybir.dt.uint32
ALU = mybir.AluOpType
ACT = mybir.ActivationFunctionType
AX = mybir.AxisListType
ds = bass.ds

D = 1024
KT = D // 128
SEQ = 1024
NB, NT = 8, 8
SAMP = NB * NT
PAST = 1024
TILES = SEQ // 128 + 1
TOK = TILES * 128
HD = 64
HG = 4
GW = HG * HD
GROUPS = ((128, 1), (512, 4), (2048, 16))
SPAN = 128
AW = 3 * GW
DI = 1024
SH = 16
SN = 128
CONV = 4
XBC = DI + 4 * SN
ZOFF = 3 * AW
XOFF = ZOFF + DI
DTOFF = XOFF + XBC
GOFF = DTOFF + SH
DIN = GOFF + 2 * D
NE = 32
FF = 512
NOVF = 16
NBLK = NE + NOVF
EPS = 1e-6
NEG = -1e30
WCOL = 416
NCH = 384


def bc(ap, shape):
    return ap.broadcast_to(shape)


def phase_norm_project(nc, T, sem):
    with ExitStack() as ctx:
        def sb(name, shape, dt=f32):
            return ctx.enter_context(nc.sbuf_tensor(name, shape, dt))

        xnT = sb("xnT", [128, KT, TOK])
        ident = sb("a_ident", [128, 128])
        w1c = sb("w1c", [128, KT])
        bgc = sb("bgc", [128, 2 * KT])
        eps = sb("a_eps", [128, 1])
        s_const, s_eps = sem("a_const"), sem("a_eps")

        with ExitStack() as c2:
            x_in = c2.enter_context(nc.sbuf_tensor("x_in", [128, 3, D], f32))
            xn = c2.enter_context(nc.sbuf_tensor("xn", [128, 3, D], f32))
            junk = c2.enter_context(nc.sbuf_tensor("a_junk", [128, D], f32))
            ms = c2.enter_context(nc.sbuf_tensor("a_ms", [128, 3, 2], f32))
            turned = c2.enter_context(nc.psum_tensor("a_turned", [128, 3, KT, 128], f32))
            s_x = [sem(f"a_x{u}") for u in range(3)]
            s_std, s_xn, s_turned, s_xfree = sem("a_std"), sem("a_xn"), sem("a_turned"), sem("a_xfree")
            s_tfree, s_cache, s_zt = sem("a_tfree"), T["s_cache"], sem("a_zt")
            zeros = c2.enter_context(nc.sbuf_tensor("a_zeros", [128, D], f32))
            with nc.Block() as block:
                @block.sync
                def _(sp):
                    sp.dma_start(ident[:, :], T["ident"]).then_inc(s_const, 16)
                    sp.dma_start(w1c[:, :], T["norm1_w"].rearrange("p a k -> p (a k)")).then_inc(s_const, 16)
                    sp.dma_start(bgc[:, :], T["b_gate"].rearrange("p a k -> p (a k)")).then_inc(s_const, 16)
                    with sp.Fori(0, 3) as j:
                        for u in range(3):
                            sp.wait_ge(s_xfree, j * 3 + u + 1)
                            sp.dma_start(x_in[:, u, :], T["x_all"][ds((j * 3 + u) * 128, 128), :]).then_inc(s_x[u], 16)

                @block.gpsimd
                def _(pool):
                    for g, (window, dil) in enumerate(GROUPS):
                        old = min(window, PAST)
                        keep = min(window, old + NT) - NT
                        for b in range(NB):
                            pool.dma_start(T["s_kv"][g][0, b, 0:keep, :, :, :].rearrange("r a h d -> r (a h d)"),
                                           T["cache"][g][0, b, old - keep:old, :, :, :].rearrange("r a h d -> r (a h d)")
                                           ).then_inc(s_cache, 16)

                @block.scalar
                def _(act):
                    act.wait_ge(s_eps, 1)
                    act.dma_start(T["o_moe"][NE * 128:, :].rearrange("(b p) c -> p b c", p=128),
                                  bc(zeros[:, :].unsqueeze(1), [128, NOVF, D])).then_inc(s_zt, 16)
                    with act.Fori(0, 3) as j:
                        for u in range(3):
                            act.wait_ge(s_x[u], (j + 1) * 16)
                            nc.scalar.activation(junk[:, :], x_in[:, u, :], ACT.Square, accum_out=ms[:, u, 0:1])
                            act.drain()
                            nc.scalar.activation(ms[:, u, 1:2], ms[:, u, 0:1], ACT.Sqrt, bias=eps[:, :],
                                                 scale=1.0 / D).then_inc(s_std, 1)
                    act.wait_ge(s_zt, 16)

                @block.vector
                def _(dve):
                    nc.vector.memset(zeros[:, :], 0.0)
                    nc.vector.memset(eps[:, :], EPS).then_inc(s_eps, 1)
                    dve.sem_inc(s_xfree, 3)
                    dve.wait_ge(s_const, 48)
                    with dve.Fori(0, 3) as j:
                        for u in range(3):
                            n = j * 3 + u
                            dve.wait_ge(s_std, n + 1)
                            nc.vector.reciprocal(ms[:, u, 1:2], ms[:, u, 1:2])
                            dve.drain()
                            nc.vector.tensor_scalar(xn[:, u, :], x_in[:, u, :], ms[:, u, 1:2], None, ALU.mult
                                                    ).then_inc(s_xn, 1)
                            dve.drain()
                            dve.sem_inc(s_xfree, 1)
                            dve.wait_ge(s_turned, n + 1)
                            for half in range(2):
                                k0 = half * KT // 2
                                nc.vector.tensor_tensor(xnT[:, k0:k0 + 4, ds(n * 128, 128)], turned[:, u, k0:k0 + 4, :],
                                                        bc(w1c[:, k0:k0 + 4].unsqueeze(2), [128, 4, 128]), ALU.mult)
                            dve.drain()
                            dve.sem_inc(s_tfree, 1)

                @block.tensor
                def _(pe):
                    pe.wait_ge(s_const, 48)
                    with pe.Fori(0, 3) as j:
                        for u in range(3):
                            pe.wait_ge(s_xn, j * 3 + u + 1)
                            pe.wait_ge(s_tfree, j * 3 + u)
                            for k in range(KT):
                                last = nc.tensor.transpose(turned[:, u, k, :], xn[:, u, k * 128:(k + 1) * 128], ident[:, :])
                            last.then_inc(s_turned, 1)

        with ExitStack() as c2:
            w_tm = c2.enter_context(nc.sbuf_tensor("w_tm", [128, 2, KT, WCOL], f32))
            w_cm = c2.enter_context(nc.sbuf_tensor("w_cm", [128, 2, KT, 256], f32))
            w_dt = c2.enter_context(nc.sbuf_tensor("w_dt", [128, KT, SH], f32))
            o_tm = c2.enter_context(nc.sbuf_tensor("o_tm", [128, 6, WCOL], f32))
            o_cm = c2.enter_context(nc.sbuf_tensor("o_cm", [128, 4, TOK], f32))
            bias = c2.enter_context(nc.sbuf_tensor("gate_bias", [128, 1], f32))
            acc = [c2.enter_context(nc.psum_tensor(f"a_acc{i}", [128, 512], f32)) for i in range(6)]
            s_wt = [sem(f"a_wt{u}") for u in range(2)]
            s_wc = [sem(f"a_wc{u}") for u in range(2)]
            s_wdt, s_wfree, s_cfree = sem("a_wdt"), sem("a_wfree"), sem("a_cfree")
            s_acc, s_out = sem("a_acc"), sem("a_out")
            s_st = [sem(f"a_st{i}") for i in range(6)]
            s_sc = [sem(f"a_sc{i}") for i in range(4)]
            n_tm = 2 * (XOFF // WCOL // 2) * TILES
            chunks = TOK // NCH
            wt_v = T["w_in"][0].rearrange("(k p) n -> p k n", p=128)

            with nc.Block() as block:
                @block.sync
                def _(sp):
                    with sp.Fori(0, XOFF // WCOL // 2) as j:
                        for u in range(2):
                            sp.wait_ge(s_wfree, j * 2 + u + 1)
                            sp.dma_start(w_tm[:, u, :, :], wt_v[:, :, ds((j * 2 + u) * WCOL, WCOL)]).then_inc(s_wt[u], 16)
                    sp.dma_start(w_dt[:, :, :], wt_v[:, :, DTOFF:DTOFF + SH]).then_inc(s_wdt, 16)
                    for base, count, off in ((0, XBC // 512, XOFF), (XBC // 512, 2 * D // 512, GOFF)):
                        with sp.Fori(0, count) as j:
                            for u in range(2):
                                sp.wait_ge(s_cfree, j * 2 + (2 * base + u + 1))
                                sp.dma_start(w_cm[:, u, :, :], wt_v[:, :, ds((j * 2 + u) * 256 + off, 256)]
                                             ).then_inc(s_wc[u], 16)

                @block.tensor
                def _(pe):
                    pe.sem_inc(s_wfree, 2)
                    pe.sem_inc(s_cfree, 2)
                    with pe.Fori(0, XOFF // WCOL // 2) as j:
                        for u in range(2):
                            pe.wait_ge(s_wt[u], (j + 1) * 16)
                            for m in range(TILES):
                                i = u * TILES + m
                                pe.wait_ge(s_out, j * (2 * TILES) + (i + 1))
                                for k in range(KT):
                                    last = nc.tensor.matmul(acc[i % 6][:, 0:WCOL], xnT[:, k, m * 128:(m + 1) * 128],
                                                            w_tm[:, u, k, :], start=(k == 0), stop=(k == KT - 1))
                                last.then_inc(s_acc, 1)
                            pe.drain()
                            pe.sem_inc(s_wfree, 1)
                    pe.wait_ge(s_wdt, 16)
                    for c in range(chunks):
                        pe.wait_ge(s_out, n_tm + c + 1)
                        for k in range(KT):
                            last = nc.tensor.matmul(acc[c][0:SH, 0:NCH], w_dt[:, k, :], xnT[:, k, c * NCH:(c + 1) * NCH],
                                                    start=(k == 0), stop=(k == KT - 1))
                        last.then_inc(s_acc, 1)
                    for base, count in ((0, XBC // 512), (XBC // 512, 2 * D // 512)):
                        with pe.Fori(0, count) as j:
                            for u in range(2):
                                pe.wait_ge(s_wc[u], (j + (base + 1)) * 16)
                                for cb in range(2):
                                    for c in range(chunks):
                                        i = (u * 2 + cb) * chunks + c
                                        bank = (i + 3) % 6
                                        pe.wait_ge(s_out, j * (4 * chunks) + (n_tm + chunks + base * 4 * chunks + i + 1))
                                        for k in range(KT):
                                            last = nc.tensor.matmul(acc[bank][:, 0:NCH], w_cm[:, u, k, cb * 128:(cb + 1) * 128],
                                                                    xnT[:, k, c * NCH:(c + 1) * NCH],
                                                                    start=(k == 0), stop=(k == KT - 1))
                                        last.then_inc(s_acc, 1)
                                pe.drain()
                                pe.sem_inc(s_cfree, 1)

                @block.scalar
                def _(act):
                    act.sem_inc(s_out, 6)
                    with act.Fori(0, XOFF // WCOL // 2) as j:
                        for u in range(2):
                            for m in range(TILES):
                                i = u * TILES + m
                                act.wait_ge(s_acc, j * (2 * TILES) + (i + 1))
                                act.wait_ge(s_st[i % 6], (j * 3 + i // 6) * 16)
                                nc.scalar.copy(o_tm[:, i % 6, :], acc[i % 6][:, 0:WCOL]).then_inc(s_out, 1)
                                act.drain()
                                act.dma_start(T["u_tm"][m * 128:(m + 1) * 128, ds((j * 2 + u) * WCOL, WCOL)],
                                              o_tm[:, i % 6, :]).then_inc(s_st[i % 6], 16)
                    for c in range(chunks):
                        act.wait_ge(s_acc, n_tm + c + 1)
                        nc.scalar.copy(T["dt_cm"][:, c * NCH:(c + 1) * NCH], acc[c][0:SH, 0:NCH]).then_inc(s_out, 1)
                    for base, count in ((0, XBC // 512), (XBC // 512, 2 * D // 512)):
                        with act.Fori(0, count) as j:
                            for q in range(4):
                                act.wait_ge(s_sc[q], (j + base) * 16)
                                if base:
                                    nc.scalar.copy(bias[:, :], bgc[:, ds(j * 4 + q, 1)])
                                    act.drain()
                                for c in range(chunks):
                                    i = q * chunks + c
                                    act.wait_ge(s_acc, j * (4 * chunks) + (n_tm + chunks + base * 4 * chunks + i + 1))
                                    dst, src = o_cm[:, q, c * NCH:(c + 1) * NCH], acc[(i + 3) % 6][:, 0:NCH]
                                    if base == 0:
                                        nc.scalar.copy(dst, src).then_inc(s_out, 1)
                                    else:
                                        nc.scalar.activation(dst, src, ACT.Sigmoid, bias=bias[:, :]
                                                             ).then_inc(s_out, 1)
                                act.drain()
                                act.dma_start(T["xbc_cm" if base == 0 else "gate_cm"][ds((j * 4 + q) * 128, 128), :],
                                              o_cm[:, q, :]).then_inc(s_sc[q], 16)
                    for i in range(6):
                        act.wait_ge(s_st[i], (XOFF // WCOL // 2) * 3 * 16)
                    for q in range(4):
                        act.wait_ge(s_sc[q], 7 * 16)


def phase_conv(nc, T, sem):
    with ExitStack() as ctx:
        def sb(name, shape, dt=f32):
            return ctx.enter_context(nc.sbuf_tensor(name, shape, dt))

        NC = XBC // 128
        HIST = CONV - 1
        ident = sb("b_ident", [128, 128])
        conv_w, conv_b = sb("conv_w", [128, NC, CONV]), sb("conv_b", [128, NC])
        xp = sb("b_prompt", [128, 2, HIST + SEQ])
        xs = sb("b_sample", [128, 2, NB, HIST + NT])
        rs = sb("b_rows", [128, 2, SAMP])
        acc = sb("b_acc", [128, 2, TOK])
        xc = sb("b_xc", [128, 2, TOK])
        xt = sb("b_xt", [128, 2, TILES, 128])
        raw = sb("b_raw", [128, 2, XBC])
        bias, a_log, neg_a = sb("dt_bias", [SH, 1]), sb("a_log", [SH, 1]), sb("neg_a", [SH, 1])
        sp_a, sp_b = sb("sp_a", [SH, TOK]), sb("sp_b", [SH, TOK])
        pt = [ctx.enter_context(nc.psum_tensor(f"b_pt{i}", [128, 4, 128], f32)) for i in range(8)]
        s_const, s_zero = sem("b_const"), sem("b_zero")
        s_in = [sem(f"b_in{u}") for u in range(2)]
        s_free, s_acc, s_xc, s_pe, s_ev = sem("b_free"), sem("b_acc"), sem("b_xc"), sem("b_pe"), sem("b_ev")
        s_out = [sem(f"b_out{u}") for u in range(2)]
        s_dt, s_dta, s_dtp, s_last = sem("b_dt"), sem("b_dta"), sem("b_dtp"), sem("b_last")
        with nc.Block() as block:
            @block.sync
            def _(sp):
                for dst, src in ((ident[:, :], T["ident"]), (conv_w[:, :, :], T["conv_w"]),
                                 (conv_b[:, :], T["conv_b"].rearrange("p a k -> p (a k)")), (bias[:, :], T["dt_bias"]),
                                 (a_log[:, :], T["A_log"])):
                    sp.dma_start(dst, src).then_inc(s_const, 16)
                sp.wait_ge(s_zero, 1)
                with sp.Fori(0, NC // 2) as j:
                    for u in range(2):
                        rows = ds((j * 2 + u) * 128, 128)
                        sp.wait_ge(s_free, j * 2 + (u + 1))
                        sp.dma_start(xp[:, u, HIST:], T["xbc_cm"][rows, 0:SEQ]).then_inc(s_in[u], 16)
                        sp.dma_start(xs[:, u, :, HIST:], T["xbc_cm"][rows, SEQ:SEQ + SAMP].rearrange("p (b t) -> p b t", b=NB)
                                     ).then_inc(s_in[u], 16)
                        sp.dma_start(rs[:, u, :], T["xbc_cm"][rows, SEQ:SEQ + SAMP]).then_inc(s_in[u], 16)
                        sp.dma_start(xs[:, u, :, 0:HIST], T["state_conv"][rows, :, :]).then_inc(s_in[u], 16)

            @block.gpsimd
            def _(pool):
                nc.gpsimd.memset(xp[:, :, 0:HIST], 0.0)
                nc.gpsimd.memset(acc[:, :, SEQ + SAMP:], 0.0).then_inc(s_zero, 1)

            @block.vector
            def _(dve):
                dve.sem_inc(s_free, 2)
                dve.wait_ge(s_const, 80)
                dve.wait_ge(s_zero, 1)
                nc.vector.tensor_scalar(sp_a[:, :], T["dt_cm"][:, :], bias[:, :], None, ALU.add)
                dve.drain()
                nc.vector.tensor_scalar(sp_b[:, :], sp_a[:, :], -1.0, None, ALU.mult)
                dve.drain()
                nc.vector.tensor_tensor(sp_b[:, :], sp_a[:, :], sp_b[:, :], ALU.min).then_inc(s_dt, 1)
                dve.wait_ge(s_dta, 1)
                nc.vector.scalar_tensor_tensor(sp_a[:, :], sp_a[:, :], 0.0, sp_b[:, :], ALU.max, ALU.add)
                nc.vector.tensor_scalar(neg_a[:, :], a_log[:, :], -1.0, None, ALU.mult)
                dve.drain()
                nc.vector.tensor_scalar(sp_b[:, :], sp_a[:, :], neg_a[:, :], None, ALU.mult).then_inc(s_dt, 1)
                with dve.Fori(0, NC // 2) as j:
                    for u in range(2):
                        c = j * 2 + u
                        dve.wait_ge(s_in[u], (j + 1) * 64)
                        dve.wait_ge(s_xc, j * 2 + u)
                        sample = acc[:, u, SEQ:SEQ + SAMP].rearrange("p (b t) -> p b t", b=NB)
                        for k in range(CONV):
                            w = conv_w[:, ds(c, 1), k:k + 1].rearrange("p a k -> p (a k)")
                            for dst, src in ((acc[:, u, 0:SEQ], xp[:, u, k:k + SEQ]), (sample, xs[:, u, :, k:k + NT])):
                                if k == 0:
                                    last = nc.vector.tensor_scalar(dst, src, w, conv_b[:, ds(c, 1)], ALU.mult, ALU.add)
                                else:
                                    last = nc.vector.scalar_tensor_tensor(dst, src, w, dst, ALU.mult, ALU.add)
                            dve.drain()
                        dve.sem_inc(s_acc, 1)
                        dve.wait_ge(s_pe, c + 1)
                        nc.vector.tensor_copy(xt[:, u, 0:4, :], pt[3 * u][:, :, :])
                        nc.vector.tensor_copy(xt[:, u, 4:8, :], pt[3 * u + 1][:, :, :])
                        nc.vector.tensor_copy(xt[:, u, 8, :], pt[3 * u + 2][:, 0, :])
                        nc.vector.tensor_copy(raw[:, 0, ds(c * 128, 128)], pt[3 * u + 2][:, 1, :])
                        nc.vector.tensor_copy(raw[0:SAMP, 1, ds(c * 128, 128)], pt[3 * u + 2][0:SAMP, 2, :])
                        dve.drain()
                        dve.sem_inc(s_ev, 1)
                        dve.sem_inc(s_free, 1)
                dve.wait_ge(s_dtp, 1)
                for q in range(2):
                    for kind, dst in ((0, T["dt_tm"]), (1, T["da_tm"])):
                        src = pt[6 + q][:, 0:2, :].rearrange("p a b -> p (a b)")
                        n = 5 if q == 0 else 4
                        nc.vector.tensor_copy(dst[:, 5 * q:5 * q + n, :],
                                              src[:, kind * 80:kind * 80 + n * SH].rearrange("p (t h) -> p t h", h=SH))
                dve.drain()
                dve.sem_inc(s_last, 1)

            @block.scalar
            def _(act):
                act.wait_ge(s_dt, 1)
                nc.scalar.activation(sp_b[:, :], sp_b[:, :], ACT.Exp)
                act.wait_ge(s_const, 80)
                nc.scalar.activation(a_log[:, :], a_log[:, :], ACT.Exp)
                act.drain()
                nc.scalar.activation(sp_b[:, :], sp_b[:, :], ACT.Ln, bias=1.0)
                act.drain()
                act.sem_inc(s_dta, 1)
                with act.Fori(0, NC // 2) as j:
                    for u in range(2):
                        c = j * 2 + u
                        act.wait_ge(s_acc, c + 1)
                        act.wait_ge(s_out[u], j * 32)
                        nc.scalar.activation(xc[:, u, :], acc[:, u, :], ACT.Silu)
                        act.drain()
                        act.sem_inc(s_xc, 1)
                        act.dma_start(T["xc_cm"][ds(c * 128, 128), :], xc[:, u, :]).then_inc(s_out[u], 16)
                        act.wait_ge(s_ev, c + 1)
                        act.dma_start(T["xc_tm"][:, ds(c * 128, 128)].rearrange("(t p) c -> p t c", p=128), xt[:, u, :, :]
                                      ).then_inc(s_out[u], 16)
                act.dma_start(T["p_conv"][0, 0, :, :], raw[128 - HIST:128, 0, :]).then_inc(s_out[0], 16)
                for b in range(NB):
                    act.dma_start(T["s_conv"][0, b, :, :], raw[b * NT + NT - HIST:(b + 1) * NT, 1, :]).then_inc(s_out[0], 16)
                act.wait_ge(s_out[0], (NC // 2) * 32 + 16 * (NB + 1))
                act.wait_ge(s_out[1], (NC // 2) * 32)

            @block.tensor
            def _(pe):
                pe.wait_ge(s_const, 80)
                pe.wait_ge(s_zero, 1)
                pe.wait_ge(s_dt, 2)
                for t in range(TILES):
                    for kind, src in ((0, sp_a), (1, sp_b)):
                        off = kind * 80 + (t % 5) * SH
                        dst = pt[6 + t // 5][:, 0:2, :].rearrange("p a b -> p (a b)")[:, off:off + SH]
                        last = nc.tensor.transpose(dst, src[:, t * 128:(t + 1) * 128], ident[0:SH, 0:SH])
                last.then_inc(s_dtp, 1)
                with pe.Fori(0, NC // 2) as j:
                    for u in range(2):
                        c = j * 2 + u
                        pe.wait_ge(s_in[u], (j + 1) * 64)
                        pe.wait_ge(s_ev, c)
                        nc.tensor.transpose(pt[3 * u + 2][:, 1, :], xp[:, u, HIST + SEQ - 128:], ident[:, :])
                        nc.tensor.transpose(pt[3 * u + 2][0:SAMP, 2, :],
                                            rs[:, u, :], ident[:, :])
                        pe.wait_ge(s_xc, c + 1)
                        for t in range(TILES):
                            last = nc.tensor.transpose(pt[3 * u + t // 4][:, t % 4, :], xc[:, u, t * 128:(t + 1) * 128],
                                                       ident[:, :])
                        last.then_inc(s_pe, 1)


def phase_attention_prompt(nc, T, sem):
    with ExitStack() as ctx:
        def sb(name, shape, dt=f32):
            return ctx.enter_context(nc.sbuf_tensor(name, shape, dt))

        def pb(name, shape):
            return ctx.enter_context(nc.psum_tensor(name, shape, f32))

        ident = sb("c_ident", [128, 128])
        rotary = sb("c_rotary", [128, 8, 3, 2 * HD])
        mask_even = sb("mask_even", [128, 4, 256])
        mask_odd = sb("mask_odd", [128, 256])
        mask_half = sb("mask_half", [128, 128])
        qk = sb("c_qk", [128, 2, 3, 2, GW])
        v = sb("c_v", [128, 2, 3, GW])
        rot = sb("c_rot", [128, 2, 3, 2, GW])
        tmp = sb("c_tmp", [128, 3, 2, 2 * HG, HD])
        qT = sb("c_qT", [128, 3, 2, 128])
        kT = sb("c_kT", [128, 3, 2, 2, 128])
        S = sb("c_S", [128, 3, HG, 256])
        P = sb("c_P", [128, 3, HG, 256])
        PT = sb("c_PT", [128, 3, HG, 2, 128])
        mx = sb("c_mx", [128, 3, HG])
        out = sb("c_out", [128, 2, 3, GW + 2 * HG])
        nmx = sb("c_nmx", [128, 3, HG])
        p_qk = pb("c_pqk", [128, 4, 128])
        p_s = [pb(f"c_ps{i}", [128, 2, 256]) for i in range(2)]
        p_t = [pb(f"c_pt{i}", [128, 4, 128]) for i in range(2)]
        p_o = pb("c_po", [128, 3, 128 * 4])
        s_const, s_zero = sem("c_const"), sem("c_zero")
        s_in = [[sem(f"c_in{u}{g}") for g in range(3)] for u in range(2)]
        s_v = [[sem(f"c_v{u}{g}") for g in range(3)] for u in range(2)]
        s_free, s_rot, s_qkt, s_qke = sem("c_free"), sem("c_rot"), sem("c_qkt"), sem("c_qke")
        s_sc, s_sce, s_p, s_pt, s_pte, s_o, s_oe = (sem(f"c_{n}") for n in ("sc", "sce", "p", "pt", "pte", "o", "oe"))
        s_nmx = sem("c_nmx")
        s_kv = [sem(f"c_kv{u}") for u in range(2)]
        s_st = [sem(f"c_st{u}") for u in range(2)]
        SC = HD ** -0.5
        def rows(g, j, u):
            if g == 0:
                return [(0, 128, ds((j * 2 + u) * 128, 128))]
            if g == 1:
                return [(0, 128, ds(j + u * 512, 128, step=4))]
            return [(64 * a, 64, ds(j * 4 + (2 * u + a), 64, step=16)) for a in range(2)]

        KV_DMAS = [4, 6]
        with nc.Block() as block:
            @block.sync
            def _(sp):
                sp.wait_ge(s_zero, 1)
                for dst, src in ((ident[:, :], T["ident"]), (rotary[:, :, :, :], T["rotary"]), (mask_even[:, :, :], T["mask_even"]),
                                 (mask_odd[:, :], T["mask_odd"]), (mask_half[:, :], T["mask_half"])):
                    sp.dma_start(dst, src).then_inc(s_const, 16)
                with sp.Fori(0, 4) as j:
                    for u in range(2):
                        sp.wait_ge(s_rot, (j * 2 + u) * 3)
                        for g in range(3):
                            if g == 2:
                                sp.wait_ge(s_kv[u], j * (16 * KV_DMAS[u]))
                            for p0, n, r in rows(g, j, u):
                                sp.dma_start(qk[p0:p0 + n, u, g, :, :],
                                             T["u_tm"][r, 0:2 * AW].rearrange("r (a c) -> r a c", a=2)[:, :, g * GW:(g + 1) * GW]
                                             ).then_inc(s_in[u][g], 16)
                        sp.wait_ge(s_free, j * 2 + (u + 1))
                        for g in range(3):
                            for p0, n, r in rows(g, j, u):
                                c0 = 2 * AW + g * GW
                                sp.dma_start(v[p0:p0 + n, u, g, :], T["u_tm"][r, c0:c0 + GW]).then_inc(s_v[u][g], 16)

            @block.gpsimd
            def _(pool):
                nc.gpsimd.memset(kT[:, :, :, :, :].rearrange("p a b c d -> p (a b c d)"), 0.0)
                nc.gpsimd.memset(v[:, 1, :, :].rearrange("p a b -> p (a b)"), 0.0).then_inc(s_zero, 1)

            @block.vector
            def _(dve):
                dve.wait_ge(s_zero, 1)
                dve.sem_inc(s_free, 1)
                dve.sem_inc(s_pte, 2)
                dve.wait_ge(s_const, 80)
                with dve.Fori(0, 4) as j:
                    for u in range(2):
                        t = j * 2 + u
                        for g in range(3):
                            dve.wait_ge(s_in[u][g], (j + 1) * (16 if g < 2 else 32))
                            if g == 0:
                                dve.wait_ge(s_qkt, t * 3)
                                dve.wait_ge(s_kv[u], j * (16 * KV_DMAS[u]))
                            x = qk[:, u, g, :, :].rearrange("p a (h c) -> p (a h) c", h=HG)
                            tab = rotary[:, ds(t, 1), g, :].rearrange("p a c -> p (a c)")
                            cos = bc(tab[:, 0:HD].unsqueeze(1), [128, 2 * HG, HD])
                            half = HD // 2
                            for a, b in ((0, half), (half, 0)):
                                sin = bc(tab[:, HD + a:HD + a + half].unsqueeze(1), [128, 2 * HG, half])
                                nc.vector.tensor_tensor(tmp[:, g, 0, :, a:a + half], x[:, :, b:b + half], sin, ALU.mult)
                            nc.vector.tensor_tensor(tmp[:, g, 1, :, :], x, cos, ALU.mult)
                            dve.drain()
                            nc.vector.tensor_tensor(rot[:, u, g, :, :].rearrange("p a (h c) -> p (a h) c", h=HG),
                                                    tmp[:, g, 0, :, :], tmp[:, g, 1, :, :], ALU.add).then_inc(s_rot, 1)
                        for g in range(3):
                            dve.wait_ge(s_qkt, t * 3 + (g + 1))
                            nc.vector.tensor_copy(qT[:, g, :, :], p_qk[:, 0:2, :])
                            nc.vector.tensor_copy(kT[:, g, :, u, :], p_qk[:, 2:4, :])
                            dve.drain()
                            dve.sem_inc(s_qke, 1)
                        for g in range(3):
                            w = 256 if g == 0 or (g == 1 and u == 1) else 128
                            if g == 0 and u == 0:
                                mask = mask_even[:, ds(j, 1), :].rearrange("p a k -> p (a k)")
                            elif g == 2:
                                mask = mask_half[:, :]
                            else:
                                mask = mask_odd[:, :] if u == 1 else mask_even[:, 0, 0:128]
                            if g == 0:
                                dve.wait_ge(s_p, t * 3)
                            dve.wait_ge(s_sc, t * 3 + (g + 1))
                            for h in range(2):
                                nc.vector.tensor_tensor(S[:, g, :, 0:w].rearrange("p (a b) k -> p a b k", b=2)[:, :, h, :],
                                                        p_s[h][:, :, 0:w], bc(mask.unsqueeze(1), [128, 2, w]), ALU.add)
                            dve.drain()
                            dve.sem_inc(s_sce, 1)
                            nc.vector.tensor_reduce(mx[:, g, :], S[:, g, :, 0:w], AX.X, ALU.max)
                            dve.drain()
                            nc.vector.tensor_scalar(nmx[:, g, :], mx[:, g, :], -SC, None, ALU.mult).then_inc(s_nmx, 1)
                        for g in range(3):
                            n = 8 if g == 0 or (g == 1 and u == 1) else 4
                            for i in range(n // 4):
                                k = (0, 2, 3 if u == 0 else 4)[g] + i
                                dve.wait_ge(s_pt, j * 9 + ((0, 4)[u] + k + 1))
                                nc.vector.tensor_copy(PT[:, g, 4 * i // (n // 4):4 * (i + 1) // (n // 4), 0:n // 4, :]
                                                      if n == 8 else PT[:, g, :, 0, :],
                                                      p_t[((0, 4)[u] + k) % 2][:, :, :].rearrange("p (h w) c -> p h w c", w=2)
                                                      if n == 8 else p_t[((0, 4)[u] + k) % 2][:, :, :]
                                                      ).then_inc(s_pte, 1)

            @block.scalar
            def _(act):
                act.sem_inc(s_oe, 2)
                with act.Fori(0, 4) as j:
                    for u in range(2):
                        t = j * 2 + u
                        act.wait_ge(s_rot, t * 3 + 3)
                        act.wait_ge(s_v[u][2], (j + 1) * 32)
                        stores = []
                        if u == 1:
                            act.wait_ge(s_v[u][1], (j + 1) * 16)
                            stores.append((T["p_kv"][1], 0, 128, 1, ds(j, 128, step=4)))
                        for p0, n, r in rows(2, j, u):
                            stores.append((T["p_kv"][2], p0, n, 2, r))
                        for dst, p0, n, g, r in stores:
                            view = dst[0, 0].rearrange("r a h c -> r a (h c)")
                            act.dma_start(view[r, 0, :], rot[p0:p0 + n, u, g, 1, :]).then_inc(s_kv[u], 16)
                            act.dma_start(view[r, 1, :], v[p0:p0 + n, u, g, :]).then_inc(s_kv[u], 16)
                        act.wait_ge(s_st[u], j * 64)
                        for g in range(3):
                            w = 256 if g == 0 or (g == 1 and u == 1) else 128
                            act.wait_ge(s_nmx, t * 3 + (g + 1))
                            if g == 0:
                                act.wait_ge(s_pt, j * 9 + (0, 4)[u])
                            for h in range(HG):
                                nc.scalar.activation(P[:, g, h, 0:w], S[:, g, h, 0:w], ACT.Exp, bias=nmx[:, g, h:h + 1],
                                                     scale=SC, accum_out=out[:, u, g, GW + HG + h:GW + HG + h + 1])
                            act.drain()
                            nc.scalar.mul(out[:, u, g, GW:GW + HG], nmx[:, g, :], -1.0).then_inc(s_p, 1)
                        for g in range(3):
                            act.wait_ge(s_o, t * 3 + (g + 1))
                            nc.scalar.copy(out[:, u, g, 0:GW], p_o[:, g, 0:GW]).then_inc(s_oe, 1)
                            act.drain()
                            for p0, n, r in rows(g, j, u):
                                act.dma_start(T["o_attn"][g, r, :], out[p0:p0 + n, u, g, :]).then_inc(s_st[u], 16)
                view = T["p_kv"][0][0, 0].rearrange("r a h c -> r a (h c)")
                act.dma_start(view[:, 0, :], rot[:, 1, 0, 1, :]).then_inc(s_kv[1], 16)
                act.dma_start(view[:, 1, :], v[:, 1, 0, :]).then_inc(s_kv[1], 16)
                act.wait_ge(s_kv[0], 4 * 16 * KV_DMAS[0])
                act.wait_ge(s_kv[1], 4 * 16 * KV_DMAS[1] + 32)
                act.wait_ge(s_st[0], 4 * 64)
                act.wait_ge(s_st[1], 4 * 64)

            @block.tensor
            def _(pe):
                pe.wait_ge(s_const, 80)
                pe.wait_ge(s_zero, 1)
                with pe.Fori(0, 4) as j:
                    for u in range(2):
                        t = j * 2 + u
                        for g in range(3):
                            pe.wait_ge(s_rot, t * 3 + (g + 1))
                            pe.wait_ge(s_qke, t * 3 + g)
                            for i in range(4):
                                last = nc.tensor.transpose(p_qk[:, i, :], rot[:, u, g, i // 2, (i % 2) * 128:(i % 2 + 1) * 128],
                                                           ident[:, :])
                            last.then_inc(s_qkt, 1)
                        for g in range(3):
                            wide = g == 0 or (g == 1 and u == 1)
                            pe.wait_ge(s_qke, t * 3 + (g + 1))
                            pe.wait_ge(s_sce, t * 3 + g)
                            for hp in range(2):
                                for h in range(2):
                                    q = qT[64 * h:64 * h + 64, g, hp, :]
                                    k = (kT[64 * h:64 * h + 64, g, hp, :, :].rearrange("p a b -> p (a b)") if wide
                                         else kT[64 * h:64 * h + 64, g, hp, u, :])
                                    last = nc.tensor.matmul(p_s[h][:, hp, 0:256 if wide else 128], q, k, start=True, stop=True)
                            last.then_inc(s_sc, 1)
                        for g in range(3):
                            wide = g == 0 or (g == 1 and u == 1)
                            n = 8 if wide else 4
                            pe.wait_ge(s_p, t * 3 + (g + 1))
                            for i in range(n // 4):
                                k = (0, 2, 3 if u == 0 else 4)[g] + i
                                first = u == 0 and k == 0
                                pe.wait_ge(s_pte, j * 9 + ((0, 4)[u] + k + 1 + first))
                                for c in range(4):
                                    h, w = (2 * i + c // 2, c % 2) if wide else (c, 0)
                                    last = nc.tensor.transpose(p_t[((0, 4)[u] + k) % 2][:, c, :],
                                                               P[:, g, h, w * 128:(w + 1) * 128], ident[:, :])
                                last.then_inc(s_pt, 1)
                            pe.wait_ge(s_pte, j * 9 + ((0, 4)[u] + (0, 2, 3 if u == 0 else 4)[g] + n // 4 + 2))
                            pe.wait_ge(s_oe, t * 3 + g)
                            pe.wait_ge(s_v[u][g], (j + 1) * (16 if g < 2 else 32))
                            slots = (u,) if not wide else ((0, 1))
                            for h in range(HG):
                                for w, slot in enumerate(slots):
                                    last = nc.tensor.matmul(p_o[:, g, h * HD:(h + 1) * HD], PT[:, g, h, w, :],
                                                            v[:, slot, g, h * HD:(h + 1) * HD],
                                                            start=(w == 0), stop=(w == len(slots) - 1))
                            last.then_inc(s_o, 1)
                        pe.drain()
                        pe.sem_inc(s_free, 1)


def phase_attention_sample(nc, T, sem):
    with ExitStack() as ctx:
        def sb(name, shape, dt=f32):
            return ctx.enter_context(nc.sbuf_tensor(name, shape, dt))

        def pb(name, shape):
            return ctx.enter_context(nc.psum_tensor(name, shape, f32))

        CT = 9
        GT = [(0, 1), (1, 5), (5, 9)]
        ident = sb("d_ident", [128, 128])
        rotary = sb("d_rotary", [128, 2 * HD])
        m_old, m_new = sb("mask_cached", [128, 3, 128]), sb("mask_new", [128, 2, 3, 128])
        new = sb("d_new", [128, 3 * AW])
        rot = sb("d_rot", [128, 2 * AW])
        tmp = sb("d_tmp", [128, 2, 2 * AW // HD, HD])
        kv = sb("d_kv", [128, 3, 2, GW])
        qbd = sb("d_qbd", [128, 3, 2, NB, 2, NT])
        kTn = sb("d_kTn", [128, 3, 2, 128])
        kc = sb("d_kc", [128, 2, CT, GW])
        kT = sb("d_kT", [128, 2, 2 * CT, 128])
        vc = sb("d_vc", [128, NB, CT, GW])
        sT = sb("d_sT", [128, 6, NB * HG * NT])
        S = sb("d_S", [128, 2, 6, 128])
        mx, den = sb("d_mx", [128, 2]), sb("d_den", [128, 2])
        p_st = pb("d_pst", [128, 6, 256])
        p_kt = [pb(f"d_pkt{i}", [128, 3, 128]) for i in range(2)]
        p_r = pb("d_pr", [128, 8, 128])
        p_o = pb("d_po", [128, NB, 2, 2, NT])
        s_const, s_new, s_rot, s_qkt, s_qbd, s_zero = (sem(f"d_{n}") for n in ("const", "new", "rot", "qkt", "qbd", "zero"))
        s_k = [sem(f"d_k{u}") for u in range(2)]
        s_v, s_kfree, s_kt, s_kte, s_st, s_ste = (sem(f"d_{n}") for n in ("v", "kfree", "kt", "kte", "st", "ste"))
        s_r, s_rm, s_p, s_pn, s_pt, s_pte, s_o, s_done, s_kv = (
            sem(f"d_{n}") for n in ("r", "rm", "p", "pn", "pt", "pte", "o", "done", "kv"))
        SC = HD ** -0.5
        G = 6

        def cache_parts(b, a):
            c = [T["cache"][g][0, b, :, a, :, :].rearrange("r h d -> r (h d)") if isinstance(b, int) else
                 T["cache"][g][0, ds(b, 1), :, a, :, :].rearrange("o r h d -> (o r) (h d)") for g in range(3)]
            parts = [((0, 128), (0, 1), c[0].rearrange("(p r) c -> p r c", r=1)),
                     ((0, 128), (1, 5), c[1].rearrange("(p r) c -> p r c", r=4))]
            c2 = c[2].rearrange("(p u a) c -> a p u c", u=8, a=2)
            return parts + [((64 * x, 64 * x + 64), (5, 9), c2[x][:, 0:4, :]) for x in range(2)]

        with nc.Block() as block:
            @block.sync
            def _(sp):
                sp.dma_start(new[:, :], T["u_tm"][SEQ:TOK, 0:3 * AW]).then_inc(s_new, 16)
                for dst, src in ((ident[:, :], T["ident"]), (rotary[:, :], T["rotary_new"]), (m_old[:, :, :], T["mask_cached"]),
                                 (m_new[:, :, :, :], T["mask_new"])):
                    sp.dma_start(dst, src).then_inc(s_const, 16)
                with sp.Fori(0, NB // 2) as j:
                    for u in range(2):
                        b = j * 2 + u
                        sp.wait_ge(s_kfree, j * 2 + (u + 1))
                        for (p0, p1), (c0, c1), src in cache_parts(b, 0):
                            sp.dma_start(kc[p0:p1, u, c0:c1, :], src).then_inc(s_k[u], 16)

            @block.gpsimd
            def _(pool):
                nc.gpsimd.memset(qbd[:, :, :, :, :, :].rearrange("p a b c d e -> p (a b c d e)"), 0.0)
                nc.gpsimd.memset(T["ya_T"][:, :, SEQ + SAMP:], 0.0).then_inc(s_zero, 1)

            @block.vector
            def _(dve):
                dve.sem_inc(s_kfree, 2)
                dve.wait_ge(s_const, 64)
                dve.wait_ge(s_new, 16)
                x = new[:, 0:2 * AW].rearrange("p (h c) -> p h c", c=HD)
                n, half = 2 * AW // HD, HD // 2
                for a, b in ((0, half), (half, 0)):
                    nc.vector.tensor_tensor(tmp[:, 0, :, a:a + half], x[:, :, b:b + half],
                                            bc(rotary[:, HD + a:HD + a + half].unsqueeze(1), [128, n, half]), ALU.mult)
                nc.vector.tensor_tensor(tmp[:, 1, :, :], x, bc(rotary[:, 0:HD].unsqueeze(1), [128, n, HD]), ALU.mult)
                dve.drain()
                nc.vector.tensor_tensor(rot[:, :].rearrange("p (h c) -> p h c", c=HD), tmp[:, 0, :, :], tmp[:, 1, :, :], ALU.add)
                dve.drain()
                dve.sem_inc(s_rot, 1)
                nc.vector.tensor_copy(kv[:, :, 0, :], rot[:, AW:].rearrange("p (g c) -> p g c", g=3))
                nc.vector.tensor_copy(kv[:, :, 1, :], new[:, 2 * AW:].rearrange("p (g c) -> p g c", g=3))
                dve.drain()
                dve.sem_inc(s_rot, 1)
                dve.wait_ge(s_zero, 1)
                dve.wait_ge(s_qkt, 1)
                pv = p_st[:, :, :].rearrange("p a (b c) -> p (a b) c", c=128)
                for g in range(3):
                    for hh in range(2):
                        r = slice(64 * hh, 64 * hh + 64)
                        for hp in range(2):
                            nc.vector.tensor_copy(qbd[r, g, hp, :, hh, :],
                                                  pv[r, 2 * g + hp, 0:SAMP].rearrange("p (b t) -> p b t", t=NT))
                nc.vector.tensor_copy(kTn[:, :, :, :].rearrange("p a b c -> p (a b) c"), pv[:, 6:12, :])
                dve.drain()
                dve.sem_inc(s_qbd, 1)
                dve.wait_ge(s_st, 1)
                nc.vector.tensor_copy(sT[:, :, :], p_st[:, :, :])
                dve.drain()
                dve.sem_inc(s_ste, 1)
                for half in range(2):
                    dve.wait_ge(s_r, half + 1)
                    nc.vector.tensor_tensor(S[:, half, 0:3, :], p_r[:, 0:3, :], m_old[:, :, :], ALU.add)
                    nc.vector.tensor_tensor(S[:, half, 3:6, :], p_r[:, 3:6, :], m_new[:, half, :, :], ALU.add)
                    dve.drain()
                    dve.sem_inc(s_rm, 1)
                    nc.vector.tensor_reduce(mx[:, half:half + 1], S[:, half, :, :].rearrange("p a k -> p (a k)"), AX.X, ALU.max)
                    dve.drain()
                    nc.vector.tensor_scalar(mx[:, half:half + 1], mx[:, half:half + 1], -SC, None, ALU.mult)
                    dve.drain()
                    dve.sem_inc(s_pn, 1)
                for half in range(2):
                    dve.wait_ge(s_p, half + 1)
                    nc.vector.reciprocal(den[:, half:half + 1], den[:, half:half + 1])
                    dve.drain()
                    nc.vector.tensor_scalar(S[:, half, :, :], S[:, half, :, :], den[:, half:half + 1], None, ALU.mult
                                            ).then_inc(s_pn, 1)
                dve.wait_ge(s_pt, 1)
                nc.vector.tensor_copy(sT[:, :, :], p_st[:, :, :])
                dve.drain()
                dve.sem_inc(s_pte, 1)
                dve.wait_ge(s_o, 1)
                for hh in range(2):
                    r = slice(64 * hh, 64 * hh + 64)
                    for hp in range(2):
                        nc.vector.tensor_copy(T["ya_T"][r, hp, SEQ:SEQ + SAMP].rearrange("p (b t) -> p b t", t=NT),
                                              p_o[r, :, hp, hh, :])
                dve.drain()
                dve.sem_inc(s_done, 1)

            @block.scalar
            def _(act):
                for b in range(NB):
                    for (p0, p1), (c0, c1), src in cache_parts(b, 1):
                        act.dma_start(vc[p0:p1, b, c0:c1, :], src).then_inc(s_v, 16)
                act.wait_ge(s_rot, 2)
                for g, (window, dil) in enumerate(GROUPS):
                    end = min(window, PAST + NT)
                    for b in range(NB):
                        act.dma_start(T["s_kv"][g][0, b, end - NT:end, :, :, :].rearrange("r a h d -> r a (h d)"),
                                      kv[b * NT:(b + 1) * NT, g, :, :]).then_inc(s_kv, 16)
                act.sem_inc(s_kte, 2)
                with act.Fori(0, NB // 2) as j:
                    for u in range(2):
                        for q in range(G):
                            n = u * G + q
                            act.wait_ge(s_kt, j * (2 * G) + (n + 1))
                            nc.scalar.copy(kT[:, u, 3 * q:3 * q + 3, :], p_kt[q % 2][:, :, :]).then_inc(s_kte, 1)
                for half in range(2):
                    act.wait_ge(s_pn, half + 1)
                    flat = S[:, half, :, :].rearrange("p a k -> p (a k)")
                    nc.scalar.activation(flat, flat, ACT.Exp, bias=mx[:, half:half + 1], scale=SC,
                                         accum_out=den[:, half:half + 1])
                    act.drain()
                    act.sem_inc(s_p, 1)
                act.wait_ge(s_kv, 16 * 3 * NB)
                act.wait_ge(T["s_cache"], 16 * 3 * NB)
                act.wait_ge(s_done, 1)

            @block.tensor
            def _(pe):
                pe.wait_ge(s_const, 64)
                pe.wait_ge(s_rot, 1)
                pv = p_st[:, :, :].rearrange("p a (b c) -> p (a b) c", c=128)
                for i in range(12):
                    last = nc.tensor.transpose(pv[:, i, :], rot[:, i * 128:(i + 1) * 128], ident[:, :])
                last.then_inc(s_qkt, 1)
                pe.wait_ge(s_qbd, 1)
                for g in range(3):
                    for hp in range(2):
                        out = p_st[:, 3 + g, :].rearrange("p (b h t) -> p b h t", h=HG, t=NT)[:, :, 2 * hp:2 * hp + 2, :]
                        nc.tensor.matmul(out, kTn[:, g, hp, :], qbd[:, g, hp, :, :, :], start=True, stop=True)
                with pe.Fori(0, NB // 2) as j:
                    for u in range(2):
                        b = j * 2 + u
                        pe.wait_ge(s_k[u], (j + 1) * 64)
                        for q in range(G):
                            pe.wait_ge(s_kte, j * (2 * G) + (u * G + q + 1))
                            for i in range(3 * q, 3 * q + 3):
                                last = nc.tensor.transpose(p_kt[q % 2][:, i % 3, :],
                                                           kc[:, u, i // 2, (i % 2) * 128:(i % 2 + 1) * 128], ident[:, :])
                            last.then_inc(s_kt, 1)
                        pe.drain()
                        pe.sem_inc(s_kfree, 1)
                        pe.wait_ge(s_kte, j * (2 * G) + ((u + 1) * G + 2))
                        for g, (c0, c1) in enumerate(GT):
                            for c in range(c0, c1):
                                for hp in range(2):
                                    t = (slice(0, NT), slice(c - c0, NT, 4), slice(2 * (c - c0), 2 * (c - c0) + 2))[g]
                                    out = p_st[:, g, ds(b * (HG * NT) + hp * 2 * NT, 2 * NT)].rearrange(
                                        "p (h t) -> p h t", t=NT)[:, :, t]
                                    q = qbd[:, g, hp, ds(b, 1), :, :].rearrange("p o h t -> p (o h) t")[:, :, t]
                                    last = nc.tensor.matmul(out, kT[:, u, 2 * c + hp, :], q, start=True, stop=True)
                pe.drain()
                pe.sem_inc(s_st, 1)
                pe.wait_ge(s_ste, 1)
                for half in range(2):
                    pe.wait_ge(s_rm, half)
                    for i in range(6):
                        last = nc.tensor.transpose(p_r[:, i, :], sT[:, i, half * 128:(half + 1) * 128], ident[:, :])
                    last.then_inc(s_r, 1)
                pe.wait_ge(s_pn, 4)
                for half in range(2):
                    for i in range(6):
                        last = nc.tensor.transpose(p_st[:, i, half * 128:(half + 1) * 128], S[:, half, i, :], ident[:, :])
                last.then_inc(s_pt, 1)
                pe.wait_ge(s_pte, 1)
                pe.wait_ge(s_v, 16 * 4 * NB)
                for b in range(NB):
                    for hp in range(2):
                        cols = slice(b * HG * NT + hp * 2 * NT, b * HG * NT + (hp + 1) * 2 * NT)
                        ch = slice(hp * 128, (hp + 1) * 128)
                        work = [(p_o[:, b, hp, :, :], vc[:, b, 0, ch], sT[:, 0, cols])]
                        for g in (1, 2):
                            for c in range(4):
                                t = slice(c, NT, 4) if g == 1 else slice(2 * c, 2 * c + 2)
                                work.append((p_o[:, b, hp, :, t], vc[:, b, GT[g][0] + c, ch],
                                             sT[:, g, cols].rearrange("p (h t) -> p h t", t=NT)[:, :, t]))
                        for g in range(3):
                            c0 = 2 * AW + g * GW + hp * 128
                            work.append((p_o[:, b, hp, :, :], new[:, c0:c0 + 128], sT[:, 3 + g, cols]))
                        for i, (out, v, p) in enumerate(work):
                            last = nc.tensor.matmul(out, v, p, start=(i == 0), stop=(i == len(work) - 1),
                                                    skip_group_check=True)
                last.then_inc(s_o, 1)


def phase_ssd(nc, T, sem, sample):
    tag = "f" if sample else "e"
    with ExitStack() as ctx:
        def sb(name, shape, dt=f32):
            return ctx.enter_context(nc.sbuf_tensor(f"{tag}_{name}", shape, dt))

        def pb(name, shape):
            return ctx.enter_context(nc.psum_tensor(f"{tag}_{name}", shape, f32))

        def sm(name):
            return sem(f"{tag}_{name}")

        GH = SH // 2
        pairs = SH // 2
        ident, ident_b = sb("ident", [128, 128]), sb("ident_b", [128, 128], bf16)
        upto, whole = sb("upto", [128, 128]), sb("whole", [128, 128])
        future, future_b = sb("future", [128, 128]), sb("future_b", [128, 128], bf16)
        d_skip = sb("d_skip", [128, SH])
        xb = sb("xb", [128, 2, DI + 2 * SN])
        bct = sb("bct", [128, 2, 4, 128])
        da = sb("da", [128, SH])
        nacs, wexp = sb("nacs", [128, SH]), sb("wexp", [128, SH])
        eacs, wend, cdec = sb("eacs", [128, SH]), sb("wend", [128, SH]), sb("cdec", [128, SH])
        E, M = sb("E", [128, 4, 4, 128]), sb("M", [128, 4, 4, 128])
        xdt, xw, xd = sb("xdt", [128, DI]), sb("xw", [128, DI]), sb("xd", [128, DI])
        y = sb("y", [128, 2, DI])
        p_misc = pb("p_misc", [128, 512])
        p_al = [pb(f"p_al{i}", [128, 4, 128]) for i in range(2)]
        p_yd, p_yo = pb("p_yd", [128, 2, 512]), pb("p_yo", [128, 2, 512])
        p_st = pb("p_st", [128, 512])
        if sample:
            seq_of, seq_cols = sb("seq_of", [128, NB]), sb("seq_cols", [128, NB, 128])
            dax = sb("dax", [128, DI])
            Bm, Cm = sb("Bm", [128, 2, NB, 128]), sb("Cm", [128, 2, NB, 128])
            h0 = sb("h0", [128, pairs, NB, SN])
            h0T = sb("h0T", [128, NB, DI])
            dec = sb("dec", [128, pairs, NB])
        else:
            hT = sb("hT", [128, DI])
            hout = sb("hout", [128, pairs, SN])
        consts = [(ident, "ident"), (upto, "upto_seq" if sample else "upto"), (future, "future_seq" if sample else "future"),
                  (d_skip, "d_skip")]
        if sample:
            consts += [(whole, "same_seq"), (seq_of, "seq_of"), (seq_cols, "seq_cols")]
        s_const, s_prep = sm("const"), sm("prep")
        s_in = [sm(f"in{u}") for u in range(2)]
        s_free, s_da, s_misc, s_nacs, s_e, s_al, s_E, s_M = (sm(n) for n in ("free", "da", "misc", "nacs", "e", "al", "E", "M"))
        s_x, s_xd, s_pe, s_st, s_ste, s_h = (sm(n) for n in ("x", "xd", "pe", "st", "ste", "h"))
        s_y, s_ho, s_hp, s_mc, s_yfree = sm("y"), sm("ho"), sm("hp"), sm("mc"), sm("yfree")
        s_out = [sm(f"out{u}") for u in range(2)]
        s_h0, s_tr, s_tre = sm("h0"), sm("tr"), sm("tre")
        y3 = lambda ap: ap.rearrange("p (h c) -> p h c", c=HD)

        def heads(ap):
            return bc(ap.unsqueeze(2), [128, SH, HD])

        def chunks(eng, body):
            if sample:
                body(0, 0, 0)
            else:
                with eng.Fori(0, SEQ // 128 // 2) as j:
                    for u in range(2):
                        body(j * 2 + u, u, j)

        def rows(n):
            return slice(SEQ, TOK) if sample else ds(n * 128, 128)

        tile_of = (lambda n: slice(TILES - 1, TILES)) if sample else (lambda n: ds(n, 1))
        NQ = 4

        with nc.Block() as block:
            @block.sync
            def _(sp):
                for dst, name in consts:
                    nd = len(dst.shape)
                    sp.dma_start(dst[:, :] if nd == 2 else dst[:, :, :], T[name]).then_inc(s_const, 16)

                def load(n, u, j):
                    sp.wait_ge(s_free, n + 1)
                    sp.dma_start(xb[:, u, :], T["xc_tm"][rows(n), 0:DI + 2 * SN]).then_inc(s_in[u], 16)
                    sp.dma_start(bct[:, u, :, :], T["xc_cm"][DI:XBC, rows(n)].rearrange("(a p) t -> p a t", p=128)
                                 ).then_inc(s_in[u], 16)
                chunks(sp, load)

            @block.gpsimd
            def _(pool):
                if not sample:
                    nc.gpsimd.memset(whole[:, :], 1.0)
                    nc.gpsimd.memset(hT[:, :], 0.0)
                pool.wait_ge(s_const, 16 * len(consts))
                nc.gpsimd.tensor_copy(ident_b[:, :], ident[:, :])
                nc.gpsimd.tensor_copy(future_b[:, :], future[:, :]).then_inc(s_prep, 1)

                def skip(n, u, j):
                    pool.wait_ge(s_in[u], (j + 1) * 32)
                    pool.wait_ge(s_y, n)
                    nc.gpsimd.tensor_tensor(y3(xd[:, :]), y3(xb[:, u, 0:DI]), heads(d_skip[:, :]), ALU.mult).then_inc(s_xd, 1)
                chunks(pool, skip)

            @block.vector
            def _(dve):
                dve.sem_inc(s_free, 2)
                dve.wait_ge(s_const, 16 * len(consts))
                dve.wait_ge(s_prep, 1)

                def work(n, u, j):
                    dt = T["dt_tm"][:, tile_of(n), :].rearrange("p a h -> p (a h)")
                    nc.vector.tensor_copy(da[:, :], T["da_tm"][:, tile_of(n), :].rearrange("p a h -> p (a h)")).then_inc(s_da, 1)
                    dve.wait_ge(s_in[u], (j + 1) * 32)
                    nc.vector.tensor_tensor(y3(xdt[:, :]), y3(xb[:, u, 0:DI]), heads(dt), ALU.mult)
                    if sample:
                        nc.vector.tensor_copy(y3(dax[:, :]), heads(T["da_tm"][:, TILES - 1, :]))
                        for g in range(2):
                            nc.vector.tensor_tensor(Cm[:, g, :, :], bc(bct[:, u, 2 + g, :].unsqueeze(1), [128, NB, 128]),
                                                    seq_cols[:, :, :], ALU.mult)
                            nc.vector.tensor_tensor(Bm[:, g, :, :],
                                                    bc(xb[:, u, DI + g * SN:DI + (g + 1) * SN].unsqueeze(1), [128, NB, 128]),
                                                    bc(seq_of[:, :].unsqueeze(2), [128, NB, 128]), ALU.mult)
                        dve.drain()
                        dve.sem_inc(s_mc, 1)
                    dve.wait_ge(s_misc, n + 1)
                    nc.vector.tensor_scalar(nacs[:, :], p_misc[:, 0:SH], -1.0, None, ALU.mult)
                    dve.drain()
                    nc.vector.tensor_tensor(wexp[:, :], p_misc[:, SH:2 * SH], nacs[:, :], ALU.add)
                    dve.drain()
                    dve.sem_inc(s_nacs, 1)
                    dve.wait_ge(s_e, n + 1)
                    nc.vector.tensor_tensor(y3(xw[:, :]), y3(xdt[:, :]), heads(wend[:, :]), ALU.mult)
                    dve.drain()
                    dve.sem_inc(s_x, 1)
                    for q in range(NQ):
                        dve.wait_ge(s_E, n * NQ + (q + 1))
                        cb = p_misc[:, 128 * (1 + q // 2):128 * (2 + q // 2)]
                        nc.vector.tensor_tensor(M[:, q, :, :], E[:, q, :, :], bc(cb.unsqueeze(1), [128, 4, 128]), ALU.mult
                                                ).then_inc(s_M, 1)
                    if not sample:
                        dve.wait_ge(s_st, n * 2 + 1)
                        for g in range(2):
                            cols = slice(g * 512, (g + 1) * 512)
                            hv = hT[:, cols].rearrange("p (h c) -> p h c", c=HD)
                            nc.vector.tensor_tensor(hv, hv, bc(cdec[:, g * GH:(g + 1) * GH].unsqueeze(2), [128, GH, HD]), ALU.mult)
                            dve.drain()
                            dve.wait_ge(s_st, n * 2 + (g + 1))
                            nc.vector.tensor_tensor(hT[:, cols], hT[:, cols], p_st[:, :], ALU.add)
                            dve.drain()
                            dve.sem_inc(s_ste, 1)
                    dve.wait_ge(s_pe, n + 1)
                    dve.wait_ge(s_out[u], j * 16)
                    yv = y[:, u, :]
                    nc.vector.tensor_tensor(y3(yv), p_yo[:, :, :].rearrange("p a (h c) -> p (a h) c", c=HD), heads(eacs[:, :]), ALU.mult)
                    dve.drain()
                    nc.vector.tensor_tensor(yv, yv, p_yd[:, :, :].rearrange("p a c -> p (a c)"), ALU.add)
                    dve.drain()
                    dve.wait_ge(s_xd, n + 1)
                    nc.vector.tensor_tensor(yv, yv, xd[:, :], ALU.add)
                    dve.drain()
                    dve.sem_inc(s_y, 1)
                    dve.sem_inc(s_free, 1)
                if sample:
                    dve.wait_ge(s_h0, 16 * NB)
                chunks(dve, work)
                if sample:
                    dve.wait_ge(s_hp, 1)
                    for i in range(2 * pairs):
                        p, half = i // 2, i % 2
                        bs = slice(4 * half, 4 * half + 4)
                        hv = h0[:, p, bs, :]
                        nc.vector.tensor_tensor(hv, hv, bc(dec[:, p, bs].unsqueeze(2), [128, 4, SN]), ALU.mult)
                        dve.drain()
                        dve.wait_ge(s_st, i + 1)
                        nc.vector.tensor_tensor(hv, hv, p_al[i % 2][:, :, :], ALU.add)
                        dve.drain()
                        dve.sem_inc(s_ste, 1)
                    dve.sem_inc(s_ho, 1)
                else:
                    dve.wait_ge(s_hp, 1)
                    for i in range(2):
                        nc.vector.tensor_copy(hout[:, 4 * i:4 * i + 4, :], p_al[i][:, :, :])
                    dve.drain()
                    dve.sem_inc(s_ho, 1)

            @block.scalar
            def _(act):
                if sample:
                    for b in range(NB):
                        act.dma_start(h0[:, :, b, :], T["state_ssm"][0, b].rearrange("(j a) c n -> (a c) j n", a=2)
                                      ).then_inc(s_h0, 16)
                    act.wait_ge(s_h0, 16 * NB)
                    for i in range(NB * 2):
                        act.wait_ge(s_tr, i + 1)
                        b, half = i // 2, i % 2
                        nc.scalar.copy(h0T[:, b, half * 512:(half + 1) * 512], p_al[i % 2][:, :, :].rearrange("p a c -> p (a c)")
                                       ).then_inc(s_tre, 1)

                def work(n, u, j):
                    act.wait_ge(s_nacs, n + 1)
                    nc.scalar.activation(eacs[:, :], p_misc[:, 0:SH], ACT.Exp)
                    nc.scalar.activation(wend[:, :], wexp[:, :], ACT.Exp)
                    nc.scalar.activation(cdec[:, :], p_misc[:, SH:2 * SH], ACT.Exp)
                    act.drain()
                    act.sem_inc(s_e, 1)
                    for q in range(NQ):
                        act.wait_ge(s_al, n * NQ + (q + 1))
                        if q == 0:
                            act.wait_ge(s_M, n * NQ)
                        for i in range(4):
                            last = nc.scalar.activation(E[:, q, i, :], p_al[q % 2][:, i, :], ACT.Exp,
                                                        bias=nacs[:, 4 * q + i:4 * q + i + 1])
                        last.then_inc(s_E, 1)
                    act.wait_ge(s_y, n + 1)
                    act.dma_start(T["y_ssd"][rows(n), :], y[:, u, :]).then_inc(s_out[u], 16)
                chunks(act, work)
                if sample:
                    act.wait_ge(s_mc, 2)
                    nc.scalar.activation(dec[:, :, :].rearrange("p a b -> p (a b)"), p_misc[:, 384:384 + pairs * NB], ACT.Exp)
                    act.drain()
                    act.sem_inc(s_hp, 1)
                    act.wait_ge(s_ho, 1)
                    for b in range(NB):
                        act.dma_start(T["s_ssm"][0, b].rearrange("(j a) c n -> (a c) j n", a=2), h0[:, :, b, :]
                                      ).then_inc(s_out[1], 16)
                    act.wait_ge(s_out[0], 16)
                    act.wait_ge(s_out[1], 16 * NB)
                else:
                    act.wait_ge(s_ho, 1)
                    act.dma_start(T["p_ssm"][0, 0].rearrange("(j a) c n -> (a c) j n", a=2), hout[:, :, :]).then_inc(s_out[0], 16)
                    act.wait_ge(s_out[0], 16 * 5)
                    act.wait_ge(s_out[1], 16 * 4)

            @block.tensor
            def _(pe):
                pe.wait_ge(s_const, 16 * len(consts))
                pe.wait_ge(s_prep, 1)
                if sample:
                    pe.wait_ge(s_h0, 16 * NB)
                    for i in range(NB * 2):
                        b, half = i // 2, i % 2
                        if i >= 2:
                            pe.wait_ge(s_tre, i - 1)
                        for k in range(4):
                            last = nc.tensor.transpose(p_al[i % 2][:, k, :], h0[:, half * 4 + k, b, :], ident[:, :])
                        last.then_inc(s_tr, 1)
                    pe.wait_ge(s_tre, NB * 2)

                def work(n, u, j):
                    pe.wait_ge(s_in[u], (j + 1) * 32)
                    pe.wait_ge(s_da, n + 1)
                    pe.wait_ge(s_M, n * NQ)
                    nc.tensor.matmul(p_misc[:, 0:SH], upto[:, :], da[:, :], start=True, stop=True)
                    nc.tensor.matmul(p_misc[:, SH:2 * SH], whole[:, :], da[:, :], start=True, stop=True)
                    for g in range(2):
                        last = nc.tensor.matmul(p_misc[:, 128 * (1 + g):128 * (2 + g)], bct[:, u, g, :], bct[:, u, 2 + g, :],
                                                start=True, stop=True)
                    last.then_inc(s_misc, 1)
                    for q in range(NQ):
                        if q >= 2:
                            pe.wait_ge(s_E, n * NQ + (q - 1))
                        for i in range(4):
                            h = 4 * q + i
                            nc.tensor.matmul(p_al[q % 2][:, i, :], ident_b[:, :], future_b[:, :], start=True, stop=False)
                            last = nc.tensor.matmul(p_al[q % 2][:, i, :], bc(da[:, h:h + 1], [128, 128]), upto[:, :],
                                                    start=False, stop=True)
                        last.then_inc(s_al, 1)
                    pe.wait_ge(s_y, n)
                    if sample:
                        pe.wait_ge(s_mc, 1)
                        for g in range(2):
                            for b in range(NB):
                                nc.tensor.matmul(p_yo[:, g, :], Cm[:, g, b, :], h0T[:, b, g * 512:(g + 1) * 512],
                                                 start=(b == 0), stop=(b == NB - 1))
                    else:
                        pe.wait_ge(s_ste, n * 2)
                        for g in range(2):
                            nc.tensor.matmul(p_yo[:, g, :], bct[:, u, 2 + g, :], hT[:, g * 512:(g + 1) * 512], start=True, stop=True)
                        pe.drain()
                        pe.wait_ge(s_x, n + 1)
                        for g in range(2):
                            pe.wait_ge(s_ste, n * 2 + g)
                            nc.tensor.matmul(p_st[:, :], xb[:, u, DI + g * SN:DI + (g + 1) * SN], xw[:, g * 512:(g + 1) * 512],
                                             start=True, stop=True).then_inc(s_st, 1)
                    for h in range(SH):
                        if h % 4 == 0:
                            pe.wait_ge(s_M, n * NQ + (h // 4 + 1))
                        last = nc.tensor.matmul(p_yd[:, h // GH, (h % GH) * HD:(h % GH + 1) * HD], M[:, h // 4, h % 4, :],
                                                xdt[:, h * HD:(h + 1) * HD], start=True, stop=True)
                    last.then_inc(s_pe, 1)
                if not sample:
                    pass
                chunks(pe, work)
                if sample:
                    pe.wait_ge(s_y, 1)
                    for p in range(pairs):
                        last = nc.tensor.matmul(p_misc[:, 384 + p * NB:384 + (p + 1) * NB], dax[:, p * 128:(p + 1) * 128],
                                                seq_of[:, :], start=True, stop=True)
                    last.then_inc(s_mc, 1)
                    pe.wait_ge(s_x, 1)
                    pe.wait_ge(s_E, NQ)
                    for i in range(2 * pairs):
                        p, half = i // 2, i % 2
                        if i >= 2:
                            pe.wait_ge(s_ste, i - 1)
                        nc.tensor.matmul(p_al[i % 2][:, :, :], xw[:, p * 128:(p + 1) * 128], Bm[:, p // 4, 4 * half:4 * half + 4, :],
                                         start=True, stop=True).then_inc(s_st, 1)
                else:
                    pe.wait_ge(s_ste, 2 * (SEQ // 128))
                    pe.wait_ge(s_E, NQ * (SEQ // 128))
                    for i in range(pairs):
                        last = nc.tensor.transpose(p_al[i // 4][:, i % 4, :], hT[:, i * 128:(i + 1) * 128], ident[:, :])
                    last.then_inc(s_hp, 1)


def phase_ssd_prompt(nc, T, sem):
    phase_ssd(nc, T, sem, False)


def phase_ssd_sample(nc, T, sem):
    phase_ssd(nc, T, sem, True)


def rows3(j, u):
    return ds((j * 3 + u) * 128, 128)


def phase_branch_inputs(nc, T, sem):
    with ExitStack() as ctx:
        def sb(name, shape, dt=f32):
            return ctx.enter_context(nc.sbuf_tensor(f"g_{name}", shape, dt))

        def sm(name):
            return sem(f"g_{name}")

        ident, nw, eps = sb("ident", [128, 128]), sb("nw", [128, KT]), sb("eps", [128, 1])
        yin, z, junk = sb("yin", [128, 3, DI]), sb("z", [128, 3, DI]), sb("junk", [128, 512])
        ms = sb("ms", [128, 3, 2])
        o = sb("o", [128, 2, 3, GW + 2 * HG])
        wt, top, ysum = sb("wt", [128, 3, HG]), sb("top", [128, HG]), sb("ysum", [128, 2, 3, GW])
        p_t = ctx.enter_context(nc.psum_tensor("g_pt", [128, 3, KT, 128], f32))
        p_a = ctx.enter_context(nc.psum_tensor("g_pa", [128, 2, 2, 128], f32))
        s_const, s_eps = sm("const"), sm("eps")
        s_in, s_o = [sm(f"in{u}") for u in range(3)], [sm(f"o{u}") for u in range(2)]
        s_free, s_silu, s_g, s_rms, s_n, s_t, s_ofree, s_top, s_w, s_ys, s_ta = (
            sm(n) for n in ("free", "silu", "gg", "rms", "n", "t", "ofree", "top", "w", "ys", "ta"))
        with nc.Block() as block:
            @block.sync
            def _(sp):
                sp.dma_start(ident[:, :], T["ident"]).then_inc(s_const, 16)
                sp.dma_start(nw[:, :], T["ssd_norm_w"].rearrange("p a k -> p (a k)")).then_inc(s_const, 16)
                with sp.Fori(0, 3) as j:
                    for u in range(3):
                        sp.wait_ge(s_free, j * 3 + (u + 1))
                        sp.dma_start(yin[:, u, :], T["y_ssd"][rows3(j, u), :]).then_inc(s_in[u], 16)
                        sp.dma_start(z[:, u, :], T["u_tm"][rows3(j, u), ZOFF:XOFF]).then_inc(s_in[u], 16)
                with sp.Fori(0, 4) as j:
                    for u in range(2):
                        sp.wait_ge(s_ofree, j * 2 + (u + 1))
                        sp.dma_start(o[:, u, :, :], T["o_attn"][:, ds((j * 2 + u) * 128, 128), :].rearrange("g r c -> r g c")
                                     ).then_inc(s_o[u], 16)

            @block.vector
            def _(dve):
                nc.vector.memset(eps[:, :], EPS).then_inc(s_eps, 1)
                dve.sem_inc(s_ofree, 2)
                dve.wait_ge(s_const, 32)
                with dve.Fori(0, 3) as j:
                    for u in range(3):
                        n = j * 3 + u
                        dve.wait_ge(s_silu, n + 1)
                        nc.vector.tensor_tensor(yin[:, u, :], yin[:, u, :], z[:, u, :], ALU.mult).then_inc(s_g, 1)
                        dve.wait_ge(s_rms, n + 1)
                        nc.vector.reciprocal(ms[:, u, :], ms[:, u, :])
                        dve.drain()
                        for g in range(2):
                            cols = slice(512 * g, 512 * g + 512)
                            last = nc.vector.tensor_scalar(z[:, u, cols], yin[:, u, cols], ms[:, u, g:g + 1], None, ALU.mult)
                        last.then_inc(s_n, 1)
                        dve.wait_ge(s_t, n + 1)
                        for half in range(2):
                            k0 = 4 * half
                            nc.vector.tensor_tensor(T["ys_T"][:, k0:k0 + 4, ds(n * 128, 128)], p_t[:, u, k0:k0 + 4, :],
                                                    bc(nw[:, k0:k0 + 4].unsqueeze(2), [128, 4, 128]), ALU.mult)
                with dve.Fori(0, 4) as j:
                    for u in range(2):
                        n = j * 2 + u
                        dve.wait_ge(s_o[u], (j + 1) * 16)
                        mx = [o[:, u, g, GW:GW + HG] for g in range(3)]
                        nc.vector.tensor_tensor(top[:, :], mx[0], mx[1], ALU.max)
                        dve.drain()
                        nc.vector.tensor_tensor(top[:, :], top[:, :], mx[2], ALU.max)
                        dve.drain()
                        nc.vector.tensor_tensor(wt[:, :, :], o[:, u, :, GW:GW + HG], bc(top[:, :].unsqueeze(1), [128, 3, HG]),
                                                ALU.subtract).then_inc(s_top, 1)
                        dve.wait_ge(s_w, n + 1)
                        den = o[:, u, :, GW + HG:]
                        nc.vector.tensor_tensor(den, den, wt[:, :, :], ALU.mult)
                        dve.drain()
                        nc.vector.tensor_tensor(top[:, :], den[:, 0, :], den[:, 1, :], ALU.add)
                        dve.drain()
                        nc.vector.tensor_tensor(top[:, :], top[:, :], den[:, 2, :], ALU.add)
                        dve.drain()
                        nc.vector.reciprocal(top[:, :], top[:, :])
                        dve.drain()
                        nc.vector.tensor_tensor(wt[:, :, :], wt[:, :, :], bc(top[:, :].unsqueeze(1), [128, 3, HG]), ALU.mult)
                        dve.drain()
                        for g in range(3):
                            nc.vector.tensor_tensor(ysum[:, u, g, :].rearrange("p (h c) -> p h c", c=HD),
                                                    o[:, u, g, 0:GW].rearrange("p (h c) -> p h c", c=HD),
                                                    bc(wt[:, g, :].unsqueeze(2), [128, HG, HD]), ALU.mult)
                        dve.drain()
                        dve.sem_inc(s_ofree, 1)
                        for g in (1, 2):
                            nc.vector.tensor_tensor(ysum[:, u, 0, :], ysum[:, u, 0, :], ysum[:, u, g, :], ALU.add)
                            dve.drain()
                        dve.sem_inc(s_ys, 1)
                        dve.wait_ge(s_ta, n + 1)
                        nc.vector.tensor_copy(T["ya_T"][:, :, ds(n * 128, 128)], p_a[:, u, :, :])

            @block.scalar
            def _(act):
                act.wait_ge(s_eps, 1)
                with act.Fori(0, 3) as j:
                    for u in range(3):
                        n = j * 3 + u
                        act.wait_ge(s_in[u], (j + 1) * 32)
                        nc.scalar.activation(z[:, u, :], z[:, u, :], ACT.Silu).then_inc(s_silu, 1)
                        act.wait_ge(s_g, n + 1)
                        for g in range(2):
                            nc.scalar.activation(junk[:, :], yin[:, u, 512 * g:512 * g + 512], ACT.Square,
                                                 accum_out=ms[:, u, g:g + 1])
                            act.drain()
                        nc.scalar.activation(ms[:, u, :], ms[:, u, :], ACT.Sqrt, bias=eps[:, :], scale=1.0 / 512)
                        act.drain()
                        act.sem_inc(s_rms, 1)
                with act.Fori(0, 4) as j:
                    for u in range(2):
                        act.wait_ge(s_top, j * 2 + (u + 1))
                        nc.scalar.activation(wt[:, :, :], wt[:, :, :], ACT.Exp)
                        act.drain()
                        act.sem_inc(s_w, 1)

            @block.tensor
            def _(pe):
                pe.sem_inc(s_free, 3)
                pe.wait_ge(s_const, 32)
                with pe.Fori(0, 3) as j:
                    for u in range(3):
                        pe.wait_ge(s_n, j * 3 + (u + 1))
                        for k in range(KT):
                            nc.tensor.transpose(p_t[:, u, k, :], z[:, u, k * 128:(k + 1) * 128], ident[:, :])
                        pe.drain()
                        pe.sem_inc(s_t, 1)
                        pe.sem_inc(s_free, 1)
                with pe.Fori(0, 4) as j:
                    for u in range(2):
                        pe.wait_ge(s_ys, j * 2 + (u + 1))
                        for hp in range(2):
                            last = nc.tensor.transpose(p_a[:, u, hp, :], ysum[:, u, 0, hp * 128:(hp + 1) * 128], ident[:, :])
                        last.then_inc(s_ta, 1)


def phase_merge(nc, T, sem):
    with ExitStack() as ctx:
        def sb(name, shape, dt=f32):
            return ctx.enter_context(nc.sbuf_tensor(f"h_{name}", shape, dt))

        def sm(name):
            return sem(f"h_{name}")

        wa, ws = sb("wa", [128, 2, 2, 128]), sb("ws", [128, 2, KT, 128])
        sig = sb("sig", [128, 2, 2, TOK])
        t1 = sb("t1", [128, 2, 3, NCH])
        p_a = ctx.enter_context(nc.psum_tensor("h_pa", [128, 3, 512], f32))
        p_s = ctx.enter_context(nc.psum_tensor("h_ps", [128, 3, 512], f32))
        s_w, s_sig = [sm(f"w{u}") for u in range(2)], [sm(f"sig{u}") for u in range(2)]
        s_wfree, s_sfree, s_mm, s_ev = sm("wfree"), sm("sfree"), sm("mm"), sm("ev")
        gates = T["gate_cm"].rearrange("(g c) t -> c g t", g=2)
        with nc.Block() as block:
            @block.sync
            def _(sp):
                with sp.Fori(0, KT // 2) as j:
                    for u in range(2):
                        cols = ds((j * 2 + u) * 128, 128)
                        sp.wait_ge(s_wfree, j * 2 + (u + 1))
                        sp.dma_start(wa[:, u, :, :], T["w_attn_br"][0].rearrange("(k p) n -> p k n", p=128)[:, :, cols]
                                     ).then_inc(s_w[u], 16)
                        sp.dma_start(ws[:, u, :, :], T["w_ssd_br"][0].rearrange("(k p) n -> p k n", p=128)[:, :, cols]
                                     ).then_inc(s_w[u], 16)
                        sp.wait_ge(s_sfree, j * 2 + (u + 1))
                        sp.dma_start(sig[:, u, :, :], gates[cols, :, :]).then_inc(s_sig[u], 16)

            @block.vector
            def _(dve):
                dve.sem_inc(s_sfree, 2)
                dve.sem_inc(s_ev, 3)
                with dve.Fori(0, KT // 2) as j:
                    for u in range(2):
                        dve.wait_ge(s_sig[u], (j + 1) * 16)
                        for c in range(3):
                            cols = slice(c * NCH, (c + 1) * NCH)
                            dve.wait_ge(s_mm, j * 6 + (u * 3 + c + 1))
                            nc.vector.tensor_tensor(t1[:, 0, c, :], p_a[:, c, 0:NCH], sig[:, u, 0, cols], ALU.mult)
                            nc.vector.tensor_tensor(t1[:, 1, c, :], p_s[:, c, 0:NCH], sig[:, u, 1, cols], ALU.mult)
                            dve.drain()
                            dve.sem_inc(s_ev, 1)
                            nc.vector.tensor_tensor(T["m_T"][:, ds(j * 2 + u, 1), cols].rearrange("p a t -> p (a t)"),
                                                    t1[:, 0, c, :], t1[:, 1, c, :], ALU.add)
                        dve.drain()
                        dve.sem_inc(s_sfree, 1)

            @block.tensor
            def _(pe):
                pe.sem_inc(s_wfree, 2)
                with pe.Fori(0, KT // 2) as j:
                    for u in range(2):
                        pe.wait_ge(s_w[u], (j + 1) * 32)
                        for c in range(3):
                            cols = slice(c * NCH, (c + 1) * NCH)
                            pe.wait_ge(s_ev, j * 6 + (u * 3 + c + 1))
                            for k in range(2):
                                nc.tensor.matmul(p_a[:, c, 0:NCH], wa[:, u, k, :], T["ya_T"][:, k, cols], start=(k == 0), stop=(k == 1))
                            for k in range(KT):
                                last = nc.tensor.matmul(p_s[:, c, 0:NCH], ws[:, u, k, :], T["ys_T"][:, k, cols],
                                                        start=(k == 0), stop=(k == KT - 1))
                            last.then_inc(s_mm, 1)
                        pe.drain()
                        pe.sem_inc(s_wfree, 1)


def phase_out_router(nc, T, sem):
    with ExitStack() as ctx:
        def sb(name, shape, dt=f32):
            return ctx.enter_context(nc.sbuf_tensor(f"i_{name}", shape, dt))

        def sm(name):
            return sem(f"i_{name}")

        NR = 36
        ident, eps, w2, br = sb("ident", [128, 128]), sb("eps", [128, 1]), sb("w2", [128, D]), sb("br", [128, NR])
        wo, wr = sb("wo", [128, KT, D]), sb("wr", [128, KT, NR])
        x, hn, junk, ms = sb("x", [128, 3, D]), sb("hn", [128, 3, D]), sb("junk", [128, D]), sb("ms", [128, 3, 2])
        hnT = sb("hnT", [128, KT, 128])
        p_h = ctx.enter_context(nc.psum_tensor("i_ph", [128, 3, 2, 512], f32))
        p_t = ctx.enter_context(nc.psum_tensor("i_pt", [128, 4, 128], f32))
        p_l = ctx.enter_context(nc.psum_tensor("i_pl", [128, 512], f32))
        s_const, s_wo, s_eps = sm("const"), [sm(f"wo{k}") for k in range(2)], sm("eps")
        s_x = [sm(f"x{u}") for u in range(3)]
        s_st, s_hn_st = [sm(f"st{u}") for u in range(3)], [sm(f"hs{u}") for u in range(3)]
        s_mm, s_h, s_rms, s_n, s_t, s_te, s_l, s_le = (sm(n) for n in ("mm", "h", "rms", "n", "t", "te", "l", "le"))
        s_xfree = sm("xfree")
        with nc.Block() as block:
            @block.sync
            def _(sp):
                for c in range(2):
                    cols = slice(512 * c, 512 * c + 512)
                    sp.dma_start(wo[:, :, cols], T["w_out"][0].rearrange("(k p) n -> p k n", p=128)[:, :, cols]).then_inc(s_wo[c], 16)
                sp.dma_start(ident[:, :], T["ident"]).then_inc(s_const, 16)
                sp.dma_start(w2[:, :], T["norm2_w"].broadcast_to([128, D])).then_inc(s_const, 16)
                sp.dma_start(br[:, :], T["b_router"].broadcast_to([128, NR])).then_inc(s_const, 16)
                sp.dma_start(wr[:, :, :], T["w_router"][0].rearrange("(k p) n -> p k n", p=128)).then_inc(s_const, 16)
                with sp.Fori(0, 3) as j:
                    for u in range(3):
                        if u == 0:
                            sp.wait_ge(s_st[u], j * 16)
                        sp.wait_ge(s_xfree, j * 3 + (u + 1))
                        if u > 0:
                            sp.wait_ge(s_st[u], j * 16)
                        sp.dma_start(x[:, u, :], T["x_all"][rows3(j, u), :]).then_inc(s_x[u], 16)

            @block.vector
            def _(dve):
                nc.vector.memset(eps[:, :], EPS).then_inc(s_eps, 1)
                dve.sem_inc(s_xfree, 3)
                dve.wait_ge(s_const, 64)
                with dve.Fori(0, 3) as j:
                    for u in range(3):
                        n = j * 3 + u
                        dve.wait_ge(s_x[u], (j + 1) * 16)
                        dve.wait_ge(s_mm, n + 1)
                        nc.vector.tensor_tensor(x[:, u, :], x[:, u, :], p_h[:, u, :, :].rearrange("p a c -> p (a c)"), ALU.add
                                                ).then_inc(s_h, 1)
                        dve.wait_ge(s_rms, n + 1)
                        nc.vector.reciprocal(ms[:, u, 1:2], ms[:, u, 1:2])
                        dve.drain()
                        dve.wait_ge(s_hn_st[u], j * 16)
                        nc.vector.scalar_tensor_tensor(hn[:, u, :], x[:, u, :], ms[:, u, 1:2], w2[:, :], ALU.mult, ALU.mult
                                                       ).then_inc(s_n, 1)
                        dve.drain()
                        dve.sem_inc(s_xfree, 1)
                        dve.wait_ge(s_l, n + 1)
                        nc.vector.tensor_tensor(T["logits"][:, ds(n, 1), 0:NR].rearrange("p a e -> p (a e)"),
                                                p_l[:, 0:NR], br[:, :], ALU.add)
                        dve.drain()
                        dve.sem_inc(s_le, 1)

            @block.scalar
            def _(act):
                act.wait_ge(s_eps, 1)
                with act.Fori(0, 3) as j:
                    for u in range(3):
                        n = j * 3 + u
                        act.wait_ge(s_h, n + 1)
                        act.dma_start(T["h"][rows3(j, u), :], x[:, u, :]).then_inc(s_st[u], 16)
                        nc.scalar.activation(junk[:, :], x[:, u, :], ACT.Square, accum_out=ms[:, u, 0:1])
                        act.drain()
                        nc.scalar.activation(ms[:, u, 1:2], ms[:, u, 0:1], ACT.Sqrt, bias=eps[:, :], scale=1.0 / D)
                        act.drain()
                        act.sem_inc(s_rms, 1)
                        act.wait_ge(s_n, n + 1)
                        act.dma_start(T["hn"][rows3(j, u), :], hn[:, u, :]).then_inc(s_hn_st[u], 16)
                        for half in range(2):
                            act.wait_ge(s_t, j * 6 + (2 * u + half + 1))
                            nc.scalar.copy(hnT[:, 4 * half:4 * half + 4, :], p_t[:, :, :]).then_inc(s_te, 1)
                for u in range(3):
                    act.wait_ge(s_st[u], 48)
                    act.wait_ge(s_hn_st[u], 48)

            @block.tensor
            def _(pe):
                def route(t):
                    pe.wait_ge(s_n, t + 1)
                    for half in range(2):
                        pe.wait_ge(s_te, 2 * t + half)
                        for k in range(4):
                            c = (4 * half + k) * 128
                            last = nc.tensor.transpose(p_t[:, k, :], hn[:, t % 3, c:c + 128], ident[:, :])
                        last.then_inc(s_t, 1)
                    pe.wait_ge(s_te, 2 * t + 2)
                    pe.wait_ge(s_le, t)
                    for k in range(KT):
                        last = nc.tensor.matmul(p_l[:, 0:NR], hnT[:, k, :], wr[:, k, :], start=(k == 0), stop=(k == KT - 1))
                    last.then_inc(s_l, 1)

                pe.wait_ge(s_const, 64)
                for t in range(TILES):
                    if t >= 3:
                        pe.wait_ge(s_h, t - 2)
                    for c in range(2):
                        if t == 0:
                            pe.wait_ge(s_wo[c], 16)
                        for k in range(KT):
                            last = nc.tensor.matmul(p_h[:, t % 3, c, :], T["m_T"][:, k, t * 128:(t + 1) * 128],
                                                    wo[:, k, 512 * c:512 * c + 512], start=(k == 0), stop=(k == KT - 1))
                    last.then_inc(s_mm, 1)
                    if t >= 1:
                        route(t - 1)
                route(TILES - 1)


def phase_route(nc, T, sem):
    with ExitStack() as ctx:
        def sb(name, shape, dt=f32):
            return ctx.enter_context(nc.sbuf_tensor(f"j_{name}", shape, dt))

        def sm(name):
            return sem(f"j_{name}")

        before, upto, ones = sb("before", [128, 128]), sb("upto", [128, 128]), sb("ones", [128, 128])
        experts, group_of, first = sb("experts", [128, NE]), sb("group_of", [128, NE]), sb("first", [128, NE])
        beyond, fills, row_id = sb("beyond", [128, NE]), sb("fills", [128, 8]), sb("row_id", [128, 1])
        tokens = sb("tokens", [128, TILES], i32)
        e4, m4, lf = sb("e4", [128, TILES, 4]), sb("m4", [128, TILES, 4]), sb("lf", [128, TILES, NE])
        t32, O = sb("t32", [128, TILES, NE]), sb("O", [128, 3, TILES, NE])
        C = sb("C", [128, TILES + 1, NE])
        top = sb("top", [128, 8, TILES])
        S, far = sb("S", [128, TILES, NE]), sb("far", [128, NE])
        slotf, ovf = sb("slotf", [128, 2, TILES]), sb("ovf", [128, 2, NE])
        col, coli = sb("col", [128, 4]), sb("coli", [128, 2], i32)
        p_pos = ctx.enter_context(nc.psum_tensor("j_pos", [128, TILES, NE], f32))
        p_s = ctx.enter_context(nc.psum_tensor("j_s", [128, 512], f32))
        consts = [(before, "before"), (upto, "upto"), (experts, "experts"), (group_of, "group_of"), (first, "first_wins"),
                  (beyond, "beyond"), (fills, "fills"), (row_id, "row_id"), (tokens, "tokens")]
        s_const, s_zero, s_v, s_a, s_ones, s_C, s_pos, s_cnt, s_nb, s_ovf, s_slot, s_sc, s_tab = (
            sm(n) for n in ("const", "zero", "v", "a", "ones", "C", "pos", "cnt", "nb", "ovf", "slot", "sc", "tab"))
        L = T["logits"]
        lc = L[:, :, 0:4]

        def over(ap, n):
            return bc(ap.unsqueeze(2), [128, TILES, n])

        def rows(ap, n):
            return bc(ap.unsqueeze(1), [128, TILES, n])

        with nc.Block() as block:
            @block.sync
            def _(sp):
                sp.dma_start(T["ids"].rearrange("(p b) a -> p (b a)", p=128), T["zero_ids"]).then_inc(s_zero, 16)
                for dst, name in consts:
                    sp.dma_start(dst[:, :], T[name]).then_inc(s_const, 16)
                sp.wait_ge(s_ovf, 1)
                sp.dma_start(T["ovf"][:, 0:NOVF].rearrange("a k -> k a"), coli[0:NOVF, 0:1]).then_inc(s_tab, 16)
                sp.dma_start(T["ovf"][:, NOVF:NOVF + 1], coli[0:1, 1:2]).then_inc(s_tab, 16)
                sp.wait_ge(s_tab, 32)

            @block.gpsimd
            def _(pool):
                nc.gpsimd.memset(ones[:, :], 1.0).then_inc(s_ones, 1)
                pool.wait_ge(s_zero, 16)
                pool.wait_ge(s_const, 16 * len(consts))
                pool.wait_ge(s_slot, 1)
                for t in range(TILES):
                    n = 128 if t < TILES - 1 else SAMP
                    for k in range(2):
                        pool.indirect_dma_start(
                            out=T["ids"], out_offset=bass.IndirectOffsetOnAxis(ap=T["slots"][0:n, t, k:k + 1], axis=0),
                            in_=tokens[0:n, t:t + 1], in_offset=None).then_inc(s_sc, 16)
                        pool.wait_ge(s_sc, 16 * (2 * t + k + 1))
                pool.wait_ge(s_sc, 32 * TILES)

            @block.scalar
            def _(act):
                act.wait_ge(s_v, 1)
                nc.scalar.activation(e4[:, :, :], e4[:, :, :], ACT.Exp).then_inc(s_a, 1)
                act.wait_ge(s_v, 2)
                nc.scalar.activation(top[:, 4, :], top[:, 4, :], ACT.Exp).then_inc(s_a, 1)

            @block.vector
            def _(dve):
                def step(instruction):
                    dve.drain()

                def tt(out, a, b, op):
                    nc.vector.tensor_tensor(out, a, b, op)
                    dve.drain()

                def ts(out, a, s1, op0, s2=None, op1=ALU.bypass):
                    nc.vector.tensor_scalar(out, a, s1, s2, op0, op1)
                    dve.drain()

                def red(out, a, op):
                    nc.vector.tensor_reduce(out, a, AX.X, op)
                    dve.drain()

                def choose(values, width, k):
                    red(top[:, k, :], values, ALU.max)
                    tt(t32[:, :, 0:width], values, over(top[:, k, :], width), ALU.is_equal)
                    tt(t32[:, :, 0:width], t32[:, :, 0:width], rows(first[:, 0:width], width), ALU.mult)
                    red(top[:, 6, :], t32[:, :, 0:width], ALU.max)
                    ts(top[:, 6, :], top[:, 6, :], -1.0, ALU.mult, float(NE), ALU.add)

                dve.wait_ge(s_const, 16 * len(consts))
                choose(lc, 4, 0)
                tt(e4[:, :, :], lc, over(top[:, 0, :], 4), ALU.subtract)
                dve.sem_inc(s_v, 1)
                tt(t32[:, :, :], rows(group_of[:, :], NE), over(top[:, 6, :], NE), ALU.not_equal)
                nc.vector.scalar_tensor_tensor(lf[:, :, :], t32[:, :, :], NEG, L[:, :, 4:4 + NE], ALU.mult, ALU.add)
                dve.drain()
                for k in range(2):
                    choose(lf[:, :, :], NE, 2 + k)
                    tt(O[:, k, :, :], rows(experts[:, :], NE), over(top[:, 6, :], NE), ALU.is_equal)
                    if k == 0:
                        nc.vector.scalar_tensor_tensor(lf[:, :, :], O[:, 0, :, :], NEG, lf[:, :, :], ALU.mult, ALU.add)
                        dve.drain()
                tt(top[:, 4, :], top[:, 3, :], top[:, 2, :], ALU.subtract)
                dve.sem_inc(s_v, 1)
                nc.vector.memset(O[SAMP:128, 0, TILES - 1, :], 0.0)
                nc.vector.memset(O[SAMP:128, 1, TILES - 1, :], 0.0)
                dve.drain()
                tt(O[:, 2, :, :], O[:, 0, :, :], O[:, 1, :, :], ALU.add)
                nc.vector.memset(C[:, 0, :], 0.0)
                dve.drain()
                for t in range(TILES):
                    tt(C[:, t + 1, :], C[:, t, :], O[:, 2, t, :], ALU.add)
                dve.sem_inc(s_C, 1)
                dve.wait_ge(s_a, 2)
                red(top[:, 1, :], e4[:, :, :], ALU.add)
                nc.vector.reciprocal(top[:, 1, :], top[:, 1, :])
                ts(top[:, 5, :], top[:, 4, :], 1.0, ALU.add)
                nc.vector.reciprocal(top[:, 5, :], top[:, 5, :])
                dve.drain()
                tt(top[:, 5, :], top[:, 5, :], top[:, 1, :], ALU.mult)
                tt(top[:, 4, :], top[:, 4, :], top[:, 5, :], ALU.mult)
                nc.vector.tensor_copy(T["gates"][:, :, 0], top[:, 5, :])
                nc.vector.tensor_copy(T["gates"][:, :, 1], top[:, 4, :])
                dve.wait_ge(s_cnt, 1)
                nc.vector.tensor_copy(col[0:NE, 0:1], p_s[0:NE, 0:1])
                dve.drain()
                ts(t32[0:NE, 0, 0:8], fills[0:NE, :], col[0:NE, 0:1], ALU.is_lt)
                red(col[0:NE, 1:2], t32[0:NE, 0, 0:8], ALU.add)
                dve.sem_inc(s_nb, 1)
                dve.wait_ge(s_nb, 2)
                nc.vector.tensor_copy(ovf[:, :, :], p_s[:, 64:128].rearrange("p (a e) -> p a e", a=2))
                dve.drain()
                ts(t32[:, 0, :], ovf[:, 1, :], row_id[:, :], ALU.is_le)
                red(col[:, 2:3], t32[:, 0, :], ALU.add)
                ts(col[:, 2:3], col[:, 2:3], float(NE - 1), ALU.min)
                nc.vector.tensor_copy(coli[:, 0:1], col[:, 2:3])
                nc.vector.tensor_copy(coli[:, 1:2], ovf[:, 1, NE - 1:NE])
                dve.drain()
                dve.sem_inc(s_ovf, 1)
                tt(far[:, :], ovf[:, 0, :], beyond[:, :], ALU.add)
                ts(far[:, :], far[:, :], 128.0, ALU.mult)
                dve.wait_ge(s_pos, 1)
                ts(S[:, :, :], p_pos[:, :, :], 128.0, ALU.is_ge)
                tt(S[:, :, :], S[:, :, :], rows(far[:, :], NE), ALU.mult)
                tt(S[:, :, :], S[:, :, :], p_pos[:, :, :], ALU.add)
                nc.vector.scalar_tensor_tensor(S[:, :, :], rows(experts[:, :], NE), 128.0, S[:, :, :], ALU.mult, ALU.add)
                dve.drain()
                for k in range(2):
                    tt(t32[:, :, :], O[:, k, :, :], S[:, :, :], ALU.mult)
                    red(slotf[:, k, :], t32[:, :, :], ALU.add)
                    nc.vector.tensor_copy(T["slots"][:, :, k], slotf[:, k, :])
                dve.drain()
                dve.sem_inc(s_slot, 1)

            @block.tensor
            def _(pe):
                pe.wait_ge(s_const, 16 * len(consts))
                pe.wait_ge(s_ones, 1)
                pe.wait_ge(s_C, 1)
                nc.tensor.matmul(p_s[0:NE, 0:1], C[:, TILES, :], ones[:, 0:1], start=True, stop=True).then_inc(s_cnt, 1)
                for t in range(TILES):
                    nc.tensor.matmul(p_pos[:, t, :], ones[:, :], C[:, t, :], start=True, stop=False)
                    last = nc.tensor.matmul(p_pos[:, t, :], before[:, :], O[:, 2, t, :], start=False, stop=True)
                last.then_inc(s_pos, 1)
                pe.wait_ge(s_nb, 1)
                nb = bc(col[0:NE, 1:2], [NE, 128])
                nc.tensor.matmul(p_s[:, 64:96], nb, before[0:NE, 0:NE], start=True, stop=True)
                nc.tensor.matmul(p_s[:, 96:128], nb, upto[0:NE, 0:NE], start=True, stop=True).then_inc(s_nb, 1)


class ExpertBuffers:

    def __init__(self, nc, ctx, tag, n):
        def sb(name, shape, dt=f32):
            return ctx.enter_context(nc.sbuf_tensor(f"{tag}_{name}", shape, dt))

        def pb(name, shape):
            return ctx.enter_context(nc.psum_tensor(f"{tag}_{name}", shape, f32))
        self.ident = sb("ident", [128, 128])
        self.ids = sb("ids", [128, n], i32)
        self.rows = sb("rows", [128, n, D])
        self.wg, self.wu = sb("wg", [128, n, KT, FF]), sb("wu", [128, n, KT, FF])
        self.wd = sb("wd", [128, n, FF // 128, D])
        self.xT = sb("xT", [128, KT, 128])
        self.act, self.hid = sb("act", [128, FF]), sb("hid", [128, FF])
        self.hT = sb("hT", [128, FF // 128, 128])
        self.out = sb("out", [128, n, D])
        self.p_x = pb("px", [128, KT, 128])
        self.p_g, self.p_u = pb("pg", [128, FF]), pb("pu", [128, FF])
        self.p_h = pb("ph", [128, FF // 128, 128])
        self.p_o = pb("po", [128, 2, 512])


def phase_experts(nc, T, sem):
    with ExitStack() as ctx:
        B = ExpertBuffers(nc, ctx, "k", 2)
        N = NE // 2

        def sm(name):
            return sem(f"k_{name}")

        s_seen = sm("seen")
        s_const = sm("const")
        s_id, s_row, s_wg, s_wd, s_out = ([sm(f"{n}{u}") for u in range(2)] for n in ("id", "row", "wgu", "wd", "out"))
        s_wgf, s_wdf, s_xt, s_xe, s_gu, s_silu, s_hid, s_ht, s_hte, s_down, s_oe = (
            sm(n) for n in ("wgf", "wdf", "xt", "xe", "gu", "silu", "hid", "ht", "hte", "down", "oe"))
        wg_v = T["w_expert_gate"][0].rearrange("e (k p) f -> p e k f", p=128)
        wu_v = T["w_expert_up"][0].rearrange("e (k p) f -> p e k f", p=128)
        wd_v = T["w_expert_down"][0].rearrange("e (k p) n -> p e k n", p=128)

        def one(ap):
            return ap.rearrange("p e k f -> p (e k) f")

        with nc.Block() as block:
            @block.sync
            def _(sp):
                sp.dma_start(B.ident[:, :], T["ident"]).then_inc(s_const, 16)
                with sp.Fori(0, N) as j:
                    for u in range(2):
                        e = ds(j * 2 + u, 1)
                        sp.wait_ge(s_wgf, j * 2 + (u + 1))
                        sp.dma_start(B.wg[:, u, :, :], one(wg_v[:, e, :, :])).then_inc(s_wg[u], 16)
                        sp.dma_start(B.wu[:, u, :, :], one(wu_v[:, e, :, :])).then_inc(s_wg[u], 16)
                        sp.wait_ge(s_wdf, j * 2 + (u + 1))
                        sp.dma_start(B.wd[:, u, :, :], one(wd_v[:, e, :, :])).then_inc(s_wd[u], 16)

            @block.gpsimd
            def _(pool):
                def fetch(n, u, i):
                    pool.wait_ge(s_xt, n + 1)
                    pool.dma_start(B.ids[:, u:u + 1], T["ids"][ds(n * 128, 128) if not isinstance(n, int) else
                                                              slice(n * 128, n * 128 + 128), :]).then_inc(s_id[u], 16)
                    pool.wait_ge(s_id[u], (i + 1) * 16)
                    pool.sem_inc(s_seen, 1)
                    pool.indirect_dma_start(out=B.rows[:, u, :], out_offset=None, in_=T["hn"],
                                            in_offset=bass.IndirectOffsetOnAxis(ap=B.ids[:, u:u + 1], axis=0)
                                            ).then_inc(s_row[u], 16)
                with pool.Fori(0, N) as j:
                    for u in range(2):
                        fetch(j * 2 + u, u, j)
                fetch(NE, 0, N)

            @block.vector
            def _(dve):
                with dve.Fori(0, N) as j:
                    for u in range(2):
                        n = j * 2 + u
                        dve.wait_ge(s_silu, n + 1)
                        nc.vector.tensor_tensor(B.hid[:, :], B.act[:, :], B.p_u[:, :], ALU.mult).then_inc(s_hid, 1)
                        dve.wait_ge(s_xt, n + 4)
                        nc.vector.tensor_copy(B.xT[:, 0:KT, :], B.p_x[:, :, :]).then_inc(s_xe, 1)
                        dve.wait_ge(s_ht, n + 1)
                        nc.vector.tensor_copy(B.hT[:, :, :], B.p_h[:, :, :]).then_inc(s_hte, 1)

            @block.scalar
            def _(act):
                act.wait_ge(s_xt, 3)
                nc.scalar.copy(B.xT[:, :, :], B.p_x[:, :, :]).then_inc(s_xe, 1)
                with act.Fori(0, N) as j:
                    for u in range(2):
                        n = j * 2 + u
                        act.wait_ge(s_gu, n + 1)
                        act.wait_ge(s_hid, n)
                        nc.scalar.activation(B.act[:, :], B.p_g[:, :], ACT.Silu).then_inc(s_silu, 1)
                        act.wait_ge(s_down, n + 1)
                        act.wait_ge(s_out[u], j * 16)
                        nc.scalar.copy(B.out[:, u, :], B.p_o[:, :, :].rearrange("p a c -> p (a c)")).then_inc(s_oe, 1)
                        act.drain()
                        act.dma_start(T["o_moe"][ds(n * 128, 128), :], B.out[:, u, :]).then_inc(s_out[u], 16)
                for u in range(2):
                    act.wait_ge(s_out[u], N * 16)

            @block.tensor
            def _(pe):
                pe.sem_inc(s_xt, 2)
                pe.sem_inc(s_wgf, 2)
                pe.sem_inc(s_wdf, 2)
                pe.wait_ge(s_const, 16)

                def turn(n, u, i):
                    pe.wait_ge(s_row[u], (i + 1) * 16)
                    for k in range(KT):
                        last = nc.tensor.transpose(B.p_x[:, k, :], B.rows[:, u, k * 128:(k + 1) * 128], B.ident[:, :])
                    last.then_inc(s_xt, 1)
                turn(0, 0, 0)
                with pe.Fori(0, N) as j:
                    for u in range(2):
                        n = j * 2 + u
                        pe.wait_ge(s_wg[u], (j + 1) * 32)
                        pe.wait_ge(s_xe, n + 1)
                        pe.wait_ge(s_hid, n)
                        for p, w in ((B.p_g, B.wg), (B.p_u, B.wu)):
                            for k in range(KT):
                                last = nc.tensor.matmul(p[:, :], B.xT[:, k, :], w[:, u, k, :], start=(k == 0), stop=(k == KT - 1))
                        last.then_inc(s_gu, 1)
                        pe.drain()
                        pe.sem_inc(s_wgf, 1)
                        turn(n + 1, 1 - u, j + u)
                        pe.wait_ge(s_hid, n + 1)
                        pe.wait_ge(s_hte, n)
                        for k in range(FF // 128):
                            last = nc.tensor.transpose(B.p_h[:, k, :], B.hid[:, k * 128:(k + 1) * 128], B.ident[:, :])
                        last.then_inc(s_ht, 1)
                        pe.wait_ge(s_hte, n + 1)
                        pe.wait_ge(s_wd[u], (j + 1) * 16)
                        pe.wait_ge(s_oe, n)
                        for c in range(2):
                            for k in range(FF // 128):
                                last = nc.tensor.matmul(B.p_o[:, c, :], B.hT[:, k, :], B.wd[:, u, k, 512 * c:512 * c + 512],
                                                        start=(k == 0), stop=(k == FF // 128 - 1))
                        last.then_inc(s_down, 1)
                        pe.drain()
                        pe.sem_inc(s_wdf, 1)


def phase_overflow(nc, T, sem):
    with ExitStack() as ctx:
        B = ExpertBuffers(nc, ctx, "l", 1)
        table = ctx.enter_context(nc.sbuf_tensor("l_table", [1, NOVF + 1], i32))

        def sm(name):
            return sem(f"l_{name}")

        s_seen = sm("seen")
        s_tab, s_id, s_row, s_w, s_xt, s_xe, s_gu, s_silu, s_hid, s_ht, s_hte, s_down, s_out, s_done = (
            sm(n) for n in ("tab", "id", "row", "w", "xt", "xe", "gu", "silu", "hid", "ht", "hte", "down", "out", "done"))
        wg_v = T["w_expert_gate"][0].rearrange("e (k p) f -> p e k f", p=128)
        wu_v = T["w_expert_up"][0].rearrange("e (k p) f -> p e k f", p=128)
        wd_v = T["w_expert_down"][0].rearrange("e (k p) n -> p e k n", p=128)

        def one(ap):
            return ap.rearrange("p e k f -> p (e k) f")

        def blocks(eng, body):
            eng.wait_ge(s_tab, 32)
            count = eng.value_load(table[0:1, NOVF:NOVF + 1], min_val=0, max_val=NOVF)
            with eng.Fori(0, NOVF) as k:
                with eng.If(k < count):
                    body(k)

        with nc.Block() as block:
            @block.sync
            def _(sp):
                sp.dma_start(table[:, :], T["ovf"][:, 0:NOVF + 1]).then_inc(s_tab, 16)
                sp.dma_start(B.ident[:, :], T["ident"]).then_inc(s_tab, 16)

                def body(k):
                    e = ds(sp.value_load(table[0:1, ds(k, 1)], min_val=0, max_val=NE - 1), 1)
                    sp.wait_ge(s_done, k)
                    sp.dma_start(B.wg[:, 0, :, :], one(wg_v[:, e, :, :])).then_inc(s_w, 16)
                    sp.dma_start(B.wu[:, 0, :, :], one(wu_v[:, e, :, :])).then_inc(s_w, 16)
                    sp.dma_start(B.wd[:, 0, :, :], one(wd_v[:, e, :, :])).then_inc(s_w, 16)
                blocks(sp, body)

            @block.gpsimd
            def _(pool):
                def body(k):
                    pool.wait_ge(s_done, k)
                    pool.dma_start(B.ids[:, 0:1], T["ids"][ds(k * 128 + NE * 128, 128), :]).then_inc(s_id, 16)
                    pool.wait_ge(s_id, (k + 1) * 16)
                    pool.sem_inc(s_seen, 1)
                    pool.indirect_dma_start(out=B.rows[:, 0, :], out_offset=None, in_=T["hn"],
                                            in_offset=bass.IndirectOffsetOnAxis(ap=B.ids[:, 0:1], axis=0)).then_inc(s_row, 16)
                blocks(pool, body)

            @block.vector
            def _(dve):
                def body(k):
                    dve.wait_ge(s_xt, k + 1)
                    nc.vector.tensor_copy(B.xT[:, :, :], B.p_x[:, :, :]).then_inc(s_xe, 1)
                    dve.wait_ge(s_silu, k + 1)
                    nc.vector.tensor_tensor(B.hid[:, :], B.act[:, :], B.p_u[:, :], ALU.mult).then_inc(s_hid, 1)
                    dve.wait_ge(s_ht, k + 1)
                    nc.vector.tensor_copy(B.hT[:, :, :], B.p_h[:, :, :]).then_inc(s_hte, 1)
                blocks(dve, body)

            @block.scalar
            def _(act):
                def body(k):
                    act.wait_ge(s_gu, k + 1)
                    nc.scalar.activation(B.act[:, :], B.p_g[:, :], ACT.Silu).then_inc(s_silu, 1)
                    act.wait_ge(s_down, k + 1)
                    nc.scalar.copy(B.out[:, 0, :], B.p_o[:, :, :].rearrange("p a c -> p (a c)"))
                    act.drain()
                    act.dma_start(T["o_moe"][ds(k * 128 + NE * 128, 128), :], B.out[:, 0, :]).then_inc(s_out, 16)
                    act.wait_ge(s_out, (k + 1) * 16)
                    act.sem_inc(s_done, 1)
                blocks(act, body)

            @block.tensor
            def _(pe):
                def body(k):
                    pe.wait_ge(s_row, (k + 1) * 16)
                    for c in range(KT):
                        last = nc.tensor.transpose(B.p_x[:, c, :], B.rows[:, 0, c * 128:(c + 1) * 128], B.ident[:, :])
                    last.then_inc(s_xt, 1)
                    pe.wait_ge(s_xe, k + 1)
                    pe.wait_ge(s_w, (k + 1) * 48)
                    for p, w in ((B.p_g, B.wg), (B.p_u, B.wu)):
                        for c in range(KT):
                            last = nc.tensor.matmul(p[:, :], B.xT[:, c, :], w[:, 0, c, :], start=(c == 0), stop=(c == KT - 1))
                    last.then_inc(s_gu, 1)
                    pe.wait_ge(s_hid, k + 1)
                    for c in range(FF // 128):
                        last = nc.tensor.transpose(B.p_h[:, c, :], B.hid[:, c * 128:(c + 1) * 128], B.ident[:, :])
                    last.then_inc(s_ht, 1)
                    pe.wait_ge(s_hte, k + 1)
                    for h in range(2):
                        for c in range(FF // 128):
                            last = nc.tensor.matmul(B.p_o[:, h, :], B.hT[:, c, :], B.wd[:, 0, c, 512 * h:512 * h + 512],
                                                    start=(c == 0), stop=(c == FF // 128 - 1))
                    last.then_inc(s_down, 1)
                blocks(pe, body)


def phase_combine(nc, T, sem):
    with ExitStack() as ctx:
        def sb(name, shape, dt=f32):
            return ctx.enter_context(nc.sbuf_tensor(f"m_{name}", shape, dt))

        def sm(name):
            return sem(f"m_{name}")

        w, eps, junk, ms = sb("w", [128, D]), sb("eps", [128, 1]), sb("junk", [128, D]), sb("ms", [128, 3, 2])
        h, o, y = sb("h", [128, 3, D]), sb("o", [128, 3, 2, D]), sb("y", [128, 3, D])
        idx, gate = sb("idx", [128, 3, 2], i32), sb("gate", [128, 3, 2])
        s_seen = sm("seen")
        s_w, s_eps, s_idx = sm("w"), sm("eps"), sm("idx")
        s_h, s_o, s_st = ([sm(f"{n}{u}") for u in range(3)] for n in ("h", "o", "st"))
        s_free, s_sum, s_rms, s_y = sm("free"), sm("sum"), sm("rms"), sm("y")
        with nc.Block() as block:
            @block.sync
            def _(sp):
                sp.dma_start(w[:, :], T["final_norm_w"].broadcast_to([128, D])).then_inc(s_w, 16)
                with sp.Fori(0, 3) as j:
                    for u in range(3):
                        sp.wait_ge(s_free, j * 3 + (u + 1))
                        sp.dma_start(h[:, u, :], T["h"][rows3(j, u), :]).then_inc(s_h[u], 16)

            @block.gpsimd
            def _(pool):
                with pool.Fori(0, 3) as j:
                    for u in range(3):
                        pool.wait_ge(s_free, j * 3 + (u + 1))
                        nc.gpsimd.tensor_copy(idx[:, u, :], T["slots"][:, ds(j * 3 + u, 1), :].rearrange("p a k -> p (a k)")
                                              ).then_inc(s_idx, 1)
                        pool.wait_ge(s_idx, j * 3 + (u + 1))
                        pool.sem_inc(s_seen, 1)
                        for k in range(2):
                            pool.indirect_dma_start(out=o[:, u, k, :], out_offset=None, in_=T["o_moe"],
                                                    in_offset=bass.IndirectOffsetOnAxis(ap=idx[:, u, k:k + 1], axis=0)
                                                    ).then_inc(s_o[u], 16)

            @block.vector
            def _(dve):
                nc.vector.memset(eps[:, :], EPS).then_inc(s_eps, 1)
                dve.sem_inc(s_free, 3)
                dve.wait_ge(s_w, 16)
                with dve.Fori(0, 3) as j:
                    for u in range(3):
                        n = j * 3 + u
                        nc.vector.tensor_copy(gate[:, u, :], T["gates"][:, ds(n, 1), :].rearrange("p a k -> p (a k)"))
                        dve.drain()
                        dve.wait_ge(s_h[u], (j + 1) * 16)
                        dve.wait_ge(s_o[u], (j + 1) * 32)
                        for k in range(2):
                            nc.vector.scalar_tensor_tensor(h[:, u, :], o[:, u, k, :], gate[:, u, k:k + 1], h[:, u, :], ALU.mult, ALU.add)
                            dve.drain()
                        dve.sem_inc(s_sum, 1)
                        dve.wait_ge(s_rms, n + 1)
                        nc.vector.reciprocal(ms[:, u, 1:2], ms[:, u, 1:2])
                        dve.drain()
                        dve.wait_ge(s_st[u], j * 16)
                        nc.vector.scalar_tensor_tensor(y[:, u, :], h[:, u, :], ms[:, u, 1:2], w[:, :], ALU.mult, ALU.mult)
                        dve.drain()
                        dve.sem_inc(s_y, 1)
                        dve.sem_inc(s_free, 1)

            @block.scalar
            def _(act):
                act.wait_ge(s_eps, 1)
                with act.Fori(0, 3) as j:
                    for u in range(3):
                        n = j * 3 + u
                        act.wait_ge(s_sum, n + 1)
                        nc.scalar.activation(junk[:, :], h[:, u, :], ACT.Square, accum_out=ms[:, u, 0:1])
                        act.drain()
                        nc.scalar.activation(ms[:, u, 1:2], ms[:, u, 0:1], ACT.Sqrt, bias=eps[:, :], scale=1.0 / D)
                        act.drain()
                        act.sem_inc(s_rms, 1)
                        act.wait_ge(s_y, n + 1)
                        act.dma_start(T["y"][rows3(j, u), :], y[:, u, :]).then_inc(s_st[u], 16)
                for u in range(3):
                    act.wait_ge(s_st[u], 48)


PHASES = [
    ([("dt_cm", [SH, TOK]), ("dt_tm", [128, TILES, SH]), ("da_tm", [128, TILES, SH])],
     [phase_norm_project, phase_conv, phase_attention_prompt, phase_attention_sample, phase_ssd_prompt, phase_ssd_sample]),
    ([("ys_T", [128, KT, TOK]), ("m_T", [128, KT, TOK])],
     [phase_branch_inputs, phase_merge, phase_out_router]),
    ([], [phase_route, phase_experts, phase_overflow, phase_combine]),
]


def output_shapes():
    keeps = [min(w, SEQ) for w, _ in GROUPS]
    news = [min(w, PAST + NT) for w, _ in GROUPS]
    return ([("y", (TOK, D))]
            + [(f"p_kv{g}", (1, 1, k, 2, HG, HD)) for g, k in enumerate(keeps)]
            + [("p_conv", (1, 1, CONV - 1, XBC)), ("p_ssm", (1, 1, SH, HD, SN))]
            + [(f"s_kv{g}", (1, NB, k, 2, HG, HD)) for g, k in enumerate(news)]
            + [("s_conv", (1, NB, CONV - 1, XBC)), ("s_ssm", (1, NB, SH, HD, SN))])


def build_program(nc, T, phases=99):
    with ExitStack() as ctx:
        used = []

        def sem(name):
            used.append(nc.alloc_semaphore(name=name))
            return used[-1]

        def scratch(name, shape, dt=f32):
            T[name] = nc.dram_tensor(f"scratch_{name}", shape, dt, kind="Internal").ap()

        scratch("u_tm", (TOK, XOFF))
        scratch("xbc_cm", (XBC, TOK))
        scratch("gate_cm", (2 * D, TOK))
        scratch("xc_tm", (TOK, XBC))
        scratch("xc_cm", (XBC, TOK))
        scratch("o_attn", (3, SEQ, GW + 8))
        scratch("y_ssd", (TOK, D))
        scratch("h", (TOK, D))
        scratch("hn", (TOK, D))
        scratch("ids", (NBLK * 128, 1), i32)
        scratch("o_moe", (NBLK * 128, D))
        scratch("ovf", (1, 32), i32)
        T["p_kv"] = [T[f"p_kv{g}"] for g in range(3)]
        T["s_kv"] = [T[f"s_kv{g}"] for g in range(3)]
        T["cache"] = [T["cache_kv_w128"], T["cache_kv_w512"], T["cache_kv_w2048"]]
        T["s_cache"] = ctx.enter_context(nc.semaphore("cache_moved"))

        def keep(name, shape, dt=f32):
            T[name] = ctx.enter_context(nc.sbuf_tensor(name, shape, dt))

        keep("ya_T", [128, 2, TOK])
        keep("logits", [128, TILES, 40])
        keep("slots", [128, TILES, 2], i32)
        keep("gates", [128, TILES, 2])
        n = 0
        for tensors, group in PHASES:
            with ExitStack() as own:
                for name, shape in tensors:
                    T[name] = own.enter_context(nc.sbuf_tensor(name, shape, f32))
                for phase in group:
                    if n < phases:
                        phase(nc, T, sem)
                        nc.clear_and_free_semaphores(used)
                        used.clear()
                        nc.all_engine_barrier()
                    n += 1


_DATA = ["norm1_w", "w_in", "w_attn_br", "w_ssd_br", "b_gate", "w_out", "conv_w", "conv_b", "dt_bias", "A_log", "D_skip",
         "ssd_norm_w", "norm2_w", "b_router_coarse", "b_router_fine", "w_expert_gate", "w_expert_up", "w_expert_down",
         "final_norm_w", "cache_kv_w128", "cache_kv_w512", "cache_kv_w2048", "state_conv", "state_ssm",
         "w_router_coarse", "w_router_fine"]


def shape_constants():
    f = np.float32
    i, j = np.arange(128)[:, None], np.arange(128)[None, :]
    c = {"ident": np.eye(128, dtype=f)}
    c["upto"] = (i <= j).astype(f)
    c["before"] = (i < j).astype(f)
    same = i // NT == j // NT
    c["upto_seq"] = ((i <= j) & same).astype(f)
    c["future"] = np.where(i <= j, 0.0, NEG).astype(f)
    c["future_seq"] = np.where((i <= j) & same, 0.0, NEG).astype(f)
    c["seq_of"] = (i // NT == np.arange(NB)[None, :]).astype(f)
    c["same_seq"] = same.astype(f)
    c["seq_cols"] = np.broadcast_to(np.arange(NB)[:, None] == np.arange(128)[None, :] // NT, (128, NB, 128)).astype(f)
    prev = np.where(j >= i, 0.0, NEG).astype(f)
    cur = np.where(j <= i, 0.0, NEG).astype(f)
    none = np.full((128, 128), NEG, f)
    first = np.stack([np.concatenate([cur, prev if n else none], 1) for n in range(4)], 1)
    c["mask_even"] = np.ascontiguousarray(first)
    c["mask_odd"] = np.concatenate([prev, cur], 1)
    c["mask_half"] = np.where((j <= i) & (i // 64 == j // 64), 0.0, NEG).astype(f)
    inv = (np.float32(10000.0) ** (-np.arange(HD // 2, dtype=f) * f(2.0 / HD))).astype(f)

    def rotary(pos):
        ang = (pos.astype(f)[..., None] * inv).astype(f)
        cs, sn = np.cos(ang), np.sin(ang)
        return np.concatenate([cs, cs, -sn, sn], -1).astype(f)
    p = np.arange(128)
    order = np.zeros((3, 8, 128), np.int64)
    for t in range(8):
        order[0, t] = t * 128 + p
        order[1, t] = t // 2 + 4 * ((t % 2) * 128 + p)
        order[2, t] = 2 * t + p // 64 + 16 * (p % 64)
    c["rotary"] = np.ascontiguousarray(rotary(order).transpose(2, 1, 0, 3))
    c["rotary_new"] = rotary(PAST + p % NT)
    t = (np.arange(128) % NT)[:, None]
    old = np.zeros((128, 3, 128), f)
    old[:, 0] = np.where(j >= t, 0.0, NEG)
    old[:, 1] = np.where(4 * j + t % 4 >= t, 0.0, NEG)
    old[:, 2] = np.where(j // 64 == t % 2, 0.0, NEG)
    c["mask_cached"] = old
    new = np.full((128, 2, 3, 128), NEG, f)
    row, key = np.arange(128)[:, None], np.arange(128)[None, :]
    for half in range(2):
        seq, tt = half * 4 + row // 32, row % NT
        ks, kt = key // NT, key % NT
        for g, ok in enumerate((kt <= tt, (kt == tt) | (kt == tt - 4), kt == tt)):
            new[:, half, g] = np.where((seq == ks) & ok & (key < SAMP), 0.0, NEG)
    c["mask_new"] = new
    c["experts"] = np.broadcast_to(np.arange(NE, dtype=f), (128, NE)).copy()
    c["group_of"] = np.broadcast_to(np.arange(NE, dtype=f) // 8, (128, NE)).copy()
    c["tokens"] = (np.arange(TILES)[None, :] * 128 + np.arange(128)[:, None]).astype(np.int32)
    c["first_wins"] = np.broadcast_to(NE - np.arange(NE, dtype=f), (128, NE)).copy()
    c["beyond"] = np.broadcast_to((NE - 1 - np.arange(NE, dtype=f)), (128, NE)).copy()
    c["fills"] = np.broadcast_to(128.0 * np.arange(1, 9, dtype=f), (128, 8)).copy()
    c["row_id"] = np.arange(128, dtype=f)[:, None].copy()
    c["zero_ids"] = np.zeros((128, NBLK), np.int32)
    return c


def kernel(**inputs):
    import numpy as _np
    import concourse.bacc as _bacc
    from concourse import mybir as _mybir
    from concourse.bass_utils import run_bass_kernel_spmd as _run

    nc = _bacc.Bacc("TRN2", target_bir_lowering=False, num_devices=1)
    x_p, x_s = _np.asarray(inputs["x_prompt"]), _np.asarray(inputs["x_sample"])
    arrays = {"x_all": _np.concatenate([x_p.reshape(SEQ, D), x_s.reshape(SAMP, D),
                                        _np.zeros((TOK - SEQ - SAMP, D), x_p.dtype)])}
    for name in _DATA:
        arrays[name] = _np.asarray(inputs[name])
    arrays["state_conv"] = _np.ascontiguousarray(arrays["state_conv"][0].transpose(2, 0, 1))
    for name in ("norm1_w", "b_gate", "ssd_norm_w", "conv_w", "conv_b"):
        a = arrays[name].reshape(-1, arrays[name].shape[-1] // 128, 128)
        arrays[name] = a.transpose(2, 1, 0) if name == "conv_w" else a.transpose(2, 0, 1)
    arrays["dt_bias"], arrays["A_log"] = arrays["dt_bias"].reshape(SH, 1), arrays["A_log"].reshape(SH, 1)
    arrays["d_skip"] = _np.broadcast_to(arrays.pop("D_skip").reshape(1, SH), (128, SH))
    arrays["b_router"] = _np.concatenate([arrays.pop("b_router_coarse"), arrays.pop("b_router_fine")], -1)
    arrays["w_router"] = _np.concatenate([arrays.pop("w_router_coarse"), arrays.pop("w_router_fine")], -1)
    arrays["final_norm_w"] = arrays["final_norm_w"].reshape(1, D)
    arrays = {f"in_{n}": _np.ascontiguousarray(a) for n, a in arrays.items()}
    arrays.update({f"const_{n}": a for n, a in shape_constants().items()})
    T = {}
    for name, a in arrays.items():
        kind = "ExternalInput"
        T[name.split("_", 1)[1]] = nc.dram_tensor(name, a.shape, _mybir.dt.from_np(a.dtype), kind=kind).ap()
    outs = output_shapes()
    for name, shape in outs:
        T[name] = nc.dram_tensor(f"out_{name}", shape, _mybir.dt.float32, kind="ExternalOutput").ap()
    build_program(nc, T)
    r = _run(nc, [arrays], core_ids=[0])
    got = [_np.asarray(r.results[0][f"out_{name}"]) for name, _ in outs]
    y = got[0]
    return (y[:SEQ].reshape(1, SEQ, D), y[SEQ:SEQ + SAMP].reshape(NB, NT, D), *got[1:])
```

```python
import concourse.bass as bass
from concourse import mybir
from contextlib import ExitStack, contextmanager
import numpy as np

f32 = mybir.dt.float32
bf16 = mybir.dt.bfloat16
f32r = mybir.dt.float32r
i32 = mybir.dt.int32
u32 = mybir.dt.uint32
ALU = mybir.AluOpType
ACT = mybir.ActivationFunctionType
AX = mybir.AxisListType
ds = bass.ds

D = 1024
KT = D // 128
SEQ = 1024
NB, NT = 8, 8
SAMP = NB * NT
PAST = 1024
TILES = SEQ // 128 + 1
TOK = TILES * 128
HD = 64
HG = 4
GW = HG * HD
GROUPS = ((128, 1), (512, 4), (2048, 16))
SPAN = 128
AW = 3 * GW
DI = 1024
SH = 16
SN = 128
CONV = 4
XBC = DI + 4 * SN
ZOFF = 3 * AW
XOFF = ZOFF + DI
DTOFF = XOFF + XBC
GOFF = DTOFF + SH
DIN = GOFF + 2 * D
NE = 32
FF = 512
NOVF = 16
NBLK = NE + NOVF
EPS = 1e-6
NEG = -1e30
WCOL = 256
HI_BITS = -4096
HIST = CONV - 1
TAIL = HIST * (1 + NB)
NCH = 384
START = 1


def bc(ap, shape):
    return ap.broadcast_to(shape)


def one_pass(ap):
    return ap.bitcast(f32r)


def split(nc, dve, value, hi, lo, upper):
    nc.vector.tensor_scalar(upper.bitcast(i32), value.bitcast(i32), HI_BITS, None, ALU.bitwise_and)
    dve.drain()
    nc.vector.tensor_copy(one_pass(hi), upper)
    nc.vector.tensor_tensor(one_pass(lo), value, upper, ALU.subtract)
    dve.drain()


def product(nc, out, pairs):
    n = len(pairs)
    for i, ((a_hi, a_lo), (b_hi, b_lo)) in enumerate(pairs):
        nc.tensor.matmul(out, one_pass(a_hi), one_pass(b_hi), start=(i == 0), stop=False)
        nc.tensor.matmul(out, one_pass(a_hi), one_pass(b_lo), start=False, stop=False)
        last = nc.tensor.matmul(out, one_pass(a_lo), one_pass(b_hi), start=False, stop=(i == n - 1))
    return last


def phase_norm_project(nc, T, sem):
    with ExitStack() as ctx:
        def sb(name, shape, dt=f32):
            return ctx.enter_context(nc.sbuf_tensor(name, shape, dt))

        x_hi, x_lo = sb("x_hi", [128, KT, TOK]), sb("x_lo", [128, KT, TOK])
        ident = sb("a_ident", [128, 128])
        w1c = sb("w1c", [128, KT])
        bgc = sb("bgc", [128, 2 * KT])
        eps = sb("a_eps", [128, 1])
        NX = XBC // 128
        conv_w, conv_b = sb("conv_w", [128, NX, CONV]), sb("conv_b", [128, NX])
        dtw = sb("dtw", [128, KT, SH])
        dt_bias, a_log = sb("dt_bias", [SH, 1]), sb("a_log", [SH, 1])
        w_in = T["w_in"][0].rearrange("(k p) n -> p k n", p=128)
        s_const, s_eps, s_cw = sem("a_const"), sem("a_eps"), sem("a_cw")

        with ExitStack() as c2:
            x_in = c2.enter_context(nc.sbuf_tensor("x_in", [128, 3, D], f32))
            xn = c2.enter_context(nc.sbuf_tensor("xn", [128, 3, D], f32))
            junk = c2.enter_context(nc.sbuf_tensor("a_junk", [128, D], f32))
            ms = c2.enter_context(nc.sbuf_tensor("a_ms", [128, 3, 2], f32))
            scaled = c2.enter_context(nc.sbuf_tensor("a_scaled", [128, KT, 128], f32))
            upper = c2.enter_context(nc.sbuf_tensor("a_upper", [128, KT, 128], f32))
            turned = c2.enter_context(nc.psum_tensor("a_turned", [128, 3, KT, 128], f32))
            s_x = [sem(f"a_x{u}") for u in range(3)]
            s_std, s_xn, s_turned, s_xfree = sem("a_std"), sem("a_xn"), sem("a_turned"), sem("a_xfree")
            s_tfree = sem("a_tfree")
            with nc.Block() as block:
                @block.sync
                def _(sp):
                    sp.dma_start(ident[:, :], T["ident"]).then_inc(s_const, 16)
                    sp.dma_start(w1c[:, :], T["norm1_w"].rearrange("p a k -> p (a k)")).then_inc(s_const, 16)
                    sp.dma_start(bgc[:, :], T["b_gate"].rearrange("p a k -> p (a k)")).then_inc(s_const, 16)
                    with sp.Fori(0, 3) as j:
                        for u in range(3):
                            sp.wait_ge(s_xfree, j * 3 + u + 1)
                            sp.dma_start(x_in[:, u, :], T["x_all"][ds((j * 3 + u) * 128, 128), :]).then_inc(s_x[u], 16)

                @block.gpsimd
                def _(pool):
                    for dst, src in ((dtw[:, :, :], w_in[:, :, DTOFF:DTOFF + SH]), (dt_bias[:, :], T["dt_bias"]),
                                     (conv_w[:, :, :], T["conv_w"]), (conv_b[:, :], T["conv_b"].rearrange("p a k -> p (a k)")),
                                     (a_log[:, :], T["A_log"])):
                        pool.dma_start(dst, src).then_inc(s_cw, 16)

                @block.scalar
                def _(act):
                    act.wait_ge(s_eps, 1)
                    with act.Fori(0, 3) as j:
                        for u in range(3):
                            act.wait_ge(s_x[u], (j + 1) * 16)
                            nc.scalar.activation(junk[:, :], x_in[:, u, :], ACT.Square, accum_out=ms[:, u, 0:1])
                            act.drain()
                            nc.scalar.activation(ms[:, u, 1:2], ms[:, u, 0:1], ACT.Sqrt, bias=eps[:, :],
                                                 scale=1.0 / D).then_inc(s_std, 1)

                @block.vector
                def _(dve):
                    nc.vector.memset(eps[:, :], EPS).then_inc(s_eps, 1)
                    dve.sem_inc(s_xfree, 3)
                    dve.wait_ge(s_const, 48)
                    for n in range(TILES + 1):
                        if n < TILES:
                            u = n % 3
                            dve.wait_ge(s_std, n + 1)
                            nc.vector.reciprocal(ms[:, u, 1:2], ms[:, u, 1:2])
                            dve.drain()
                            nc.vector.tensor_scalar(xn[:, u, :], x_in[:, u, :], ms[:, u, 1:2], None, ALU.mult
                                                    ).then_inc(s_xn, 1)
                            dve.drain()
                            dve.sem_inc(s_xfree, 1)
                        if n > 0:
                            cols, u = slice((n - 1) * 128, n * 128), (n - 1) % 3
                            dve.wait_ge(s_turned, n)
                            for k0 in (0, KT // 2):
                                nc.vector.tensor_tensor(scaled[:, k0:k0 + 4, :], turned[:, u, k0:k0 + 4, :],
                                                        bc(w1c[:, k0:k0 + 4].unsqueeze(2), [128, 4, 128]), ALU.mult)
                            dve.drain()
                            dve.sem_inc(s_tfree, 1)
                            split(nc, dve, scaled[:, :, :], x_hi[:, :, cols], x_lo[:, :, cols], upper[:, :, :])

                @block.tensor
                def _(pe):
                    pe.sem_inc(s_tfree, 3)
                    pe.wait_ge(s_const, 48)
                    with pe.Fori(0, 3) as j:
                        for u in range(3):
                            pe.wait_ge(s_xn, j * 3 + u + 1)
                            pe.wait_ge(s_tfree, j * 3 + u + 1)
                            for k in range(KT):
                                last = nc.tensor.transpose(turned[:, u, k, :], xn[:, u, k * 128:(k + 1) * 128], ident[:, :])
                            last.then_inc(s_turned, 1)

        with ExitStack() as c2:
            def sb2(name, shape):
                return c2.enter_context(nc.sbuf_tensor(name, shape, f32))

            w = sb2("w", [128, KT * WCOL])
            w_lo, w_hi = sb2("w_lo", [128, 2, KT * WCOL]), sb2("w_hi", [128, 2, KT * WCOL])
            upper = sb2("w_upper", [128, KT * WCOL // 2])
            dtw_lo, dtw_hi = sb2("dtw_lo", [128, KT, SH]), sb2("dtw_hi", [128, KT, SH])
            o_tm = sb2("o_tm", [128, 6, WCOL])
            o_gate = sb2("o_gate", [128, 2, TOK])
            bias = sb2("gate_bias", [128, 1])
            xr = sb2("xr", [128, 2, HIST + SEQ])
            xs = sb2("xs", [128, 2, NB, HIST + NT])
            tail = sb2("tail", [128, 2, TAIL])
            sums = sb2("sums", [128, TOK])
            xc = sb2("xc", [128, 2, TOK])
            xt = sb2("xt", [128, 2, TILES, 128])
            tails = sb2("tails", [TAIL, XBC])
            neg_a = sb2("neg_a", [SH, 1])
            dt_cm, da_cm = sb2("dt_cm", [SH, TOK]), sums[0:SH, :]
            acc = [c2.enter_context(nc.psum_tensor(f"a_acc{i}", [128, 512], f32)) for i in range(6)]
            pt = [c2.enter_context(nc.psum_tensor(f"a_pt{i}", [128, 4, 128], f32)) for i in range(2)]
            s_w, s_rfree = sem("a_w"), sem("a_rfree")
            s_dtw, s_split, s_wfree = sem("a_dtw"), sem("a_split"), sem("a_wfree")
            s_acc, s_out, s_zero = sem("a_acc"), sem("a_out"), sem("a_zero")
            s_st = [sem(f"a_st{i}") for i in range(6)]
            s_gst, s_hist, s_cst, s_tst = ([sem(f"a_{n}{i}") for i in range(2)] for n in ("gst", "hist", "cst", "tst"))
            s_stored, s_dt, s_dta, s_dtp = sem("a_stored"), sem("a_dt"), sem("a_dta"), sem("a_dtp")
            s_free, s_xr, s_sums, s_xc, s_pe, s_ev, s_xt = (sem(f"a_{n}") for n in ("free", "xr", "sums", "xc", "pe", "ev", "xt"))
            for s in (*s_st, *s_gst, *s_cst, s_xc):
                nc.sync.sem_inc(s, START)
            chunks = TOK // NCH
            n_tm = XOFF // WCOL
            TM, CM = chunks, chunks + n_tm * TILES

            def tm(w):
                return w.rearrange("p (k n) -> p k n", n=WCOL)

            def cm(w, a):
                return w[:, a * KT * 128:(a + 1) * KT * 128].rearrange("p (k n) -> p k n", n=128)

            def tm_blocks(eng, body):
                with eng.Fori(0, n_tm // 2) as j:
                    for u in range(2):
                        body(j * 2 + u, u, j)
                body(n_tm - 1, 0, n_tm // 2)

            with nc.Block() as block:
                @block.sync
                def _(sp):

                    def load_tm(n, u, j):
                        sp.wait_ge(s_rfree, n + 1)
                        sp.dma_start(tm(w[:, :]), w_in[:, :, ds(n * WCOL, WCOL)]).then_inc(s_w, 16)
                    tm_blocks(sp, load_tm)

                    def load(n, first, second):
                        sp.wait_ge(s_rfree, n + (n_tm + 1))
                        for a, off in enumerate((first, second)):
                            sp.dma_start(cm(w, a), w_in[:, :, ds(off, 128)]).then_inc(s_w, 16)
                    with sp.Fori(0, NX // 2) as j:
                        for u in range(2):
                            n = j * 2 + u
                            load(n, n * 128 + XOFF, n * 128 + GOFF)
                            sp.wait_ge(s_free, n + 1)
                            sp.dma_start(xs[:, u, :, 0:HIST], T["state_conv"][ds(n * 128, 128), :, :]).then_inc(s_hist[u], 16)
                    for u in range(2):
                        load(NX + u, GOFF + (NX + 2 * u) * 128, GOFF + (NX + 2 * u + 1) * 128)

                @block.gpsimd
                def _(pool):
                    nc.gpsimd.memset(xr[:, :, 0:HIST], 0.0).then_inc(s_zero, 1)
                    for b in range(NB):
                        pool.wait_ge(s_split, b + 1)
                        for g, (window, dil) in enumerate(GROUPS):
                            old = min(window, PAST)
                            keep = min(window, old + NT) - NT
                            pool.dma_start(T["s_kv"][g][0, b, 0:keep, :, :, :].rearrange("r a h d -> r (a h d)"),
                                           T["cache"][g][0, b, old - keep:old, :, :, :].rearrange("r a h d -> r (a h d)")
                                           ).then_inc(T["s_cache"], 16)
                    with pool.Fori(0, NX // 2) as j:
                        for u in range(2):
                            n = j * 2 + u
                            pool.wait_ge(s_xt, n + 1)
                            pool.dma_start(T["xc_tm"][:, ds(n * 128, 128)].rearrange("(t p) c -> p t c", p=128),
                                           xt[:, u, :, :]).then_inc(s_tst[u], 16)
                            pool.wait_ge(s_tst[u], (j + 1) * 16)
                            pool.sem_inc(s_stored, 1)
                    pool.dma_start(T["p_conv"][0, 0, :, :], tails[0:HIST, :]).then_inc(s_tst[0], 16)
                    pool.dma_start(T["s_conv"][0].rearrange("b r c -> (b r) c"), tails[HIST:, :]).then_inc(s_tst[1], 16)
                    for u in range(2):
                        pool.wait_ge(s_tst[u], (NX // 2 + 1) * 16)

                @block.vector
                def _(dve):
                    dve.sem_inc(s_ev, 1)
                    dve.sem_inc(s_free, 2)
                    dve.sem_inc(s_rfree, 1)
                    dve.sem_inc(s_stored, 2)
                    dve.wait_ge(s_cw, 80)
                    split(nc, dve, dtw[:, :, :], dtw_hi[:, :, :], dtw_lo[:, :, :], upper[:, 0:KT * SH].rearrange("p (k n) -> p k n", n=SH))
                    dve.sem_inc(s_dtw, 1)
                    dve.wait_ge(s_dta, 1)
                    nc.vector.tensor_scalar(dt_cm[:, :], dt_cm[:, :], dt_bias[:, :], None, ALU.add)
                    dve.drain()
                    nc.vector.tensor_scalar(da_cm, dt_cm[:, :], -1.0, None, ALU.mult)
                    dve.drain()
                    nc.vector.tensor_tensor(da_cm, dt_cm[:, :], da_cm, ALU.min).then_inc(s_dt, 1)
                    dve.wait_ge(s_dta, 2)
                    nc.vector.scalar_tensor_tensor(dt_cm[:, :], dt_cm[:, :], 0.0, da_cm, ALU.max, ALU.add)
                    nc.vector.tensor_scalar(neg_a[:, :], a_log[:, :], -1.0, None, ALU.mult)
                    dve.drain()
                    nc.vector.tensor_scalar(da_cm, dt_cm[:, :], neg_a[:, :], None, ALU.mult).then_inc(s_dt, 1)

                    def split_block(u):
                        for half in range(2):
                            cols = slice(half * KT * WCOL // 2, (half + 1) * KT * WCOL // 2)
                            split(nc, dve, w[:, cols], w_hi[:, u, cols], w_lo[:, u, cols], upper[:, :])
                        dve.sem_inc(s_rfree, 1)
                        dve.sem_inc(s_split, 1)

                    def prepare_tm(n, u, j):
                        dve.wait_ge(s_w, (n + 1) * 16)
                        dve.wait_ge(s_wfree, n + 1)
                        split_block(u)
                    tm_blocks(dve, prepare_tm)
                    dve.wait_ge(s_dtp, 1)
                    for kind, dst in enumerate((T["dt_tm"], T["da_tm"])):
                        nc.vector.tensor_copy(dst[:, :, :], pt[1][:, :, :].rearrange("p a b -> p (a b)")
                                              [:, kind * TILES * SH:(kind + 1) * TILES * SH].rearrange("p (t h) -> p t h", h=SH))
                    dve.drain()
                    dve.sem_inc(s_ev, 1)
                    nc.vector.memset(sums[:, SEQ + SAMP:], 0.0)

                    def prepare(n, u):
                        dve.wait_ge(s_w, n * 32 + (n_tm * 16 + 32))
                        dve.wait_ge(s_wfree, n + (n_tm + 1))
                        split_block((n_tm + u) % 2)
                    prepare(0, 0)
                    dve.wait_ge(s_zero, 1)
                    with dve.Fori(0, NX // 2) as j:
                        for u in range(2):
                            n = j * 2 + u
                            prepare(j * 2 + (u + 1), 1 - u)
                            dve.wait_ge(s_xr, n + 1)
                            dve.wait_ge(s_hist[u], (j + 1) * 16)
                            dve.wait_ge(s_xc, n + START)
                            sample = sums[:, SEQ:SEQ + SAMP].rearrange("p (b t) -> p b t", b=NB)
                            for k in range(CONV):
                                tap = conv_w[:, ds(n, 1), k:k + 1].rearrange("p a k -> p (a k)")
                                for dst, src in ((sums[:, 0:SEQ], xr[:, u, k:k + SEQ]), (sample, xs[:, u, :, k:k + NT])):
                                    if k == 0:
                                        nc.vector.tensor_scalar(dst, src, tap, conv_b[:, ds(n, 1)], ALU.mult, ALU.add)
                                    else:
                                        nc.vector.scalar_tensor_tensor(dst, src, tap, dst, ALU.mult, ALU.add)
                                dve.drain()
                            dve.sem_inc(s_sums, 1)
                            dve.wait_ge(s_stored, n + 1)
                            for f in range(3):
                                p = pt[(u + f) % 2]
                                dve.wait_ge(s_pe, j * 6 + (3 * u + f + 1))
                                if f < 2:
                                    nc.vector.tensor_copy(xt[:, u, 4 * f:4 * f + 4, :], p[:, :, :])
                                else:
                                    nc.vector.tensor_copy(xt[:, u, 8, :], p[:, 0, :])
                                    nc.vector.tensor_copy(tails[:, ds(n * 128, 128)], p[0:TAIL, 1, :])
                                dve.drain()
                                dve.sem_inc(s_ev, 1)
                            dve.sem_inc(s_xt, 1)
                            dve.sem_inc(s_free, 1)
                    prepare(NX + 1, 1)

                @block.scalar
                def _(act):
                    act.sem_inc(s_out, 6)
                    for c in range(chunks):
                        act.wait_ge(s_acc, c + 1)
                        nc.scalar.copy(dt_cm[:, c * NCH:(c + 1) * NCH], acc[c][0:SH, 0:NCH]).then_inc(s_out, 1)
                    act.drain()
                    act.sem_inc(s_dta, 1)
                    act.wait_ge(s_cw, 80)
                    nc.scalar.activation(a_log[:, :], a_log[:, :], ACT.Exp)
                    act.wait_ge(s_dt, 1)
                    nc.scalar.activation(da_cm, da_cm, ACT.Exp)
                    act.drain()
                    nc.scalar.activation(da_cm, da_cm, ACT.Ln, bias=1.0)
                    act.drain()
                    act.sem_inc(s_dta, 1)

                    def take_tm(n, u, j):
                        for m in range(TILES):
                            i = u * TILES + m
                            act.wait_ge(s_acc, j * (2 * TILES) + (TM + i + 1))
                            act.wait_ge(s_st[i % 6], (j * 3 + i // 6) * 16 + START)
                            nc.scalar.copy(o_tm[:, i % 6, :], acc[(TM + i) % 6][:, 0:WCOL]).then_inc(s_out, 1)
                            act.drain()
                            act.dma_start(T["u_tm"][m * 128:(m + 1) * 128, ds(n * WCOL, WCOL)], o_tm[:, i % 6, :]
                                          ).then_inc(s_st[i % 6], 16)
                    tm_blocks(act, take_tm)

                    def gate(block, slot, stored, products, part, cs):
                        if cs[0] == 0:
                            act.wait_ge(s_gst[slot], stored)
                            nc.scalar.copy(bias[:, :], bgc[:, ds(block, 1)])
                            act.drain()
                        for c in cs:
                            act.wait_ge(s_acc, products + (part * chunks + c + 1))
                            nc.scalar.activation(o_gate[:, slot, c * NCH:(c + 1) * NCH], acc[(CM + part * chunks + c) % 6][:, 0:NCH],
                                                 ACT.Sigmoid, bias=bias[:, :]).then_inc(s_out, 1)
                        if cs[-1] == chunks - 1:
                            act.drain()
                            act.dma_start(T["gate_cm"][ds(block * 128, 128), :], o_gate[:, slot, :]).then_inc(s_gst[slot], 16)

                    with act.Fori(0, NX // 2) as j:
                        for u in range(2):
                            n = j * 2 + u
                            before = j * (4 * chunks) + (CM + 2 * chunks * u)
                            act.wait_ge(s_free, n + 1)
                            for c in range(chunks):
                                act.wait_ge(s_acc, j * (4 * chunks) + (CM + 2 * chunks * u + c + 1))
                                src = acc[(CM + c) % 6]
                                m = min(NCH, SEQ - c * NCH)
                                last = nc.scalar.copy(xr[:, u, HIST + c * NCH:HIST + c * NCH + m], src[:, 0:m])
                                if c == chunks - 1:
                                    new = src[:, m:m + SAMP].rearrange("p (b t) -> p b t", b=NB)
                                    nc.scalar.copy(xs[:, u, :, HIST:], new)
                                    nc.scalar.copy(tail[:, u, 0:HIST], src[:, m - HIST:m])
                                    last = nc.scalar.copy(tail[:, u, HIST:].rearrange("p (b t) -> p b t", b=NB), new[:, :, NT - HIST:])
                                last.then_inc(s_out, 1)
                            act.drain()
                            act.sem_inc(s_xr, 1)
                            gate(n, u, j * 16 + START, before, 1, (0, 1))
                            act.wait_ge(s_sums, n + 1)
                            act.wait_ge(s_cst[u], j * 16 + START)
                            nc.scalar.activation(xc[:, u, :], sums[:, :], ACT.Silu)
                            act.drain()
                            act.sem_inc(s_xc, 1)
                            act.dma_start(T["xc_cm"][ds(n * 128, 128), :], xc[:, u, :]).then_inc(s_cst[u], 16)
                            gate(n, u, 0, before, 1, (2,))
                    for i in range(4):
                        gate(NX + i, i % 2, (NX // 2 + i // 2) * 16 + START, CM + (2 * NX + i // 2 * 2) * chunks, i % 2, range(chunks))
                    for i in range(6):
                        act.wait_ge(s_st[i], len(range(i, n_tm * TILES, 6)) * 16 + START)
                    for u in range(2):
                        act.wait_ge(s_gst[u], (NX // 2 + 2) * 16 + START)
                        act.wait_ge(s_cst[u], NX // 2 * 16 + START)

                @block.tensor
                def _(pe):
                    pe.sem_inc(s_wfree, 2)
                    pe.wait_ge(s_dtw, 1)
                    for c in range(chunks):
                        pe.wait_ge(s_out, c + 1)
                        cols = slice(c * NCH, (c + 1) * NCH)
                        product(nc, acc[c][0:SH, 0:NCH], [((dtw_hi[:, k, :], dtw_lo[:, k, :]), (x_hi[:, k, cols], x_lo[:, k, cols]))
                                                          for k in range(KT)]).then_inc(s_acc, 1)

                    def products_tm(n, u, j):
                        hi, lo = tm(w_hi[:, u, :]), tm(w_lo[:, u, :])
                        pe.wait_ge(s_split, n + 1)
                        for m in range(TILES):
                            i = u * TILES + m
                            rows = slice(m * 128, (m + 1) * 128)
                            pe.wait_ge(s_out, j * (2 * TILES) + (TM + i + 1))
                            product(nc, acc[(TM + i) % 6][:, 0:WCOL],
                                    [((x_hi[:, k, rows], x_lo[:, k, rows]), (hi[:, k, :], lo[:, k, :])) for k in range(KT)]
                                    ).then_inc(s_acc, 1)
                        pe.drain()
                        pe.sem_inc(s_wfree, 1)
                    tm_blocks(pe, products_tm)
                    pe.wait_ge(s_dt, 2)
                    for t in range(TILES):
                        for kind, src in ((0, dt_cm[:, :]), (1, da_cm)):
                            off = (kind * TILES + t) * SH
                            last = nc.tensor.transpose(pt[1][:, :, :].rearrange("p a b -> p (a b)")[:, off:off + SH],
                                                       src[:, t * 128:(t + 1) * 128], ident[0:SH, 0:SH])
                    last.then_inc(s_dtp, 1)

                    def block_products(u, before):
                        slot = (n_tm + u) % 2
                        for a in range(2):
                            hi, lo = cm(w_hi[:, slot, :], a), cm(w_lo[:, slot, :], a)
                            for c in range(chunks):
                                cols = slice(c * NCH, (c + 1) * NCH)
                                pe.wait_ge(s_out, before + (a * chunks + c + 1))
                                product(nc, acc[(CM + a * chunks + c) % 6][:, 0:NCH],
                                        [((hi[:, k, :], lo[:, k, :]), (x_hi[:, k, cols], x_lo[:, k, cols])) for k in range(KT)]
                                        ).then_inc(s_acc, 1)
                        pe.drain()
                        pe.sem_inc(s_wfree, 1)
                    with pe.Fori(0, NX // 2) as j:
                        for u in range(2):
                            n = j * 2 + u
                            pe.wait_ge(s_split, n + (n_tm + 1))
                            block_products(u, j * (4 * chunks) + (CM + 2 * chunks * u))
                            pe.wait_ge(s_xc, n + (1 + START))
                            for f in range(3):
                                pe.wait_ge(s_ev, j * 6 + (3 * u + f + 1))
                                p = pt[(u + f) % 2]
                                for t in range(4 * f, min(4 * f + 4, TILES)):
                                    last = nc.tensor.transpose(p[:, t % 4, :], xc[:, u, t * 128:(t + 1) * 128], ident[:, :])
                                if f == 2:
                                    last = nc.tensor.transpose(p[0:TAIL, 1, :], tail[:, u, :], ident[:, :])
                                last.then_inc(s_pe, 1)
                    for u in range(2):
                        pe.wait_ge(s_split, n_tm + NX + u + 1)
                        block_products(u, CM + (2 * NX + 2 * u) * chunks)


def phase_attention_prompt(nc, T, sem):
    with ExitStack() as ctx:
        def sb(name, shape, dt=f32):
            return ctx.enter_context(nc.sbuf_tensor(name, shape, dt))

        def pb(name, shape):
            return ctx.enter_context(nc.psum_tensor(name, shape, f32))

        ident = sb("c_ident", [128, 128])
        rotary = sb("c_rotary", [128, 8, 3, 2 * HD])
        mask_even = sb("mask_even", [128, 4, 256])
        mask_odd = sb("mask_odd", [128, 256])
        mask_half = sb("mask_half", [128, 128])
        qk = sb("c_qk", [128, 2, 3, 2, GW])
        v = sb("c_v", [128, 2, 3, GW])
        rot = sb("c_rot", [128, 2, 3, 2, GW])
        tmp = sb("c_tmp", [128, 3, 2, 2 * HG, HD])
        qT = sb("c_qT", [128, 3, 2, 128])
        kT = sb("c_kT", [128, 3, 2, 2, 128])
        S = sb("c_S", [128, 3, HG, 256])
        P = sb("c_P", [128, 3, HG, 256])
        PT = sb("c_PT", [128, 3, HG, 2, 128])
        mx = sb("c_mx", [128, 3, HG])
        out = sb("c_out", [128, 2, 3, GW + 2 * HG])
        nmx = sb("c_nmx", [128, 3, HG])
        zeros = sb("c_zeros", [128, D])
        p_qk = pb("c_pqk", [128, 4, 128])
        p_s = [pb(f"c_ps{i}", [128, 2, 256]) for i in range(2)]
        p_t = [pb(f"c_pt{i}", [128, 4, 128]) for i in range(2)]
        p_o = pb("c_po", [128, 3, 128 * 4])
        s_const, s_zero = sem("c_const"), sem("c_zero")
        s_in = [[sem(f"c_in{u}{g}") for g in range(3)] for u in range(2)]
        s_v = [[sem(f"c_v{u}{g}") for g in range(3)] for u in range(2)]
        s_free, s_rot, s_qkt, s_qke = sem("c_free"), sem("c_rot"), sem("c_qkt"), sem("c_qke")
        s_sc, s_sce, s_p, s_pt, s_pte, s_o, s_oe = (sem(f"c_{n}") for n in ("sc", "sce", "p", "pt", "pte", "o", "oe"))
        s_nmx, s_zeros, s_unused = sem("c_nmx"), sem("c_zeros"), sem("c_unused")
        s_kv = [sem(f"c_kv{u}") for u in range(2)]
        s_st = [sem(f"c_st{u}") for u in range(2)]
        for s in (s_rot, *s_kv, s_qkt, s_p, *s_st, s_pt, s_qke, s_sce, s_oe):
            nc.sync.sem_inc(s, START)
        SC = HD ** -0.5
        def rows(g, j, u):
            if g == 0:
                return [(0, 128, ds((j * 2 + u) * 128, 128))]
            if g == 1:
                return [(0, 128, ds(j + u * 512, 128, step=4))]
            return [(64 * a, 64, ds(j * 4 + (2 * u + a), 64, step=16)) for a in range(2)]

        KV_DMAS = [4, 6]
        with nc.Block() as block:
            @block.sync
            def _(sp):
                sp.wait_ge(s_zero, 1)
                for dst, src in ((ident[:, :], T["ident"]), (rotary[:, :, :, :], T["rotary"]), (mask_even[:, :, :], T["mask_even"]),
                                 (mask_odd[:, :], T["mask_odd"]), (mask_half[:, :], T["mask_half"])):
                    sp.dma_start(dst, src).then_inc(s_const, 16)
                with sp.Fori(0, 4) as j:
                    for u in range(2):
                        sp.wait_ge(s_rot, (j * 2 + u) * 3 + START)
                        for g in range(3):
                            if g == 2:
                                sp.wait_ge(s_kv[u], j * (16 * KV_DMAS[u]) + START)
                            for p0, n, r in rows(g, j, u):
                                sp.dma_start(qk[p0:p0 + n, u, g, :, :],
                                             T["u_tm"][r, 0:2 * AW].rearrange("r (a c) -> r a c", a=2)[:, :, g * GW:(g + 1) * GW]
                                             ).then_inc(s_in[u][g], 16)
                        sp.wait_ge(s_free, j * 2 + (u + 1))
                        for g in range(3):
                            for p0, n, r in rows(g, j, u):
                                c0 = 2 * AW + g * GW
                                sp.dma_start(v[p0:p0 + n, u, g, :], T["u_tm"][r, c0:c0 + GW]).then_inc(s_v[u][g], 16)

            @block.gpsimd
            def _(pool):
                nc.gpsimd.memset(kT[:, :, :, :, :].rearrange("p a b c d -> p (a b c d)"), 0.0)
                nc.gpsimd.memset(v[:, 1, :, :].rearrange("p a b -> p (a b)"), 0.0).then_inc(s_zero, 1)
                nc.gpsimd.memset(zeros[:, :], 0.0).then_inc(s_zeros, 1)
                pool.wait_ge(s_zeros, 1)
                pool.dma_start(T["o_moe"][NE * 128:, :].rearrange("(b p) c -> p b c", p=128),
                               bc(zeros[:, :].unsqueeze(1), [128, NOVF, D])).then_inc(s_unused, 16)
                pool.wait_ge(s_unused, 16)

            @block.vector
            def _(dve):
                dve.wait_ge(s_zero, 1)
                dve.sem_inc(s_free, 1)
                dve.sem_inc(s_pte, 2)
                dve.wait_ge(s_const, 80)
                with dve.Fori(0, 4) as j:
                    for u in range(2):
                        t = j * 2 + u
                        for g in range(3):
                            dve.wait_ge(s_in[u][g], (j + 1) * (16 if g < 2 else 32))
                            if g == 0:
                                dve.wait_ge(s_qkt, t * 3 + START)
                                dve.wait_ge(s_kv[u], j * (16 * KV_DMAS[u]) + START)
                            x = qk[:, u, g, :, :].rearrange("p a (h c) -> p (a h) c", h=HG)
                            tab = rotary[:, ds(t, 1), g, :].rearrange("p a c -> p (a c)")
                            cos = bc(tab[:, 0:HD].unsqueeze(1), [128, 2 * HG, HD])
                            half = HD // 2
                            for a, b in ((0, half), (half, 0)):
                                sin = bc(tab[:, HD + a:HD + a + half].unsqueeze(1), [128, 2 * HG, half])
                                nc.vector.tensor_tensor(tmp[:, g, 0, :, a:a + half], x[:, :, b:b + half], sin, ALU.mult)
                            nc.vector.tensor_tensor(tmp[:, g, 1, :, :], x, cos, ALU.mult)
                            dve.drain()
                            nc.vector.tensor_tensor(rot[:, u, g, :, :].rearrange("p a (h c) -> p (a h) c", h=HG),
                                                    tmp[:, g, 0, :, :], tmp[:, g, 1, :, :], ALU.add).then_inc(s_rot, 1)
                        for g in range(3):
                            dve.wait_ge(s_qkt, t * 3 + (g + 1 + START))
                            nc.vector.tensor_copy(qT[:, g, :, :], p_qk[:, 0:2, :])
                            nc.vector.tensor_copy(kT[:, g, :, u, :], p_qk[:, 2:4, :])
                            dve.drain()
                            dve.sem_inc(s_qke, 1)
                        for g in range(3):
                            w = 256 if g == 0 or (g == 1 and u == 1) else 128
                            if g == 0 and u == 0:
                                mask = mask_even[:, ds(j, 1), :].rearrange("p a k -> p (a k)")
                            elif g == 2:
                                mask = mask_half[:, :]
                            else:
                                mask = mask_odd[:, :] if u == 1 else mask_even[:, 0, 0:128]
                            if g == 0:
                                dve.wait_ge(s_p, t * 3 + START)
                            dve.wait_ge(s_sc, t * 3 + (g + 1))
                            for h in range(2):
                                nc.vector.tensor_tensor(S[:, g, :, 0:w].rearrange("p (a b) k -> p a b k", b=2)[:, :, h, :],
                                                        p_s[h][:, :, 0:w], bc(mask.unsqueeze(1), [128, 2, w]), ALU.add)
                            dve.drain()
                            dve.sem_inc(s_sce, 1)
                            nc.vector.tensor_reduce(mx[:, g, :], S[:, g, :, 0:w], AX.X, ALU.max)
                            dve.drain()
                            nc.vector.tensor_scalar(nmx[:, g, :], mx[:, g, :], -SC, None, ALU.mult).then_inc(s_nmx, 1)
                        for g in range(3):
                            n = 8 if g == 0 or (g == 1 and u == 1) else 4
                            for i in range(n // 4):
                                k = (0, 2, 3 if u == 0 else 4)[g] + i
                                dve.wait_ge(s_pt, j * 9 + ((0, 4)[u] + k + 1 + START))
                                nc.vector.tensor_copy(PT[:, g, 4 * i // (n // 4):4 * (i + 1) // (n // 4), 0:n // 4, :]
                                                      if n == 8 else PT[:, g, :, 0, :],
                                                      p_t[((0, 4)[u] + k) % 2][:, :, :].rearrange("p (h w) c -> p h w c", w=2)
                                                      if n == 8 else p_t[((0, 4)[u] + k) % 2][:, :, :]
                                                      ).then_inc(s_pte, 1)

            @block.scalar
            def _(act):
                act.sem_inc(s_oe, 2)
                with act.Fori(0, 4) as j:
                    for u in range(2):
                        t = j * 2 + u
                        act.wait_ge(s_rot, t * 3 + (3 + START))
                        act.wait_ge(s_v[u][2], (j + 1) * 32)
                        stores = []
                        if u == 1:
                            act.wait_ge(s_v[u][1], (j + 1) * 16)
                            stores.append((T["p_kv"][1], 0, 128, 1, ds(j, 128, step=4)))
                        for p0, n, r in rows(2, j, u):
                            stores.append((T["p_kv"][2], p0, n, 2, r))
                        for dst, p0, n, g, r in stores:
                            view = dst[0, 0].rearrange("r a h c -> r a (h c)")
                            act.dma_start(view[r, 0, :], rot[p0:p0 + n, u, g, 1, :]).then_inc(s_kv[u], 16)
                            act.dma_start(view[r, 1, :], v[p0:p0 + n, u, g, :]).then_inc(s_kv[u], 16)
                        act.wait_ge(s_st[u], j * 64 + START)
                        for g in range(3):
                            w = 256 if g == 0 or (g == 1 and u == 1) else 128
                            act.wait_ge(s_nmx, t * 3 + (g + 1))
                            if g == 0:
                                act.wait_ge(s_pt, j * 9 + (0, 4)[u] + START)
                            for h in range(HG):
                                nc.scalar.activation(P[:, g, h, 0:w], S[:, g, h, 0:w], ACT.Exp, bias=nmx[:, g, h:h + 1],
                                                     scale=SC, accum_out=out[:, u, g, GW + HG + h:GW + HG + h + 1])
                            act.drain()
                            nc.scalar.mul(out[:, u, g, GW:GW + HG], nmx[:, g, :], -1.0).then_inc(s_p, 1)
                        for g in range(3):
                            act.wait_ge(s_o, t * 3 + (g + 1))
                            nc.scalar.copy(out[:, u, g, 0:GW], p_o[:, g, 0:GW]).then_inc(s_oe, 1)
                            act.drain()
                            for p0, n, r in rows(g, j, u):
                                act.dma_start(T["o_attn"][g, r, :], out[p0:p0 + n, u, g, :]).then_inc(s_st[u], 16)
                view = T["p_kv"][0][0, 0].rearrange("r a h c -> r a (h c)")
                act.dma_start(view[:, 0, :], rot[:, 1, 0, 1, :]).then_inc(s_kv[1], 16)
                act.dma_start(view[:, 1, :], v[:, 1, 0, :]).then_inc(s_kv[1], 16)
                act.wait_ge(s_kv[0], 4 * 16 * KV_DMAS[0] + START)
                act.wait_ge(s_kv[1], 4 * 16 * KV_DMAS[1] + (32 + START))
                act.wait_ge(s_st[0], 4 * 64 + START)
                act.wait_ge(s_st[1], 4 * 64 + START)

            @block.tensor
            def _(pe):
                pe.wait_ge(s_const, 80)
                pe.wait_ge(s_zero, 1)
                with pe.Fori(0, 4) as j:
                    for u in range(2):
                        t = j * 2 + u
                        for g in range(3):
                            pe.wait_ge(s_rot, t * 3 + (g + 1 + START))
                            pe.wait_ge(s_qke, t * 3 + (g + START))
                            for i in range(4):
                                last = nc.tensor.transpose(p_qk[:, i, :], rot[:, u, g, i // 2, (i % 2) * 128:(i % 2 + 1) * 128],
                                                           ident[:, :])
                            last.then_inc(s_qkt, 1)
                        for g in range(3):
                            wide = g == 0 or (g == 1 and u == 1)
                            pe.wait_ge(s_qke, t * 3 + (g + 1 + START))
                            pe.wait_ge(s_sce, t * 3 + (g + START))
                            for hp in range(2):
                                for h in range(2):
                                    q = qT[64 * h:64 * h + 64, g, hp, :]
                                    k = (kT[64 * h:64 * h + 64, g, hp, :, :].rearrange("p a b -> p (a b)") if wide
                                         else kT[64 * h:64 * h + 64, g, hp, u, :])
                                    last = nc.tensor.matmul(p_s[h][:, hp, 0:256 if wide else 128], q, k, start=True, stop=True)
                            last.then_inc(s_sc, 1)
                        for g in range(3):
                            wide = g == 0 or (g == 1 and u == 1)
                            n = 8 if wide else 4
                            pe.wait_ge(s_p, t * 3 + (g + 1 + START))
                            for i in range(n // 4):
                                k = (0, 2, 3 if u == 0 else 4)[g] + i
                                first = u == 0 and k == 0
                                pe.wait_ge(s_pte, j * 9 + ((0, 4)[u] + k + 1 + first))
                                for c in range(4):
                                    h, w = (2 * i + c // 2, c % 2) if wide else (c, 0)
                                    last = nc.tensor.transpose(p_t[((0, 4)[u] + k) % 2][:, c, :],
                                                               P[:, g, h, w * 128:(w + 1) * 128], ident[:, :])
                                last.then_inc(s_pt, 1)
                            pe.wait_ge(s_pte, j * 9 + ((0, 4)[u] + (0, 2, 3 if u == 0 else 4)[g] + n // 4 + 2))
                            pe.wait_ge(s_oe, t * 3 + (g + START))
                            pe.wait_ge(s_v[u][g], (j + 1) * (16 if g < 2 else 32))
                            slots = (u,) if not wide else ((0, 1))
                            for h in range(HG):
                                for w, slot in enumerate(slots):
                                    last = nc.tensor.matmul(p_o[:, g, h * HD:(h + 1) * HD], PT[:, g, h, w, :],
                                                            v[:, slot, g, h * HD:(h + 1) * HD],
                                                            start=(w == 0), stop=(w == len(slots) - 1))
                            last.then_inc(s_o, 1)
                        pe.drain()
                        pe.sem_inc(s_free, 1)


def phase_attention_sample(nc, T, sem):
    with ExitStack() as ctx:
        def sb(name, shape, dt=f32):
            return ctx.enter_context(nc.sbuf_tensor(name, shape, dt))

        def pb(name, shape):
            return ctx.enter_context(nc.psum_tensor(name, shape, f32))

        CT = 9
        GT = [(0, 1), (1, 5), (5, 9)]
        ident = sb("d_ident", [128, 128])
        rotary = sb("d_rotary", [128, 2 * HD])
        m_old, m_new = sb("mask_cached", [128, 3, 128]), sb("mask_new", [128, 2, 3, 128])
        new = sb("d_new", [128, 3 * AW])
        rot = sb("d_rot", [128, 2 * AW])
        tmp = sb("d_tmp", [128, 2, 2 * AW // HD, HD])
        kv = sb("d_kv", [128, 3, 2, GW])
        qbd = sb("d_qbd", [128, 3, 2, NB, 2, NT])
        kTn = sb("d_kTn", [128, 3, 2, 128])
        kc = sb("d_kc", [128, 2, CT, GW])
        kT = sb("d_kT", [128, 2, 2 * CT, 128])
        vc = sb("d_vc", [128, NB, CT, GW])
        sT = sb("d_sT", [128, 6, NB * HG * NT])
        S = sb("d_S", [128, 2, 6, 128])
        mx, den = sb("d_mx", [128, 2]), sb("d_den", [128, 2])
        p_st = pb("d_pst", [128, 6, 256])
        p_kt = [pb(f"d_pkt{i}", [128, 3, 128]) for i in range(2)]
        p_r = pb("d_pr", [128, 8, 128])
        p_o = pb("d_po", [128, NB, 2, 2, NT])
        s_const, s_new, s_rot, s_qkt, s_qbd, s_zero = (sem(f"d_{n}") for n in ("const", "new", "rot", "qkt", "qbd", "zero"))
        s_k = [sem(f"d_k{u}") for u in range(2)]
        s_v, s_kfree, s_kt, s_kte, s_st, s_ste = (sem(f"d_{n}") for n in ("v", "kfree", "kt", "kte", "st", "ste"))
        s_r, s_rm, s_p, s_pn, s_pt, s_pte, s_o, s_done, s_kv = (
            sem(f"d_{n}") for n in ("r", "rm", "p", "pn", "pt", "pte", "o", "done", "kv"))
        SC = HD ** -0.5
        G = 6

        def cache_parts(b, a):
            c = [T["cache"][g][0, b, :, a, :, :].rearrange("r h d -> r (h d)") if isinstance(b, int) else
                 T["cache"][g][0, ds(b, 1), :, a, :, :].rearrange("o r h d -> (o r) (h d)") for g in range(3)]
            parts = [((0, 128), (0, 1), c[0].rearrange("(p r) c -> p r c", r=1)),
                     ((0, 128), (1, 5), c[1].rearrange("(p r) c -> p r c", r=4))]
            c2 = c[2].rearrange("(p u a) c -> a p u c", u=8, a=2)
            return parts + [((64 * x, 64 * x + 64), (5, 9), c2[x][:, 0:4, :]) for x in range(2)]

        with nc.Block() as block:
            @block.sync
            def _(sp):
                sp.dma_start(new[:, :], T["u_tm"][SEQ:TOK, 0:3 * AW]).then_inc(s_new, 16)
                for dst, src in ((ident[:, :], T["ident"]), (rotary[:, :], T["rotary_new"]), (m_old[:, :, :], T["mask_cached"]),
                                 (m_new[:, :, :, :], T["mask_new"])):
                    sp.dma_start(dst, src).then_inc(s_const, 16)
                with sp.Fori(0, NB // 2) as j:
                    for u in range(2):
                        b = j * 2 + u
                        sp.wait_ge(s_kfree, j * 2 + (u + 1))
                        for (p0, p1), (c0, c1), src in cache_parts(b, 0):
                            sp.dma_start(kc[p0:p1, u, c0:c1, :], src).then_inc(s_k[u], 16)

            @block.gpsimd
            def _(pool):
                nc.gpsimd.memset(qbd[:, :, :, :, :, :].rearrange("p a b c d e -> p (a b c d e)"), 0.0)
                nc.gpsimd.memset(T["ya_T"][:, :, SEQ + SAMP:], 0.0).then_inc(s_zero, 1)

            @block.vector
            def _(dve):
                dve.sem_inc(s_kfree, 2)
                dve.wait_ge(s_const, 64)
                dve.wait_ge(s_new, 16)
                x = new[:, 0:2 * AW].rearrange("p (h c) -> p h c", c=HD)
                n, half = 2 * AW // HD, HD // 2
                for a, b in ((0, half), (half, 0)):
                    nc.vector.tensor_tensor(tmp[:, 0, :, a:a + half], x[:, :, b:b + half],
                                            bc(rotary[:, HD + a:HD + a + half].unsqueeze(1), [128, n, half]), ALU.mult)
                nc.vector.tensor_tensor(tmp[:, 1, :, :], x, bc(rotary[:, 0:HD].unsqueeze(1), [128, n, HD]), ALU.mult)
                dve.drain()
                nc.vector.tensor_tensor(rot[:, :].rearrange("p (h c) -> p h c", c=HD), tmp[:, 0, :, :], tmp[:, 1, :, :], ALU.add)
                dve.drain()
                dve.sem_inc(s_rot, 1)
                nc.vector.tensor_copy(kv[:, :, 0, :], rot[:, AW:].rearrange("p (g c) -> p g c", g=3))
                nc.vector.tensor_copy(kv[:, :, 1, :], new[:, 2 * AW:].rearrange("p (g c) -> p g c", g=3))
                dve.drain()
                dve.sem_inc(s_rot, 1)
                dve.wait_ge(s_zero, 1)
                dve.wait_ge(s_qkt, 1)
                pv = p_st[:, :, :].rearrange("p a (b c) -> p (a b) c", c=128)
                for g in range(3):
                    for hh in range(2):
                        r = slice(64 * hh, 64 * hh + 64)
                        for hp in range(2):
                            nc.vector.tensor_copy(qbd[r, g, hp, :, hh, :],
                                                  pv[r, 2 * g + hp, 0:SAMP].rearrange("p (b t) -> p b t", t=NT))
                nc.vector.tensor_copy(kTn[:, :, :, :].rearrange("p a b c -> p (a b) c"), pv[:, 6:12, :])
                dve.drain()
                dve.sem_inc(s_qbd, 1)
                dve.wait_ge(s_st, 1)
                nc.vector.tensor_copy(sT[:, :, :], p_st[:, :, :])
                dve.drain()
                dve.sem_inc(s_ste, 1)
                for half in range(2):
                    dve.wait_ge(s_r, half + 1)
                    nc.vector.tensor_tensor(S[:, half, 0:3, :], p_r[:, 0:3, :], m_old[:, :, :], ALU.add)
                    nc.vector.tensor_tensor(S[:, half, 3:6, :], p_r[:, 3:6, :], m_new[:, half, :, :], ALU.add)
                    dve.drain()
                    dve.sem_inc(s_rm, 1)
                    nc.vector.tensor_reduce(mx[:, half:half + 1], S[:, half, :, :].rearrange("p a k -> p (a k)"), AX.X, ALU.max)
                    dve.drain()
                    nc.vector.tensor_scalar(mx[:, half:half + 1], mx[:, half:half + 1], -SC, None, ALU.mult)
                    dve.drain()
                    dve.sem_inc(s_pn, 1)
                for half in range(2):
                    dve.wait_ge(s_p, half + 1)
                    nc.vector.reciprocal(den[:, half:half + 1], den[:, half:half + 1])
                    dve.drain()
                    nc.vector.tensor_scalar(S[:, half, :, :], S[:, half, :, :], den[:, half:half + 1], None, ALU.mult
                                            ).then_inc(s_pn, 1)
                dve.wait_ge(s_pt, 1)
                nc.vector.tensor_copy(sT[:, :, :], p_st[:, :, :])
                dve.drain()
                dve.sem_inc(s_pte, 1)
                dve.wait_ge(s_o, 1)
                for hh in range(2):
                    r = slice(64 * hh, 64 * hh + 64)
                    for hp in range(2):
                        nc.vector.tensor_copy(T["ya_T"][r, hp, SEQ:SEQ + SAMP].rearrange("p (b t) -> p b t", t=NT),
                                              p_o[r, :, hp, hh, :])
                dve.drain()
                dve.sem_inc(s_done, 1)

            @block.scalar
            def _(act):
                for b in range(NB):
                    for (p0, p1), (c0, c1), src in cache_parts(b, 1):
                        act.dma_start(vc[p0:p1, b, c0:c1, :], src).then_inc(s_v, 16)
                act.wait_ge(s_rot, 2)
                for g, (window, dil) in enumerate(GROUPS):
                    end = min(window, PAST + NT)
                    for b in range(NB):
                        act.dma_start(T["s_kv"][g][0, b, end - NT:end, :, :, :].rearrange("r a h d -> r a (h d)"),
                                      kv[b * NT:(b + 1) * NT, g, :, :]).then_inc(s_kv, 16)
                act.sem_inc(s_kte, 2)
                with act.Fori(0, NB // 2) as j:
                    for u in range(2):
                        for q in range(G):
                            n = u * G + q
                            act.wait_ge(s_kt, j * (2 * G) + (n + 1))
                            nc.scalar.copy(kT[:, u, 3 * q:3 * q + 3, :], p_kt[q % 2][:, :, :]).then_inc(s_kte, 1)
                for half in range(2):
                    act.wait_ge(s_pn, half + 1)
                    flat = S[:, half, :, :].rearrange("p a k -> p (a k)")
                    nc.scalar.activation(flat, flat, ACT.Exp, bias=mx[:, half:half + 1], scale=SC,
                                         accum_out=den[:, half:half + 1])
                    act.drain()
                    act.sem_inc(s_p, 1)
                act.wait_ge(s_kv, 16 * 3 * NB)
                act.wait_ge(T["s_cache"], 16 * 3 * NB)
                act.wait_ge(s_done, 1)

            @block.tensor
            def _(pe):
                pe.wait_ge(s_const, 64)
                pe.wait_ge(s_rot, 1)
                pv = p_st[:, :, :].rearrange("p a (b c) -> p (a b) c", c=128)
                for i in range(12):
                    last = nc.tensor.transpose(pv[:, i, :], rot[:, i * 128:(i + 1) * 128], ident[:, :])
                last.then_inc(s_qkt, 1)
                pe.wait_ge(s_qbd, 1)
                for g in range(3):
                    for hp in range(2):
                        out = p_st[:, 3 + g, :].rearrange("p (b h t) -> p b h t", h=HG, t=NT)[:, :, 2 * hp:2 * hp + 2, :]
                        nc.tensor.matmul(out, kTn[:, g, hp, :], qbd[:, g, hp, :, :, :], start=True, stop=True)
                with pe.Fori(0, NB // 2) as j:
                    for u in range(2):
                        b = j * 2 + u
                        pe.wait_ge(s_k[u], (j + 1) * 64)
                        for q in range(G):
                            pe.wait_ge(s_kte, j * (2 * G) + (u * G + q + 1))
                            for i in range(3 * q, 3 * q + 3):
                                last = nc.tensor.transpose(p_kt[q % 2][:, i % 3, :],
                                                           kc[:, u, i // 2, (i % 2) * 128:(i % 2 + 1) * 128], ident[:, :])
                            last.then_inc(s_kt, 1)
                        pe.drain()
                        pe.sem_inc(s_kfree, 1)
                        pe.wait_ge(s_kte, j * (2 * G) + ((u + 1) * G + 2))
                        for g, (c0, c1) in enumerate(GT):
                            for c in range(c0, c1):
                                for hp in range(2):
                                    t = (slice(0, NT), slice(c - c0, NT, 4), slice(2 * (c - c0), 2 * (c - c0) + 2))[g]
                                    out = p_st[:, g, ds(b * (HG * NT) + hp * 2 * NT, 2 * NT)].rearrange(
                                        "p (h t) -> p h t", t=NT)[:, :, t]
                                    q = qbd[:, g, hp, ds(b, 1), :, :].rearrange("p o h t -> p (o h) t")[:, :, t]
                                    last = nc.tensor.matmul(out, kT[:, u, 2 * c + hp, :], q, start=True, stop=True)
                pe.drain()
                pe.sem_inc(s_st, 1)
                pe.wait_ge(s_ste, 1)
                for half in range(2):
                    if half:
                        pe.wait_ge(s_rm, half)
                    for i in range(6):
                        last = nc.tensor.transpose(p_r[:, i, :], sT[:, i, half * 128:(half + 1) * 128], ident[:, :])
                    last.then_inc(s_r, 1)
                pe.wait_ge(s_pn, 4)
                for half in range(2):
                    for i in range(6):
                        last = nc.tensor.transpose(p_st[:, i, half * 128:(half + 1) * 128], S[:, half, i, :], ident[:, :])
                last.then_inc(s_pt, 1)
                pe.wait_ge(s_pte, 1)
                pe.wait_ge(s_v, 16 * 4 * NB)
                for b in range(NB):
                    for hp in range(2):
                        cols = slice(b * HG * NT + hp * 2 * NT, b * HG * NT + (hp + 1) * 2 * NT)
                        ch = slice(hp * 128, (hp + 1) * 128)
                        work = [(p_o[:, b, hp, :, :], vc[:, b, 0, ch], sT[:, 0, cols])]
                        for g in (1, 2):
                            for c in range(4):
                                t = slice(c, NT, 4) if g == 1 else slice(2 * c, 2 * c + 2)
                                work.append((p_o[:, b, hp, :, t], vc[:, b, GT[g][0] + c, ch],
                                             sT[:, g, cols].rearrange("p (h t) -> p h t", t=NT)[:, :, t]))
                        for g in range(3):
                            c0 = 2 * AW + g * GW + hp * 128
                            work.append((p_o[:, b, hp, :, :], new[:, c0:c0 + 128], sT[:, 3 + g, cols]))
                        for i, (out, v, p) in enumerate(work):
                            last = nc.tensor.matmul(out, v, p, start=(i == 0), stop=(i == len(work) - 1),
                                                    skip_group_check=True)
                last.then_inc(s_o, 1)


def phase_ssd(nc, T, sem, sample):
    tag = "f" if sample else "e"
    with ExitStack() as ctx:
        def sb(name, shape, dt=f32):
            return ctx.enter_context(nc.sbuf_tensor(f"{tag}_{name}", shape, dt))

        def pb(name, shape):
            return ctx.enter_context(nc.psum_tensor(f"{tag}_{name}", shape, f32))

        def sm(name):
            return sem(f"{tag}_{name}")

        GH = SH // 2
        pairs = SH // 2
        ident, ident_b = sb("ident", [128, 128]), sb("ident_b", [128, 128], bf16)
        upto, whole = sb("upto", [128, 128]), sb("whole", [128, 128])
        future, future_b = sb("future", [128, 128]), sb("future_b", [128, 128], bf16)
        d_skip = sb("d_skip", [128, SH])
        xb = sb("xb", [128, 2, DI + 2 * SN])
        bct = sb("bct", [128, 2, 4, 128])
        da = sb("da", [128, SH])
        nacs, wexp = sb("nacs", [128, SH]), sb("wexp", [128, SH])
        eacs, wend, cdec = sb("eacs", [128, SH]), sb("wend", [128, SH]), sb("cdec", [128, SH])
        E, M = sb("E", [128, 4, 4, 128]), sb("M", [128, 4, 4, 128])
        xdt, xw, xd = sb("xdt", [128, DI]), sb("xw", [128, DI]), sb("xd", [128, DI])
        y = sb("y", [128, 2, DI])
        p_misc = pb("p_misc", [128, 512])
        p_al = [pb(f"p_al{i}", [128, 4, 128]) for i in range(2)]
        p_yd, p_yo = pb("p_yd", [128, 2, 512]), pb("p_yo", [128, 2, 512])
        p_st = pb("p_st", [128, 512])
        if sample:
            seq_of, seq_cols = sb("seq_of", [128, NB]), sb("seq_cols", [128, NB, 128])
            dax = sb("dax", [128, DI])
            Bm, Cm = sb("Bm", [128, 2, NB, 128]), sb("Cm", [128, 2, NB, 128])
            h0 = sb("h0", [128, pairs, NB, SN])
            h0T = sb("h0T", [128, NB, DI])
            dec = sb("dec", [128, pairs, NB])
        else:
            hT = sb("hT", [128, DI])
            hout = sb("hout", [128, pairs, SN])
        consts = [(ident, "ident"), (upto, "upto_seq" if sample else "upto"), (future, "future_seq" if sample else "future"),
                  (d_skip, "d_skip")]
        if sample:
            consts += [(whole, "same_seq"), (seq_of, "seq_of"), (seq_cols, "seq_cols")]
        s_const, s_prep = sm("const"), sm("prep")
        s_in = [sm(f"in{u}") for u in range(2)]
        s_free, s_da, s_misc, s_nacs, s_e, s_al, s_E, s_M = (sm(n) for n in ("free", "da", "misc", "nacs", "e", "al", "E", "M"))
        s_x, s_xd, s_pe, s_st, s_ste, s_h = (sm(n) for n in ("x", "xd", "pe", "st", "ste", "h"))
        s_y, s_ho, s_hp, s_mc, s_yfree = sm("y"), sm("ho"), sm("hp"), sm("mc"), sm("yfree")
        s_out = [sm(f"out{u}") for u in range(2)]
        s_h0, s_tr, s_tre = sm("h0"), sm("tr"), sm("tre")
        for s in (s_y, *s_out, s_M, s_ste):
            nc.sync.sem_inc(s, START)
        y3 = lambda ap: ap.rearrange("p (h c) -> p h c", c=HD)

        def heads(ap):
            return bc(ap.unsqueeze(2), [128, SH, HD])

        def chunks(eng, body):
            if sample:
                body(0, 0, 0)
            else:
                with eng.Fori(0, SEQ // 128 // 2) as j:
                    for u in range(2):
                        body(j * 2 + u, u, j)

        def rows(n):
            return slice(SEQ, TOK) if sample else ds(n * 128, 128)

        tile_of = (lambda n: slice(TILES - 1, TILES)) if sample else (lambda n: ds(n, 1))
        NQ = 4

        with nc.Block() as block:
            @block.sync
            def _(sp):
                for dst, name in consts:
                    nd = len(dst.shape)
                    sp.dma_start(dst[:, :] if nd == 2 else dst[:, :, :], T[name]).then_inc(s_const, 16)

                def load(n, u, j):
                    sp.wait_ge(s_free, n + 1)
                    sp.dma_start(xb[:, u, :], T["xc_tm"][rows(n), 0:DI + 2 * SN]).then_inc(s_in[u], 16)
                    sp.dma_start(bct[:, u, :, :], T["xc_cm"][DI:XBC, rows(n)].rearrange("(a p) t -> p a t", p=128)
                                 ).then_inc(s_in[u], 16)
                chunks(sp, load)

            @block.gpsimd
            def _(pool):
                if not sample:
                    nc.gpsimd.memset(whole[:, :], 1.0)
                    nc.gpsimd.memset(hT[:, :], 0.0)
                pool.wait_ge(s_const, 16 * len(consts))
                nc.gpsimd.tensor_copy(ident_b[:, :], ident[:, :])
                nc.gpsimd.tensor_copy(future_b[:, :], future[:, :]).then_inc(s_prep, 1)

                def skip(n, u, j):
                    pool.wait_ge(s_in[u], (j + 1) * 32)
                    pool.wait_ge(s_y, n + START)
                    nc.gpsimd.tensor_tensor(y3(xd[:, :]), y3(xb[:, u, 0:DI]), heads(d_skip[:, :]), ALU.mult).then_inc(s_xd, 1)
                chunks(pool, skip)

            @block.vector
            def _(dve):
                dve.sem_inc(s_free, 2)
                dve.wait_ge(s_const, 16 * len(consts))
                dve.wait_ge(s_prep, 1)

                def work(n, u, j):
                    dt = T["dt_tm"][:, tile_of(n), :].rearrange("p a h -> p (a h)")
                    nc.vector.tensor_copy(da[:, :], T["da_tm"][:, tile_of(n), :].rearrange("p a h -> p (a h)")).then_inc(s_da, 1)
                    dve.wait_ge(s_in[u], (j + 1) * 32)
                    nc.vector.tensor_tensor(y3(xdt[:, :]), y3(xb[:, u, 0:DI]), heads(dt), ALU.mult)
                    if sample:
                        nc.vector.tensor_copy(y3(dax[:, :]), heads(T["da_tm"][:, TILES - 1, :]))
                        for g in range(2):
                            nc.vector.tensor_tensor(Cm[:, g, :, :], bc(bct[:, u, 2 + g, :].unsqueeze(1), [128, NB, 128]),
                                                    seq_cols[:, :, :], ALU.mult)
                            nc.vector.tensor_tensor(Bm[:, g, :, :],
                                                    bc(xb[:, u, DI + g * SN:DI + (g + 1) * SN].unsqueeze(1), [128, NB, 128]),
                                                    bc(seq_of[:, :].unsqueeze(2), [128, NB, 128]), ALU.mult)
                        dve.drain()
                        dve.sem_inc(s_mc, 1)
                    dve.wait_ge(s_misc, n + 1)
                    nc.vector.tensor_scalar(nacs[:, :], p_misc[:, 0:SH], -1.0, None, ALU.mult)
                    dve.drain()
                    nc.vector.tensor_tensor(wexp[:, :], p_misc[:, SH:2 * SH], nacs[:, :], ALU.add)
                    dve.drain()
                    dve.sem_inc(s_nacs, 1)
                    dve.wait_ge(s_e, n + 1)
                    nc.vector.tensor_tensor(y3(xw[:, :]), y3(xdt[:, :]), heads(wend[:, :]), ALU.mult)
                    dve.drain()
                    dve.sem_inc(s_x, 1)
                    for q in range(NQ):
                        dve.wait_ge(s_E, n * NQ + (q + 1))
                        cb = p_misc[:, 128 * (1 + q // 2):128 * (2 + q // 2)]
                        nc.vector.tensor_tensor(M[:, q, :, :], E[:, q, :, :], bc(cb.unsqueeze(1), [128, 4, 128]), ALU.mult
                                                ).then_inc(s_M, 1)
                    if not sample:
                        dve.wait_ge(s_st, n * 2 + 1)
                        for g in range(2):
                            cols = slice(g * 512, (g + 1) * 512)
                            hv = hT[:, cols].rearrange("p (h c) -> p h c", c=HD)
                            nc.vector.tensor_tensor(hv, hv, bc(cdec[:, g * GH:(g + 1) * GH].unsqueeze(2), [128, GH, HD]), ALU.mult)
                            dve.drain()
                            dve.wait_ge(s_st, n * 2 + (g + 1))
                            nc.vector.tensor_tensor(hT[:, cols], hT[:, cols], p_st[:, :], ALU.add)
                            dve.drain()
                            dve.sem_inc(s_ste, 1)
                    dve.wait_ge(s_pe, n + 1)
                    dve.wait_ge(s_out[u], j * 16 + START)
                    yv = y[:, u, :]
                    nc.vector.tensor_tensor(y3(yv), p_yo[:, :, :].rearrange("p a (h c) -> p (a h) c", c=HD), heads(eacs[:, :]), ALU.mult)
                    dve.drain()
                    nc.vector.tensor_tensor(yv, yv, p_yd[:, :, :].rearrange("p a c -> p (a c)"), ALU.add)
                    dve.drain()
                    dve.wait_ge(s_xd, n + 1)
                    nc.vector.tensor_tensor(yv, yv, xd[:, :], ALU.add)
                    dve.drain()
                    dve.sem_inc(s_y, 1)
                    dve.sem_inc(s_free, 1)
                if sample:
                    dve.wait_ge(s_h0, 16 * NB)
                chunks(dve, work)
                if sample:
                    dve.wait_ge(s_hp, 1)
                    for i in range(2 * pairs):
                        p, half = i // 2, i % 2
                        bs = slice(4 * half, 4 * half + 4)
                        hv = h0[:, p, bs, :]
                        nc.vector.tensor_tensor(hv, hv, bc(dec[:, p, bs].unsqueeze(2), [128, 4, SN]), ALU.mult)
                        dve.drain()
                        dve.wait_ge(s_st, i + 1)
                        nc.vector.tensor_tensor(hv, hv, p_al[i % 2][:, :, :], ALU.add)
                        dve.drain()
                        dve.sem_inc(s_ste, 1)
                    dve.sem_inc(s_ho, 1)
                else:
                    dve.wait_ge(s_hp, 1)
                    for i in range(2):
                        nc.vector.tensor_copy(hout[:, 4 * i:4 * i + 4, :], p_al[i][:, :, :])
                    dve.drain()
                    dve.sem_inc(s_ho, 1)

            @block.scalar
            def _(act):
                if sample:
                    for b in range(NB):
                        act.dma_start(h0[:, :, b, :], T["state_ssm"][0, b].rearrange("(j a) c n -> (a c) j n", a=2)
                                      ).then_inc(s_h0, 16)
                    act.wait_ge(s_h0, 16 * NB)
                    for i in range(NB * 2):
                        act.wait_ge(s_tr, i + 1)
                        b, half = i // 2, i % 2
                        nc.scalar.copy(h0T[:, b, half * 512:(half + 1) * 512], p_al[i % 2][:, :, :].rearrange("p a c -> p (a c)")
                                       ).then_inc(s_tre, 1)

                def work(n, u, j):
                    act.wait_ge(s_nacs, n + 1)
                    nc.scalar.activation(eacs[:, :], p_misc[:, 0:SH], ACT.Exp)
                    nc.scalar.activation(wend[:, :], wexp[:, :], ACT.Exp)
                    nc.scalar.activation(cdec[:, :], p_misc[:, SH:2 * SH], ACT.Exp)
                    act.drain()
                    act.sem_inc(s_e, 1)
                    for q in range(NQ):
                        act.wait_ge(s_al, n * NQ + (q + 1))
                        if q == 0:
                            act.wait_ge(s_M, n * NQ + START)
                        for i in range(4):
                            last = nc.scalar.activation(E[:, q, i, :], p_al[q % 2][:, i, :], ACT.Exp,
                                                        bias=nacs[:, 4 * q + i:4 * q + i + 1])
                        last.then_inc(s_E, 1)
                    act.wait_ge(s_y, n + (1 + START))
                    act.dma_start(T["y_ssd"][rows(n), :], y[:, u, :]).then_inc(s_out[u], 16)
                chunks(act, work)
                if sample:
                    act.wait_ge(s_mc, 2)
                    nc.scalar.activation(dec[:, :, :].rearrange("p a b -> p (a b)"), p_misc[:, 384:384 + pairs * NB], ACT.Exp)
                    act.drain()
                    act.sem_inc(s_hp, 1)
                    act.wait_ge(s_ho, 1)
                    for b in range(NB):
                        act.dma_start(T["s_ssm"][0, b].rearrange("(j a) c n -> (a c) j n", a=2), h0[:, :, b, :]
                                      ).then_inc(s_out[1], 16)
                    act.wait_ge(s_out[0], START + 16)
                    act.wait_ge(s_out[1], 16 * NB + START)
                else:
                    act.wait_ge(s_ho, 1)
                    act.dma_start(T["p_ssm"][0, 0].rearrange("(j a) c n -> (a c) j n", a=2), hout[:, :, :]).then_inc(s_out[0], 16)
                    act.wait_ge(s_out[0], 16 * 5 + START)
                    act.wait_ge(s_out[1], 16 * 4 + START)

            @block.tensor
            def _(pe):
                pe.wait_ge(s_const, 16 * len(consts))
                pe.wait_ge(s_prep, 1)
                if sample:
                    pe.wait_ge(s_h0, 16 * NB)
                    for i in range(NB * 2):
                        b, half = i // 2, i % 2
                        if i >= 2:
                            pe.wait_ge(s_tre, i - 1)
                        for k in range(4):
                            last = nc.tensor.transpose(p_al[i % 2][:, k, :], h0[:, half * 4 + k, b, :], ident[:, :])
                        last.then_inc(s_tr, 1)
                    pe.wait_ge(s_tre, NB * 2)

                def work(n, u, j):
                    pe.wait_ge(s_in[u], (j + 1) * 32)
                    pe.wait_ge(s_da, n + 1)
                    pe.wait_ge(s_M, n * NQ + START)
                    nc.tensor.matmul(p_misc[:, 0:SH], upto[:, :], da[:, :], start=True, stop=True)
                    nc.tensor.matmul(p_misc[:, SH:2 * SH], whole[:, :], da[:, :], start=True, stop=True)
                    for g in range(2):
                        last = nc.tensor.matmul(p_misc[:, 128 * (1 + g):128 * (2 + g)], bct[:, u, g, :], bct[:, u, 2 + g, :],
                                                start=True, stop=True)
                    last.then_inc(s_misc, 1)
                    for q in range(NQ):
                        if q >= 2:
                            pe.wait_ge(s_E, n * NQ + (q - 1))
                        for i in range(4):
                            h = 4 * q + i
                            nc.tensor.matmul(p_al[q % 2][:, i, :], ident_b[:, :], future_b[:, :], start=True, stop=False)
                            last = nc.tensor.matmul(p_al[q % 2][:, i, :], bc(da[:, h:h + 1], [128, 128]), upto[:, :],
                                                    start=False, stop=True)
                        last.then_inc(s_al, 1)
                    pe.wait_ge(s_y, n + START)
                    if sample:
                        pe.wait_ge(s_mc, 1)
                        for g in range(2):
                            for b in range(NB):
                                nc.tensor.matmul(p_yo[:, g, :], Cm[:, g, b, :], h0T[:, b, g * 512:(g + 1) * 512],
                                                 start=(b == 0), stop=(b == NB - 1))
                    else:
                        pe.wait_ge(s_ste, n * 2 + START)
                        for g in range(2):
                            nc.tensor.matmul(p_yo[:, g, :], bct[:, u, 2 + g, :], hT[:, g * 512:(g + 1) * 512], start=True, stop=True)
                        pe.drain()
                        pe.wait_ge(s_x, n + 1)
                        for g in range(2):
                            pe.wait_ge(s_ste, n * 2 + (g + START))
                            nc.tensor.matmul(p_st[:, :], xb[:, u, DI + g * SN:DI + (g + 1) * SN], xw[:, g * 512:(g + 1) * 512],
                                             start=True, stop=True).then_inc(s_st, 1)
                    for h in range(SH):
                        if h % 4 == 0:
                            pe.wait_ge(s_M, n * NQ + (h // 4 + 1 + START))
                        last = nc.tensor.matmul(p_yd[:, h // GH, (h % GH) * HD:(h % GH + 1) * HD], M[:, h // 4, h % 4, :],
                                                xdt[:, h * HD:(h + 1) * HD], start=True, stop=True)
                    last.then_inc(s_pe, 1)
                chunks(pe, work)
                if sample:
                    pe.wait_ge(s_y, START + 1)
                    for p in range(pairs):
                        last = nc.tensor.matmul(p_misc[:, 384 + p * NB:384 + (p + 1) * NB], dax[:, p * 128:(p + 1) * 128],
                                                seq_of[:, :], start=True, stop=True)
                    last.then_inc(s_mc, 1)
                    pe.wait_ge(s_x, 1)
                    pe.wait_ge(s_E, NQ)
                    for i in range(2 * pairs):
                        p, half = i // 2, i % 2
                        if i >= 2:
                            pe.wait_ge(s_ste, i - 1 + START)
                        nc.tensor.matmul(p_al[i % 2][:, :, :], xw[:, p * 128:(p + 1) * 128], Bm[:, p // 4, 4 * half:4 * half + 4, :],
                                         start=True, stop=True).then_inc(s_st, 1)
                else:
                    pe.wait_ge(s_ste, 2 * (SEQ // 128) + START)
                    pe.wait_ge(s_E, NQ * (SEQ // 128))
                    for i in range(pairs):
                        last = nc.tensor.transpose(p_al[i // 4][:, i % 4, :], hT[:, i * 128:(i + 1) * 128], ident[:, :])
                    last.then_inc(s_hp, 1)


def phase_ssd_prompt(nc, T, sem):
    phase_ssd(nc, T, sem, False)


def phase_ssd_sample(nc, T, sem):
    phase_ssd(nc, T, sem, True)


def rows3(j, u):
    return ds((j * 3 + u) * 128, 128)


def phase_branch_inputs(nc, T, sem):
    with ExitStack() as ctx:
        def sb(name, shape, dt=f32):
            return ctx.enter_context(nc.sbuf_tensor(f"g_{name}", shape, dt))

        def sm(name):
            return sem(f"g_{name}")

        ident, nw, eps = sb("ident", [128, 128]), sb("nw", [128, KT]), sb("eps", [128, 1])
        yin, z, junk = sb("yin", [128, 3, DI]), sb("z", [128, 3, DI]), sb("junk", [128, 512])
        ms = sb("ms", [128, 3, 2])
        o = sb("o", [128, 2, 3, GW + 2 * HG])
        wt, top, ysum = sb("wt", [128, 3, HG]), sb("top", [128, HG]), sb("ysum", [128, 2, 3, GW])
        p_t = ctx.enter_context(nc.psum_tensor("g_pt", [128, 3, KT, 128], f32))
        p_a = ctx.enter_context(nc.psum_tensor("g_pa", [128, 2, 2, 128], f32))
        s_const, s_eps = sm("const"), sm("eps")
        s_in, s_o = [sm(f"in{u}") for u in range(3)], [sm(f"o{u}") for u in range(2)]
        s_free, s_silu, s_g, s_rms, s_n, s_t, s_ofree, s_top, s_w, s_ys, s_ta = (
            sm(n) for n in ("free", "silu", "gg", "rms", "n", "t", "ofree", "top", "w", "ys", "ta"))
        with nc.Block() as block:
            @block.sync
            def _(sp):
                sp.dma_start(ident[:, :], T["ident"]).then_inc(s_const, 16)
                sp.dma_start(nw[:, :], T["ssd_norm_w"].rearrange("p a k -> p (a k)")).then_inc(s_const, 16)
                with sp.Fori(0, 3) as j:
                    for u in range(3):
                        sp.wait_ge(s_free, j * 3 + (u + 1))
                        sp.dma_start(yin[:, u, :], T["y_ssd"][rows3(j, u), :]).then_inc(s_in[u], 16)
                        sp.dma_start(z[:, u, :], T["u_tm"][rows3(j, u), ZOFF:XOFF]).then_inc(s_in[u], 16)
                with sp.Fori(0, 4) as j:
                    for u in range(2):
                        sp.wait_ge(s_ofree, j * 2 + (u + 1))
                        sp.dma_start(o[:, u, :, :], T["o_attn"][:, ds((j * 2 + u) * 128, 128), :].rearrange("g r c -> r g c")
                                     ).then_inc(s_o[u], 16)

            @block.vector
            def _(dve):
                nc.vector.memset(eps[:, :], EPS).then_inc(s_eps, 1)
                dve.sem_inc(s_ofree, 2)
                dve.wait_ge(s_const, 32)
                with dve.Fori(0, 3) as j:
                    for u in range(3):
                        n = j * 3 + u
                        dve.wait_ge(s_silu, n + 1)
                        nc.vector.tensor_tensor(yin[:, u, :], yin[:, u, :], z[:, u, :], ALU.mult).then_inc(s_g, 1)
                        dve.wait_ge(s_rms, n + 1)
                        nc.vector.reciprocal(ms[:, u, :], ms[:, u, :])
                        dve.drain()
                        for g in range(2):
                            cols = slice(512 * g, 512 * g + 512)
                            last = nc.vector.tensor_scalar(z[:, u, cols], yin[:, u, cols], ms[:, u, g:g + 1], None, ALU.mult)
                        last.then_inc(s_n, 1)
                        dve.wait_ge(s_t, n + 1)
                        for half in range(2):
                            k0 = 4 * half
                            nc.vector.tensor_tensor(T["ys_T"][:, k0:k0 + 4, ds(n * 128, 128)], p_t[:, u, k0:k0 + 4, :],
                                                    bc(nw[:, k0:k0 + 4].unsqueeze(2), [128, 4, 128]), ALU.mult)
                with dve.Fori(0, 4) as j:
                    for u in range(2):
                        n = j * 2 + u
                        dve.wait_ge(s_o[u], (j + 1) * 16)
                        mx = [o[:, u, g, GW:GW + HG] for g in range(3)]
                        nc.vector.tensor_tensor(top[:, :], mx[0], mx[1], ALU.max)
                        dve.drain()
                        nc.vector.tensor_tensor(top[:, :], top[:, :], mx[2], ALU.max)
                        dve.drain()
                        nc.vector.tensor_tensor(wt[:, :, :], o[:, u, :, GW:GW + HG], bc(top[:, :].unsqueeze(1), [128, 3, HG]),
                                                ALU.subtract).then_inc(s_top, 1)
                        dve.wait_ge(s_w, n + 1)
                        den = o[:, u, :, GW + HG:]
                        nc.vector.tensor_tensor(den, den, wt[:, :, :], ALU.mult)
                        dve.drain()
                        nc.vector.tensor_tensor(top[:, :], den[:, 0, :], den[:, 1, :], ALU.add)
                        dve.drain()
                        nc.vector.tensor_tensor(top[:, :], top[:, :], den[:, 2, :], ALU.add)
                        dve.drain()
                        nc.vector.reciprocal(top[:, :], top[:, :])
                        dve.drain()
                        nc.vector.tensor_tensor(wt[:, :, :], wt[:, :, :], bc(top[:, :].unsqueeze(1), [128, 3, HG]), ALU.mult)
                        dve.drain()
                        for g in range(3):
                            nc.vector.tensor_tensor(ysum[:, u, g, :].rearrange("p (h c) -> p h c", c=HD),
                                                    o[:, u, g, 0:GW].rearrange("p (h c) -> p h c", c=HD),
                                                    bc(wt[:, g, :].unsqueeze(2), [128, HG, HD]), ALU.mult)
                        dve.drain()
                        dve.sem_inc(s_ofree, 1)
                        for g in (1, 2):
                            nc.vector.tensor_tensor(ysum[:, u, 0, :], ysum[:, u, 0, :], ysum[:, u, g, :], ALU.add)
                            dve.drain()
                        dve.sem_inc(s_ys, 1)
                        dve.wait_ge(s_ta, n + 1)
                        nc.vector.tensor_copy(T["ya_T"][:, :, ds(n * 128, 128)], p_a[:, u, :, :])

            @block.scalar
            def _(act):
                act.wait_ge(s_eps, 1)
                with act.Fori(0, 3) as j:
                    for u in range(3):
                        n = j * 3 + u
                        act.wait_ge(s_in[u], (j + 1) * 32)
                        nc.scalar.activation(z[:, u, :], z[:, u, :], ACT.Silu).then_inc(s_silu, 1)
                        act.wait_ge(s_g, n + 1)
                        for g in range(2):
                            nc.scalar.activation(junk[:, :], yin[:, u, 512 * g:512 * g + 512], ACT.Square,
                                                 accum_out=ms[:, u, g:g + 1])
                            act.drain()
                        nc.scalar.activation(ms[:, u, :], ms[:, u, :], ACT.Sqrt, bias=eps[:, :], scale=1.0 / 512)
                        act.drain()
                        act.sem_inc(s_rms, 1)
                with act.Fori(0, 4) as j:
                    for u in range(2):
                        act.wait_ge(s_top, j * 2 + (u + 1))
                        nc.scalar.activation(wt[:, :, :], wt[:, :, :], ACT.Exp)
                        act.drain()
                        act.sem_inc(s_w, 1)

            @block.tensor
            def _(pe):
                pe.sem_inc(s_free, 3)
                pe.wait_ge(s_const, 32)
                with pe.Fori(0, 3) as j:
                    for u in range(3):
                        pe.wait_ge(s_n, j * 3 + (u + 1))
                        for k in range(KT):
                            nc.tensor.transpose(p_t[:, u, k, :], z[:, u, k * 128:(k + 1) * 128], ident[:, :])
                        pe.drain()
                        pe.sem_inc(s_t, 1)
                        pe.sem_inc(s_free, 1)
                with pe.Fori(0, 4) as j:
                    for u in range(2):
                        pe.wait_ge(s_ys, j * 2 + (u + 1))
                        for hp in range(2):
                            last = nc.tensor.transpose(p_a[:, u, hp, :], ysum[:, u, 0, hp * 128:(hp + 1) * 128], ident[:, :])
                        last.then_inc(s_ta, 1)


def phase_merge(nc, T, sem):
    with ExitStack() as ctx:
        def sb(name, shape, dt=f32):
            return ctx.enter_context(nc.sbuf_tensor(f"h_{name}", shape, dt))

        def sm(name):
            return sem(f"h_{name}")

        wa, ws = sb("wa", [128, 2, 2, 128]), sb("ws", [128, 2, KT, 128])
        sig = sb("sig", [128, 2, 2, TOK])
        t1 = sb("t1", [128, 2, 3, NCH])
        p_a = ctx.enter_context(nc.psum_tensor("h_pa", [128, 3, 512], f32))
        p_s = ctx.enter_context(nc.psum_tensor("h_ps", [128, 3, 512], f32))
        s_w, s_sig = [sm(f"w{u}") for u in range(2)], [sm(f"sig{u}") for u in range(2)]
        s_wfree, s_sfree, s_mm, s_ev = sm("wfree"), sm("sfree"), sm("mm"), sm("ev")
        gates = T["gate_cm"].rearrange("(g c) t -> c g t", g=2)
        with nc.Block() as block:
            @block.sync
            def _(sp):
                with sp.Fori(0, KT // 2) as j:
                    for u in range(2):
                        cols = ds((j * 2 + u) * 128, 128)
                        sp.wait_ge(s_wfree, j * 2 + (u + 1))
                        sp.dma_start(wa[:, u, :, :], T["w_attn_br"][0].rearrange("(k p) n -> p k n", p=128)[:, :, cols]
                                     ).then_inc(s_w[u], 16)
                        sp.dma_start(ws[:, u, :, :], T["w_ssd_br"][0].rearrange("(k p) n -> p k n", p=128)[:, :, cols]
                                     ).then_inc(s_w[u], 16)
                        sp.wait_ge(s_sfree, j * 2 + (u + 1))
                        sp.dma_start(sig[:, u, :, :], gates[cols, :, :]).then_inc(s_sig[u], 16)

            @block.vector
            def _(dve):
                dve.sem_inc(s_sfree, 2)
                dve.sem_inc(s_ev, 3)
                with dve.Fori(0, KT // 2) as j:
                    for u in range(2):
                        dve.wait_ge(s_sig[u], (j + 1) * 16)
                        for c in range(3):
                            cols = slice(c * NCH, (c + 1) * NCH)
                            dve.wait_ge(s_mm, j * 6 + (u * 3 + c + 1))
                            nc.vector.tensor_tensor(t1[:, 0, c, :], p_a[:, c, 0:NCH], sig[:, u, 0, cols], ALU.mult)
                            nc.vector.tensor_tensor(t1[:, 1, c, :], p_s[:, c, 0:NCH], sig[:, u, 1, cols], ALU.mult)
                            dve.drain()
                            dve.sem_inc(s_ev, 1)
                            nc.vector.tensor_tensor(T["m_T"][:, ds(j * 2 + u, 1), cols].rearrange("p a t -> p (a t)"),
                                                    t1[:, 0, c, :], t1[:, 1, c, :], ALU.add)
                        dve.drain()
                        dve.sem_inc(s_sfree, 1)

            @block.tensor
            def _(pe):
                pe.sem_inc(s_wfree, 2)
                with pe.Fori(0, KT // 2) as j:
                    for u in range(2):
                        pe.wait_ge(s_w[u], (j + 1) * 32)
                        for c in range(3):
                            cols = slice(c * NCH, (c + 1) * NCH)
                            pe.wait_ge(s_ev, j * 6 + (u * 3 + c + 1))
                            for k in range(2):
                                nc.tensor.matmul(p_a[:, c, 0:NCH], wa[:, u, k, :], T["ya_T"][:, k, cols], start=(k == 0), stop=(k == 1))
                            for k in range(KT):
                                last = nc.tensor.matmul(p_s[:, c, 0:NCH], ws[:, u, k, :], T["ys_T"][:, k, cols],
                                                        start=(k == 0), stop=(k == KT - 1))
                            last.then_inc(s_mm, 1)
                        pe.drain()
                        pe.sem_inc(s_wfree, 1)


def phase_out_router(nc, T, sem):
    with ExitStack() as ctx:
        def sb(name, shape, dt=f32):
            return ctx.enter_context(nc.sbuf_tensor(f"i_{name}", shape, dt))

        def sm(name):
            return sem(f"i_{name}")

        NR = 36
        ident, eps, w2, br = sb("ident", [128, 128]), sb("eps", [128, 1]), sb("w2", [128, D]), sb("br", [128, NR])
        wo, wr = sb("wo", [128, KT, D]), sb("wr", [128, KT, NR])
        x, hn, junk, ms = sb("x", [128, 3, D]), sb("hn", [128, 3, D]), sb("junk", [128, D]), sb("ms", [128, 3, 2])
        hnT = sb("hnT", [128, KT, 128])
        p_h = ctx.enter_context(nc.psum_tensor("i_ph", [128, 3, 2, 512], f32))
        p_t = ctx.enter_context(nc.psum_tensor("i_pt", [128, 4, 128], f32))
        p_l = ctx.enter_context(nc.psum_tensor("i_pl", [128, 512], f32))
        s_const, s_wo, s_eps = sm("const"), [sm(f"wo{k}") for k in range(2)], sm("eps")
        s_x = [sm(f"x{u}") for u in range(3)]
        s_st, s_hn_st = [sm(f"st{u}") for u in range(3)], [sm(f"hs{u}") for u in range(3)]
        s_mm, s_h, s_rms, s_n, s_t, s_te, s_l, s_le = (sm(n) for n in ("mm", "h", "rms", "n", "t", "te", "l", "le"))
        s_xfree = sm("xfree")
        for s in (*s_st, *s_hn_st, s_te, s_le):
            nc.sync.sem_inc(s, START)
        with nc.Block() as block:
            @block.sync
            def _(sp):
                for c in range(2):
                    cols = slice(512 * c, 512 * c + 512)
                    sp.dma_start(wo[:, :, cols], T["w_out"][0].rearrange("(k p) n -> p k n", p=128)[:, :, cols]).then_inc(s_wo[c], 16)
                sp.dma_start(ident[:, :], T["ident"]).then_inc(s_const, 16)
                sp.dma_start(w2[:, :], T["norm2_w"].broadcast_to([128, D])).then_inc(s_const, 16)
                sp.dma_start(br[:, :], T["b_router"].broadcast_to([128, NR])).then_inc(s_const, 16)
                sp.dma_start(wr[:, :, :], T["w_router"][0].rearrange("(k p) n -> p k n", p=128)).then_inc(s_const, 16)
                with sp.Fori(0, 3) as j:
                    for u in range(3):
                        if u == 0:
                            sp.wait_ge(s_st[u], j * 16 + START)
                        sp.wait_ge(s_xfree, j * 3 + (u + 1))
                        if u > 0:
                            sp.wait_ge(s_st[u], j * 16 + START)
                        sp.dma_start(x[:, u, :], T["x_all"][rows3(j, u), :]).then_inc(s_x[u], 16)

            @block.vector
            def _(dve):
                nc.vector.memset(eps[:, :], EPS).then_inc(s_eps, 1)
                dve.sem_inc(s_xfree, 3)
                dve.wait_ge(s_const, 64)
                with dve.Fori(0, 3) as j:
                    for u in range(3):
                        n = j * 3 + u
                        dve.wait_ge(s_x[u], (j + 1) * 16)
                        dve.wait_ge(s_mm, n + 1)
                        nc.vector.tensor_tensor(x[:, u, :], x[:, u, :], p_h[:, u, :, :].rearrange("p a c -> p (a c)"), ALU.add
                                                ).then_inc(s_h, 1)
                        dve.wait_ge(s_rms, n + 1)
                        nc.vector.reciprocal(ms[:, u, 1:2], ms[:, u, 1:2])
                        dve.drain()
                        dve.wait_ge(s_hn_st[u], j * 16 + START)
                        nc.vector.scalar_tensor_tensor(hn[:, u, :], x[:, u, :], ms[:, u, 1:2], w2[:, :], ALU.mult, ALU.mult
                                                       ).then_inc(s_n, 1)
                        dve.drain()
                        dve.sem_inc(s_xfree, 1)
                        dve.wait_ge(s_l, n + 1)
                        nc.vector.tensor_tensor(T["logits"][:, ds(n, 1), 0:NR].rearrange("p a e -> p (a e)"),
                                                p_l[:, 0:NR], br[:, :], ALU.add)
                        dve.drain()
                        dve.sem_inc(s_le, 1)

            @block.scalar
            def _(act):
                act.wait_ge(s_eps, 1)
                with act.Fori(0, 3) as j:
                    for u in range(3):
                        n = j * 3 + u
                        act.wait_ge(s_h, n + 1)
                        act.dma_start(T["h"][rows3(j, u), :], x[:, u, :]).then_inc(s_st[u], 16)
                        nc.scalar.activation(junk[:, :], x[:, u, :], ACT.Square, accum_out=ms[:, u, 0:1])
                        act.drain()
                        nc.scalar.activation(ms[:, u, 1:2], ms[:, u, 0:1], ACT.Sqrt, bias=eps[:, :], scale=1.0 / D)
                        act.drain()
                        act.sem_inc(s_rms, 1)
                        act.wait_ge(s_n, n + 1)
                        act.dma_start(T["hn"][rows3(j, u), :], hn[:, u, :]).then_inc(s_hn_st[u], 16)
                        for half in range(2):
                            act.wait_ge(s_t, j * 6 + (2 * u + half + 1))
                            nc.scalar.copy(hnT[:, 4 * half:4 * half + 4, :], p_t[:, :, :]).then_inc(s_te, 1)
                for u in range(3):
                    act.wait_ge(s_st[u], START + 48)
                    act.wait_ge(s_hn_st[u], START + 48)

            @block.tensor
            def _(pe):
                def route(t):
                    pe.wait_ge(s_n, t + 1)
                    for half in range(2):
                        pe.wait_ge(s_te, 2 * t + half + START)
                        for k in range(4):
                            c = (4 * half + k) * 128
                            last = nc.tensor.transpose(p_t[:, k, :], hn[:, t % 3, c:c + 128], ident[:, :])
                        last.then_inc(s_t, 1)
                    pe.wait_ge(s_te, 2 * t + (2 + START))
                    pe.wait_ge(s_le, t + START)
                    for k in range(KT):
                        last = nc.tensor.matmul(p_l[:, 0:NR], hnT[:, k, :], wr[:, k, :], start=(k == 0), stop=(k == KT - 1))
                    last.then_inc(s_l, 1)

                pe.wait_ge(s_const, 64)
                for t in range(TILES):
                    if t >= 3:
                        pe.wait_ge(s_h, t - 2)
                    for c in range(2):
                        if t == 0:
                            pe.wait_ge(s_wo[c], 16)
                        for k in range(KT):
                            last = nc.tensor.matmul(p_h[:, t % 3, c, :], T["m_T"][:, k, t * 128:(t + 1) * 128],
                                                    wo[:, k, 512 * c:512 * c + 512], start=(k == 0), stop=(k == KT - 1))
                    last.then_inc(s_mm, 1)
                    if t >= 1:
                        route(t - 1)
                route(TILES - 1)


def phase_route(nc, T, sem):
    with ExitStack() as ctx:
        def sb(name, shape, dt=f32):
            return ctx.enter_context(nc.sbuf_tensor(f"j_{name}", shape, dt))

        def sm(name):
            return sem(f"j_{name}")

        before, upto, ones = sb("before", [128, 128]), sb("upto", [128, 128]), sb("ones", [128, 128])
        experts, group_of, first = sb("experts", [128, NE]), sb("group_of", [128, NE]), sb("first", [128, NE])
        beyond, fills, row_id = sb("beyond", [128, NE]), sb("fills", [128, 8]), sb("row_id", [128, 1])
        tokens = sb("tokens", [128, TILES], i32)
        e4, m4, lf = sb("e4", [128, TILES, 4]), sb("m4", [128, TILES, 4]), sb("lf", [128, TILES, NE])
        t32, O = sb("t32", [128, TILES, NE]), sb("O", [128, 3, TILES, NE])
        C = sb("C", [128, TILES + 1, NE])
        top = sb("top", [128, 8, TILES])
        S, far = sb("S", [128, TILES, NE]), sb("far", [128, NE])
        slotf, ovf = sb("slotf", [128, 2, TILES]), sb("ovf", [128, 2, NE])
        col, coli = sb("col", [128, 4]), sb("coli", [128, 2], i32)
        p_pos = ctx.enter_context(nc.psum_tensor("j_pos", [128, TILES, NE], f32))
        p_s = ctx.enter_context(nc.psum_tensor("j_s", [128, 512], f32))
        consts = [(before, "before"), (upto, "upto"), (experts, "experts"), (group_of, "group_of"), (first, "first_wins"),
                  (beyond, "beyond"), (fills, "fills"), (row_id, "row_id"), (tokens, "tokens")]
        s_const, s_zero, s_v, s_a, s_ones, s_C, s_pos, s_cnt, s_nb, s_ovf, s_slot, s_sc, s_tab = (
            sm(n) for n in ("const", "zero", "v", "a", "ones", "C", "pos", "cnt", "nb", "ovf", "slot", "sc", "tab"))
        L = T["logits"]
        lc = L[:, :, 0:4]

        def over(ap, n):
            return bc(ap.unsqueeze(2), [128, TILES, n])

        def rows(ap, n):
            return bc(ap.unsqueeze(1), [128, TILES, n])

        with nc.Block() as block:
            @block.sync
            def _(sp):
                sp.dma_start(T["ids"].rearrange("(p b) a -> p (b a)", p=128), T["zero_ids"]).then_inc(s_zero, 16)
                for dst, name in consts:
                    sp.dma_start(dst[:, :], T[name]).then_inc(s_const, 16)
                sp.wait_ge(s_ovf, 1)
                sp.dma_start(T["ovf"][:, 0:NOVF].rearrange("a k -> k a"), coli[0:NOVF, 0:1]).then_inc(s_tab, 16)
                sp.dma_start(T["ovf"][:, NOVF:NOVF + 1], coli[0:1, 1:2]).then_inc(s_tab, 16)
                sp.wait_ge(s_tab, 32)

            @block.gpsimd
            def _(pool):
                nc.gpsimd.memset(ones[:, :], 1.0).then_inc(s_ones, 1)
                pool.wait_ge(s_zero, 16)
                pool.wait_ge(s_const, 16 * len(consts))
                pool.wait_ge(s_slot, 1)
                for t in range(TILES):
                    n = 128 if t < TILES - 1 else SAMP
                    for k in range(2):
                        pool.indirect_dma_start(
                            out=T["ids"], out_offset=bass.IndirectOffsetOnAxis(ap=T["slots"][0:n, t, k:k + 1], axis=0),
                            in_=tokens[0:n, t:t + 1], in_offset=None).then_inc(s_sc, 16)
                        pool.wait_ge(s_sc, 16 * (2 * t + k + 1))
                pool.wait_ge(s_sc, 32 * TILES)

            @block.scalar
            def _(act):
                act.wait_ge(s_v, 1)
                nc.scalar.activation(e4[:, :, :], e4[:, :, :], ACT.Exp).then_inc(s_a, 1)
                act.wait_ge(s_v, 2)
                nc.scalar.activation(top[:, 4, :], top[:, 4, :], ACT.Exp).then_inc(s_a, 1)

            @block.vector
            def _(dve):
                def tt(out, a, b, op):
                    nc.vector.tensor_tensor(out, a, b, op)
                    dve.drain()

                def ts(out, a, s1, op0, s2=None, op1=ALU.bypass):
                    nc.vector.tensor_scalar(out, a, s1, s2, op0, op1)
                    dve.drain()

                def red(out, a, op):
                    nc.vector.tensor_reduce(out, a, AX.X, op)
                    dve.drain()

                def choose(values, width, k):
                    red(top[:, k, :], values, ALU.max)
                    tt(t32[:, :, 0:width], values, over(top[:, k, :], width), ALU.is_equal)
                    tt(t32[:, :, 0:width], t32[:, :, 0:width], rows(first[:, 0:width], width), ALU.mult)
                    red(top[:, 6, :], t32[:, :, 0:width], ALU.max)
                    ts(top[:, 6, :], top[:, 6, :], -1.0, ALU.mult, float(NE), ALU.add)

                dve.wait_ge(s_const, 16 * len(consts))
                choose(lc, 4, 0)
                tt(e4[:, :, :], lc, over(top[:, 0, :], 4), ALU.subtract)
                dve.sem_inc(s_v, 1)
                tt(t32[:, :, :], rows(group_of[:, :], NE), over(top[:, 6, :], NE), ALU.not_equal)
                nc.vector.scalar_tensor_tensor(lf[:, :, :], t32[:, :, :], NEG, L[:, :, 4:4 + NE], ALU.mult, ALU.add)
                dve.drain()
                for k in range(2):
                    choose(lf[:, :, :], NE, 2 + k)
                    tt(O[:, k, :, :], rows(experts[:, :], NE), over(top[:, 6, :], NE), ALU.is_equal)
                    if k == 0:
                        nc.vector.scalar_tensor_tensor(lf[:, :, :], O[:, 0, :, :], NEG, lf[:, :, :], ALU.mult, ALU.add)
                        dve.drain()
                tt(top[:, 4, :], top[:, 3, :], top[:, 2, :], ALU.subtract)
                dve.sem_inc(s_v, 1)
                nc.vector.memset(O[SAMP:128, 0, TILES - 1, :], 0.0)
                nc.vector.memset(O[SAMP:128, 1, TILES - 1, :], 0.0)
                dve.drain()
                tt(O[:, 2, :, :], O[:, 0, :, :], O[:, 1, :, :], ALU.add)
                nc.vector.memset(C[:, 0, :], 0.0)
                dve.drain()
                for t in range(TILES):
                    tt(C[:, t + 1, :], C[:, t, :], O[:, 2, t, :], ALU.add)
                dve.sem_inc(s_C, 1)
                dve.wait_ge(s_a, 2)
                red(top[:, 1, :], e4[:, :, :], ALU.add)
                nc.vector.reciprocal(top[:, 1, :], top[:, 1, :])
                ts(top[:, 5, :], top[:, 4, :], 1.0, ALU.add)
                nc.vector.reciprocal(top[:, 5, :], top[:, 5, :])
                dve.drain()
                tt(top[:, 5, :], top[:, 5, :], top[:, 1, :], ALU.mult)
                tt(top[:, 4, :], top[:, 4, :], top[:, 5, :], ALU.mult)
                nc.vector.tensor_copy(T["gates"][:, :, 0], top[:, 5, :])
                nc.vector.tensor_copy(T["gates"][:, :, 1], top[:, 4, :])
                dve.wait_ge(s_cnt, 1)
                nc.vector.tensor_copy(col[0:NE, 0:1], p_s[0:NE, 0:1])
                dve.drain()
                ts(t32[0:NE, 0, 0:8], fills[0:NE, :], col[0:NE, 0:1], ALU.is_lt)
                red(col[0:NE, 1:2], t32[0:NE, 0, 0:8], ALU.add)
                dve.sem_inc(s_nb, 1)
                dve.wait_ge(s_nb, 2)
                nc.vector.tensor_copy(ovf[:, :, :], p_s[:, 64:128].rearrange("p (a e) -> p a e", a=2))
                dve.drain()
                ts(t32[:, 0, :], ovf[:, 1, :], row_id[:, :], ALU.is_le)
                red(col[:, 2:3], t32[:, 0, :], ALU.add)
                ts(col[:, 2:3], col[:, 2:3], float(NE - 1), ALU.min)
                nc.vector.tensor_copy(coli[:, 0:1], col[:, 2:3])
                nc.vector.tensor_copy(coli[:, 1:2], ovf[:, 1, NE - 1:NE])
                dve.drain()
                dve.sem_inc(s_ovf, 1)
                tt(far[:, :], ovf[:, 0, :], beyond[:, :], ALU.add)
                ts(far[:, :], far[:, :], 128.0, ALU.mult)
                dve.wait_ge(s_pos, 1)
                ts(S[:, :, :], p_pos[:, :, :], 128.0, ALU.is_ge)
                tt(S[:, :, :], S[:, :, :], rows(far[:, :], NE), ALU.mult)
                tt(S[:, :, :], S[:, :, :], p_pos[:, :, :], ALU.add)
                nc.vector.scalar_tensor_tensor(S[:, :, :], rows(experts[:, :], NE), 128.0, S[:, :, :], ALU.mult, ALU.add)
                dve.drain()
                for k in range(2):
                    tt(t32[:, :, :], O[:, k, :, :], S[:, :, :], ALU.mult)
                    red(slotf[:, k, :], t32[:, :, :], ALU.add)
                    nc.vector.tensor_copy(T["slots"][:, :, k], slotf[:, k, :])
                dve.drain()
                dve.sem_inc(s_slot, 1)

            @block.tensor
            def _(pe):
                pe.wait_ge(s_const, 16 * len(consts))
                pe.wait_ge(s_ones, 1)
                pe.wait_ge(s_C, 1)
                nc.tensor.matmul(p_s[0:NE, 0:1], C[:, TILES, :], ones[:, 0:1], start=True, stop=True).then_inc(s_cnt, 1)
                for t in range(TILES):
                    nc.tensor.matmul(p_pos[:, t, :], ones[:, :], C[:, t, :], start=True, stop=False)
                    last = nc.tensor.matmul(p_pos[:, t, :], before[:, :], O[:, 2, t, :], start=False, stop=True)
                last.then_inc(s_pos, 1)
                pe.wait_ge(s_nb, 1)
                nb = bc(col[0:NE, 1:2], [NE, 128])
                nc.tensor.matmul(p_s[:, 64:96], nb, before[0:NE, 0:NE], start=True, stop=True)
                nc.tensor.matmul(p_s[:, 96:128], nb, upto[0:NE, 0:NE], start=True, stop=True).then_inc(s_nb, 1)


class ExpertBuffers:

    def __init__(self, nc, ctx, tag, n):
        def sb(name, shape, dt=f32):
            return ctx.enter_context(nc.sbuf_tensor(f"{tag}_{name}", shape, dt))

        def pb(name, shape):
            return ctx.enter_context(nc.psum_tensor(f"{tag}_{name}", shape, f32))
        self.ident = sb("ident", [128, 128])
        self.ids = sb("ids", [128, n], i32)
        self.rows = sb("rows", [128, n, D])
        self.wg, self.wu = sb("wg", [128, n, KT, FF]), sb("wu", [128, n, KT, FF])
        self.wd = sb("wd", [128, n, FF // 128, D])
        self.xT = sb("xT", [128, KT, 128])
        self.act, self.hid = sb("act", [128, FF]), sb("hid", [128, FF])
        self.hT = sb("hT", [128, FF // 128, 128])
        self.out = sb("out", [128, n, D])
        self.p_x = pb("px", [128, KT, 128])
        self.p_g, self.p_u = pb("pg", [128, FF]), pb("pu", [128, FF])
        self.p_h = pb("ph", [128, FF // 128, 128])
        self.p_o = pb("po", [128, 2, 512])


def phase_experts(nc, T, sem):
    with ExitStack() as ctx:
        B = ExpertBuffers(nc, ctx, "k", 2)
        N = NE // 2

        def sm(name):
            return sem(f"k_{name}")

        s_seen = sm("seen")
        s_const = sm("const")
        s_id, s_row, s_wg, s_wd, s_out = ([sm(f"{n}{u}") for u in range(2)] for n in ("id", "row", "wgu", "wd", "out"))
        s_wgf, s_wdf, s_xt, s_xe, s_gu, s_silu, s_hid, s_ht, s_hte, s_down, s_oe = (
            sm(n) for n in ("wgf", "wdf", "xt", "xe", "gu", "silu", "hid", "ht", "hte", "down", "oe"))
        for s in (s_hid, *s_out, s_hte, s_oe):
            nc.sync.sem_inc(s, START)
        wg_v = T["w_expert_gate"][0].rearrange("e (k p) f -> p e k f", p=128)
        wu_v = T["w_expert_up"][0].rearrange("e (k p) f -> p e k f", p=128)
        wd_v = T["w_expert_down"][0].rearrange("e (k p) n -> p e k n", p=128)

        def one(ap):
            return ap.rearrange("p e k f -> p (e k) f")

        with nc.Block() as block:
            @block.sync
            def _(sp):
                sp.dma_start(B.ident[:, :], T["ident"]).then_inc(s_const, 16)
                with sp.Fori(0, N) as j:
                    for u in range(2):
                        e = ds(j * 2 + u, 1)
                        sp.wait_ge(s_wgf, j * 2 + (u + 1))
                        sp.dma_start(B.wg[:, u, :, :], one(wg_v[:, e, :, :])).then_inc(s_wg[u], 16)
                        sp.dma_start(B.wu[:, u, :, :], one(wu_v[:, e, :, :])).then_inc(s_wg[u], 16)
                        sp.wait_ge(s_wdf, j * 2 + (u + 1))
                        sp.dma_start(B.wd[:, u, :, :], one(wd_v[:, e, :, :])).then_inc(s_wd[u], 16)

            @block.gpsimd
            def _(pool):
                def fetch(n, u, i):
                    pool.wait_ge(s_xt, n + 1)
                    pool.dma_start(B.ids[:, u:u + 1], T["ids"][ds(n * 128, 128) if not isinstance(n, int) else
                                                              slice(n * 128, n * 128 + 128), :]).then_inc(s_id[u], 16)
                    pool.wait_ge(s_id[u], (i + 1) * 16)
                    pool.sem_inc(s_seen, 1)
                    pool.indirect_dma_start(out=B.rows[:, u, :], out_offset=None, in_=T["hn"],
                                            in_offset=bass.IndirectOffsetOnAxis(ap=B.ids[:, u:u + 1], axis=0)
                                            ).then_inc(s_row[u], 16)
                with pool.Fori(0, N) as j:
                    for u in range(2):
                        fetch(j * 2 + u, u, j)
                fetch(NE, 0, N)

            @block.vector
            def _(dve):
                with dve.Fori(0, N) as j:
                    for u in range(2):
                        n = j * 2 + u
                        dve.wait_ge(s_silu, n + 1)
                        nc.vector.tensor_tensor(B.hid[:, :], B.act[:, :], B.p_u[:, :], ALU.mult).then_inc(s_hid, 1)
                        dve.wait_ge(s_xt, n + 4)
                        nc.vector.tensor_copy(B.xT[:, 0:KT, :], B.p_x[:, :, :]).then_inc(s_xe, 1)
                        dve.wait_ge(s_ht, n + 1)
                        nc.vector.tensor_copy(B.hT[:, :, :], B.p_h[:, :, :]).then_inc(s_hte, 1)

            @block.scalar
            def _(act):
                act.wait_ge(s_xt, 3)
                nc.scalar.copy(B.xT[:, :, :], B.p_x[:, :, :]).then_inc(s_xe, 1)
                with act.Fori(0, N) as j:
                    for u in range(2):
                        n = j * 2 + u
                        act.wait_ge(s_gu, n + 1)
                        act.wait_ge(s_hid, n + START)
                        nc.scalar.activation(B.act[:, :], B.p_g[:, :], ACT.Silu).then_inc(s_silu, 1)
                        act.wait_ge(s_down, n + 1)
                        act.wait_ge(s_out[u], j * 16 + START)
                        nc.scalar.copy(B.out[:, u, :], B.p_o[:, :, :].rearrange("p a c -> p (a c)")).then_inc(s_oe, 1)
                        act.drain()
                        act.dma_start(T["o_moe"][ds(n * 128, 128), :], B.out[:, u, :]).then_inc(s_out[u], 16)
                for u in range(2):
                    act.wait_ge(s_out[u], N * 16 + START)

            @block.tensor
            def _(pe):
                pe.sem_inc(s_xt, 2)
                pe.sem_inc(s_wgf, 2)
                pe.sem_inc(s_wdf, 2)
                pe.wait_ge(s_const, 16)

                def turn(n, u, i):
                    pe.wait_ge(s_row[u], (i + 1) * 16)
                    for k in range(KT):
                        last = nc.tensor.transpose(B.p_x[:, k, :], B.rows[:, u, k * 128:(k + 1) * 128], B.ident[:, :])
                    last.then_inc(s_xt, 1)
                turn(0, 0, 0)
                with pe.Fori(0, N) as j:
                    for u in range(2):
                        n = j * 2 + u
                        pe.wait_ge(s_wg[u], (j + 1) * 32)
                        pe.wait_ge(s_xe, n + 1)
                        pe.wait_ge(s_hid, n + START)
                        for p, w in ((B.p_g, B.wg), (B.p_u, B.wu)):
                            for k in range(KT):
                                last = nc.tensor.matmul(p[:, :], B.xT[:, k, :], w[:, u, k, :], start=(k == 0), stop=(k == KT - 1))
                        last.then_inc(s_gu, 1)
                        pe.drain()
                        pe.sem_inc(s_wgf, 1)
                        turn(n + 1, 1 - u, j + u)
                        pe.wait_ge(s_hid, n + (1 + START))
                        pe.wait_ge(s_hte, n + START)
                        for k in range(FF // 128):
                            last = nc.tensor.transpose(B.p_h[:, k, :], B.hid[:, k * 128:(k + 1) * 128], B.ident[:, :])
                        last.then_inc(s_ht, 1)
                        pe.wait_ge(s_hte, n + (1 + START))
                        pe.wait_ge(s_wd[u], (j + 1) * 16)
                        pe.wait_ge(s_oe, n + START)
                        for c in range(2):
                            for k in range(FF // 128):
                                last = nc.tensor.matmul(B.p_o[:, c, :], B.hT[:, k, :], B.wd[:, u, k, 512 * c:512 * c + 512],
                                                        start=(k == 0), stop=(k == FF // 128 - 1))
                        last.then_inc(s_down, 1)
                        pe.drain()
                        pe.sem_inc(s_wdf, 1)


def phase_overflow(nc, T, sem):
    with ExitStack() as ctx:
        B = ExpertBuffers(nc, ctx, "l", 1)
        table = ctx.enter_context(nc.sbuf_tensor("l_table", [1, NOVF + 1], i32))

        def sm(name):
            return sem(f"l_{name}")

        s_seen = sm("seen")
        s_tab, s_id, s_row, s_w, s_xt, s_xe, s_gu, s_silu, s_hid, s_ht, s_hte, s_down, s_out, s_done = (
            sm(n) for n in ("tab", "id", "row", "w", "xt", "xe", "gu", "silu", "hid", "ht", "hte", "down", "out", "done"))
        for s in (s_done,):
            nc.sync.sem_inc(s, START)
        wg_v = T["w_expert_gate"][0].rearrange("e (k p) f -> p e k f", p=128)
        wu_v = T["w_expert_up"][0].rearrange("e (k p) f -> p e k f", p=128)
        wd_v = T["w_expert_down"][0].rearrange("e (k p) n -> p e k n", p=128)

        def one(ap):
            return ap.rearrange("p e k f -> p (e k) f")

        def blocks(eng, body):
            eng.wait_ge(s_tab, 32)
            count = eng.value_load(table[0:1, NOVF:NOVF + 1], min_val=0, max_val=NOVF)
            with eng.Fori(0, NOVF) as k:
                with eng.If(k < count):
                    body(k)

        with nc.Block() as block:
            @block.sync
            def _(sp):
                sp.dma_start(table[:, :], T["ovf"][:, 0:NOVF + 1]).then_inc(s_tab, 16)
                sp.dma_start(B.ident[:, :], T["ident"]).then_inc(s_tab, 16)

                def body(k):
                    e = ds(sp.value_load(table[0:1, ds(k, 1)], min_val=0, max_val=NE - 1), 1)
                    sp.wait_ge(s_done, k + START)
                    sp.dma_start(B.wg[:, 0, :, :], one(wg_v[:, e, :, :])).then_inc(s_w, 16)
                    sp.dma_start(B.wu[:, 0, :, :], one(wu_v[:, e, :, :])).then_inc(s_w, 16)
                    sp.dma_start(B.wd[:, 0, :, :], one(wd_v[:, e, :, :])).then_inc(s_w, 16)
                blocks(sp, body)

            @block.gpsimd
            def _(pool):
                def body(k):
                    pool.wait_ge(s_done, k + START)
                    pool.dma_start(B.ids[:, 0:1], T["ids"][ds(k * 128 + NE * 128, 128), :]).then_inc(s_id, 16)
                    pool.wait_ge(s_id, (k + 1) * 16)
                    pool.sem_inc(s_seen, 1)
                    pool.indirect_dma_start(out=B.rows[:, 0, :], out_offset=None, in_=T["hn"],
                                            in_offset=bass.IndirectOffsetOnAxis(ap=B.ids[:, 0:1], axis=0)).then_inc(s_row, 16)
                blocks(pool, body)

            @block.vector
            def _(dve):
                def body(k):
                    dve.wait_ge(s_xt, k + 1)
                    nc.vector.tensor_copy(B.xT[:, :, :], B.p_x[:, :, :]).then_inc(s_xe, 1)
                    dve.wait_ge(s_silu, k + 1)
                    nc.vector.tensor_tensor(B.hid[:, :], B.act[:, :], B.p_u[:, :], ALU.mult).then_inc(s_hid, 1)
                    dve.wait_ge(s_ht, k + 1)
                    nc.vector.tensor_copy(B.hT[:, :, :], B.p_h[:, :, :]).then_inc(s_hte, 1)
                blocks(dve, body)

            @block.scalar
            def _(act):
                def body(k):
                    act.wait_ge(s_gu, k + 1)
                    nc.scalar.activation(B.act[:, :], B.p_g[:, :], ACT.Silu).then_inc(s_silu, 1)
                    act.wait_ge(s_down, k + 1)
                    nc.scalar.copy(B.out[:, 0, :], B.p_o[:, :, :].rearrange("p a c -> p (a c)"))
                    act.drain()
                    act.dma_start(T["o_moe"][ds(k * 128 + NE * 128, 128), :], B.out[:, 0, :]).then_inc(s_out, 16)
                    act.wait_ge(s_out, (k + 1) * 16)
                    act.sem_inc(s_done, 1)
                blocks(act, body)

            @block.tensor
            def _(pe):
                def body(k):
                    pe.wait_ge(s_row, (k + 1) * 16)
                    for c in range(KT):
                        last = nc.tensor.transpose(B.p_x[:, c, :], B.rows[:, 0, c * 128:(c + 1) * 128], B.ident[:, :])
                    last.then_inc(s_xt, 1)
                    pe.wait_ge(s_xe, k + 1)
                    pe.wait_ge(s_w, (k + 1) * 48)
                    for p, w in ((B.p_g, B.wg), (B.p_u, B.wu)):
                        for c in range(KT):
                            last = nc.tensor.matmul(p[:, :], B.xT[:, c, :], w[:, 0, c, :], start=(c == 0), stop=(c == KT - 1))
                    last.then_inc(s_gu, 1)
                    pe.wait_ge(s_hid, k + 1)
                    for c in range(FF // 128):
                        last = nc.tensor.transpose(B.p_h[:, c, :], B.hid[:, c * 128:(c + 1) * 128], B.ident[:, :])
                    last.then_inc(s_ht, 1)
                    pe.wait_ge(s_hte, k + 1)
                    for h in range(2):
                        for c in range(FF // 128):
                            last = nc.tensor.matmul(B.p_o[:, h, :], B.hT[:, c, :], B.wd[:, 0, c, 512 * h:512 * h + 512],
                                                    start=(c == 0), stop=(c == FF // 128 - 1))
                    last.then_inc(s_down, 1)
                blocks(pe, body)


def phase_combine(nc, T, sem):
    with ExitStack() as ctx:
        def sb(name, shape, dt=f32):
            return ctx.enter_context(nc.sbuf_tensor(f"m_{name}", shape, dt))

        def sm(name):
            return sem(f"m_{name}")

        w, eps, junk, ms = sb("w", [128, D]), sb("eps", [128, 1]), sb("junk", [128, D]), sb("ms", [128, 3, 2])
        h, o, y = sb("h", [128, 3, D]), sb("o", [128, 3, 2, D]), sb("y", [128, 3, D])
        idx, gate = sb("idx", [128, 3, 2], i32), sb("gate", [128, 3, 2])
        s_seen = sm("seen")
        s_w, s_eps, s_idx = sm("w"), sm("eps"), sm("idx")
        s_h, s_o, s_st = ([sm(f"{n}{u}") for u in range(3)] for n in ("h", "o", "st"))
        s_free, s_sum, s_rms, s_y = sm("free"), sm("sum"), sm("rms"), sm("y")
        for s in (*s_st,):
            nc.sync.sem_inc(s, START)
        with nc.Block() as block:
            @block.sync
            def _(sp):
                sp.dma_start(w[:, :], T["final_norm_w"].broadcast_to([128, D])).then_inc(s_w, 16)
                with sp.Fori(0, 3) as j:
                    for u in range(3):
                        sp.wait_ge(s_free, j * 3 + (u + 1))
                        sp.dma_start(h[:, u, :], T["h"][rows3(j, u), :]).then_inc(s_h[u], 16)

            @block.gpsimd
            def _(pool):
                with pool.Fori(0, 3) as j:
                    for u in range(3):
                        pool.wait_ge(s_free, j * 3 + (u + 1))
                        nc.gpsimd.tensor_copy(idx[:, u, :], T["slots"][:, ds(j * 3 + u, 1), :].rearrange("p a k -> p (a k)")
                                              ).then_inc(s_idx, 1)
                        pool.wait_ge(s_idx, j * 3 + (u + 1))
                        pool.sem_inc(s_seen, 1)
                        for k in range(2):
                            pool.indirect_dma_start(out=o[:, u, k, :], out_offset=None, in_=T["o_moe"],
                                                    in_offset=bass.IndirectOffsetOnAxis(ap=idx[:, u, k:k + 1], axis=0)
                                                    ).then_inc(s_o[u], 16)

            @block.vector
            def _(dve):
                nc.vector.memset(eps[:, :], EPS).then_inc(s_eps, 1)
                dve.sem_inc(s_free, 3)
                dve.wait_ge(s_w, 16)
                with dve.Fori(0, 3) as j:
                    for u in range(3):
                        n = j * 3 + u
                        nc.vector.tensor_copy(gate[:, u, :], T["gates"][:, ds(n, 1), :].rearrange("p a k -> p (a k)"))
                        dve.drain()
                        dve.wait_ge(s_h[u], (j + 1) * 16)
                        dve.wait_ge(s_o[u], (j + 1) * 32)
                        for k in range(2):
                            nc.vector.scalar_tensor_tensor(h[:, u, :], o[:, u, k, :], gate[:, u, k:k + 1], h[:, u, :], ALU.mult, ALU.add)
                            dve.drain()
                        dve.sem_inc(s_sum, 1)
                        dve.wait_ge(s_rms, n + 1)
                        nc.vector.reciprocal(ms[:, u, 1:2], ms[:, u, 1:2])
                        dve.drain()
                        dve.wait_ge(s_st[u], j * 16 + START)
                        nc.vector.scalar_tensor_tensor(y[:, u, :], h[:, u, :], ms[:, u, 1:2], w[:, :], ALU.mult, ALU.mult)
                        dve.drain()
                        dve.sem_inc(s_y, 1)
                        dve.sem_inc(s_free, 1)

            @block.scalar
            def _(act):
                act.wait_ge(s_eps, 1)
                with act.Fori(0, 3) as j:
                    for u in range(3):
                        n = j * 3 + u
                        act.wait_ge(s_sum, n + 1)
                        nc.scalar.activation(junk[:, :], h[:, u, :], ACT.Square, accum_out=ms[:, u, 0:1])
                        act.drain()
                        nc.scalar.activation(ms[:, u, 1:2], ms[:, u, 0:1], ACT.Sqrt, bias=eps[:, :], scale=1.0 / D)
                        act.drain()
                        act.sem_inc(s_rms, 1)
                        act.wait_ge(s_y, n + 1)
                        act.dma_start(T["y"][rows3(j, u), :], y[:, u, :]).then_inc(s_st[u], 16)
                for u in range(3):
                    act.wait_ge(s_st[u], START + 48)


def output_shapes():
    keeps = [min(w, SEQ) for w, _ in GROUPS]
    news = [min(w, PAST + NT) for w, _ in GROUPS]
    return ([("y", (TOK, D))]
            + [(f"p_kv{g}", (1, 1, k, 2, HG, HD)) for g, k in enumerate(keeps)]
            + [("p_conv", (1, 1, CONV - 1, XBC)), ("p_ssm", (1, 1, SH, HD, SN))]
            + [(f"s_kv{g}", (1, NB, k, 2, HG, HD)) for g, k in enumerate(news)]
            + [("s_conv", (1, NB, CONV - 1, XBC)), ("s_ssm", (1, NB, SH, HD, SN))])


def build_program(nc, T):
    with ExitStack() as ctx:
        used = []

        def sem(name):
            used.append(nc.alloc_semaphore(name=name))
            return used[-1]

        def scratch(name, shape, dt=f32):
            T[name] = nc.dram_tensor(f"scratch_{name}", shape, dt, kind="Internal").ap()

        scratch("u_tm", (TOK, XOFF))
        scratch("gate_cm", (2 * D, TOK))
        scratch("xc_tm", (TOK, XBC))
        scratch("xc_cm", (XBC, TOK))
        scratch("o_attn", (3, SEQ, GW + 8))
        scratch("y_ssd", (TOK, D))
        scratch("h", (TOK, D))
        scratch("hn", (TOK, D))
        scratch("ids", (NBLK * 128, 1), i32)
        scratch("o_moe", (NBLK * 128, D))
        scratch("ovf", (1, 32), i32)
        T["p_kv"] = [T[f"p_kv{g}"] for g in range(3)]
        T["s_kv"] = [T[f"s_kv{g}"] for g in range(3)]
        T["cache"] = [T["cache_kv_w128"], T["cache_kv_w512"], T["cache_kv_w2048"]]
        T["s_cache"] = ctx.enter_context(nc.semaphore("cache_moved"))

        def keep(name, shape, dt=f32):
            T[name] = ctx.enter_context(nc.sbuf_tensor(name, shape, dt))

        keep("logits", [128, TILES, 40])
        keep("slots", [128, TILES, 2], i32)
        keep("gates", [128, TILES, 2])
        keep("dt_tm", [128, TILES, SH])
        keep("da_tm", [128, TILES, SH])

        @contextmanager
        def living(*tensors):
            with ExitStack() as own:
                for name, shape in tensors:
                    T[name] = own.enter_context(nc.sbuf_tensor(name, shape, f32))
                yield

        def run(*steps):
            for phase in steps:
                phase(nc, T, sem)
                nc.clear_and_free_semaphores(used)
                used.clear()
                nc.all_engine_barrier()

        run(phase_norm_project)
        with living(("ya_T", [128, 2, TOK])):
            run(phase_attention_prompt, phase_attention_sample, phase_ssd_prompt, phase_ssd_sample)
            with living(("ys_T", [128, KT, TOK]), ("m_T", [128, KT, TOK])):
                run(phase_branch_inputs, phase_merge, phase_out_router)
        run(phase_route, phase_experts, phase_overflow, phase_combine)




_DATA = ["norm1_w", "w_in", "w_attn_br", "w_ssd_br", "b_gate", "w_out", "conv_w", "conv_b", "dt_bias", "A_log", "D_skip",
         "ssd_norm_w", "norm2_w", "b_router_coarse", "b_router_fine", "w_expert_gate", "w_expert_up", "w_expert_down",
         "final_norm_w", "cache_kv_w128", "cache_kv_w512", "cache_kv_w2048", "state_conv", "state_ssm",
         "w_router_coarse", "w_router_fine"]


def shape_constants():
    f = np.float32
    i, j = np.arange(128)[:, None], np.arange(128)[None, :]
    c = {"ident": np.eye(128, dtype=f)}
    c["upto"] = (i <= j).astype(f)
    c["before"] = (i < j).astype(f)
    same = i // NT == j // NT
    c["upto_seq"] = ((i <= j) & same).astype(f)
    c["future"] = np.where(i <= j, 0.0, NEG).astype(f)
    c["future_seq"] = np.where((i <= j) & same, 0.0, NEG).astype(f)
    c["seq_of"] = (i // NT == np.arange(NB)[None, :]).astype(f)
    c["same_seq"] = same.astype(f)
    c["seq_cols"] = np.broadcast_to(np.arange(NB)[:, None] == np.arange(128)[None, :] // NT, (128, NB, 128)).astype(f)
    prev = np.where(j >= i, 0.0, NEG).astype(f)
    cur = np.where(j <= i, 0.0, NEG).astype(f)
    none = np.full((128, 128), NEG, f)
    first = np.stack([np.concatenate([cur, prev if n else none], 1) for n in range(4)], 1)
    c["mask_even"] = np.ascontiguousarray(first)
    c["mask_odd"] = np.concatenate([prev, cur], 1)
    c["mask_half"] = np.where((j <= i) & (i // 64 == j // 64), 0.0, NEG).astype(f)
    inv = (np.float32(10000.0) ** (-np.arange(HD // 2, dtype=f) * f(2.0 / HD))).astype(f)

    def rotary(pos):
        ang = (pos.astype(f)[..., None] * inv).astype(f)
        cs, sn = np.cos(ang), np.sin(ang)
        return np.concatenate([cs, cs, -sn, sn], -1).astype(f)
    p = np.arange(128)
    order = np.zeros((3, 8, 128), np.int64)
    for t in range(8):
        order[0, t] = t * 128 + p
        order[1, t] = t // 2 + 4 * ((t % 2) * 128 + p)
        order[2, t] = 2 * t + p // 64 + 16 * (p % 64)
    c["rotary"] = np.ascontiguousarray(rotary(order).transpose(2, 1, 0, 3))
    c["rotary_new"] = rotary(PAST + p % NT)
    t = (np.arange(128) % NT)[:, None]
    old = np.zeros((128, 3, 128), f)
    old[:, 0] = np.where(j >= t, 0.0, NEG)
    old[:, 1] = np.where(4 * j + t % 4 >= t, 0.0, NEG)
    old[:, 2] = np.where(j // 64 == t % 2, 0.0, NEG)
    c["mask_cached"] = old
    new = np.full((128, 2, 3, 128), NEG, f)
    row, key = np.arange(128)[:, None], np.arange(128)[None, :]
    for half in range(2):
        seq, tt = half * 4 + row // 32, row % NT
        ks, kt = key // NT, key % NT
        for g, ok in enumerate((kt <= tt, (kt == tt) | (kt == tt - 4), kt == tt)):
            new[:, half, g] = np.where((seq == ks) & ok & (key < SAMP), 0.0, NEG)
    c["mask_new"] = new
    c["experts"] = np.broadcast_to(np.arange(NE, dtype=f), (128, NE)).copy()
    c["group_of"] = np.broadcast_to(np.arange(NE, dtype=f) // 8, (128, NE)).copy()
    c["tokens"] = (np.arange(TILES)[None, :] * 128 + np.arange(128)[:, None]).astype(np.int32)
    c["first_wins"] = np.broadcast_to(NE - np.arange(NE, dtype=f), (128, NE)).copy()
    c["beyond"] = np.broadcast_to((NE - 1 - np.arange(NE, dtype=f)), (128, NE)).copy()
    c["fills"] = np.broadcast_to(128.0 * np.arange(1, 9, dtype=f), (128, 8)).copy()
    c["row_id"] = np.arange(128, dtype=f)[:, None].copy()
    c["zero_ids"] = np.zeros((128, NBLK), np.int32)
    return c


def kernel(**inputs):
    import numpy as _np
    import concourse.bacc as _bacc
    from concourse import mybir as _mybir
    from concourse.bass_utils import run_bass_kernel_spmd as _run

    nc = _bacc.Bacc("TRN2", target_bir_lowering=False, num_devices=1)
    x_p, x_s = _np.asarray(inputs["x_prompt"]), _np.asarray(inputs["x_sample"])
    arrays = {"x_all": _np.concatenate([x_p.reshape(SEQ, D), x_s.reshape(SAMP, D),
                                        _np.zeros((TOK - SEQ - SAMP, D), x_p.dtype)])}
    for name in _DATA:
        arrays[name] = _np.asarray(inputs[name])
    arrays["state_conv"] = _np.ascontiguousarray(arrays["state_conv"][0].transpose(2, 0, 1))
    for name in ("norm1_w", "b_gate", "ssd_norm_w", "conv_w", "conv_b"):
        a = arrays[name].reshape(-1, arrays[name].shape[-1] // 128, 128)
        arrays[name] = a.transpose(2, 1, 0) if name == "conv_w" else a.transpose(2, 0, 1)
    arrays["dt_bias"], arrays["A_log"] = arrays["dt_bias"].reshape(SH, 1), arrays["A_log"].reshape(SH, 1)
    arrays["d_skip"] = _np.broadcast_to(arrays.pop("D_skip").reshape(1, SH), (128, SH))
    arrays["b_router"] = _np.concatenate([arrays.pop("b_router_coarse"), arrays.pop("b_router_fine")], -1)
    arrays["w_router"] = _np.concatenate([arrays.pop("w_router_coarse"), arrays.pop("w_router_fine")], -1)
    arrays["final_norm_w"] = arrays["final_norm_w"].reshape(1, D)
    arrays = {f"in_{n}": _np.ascontiguousarray(a) for n, a in arrays.items()}
    arrays.update({f"const_{n}": a for n, a in shape_constants().items()})
    T = {}
    for name, a in arrays.items():
        kind = "ExternalInput"
        T[name.split("_", 1)[1]] = nc.dram_tensor(name, a.shape, _mybir.dt.from_np(a.dtype), kind=kind).ap()
    outs = output_shapes()
    for name, shape in outs:
        T[name] = nc.dram_tensor(f"out_{name}", shape, _mybir.dt.float32, kind="ExternalOutput").ap()
    build_program(nc, T)
    r = _run(nc, [arrays], core_ids=[0])
    got = [_np.asarray(r.results[0][f"out_{name}"]) for name, _ in outs]
    y = got[0]
    return (y[:SEQ].reshape(1, SEQ, D), y[SEQ:SEQ + SAMP].reshape(NB, NT, D), *got[1:])
```

```python
import concourse.bass as bass
from concourse import mybir
from contextlib import ExitStack, contextmanager
import numpy as np

f32 = mybir.dt.float32
bf16 = mybir.dt.bfloat16
f32r = mybir.dt.float32r
i32 = mybir.dt.int32
ALU = mybir.AluOpType
ACT = mybir.ActivationFunctionType
AX = mybir.AxisListType
ds = bass.ds

D = 1024
KT = D // 128
SEQ = 1024
NB, NT = 8, 8
SAMP = NB * NT
PAST = 1024
TILES = SEQ // 128 + 1
TOK = TILES * 128
HD = 64
HG = 4
GW = HG * HD
GROUPS = ((128, 1), (512, 4), (2048, 16))
AW = 3 * GW
DI = 1024
SH = 16
SN = 128
CONV = 4
XBC = DI + 4 * SN
ZOFF = 3 * AW
XOFF = ZOFF + DI
DTOFF = XOFF + XBC
GOFF = DTOFF + SH
NE = 32
FF = 512
NOVF = 16
NBLK = NE + NOVF
EPS = 1e-6
NEG = -1e30
WCOL = 256
HI_BITS = -4096
HIST = CONV - 1
TAIL = HIST * (1 + NB)
NCH = 384
START = 1


def bc(ap, shape):
    return ap.broadcast_to(shape)


def one_pass(ap):
    return ap.bitcast(f32r)


def split(nc, dve, value, hi, lo, upper):
    nc.vector.tensor_scalar(upper.bitcast(i32), value.bitcast(i32), HI_BITS, None, ALU.bitwise_and)
    dve.drain()
    nc.vector.tensor_copy(one_pass(hi), upper)
    nc.vector.tensor_tensor(one_pass(lo), value, upper, ALU.subtract)
    dve.drain()


def product(nc, out, pairs):
    n = len(pairs)
    for i, ((a_hi, a_lo), (b_hi, b_lo)) in enumerate(pairs):
        nc.tensor.matmul(out, one_pass(a_hi), one_pass(b_hi), start=(i == 0), stop=False)
        nc.tensor.matmul(out, one_pass(a_hi), one_pass(b_lo), start=False, stop=False)
        last = nc.tensor.matmul(out, one_pass(a_lo), one_pass(b_hi), start=False, stop=(i == n - 1))
    return last


def phase_norm_project(nc, T, sem):
    with ExitStack() as ctx:
        def sb(name, shape, dt=f32):
            return ctx.enter_context(nc.sbuf_tensor(name, shape, dt))

        x_hi, x_lo = sb("x_hi", [128, KT, TOK]), sb("x_lo", [128, KT, TOK])
        ident = sb("a_ident", [128, 128])
        w1c = sb("w1c", [128, KT])
        bgc = sb("bgc", [128, 2 * KT])
        eps = sb("a_eps", [128, 1])
        NX = XBC // 128
        conv_w, conv_b = sb("conv_w", [128, NX, CONV]), sb("conv_b", [128, NX])
        dtw = sb("dtw", [128, KT, SH])
        dt_bias, a_log = sb("dt_bias", [SH, 1]), sb("a_log", [SH, 1])
        w_in = T["w_in"][0].rearrange("(k p) n -> p k n", p=128)
        w = sb("w", [128, KT * WCOL])
        s_const, s_eps, s_cw, s_w = sem("a_const"), sem("a_eps"), sem("a_cw"), sem("a_w")

        def tm(w):
            return w.rearrange("p (k n) -> p k n", n=WCOL)

        with ExitStack() as c2:
            x_in = c2.enter_context(nc.sbuf_tensor("x_in", [128, 3, D], f32))
            xn = c2.enter_context(nc.sbuf_tensor("xn", [128, 3, D], f32))
            junk = c2.enter_context(nc.sbuf_tensor("a_junk", [128, D], f32))
            ms = c2.enter_context(nc.sbuf_tensor("a_ms", [128, 3, 2], f32))
            scaled = c2.enter_context(nc.sbuf_tensor("a_scaled", [128, KT, 128], f32))
            upper = c2.enter_context(nc.sbuf_tensor("a_upper", [128, KT, 128], f32))
            turned = c2.enter_context(nc.psum_tensor("a_turned", [128, 3, KT, 128], f32))
            s_x = [sem(f"a_x{u}") for u in range(3)]
            s_std, s_xn, s_turned, s_xfree = sem("a_std"), sem("a_xn"), sem("a_turned"), sem("a_xfree")
            s_tfree = sem("a_tfree")
            with nc.Block() as block:
                @block.sync
                def _(sp):
                    sp.dma_start(ident[:, :], T["ident"]).then_inc(s_const, 16)
                    sp.dma_start(w1c[:, :], T["norm1_w"].rearrange("p a k -> p (a k)")).then_inc(s_const, 16)
                    sp.dma_start(bgc[:, :], T["b_gate"].rearrange("p a k -> p (a k)")).then_inc(s_const, 16)
                    with sp.Fori(0, 3) as j:
                        for u in range(3):
                            sp.wait_ge(s_xfree, j * 3 + u + 1)
                            sp.dma_start(x_in[:, u, :], T["x_all"][ds((j * 3 + u) * 128, 128), :]).then_inc(s_x[u], 16)
                    sp.dma_start(tm(w[:, :]), w_in[:, :, 0:WCOL]).then_inc(s_w, 16)

                @block.gpsimd
                def _(pool):
                    for dst, src in ((dtw[:, :, :], w_in[:, :, DTOFF:DTOFF + SH]), (dt_bias[:, :], T["dt_bias"]),
                                     (conv_w[:, :, :], T["conv_w"]), (conv_b[:, :], T["conv_b"].rearrange("p a k -> p (a k)")),
                                     (a_log[:, :], T["A_log"])):
                        pool.dma_start(dst, src).then_inc(s_cw, 16)

                @block.scalar
                def _(act):
                    act.wait_ge(s_eps, 1)
                    with act.Fori(0, 3) as j:
                        for u in range(3):
                            act.wait_ge(s_x[u], (j + 1) * 16)
                            nc.scalar.activation(junk[:, :], x_in[:, u, :], ACT.Square, accum_out=ms[:, u, 0:1])
                            act.drain()
                            nc.scalar.activation(ms[:, u, 1:2], ms[:, u, 0:1], ACT.Sqrt, bias=eps[:, :],
                                                 scale=1.0 / D).then_inc(s_std, 1)

                @block.vector
                def _(dve):
                    nc.vector.memset(eps[:, :], EPS).then_inc(s_eps, 1)
                    dve.sem_inc(s_xfree, 3)
                    dve.wait_ge(s_const, 48)
                    for n in range(TILES + 1):
                        if n < TILES:
                            u = n % 3
                            dve.wait_ge(s_std, n + 1)
                            nc.vector.reciprocal(ms[:, u, 1:2], ms[:, u, 1:2])
                            dve.drain()
                            nc.vector.tensor_scalar(xn[:, u, :], x_in[:, u, :], ms[:, u, 1:2], None, ALU.mult
                                                    ).then_inc(s_xn, 1)
                            dve.drain()
                            dve.sem_inc(s_xfree, 1)
                        if n > 0:
                            cols, u = slice((n - 1) * 128, n * 128), (n - 1) % 3
                            dve.wait_ge(s_turned, n)
                            for k0 in (0, KT // 2):
                                nc.vector.tensor_tensor(scaled[:, k0:k0 + 4, :], turned[:, u, k0:k0 + 4, :],
                                                        bc(w1c[:, k0:k0 + 4].unsqueeze(2), [128, 4, 128]), ALU.mult)
                            dve.drain()
                            dve.sem_inc(s_tfree, 1)
                            split(nc, dve, scaled[:, :, :], x_hi[:, :, cols], x_lo[:, :, cols], upper[:, :, :])

                @block.tensor
                def _(pe):
                    pe.sem_inc(s_tfree, 3)
                    pe.wait_ge(s_const, 48)
                    with pe.Fori(0, 3) as j:
                        for u in range(3):
                            pe.wait_ge(s_xn, j * 3 + u + 1)
                            pe.wait_ge(s_tfree, j * 3 + u + 1)
                            for k in range(KT):
                                last = nc.tensor.transpose(turned[:, u, k, :], xn[:, u, k * 128:(k + 1) * 128], ident[:, :])
                            last.then_inc(s_turned, 1)

        with ExitStack() as c2:
            def sb2(name, shape):
                return c2.enter_context(nc.sbuf_tensor(name, shape, f32))

            w_lo, w_hi = sb2("w_lo", [128, 2, KT * WCOL]), sb2("w_hi", [128, 2, KT * WCOL])
            upper = sb2("w_upper", [128, KT * WCOL // 2])
            dtw_lo, dtw_hi = sb2("dtw_lo", [128, KT, SH]), sb2("dtw_hi", [128, KT, SH])
            o_tm = sb2("o_tm", [128, 6, WCOL])
            o_gate = sb2("o_gate", [128, 2, TOK])
            bias = sb2("gate_bias", [128, 1])
            xr = sb2("xr", [128, 2, HIST + SEQ])
            xs = sb2("xs", [128, 2, NB, HIST + NT])
            tail = sb2("tail", [128, 2, TAIL])
            sums = sb2("sums", [128, TOK])
            xc = sb2("xc", [128, 2, TOK])
            xt = sb2("xt", [128, 2, TILES, 128])
            tails = sb2("tails", [TAIL, XBC])
            neg_a = sb2("neg_a", [SH, 1])
            dt_cm, da_cm = sb2("dt_cm", [SH, TOK]), sums[0:SH, :]
            acc = [c2.enter_context(nc.psum_tensor(f"a_acc{i}", [128, 512], f32)) for i in range(6)]
            pt = [c2.enter_context(nc.psum_tensor(f"a_pt{i}", [128, 4, 128], f32)) for i in range(2)]
            s_rfree = sem("a_rfree")
            s_dtw, s_split, s_wfree = sem("a_dtw"), sem("a_split"), sem("a_wfree")
            s_acc, s_out, s_zero = sem("a_acc"), sem("a_out"), sem("a_zero")
            s_st = [sem(f"a_st{i}") for i in range(6)]
            s_gst, s_hist, s_cst, s_tst = ([sem(f"a_{n}{i}") for i in range(2)] for n in ("gst", "hist", "cst", "tst"))
            s_stored, s_dt, s_dta, s_dtp = sem("a_stored"), sem("a_dt"), sem("a_dta"), sem("a_dtp")
            s_free, s_xr, s_sums, s_xc, s_pe, s_ev, s_xt = (sem(f"a_{n}") for n in ("free", "xr", "sums", "xc", "pe", "ev", "xt"))
            for s in (*s_st, *s_gst, *s_cst, s_xc):
                nc.sync.sem_inc(s, START)
            chunks = TOK // NCH
            n_tm = XOFF // WCOL
            TM, CM = chunks, chunks + n_tm * TILES

            def cm(w, a):
                return w[:, a * KT * 128:(a + 1) * KT * 128].rearrange("p (k n) -> p k n", n=128)

            def tm_blocks(eng, body):
                with eng.Fori(0, n_tm // 2) as j:
                    for u in range(2):
                        body(j * 2 + u, u, j)
                body(n_tm - 1, 0, n_tm // 2)

            with nc.Block() as block:
                @block.sync
                def _(sp):
                    with sp.Fori(0, n_tm // 2) as j:
                        for u in range(2):
                            n = j * 2 + (u + 1)
                            sp.wait_ge(s_rfree, n + 1)
                            sp.dma_start(tm(w[:, :]), w_in[:, :, ds(n * WCOL, WCOL)]).then_inc(s_w, 16)

                    def load(n, first, second):
                        sp.wait_ge(s_rfree, n + (n_tm + 1))
                        for a, off in enumerate((first, second)):
                            sp.dma_start(cm(w, a), w_in[:, :, ds(off, 128)]).then_inc(s_w, 16)
                    with sp.Fori(0, NX // 2) as j:
                        for u in range(2):
                            n = j * 2 + u
                            load(n, n * 128 + XOFF, n * 128 + GOFF)
                            sp.wait_ge(s_free, n + 1)
                            sp.dma_start(xs[:, u, :, 0:HIST], T["state_conv"][ds(n * 128, 128), :, :]).then_inc(s_hist[u], 16)
                    for u in range(2):
                        load(NX + u, GOFF + (NX + 2 * u) * 128, GOFF + (NX + 2 * u + 1) * 128)

                @block.gpsimd
                def _(pool):
                    nc.gpsimd.memset(xr[:, :, 0:HIST], 0.0).then_inc(s_zero, 1)
                    for b in range(NB):
                        pool.wait_ge(s_split, b + 1)
                        for g, (window, _) in enumerate(GROUPS):
                            old = min(window, PAST)
                            keep = min(window, old + NT) - NT
                            pool.dma_start(T["s_kv"][g][0, b, 0:keep, :, :, :].rearrange("r a h d -> r (a h d)"),
                                           T["cache"][g][0, b, old - keep:old, :, :, :].rearrange("r a h d -> r (a h d)")
                                           ).then_inc(T["s_cache"], 16)
                    with pool.Fori(0, NX // 2) as j:
                        for u in range(2):
                            n = j * 2 + u
                            pool.wait_ge(s_xt, n + 1)
                            pool.dma_start(T["xc_tm"][:, ds(n * 128, 128)].rearrange("(t p) c -> p t c", p=128),
                                           xt[:, u, :, :]).then_inc(s_tst[u], 16)
                            pool.wait_ge(s_tst[u], (j + 1) * 16)
                            pool.sem_inc(s_stored, 1)
                    pool.dma_start(T["p_conv"][0, 0, :, :], tails[0:HIST, :]).then_inc(s_tst[0], 16)
                    pool.dma_start(T["s_conv"][0].rearrange("b r c -> (b r) c"), tails[HIST:, :]).then_inc(s_tst[1], 16)
                    for u in range(2):
                        pool.wait_ge(s_tst[u], (NX // 2 + 1) * 16)

                @block.vector
                def _(dve):
                    dve.sem_inc(s_ev, 1)
                    dve.sem_inc(s_free, 2)
                    dve.sem_inc(s_rfree, 1)
                    dve.sem_inc(s_stored, 2)
                    dve.wait_ge(s_cw, 80)
                    split(nc, dve, dtw[:, :, :], dtw_hi[:, :, :], dtw_lo[:, :, :], upper[:, 0:KT * SH].rearrange("p (k n) -> p k n", n=SH))
                    dve.sem_inc(s_dtw, 1)
                    def split_block(u):
                        for half in range(2):
                            cols = slice(half * KT * WCOL // 2, (half + 1) * KT * WCOL // 2)
                            split(nc, dve, w[:, cols], w_hi[:, u, cols], w_lo[:, u, cols], upper[:, :])
                        dve.sem_inc(s_rfree, 1)
                        dve.sem_inc(s_split, 1)

                    def prepare_tm(n, u):
                        dve.wait_ge(s_w, (n + 1) * 16)
                        dve.wait_ge(s_wfree, n + 1)
                        split_block(u)
                    prepare_tm(0, 0)
                    dve.wait_ge(s_dta, 1)
                    nc.vector.tensor_scalar(dt_cm[:, :], dt_cm[:, :], dt_bias[:, :], None, ALU.add)
                    dve.drain()
                    nc.vector.tensor_scalar(da_cm, dt_cm[:, :], -1.0, None, ALU.mult)
                    dve.drain()
                    nc.vector.tensor_tensor(da_cm, dt_cm[:, :], da_cm, ALU.min).then_inc(s_dt, 1)
                    dve.wait_ge(s_dta, 2)
                    nc.vector.scalar_tensor_tensor(dt_cm[:, :], dt_cm[:, :], 0.0, da_cm, ALU.max, ALU.add)
                    nc.vector.tensor_scalar(neg_a[:, :], a_log[:, :], -1.0, None, ALU.mult)
                    dve.drain()
                    nc.vector.tensor_scalar(da_cm, dt_cm[:, :], neg_a[:, :], None, ALU.mult).then_inc(s_dt, 1)

                    with dve.Fori(0, n_tm // 2) as j:
                        for u in range(2):
                            prepare_tm(j * 2 + (u + 1), 1 - u)
                    dve.wait_ge(s_dtp, 1)
                    for kind, dst in enumerate((T["dt_tm"], T["da_tm"])):
                        nc.vector.tensor_copy(dst[:, :, :], pt[1][:, :, :].rearrange("p a b -> p (a b)")
                                              [:, kind * TILES * SH:(kind + 1) * TILES * SH].rearrange("p (t h) -> p t h", h=SH))
                    dve.drain()
                    dve.sem_inc(s_ev, 1)
                    nc.vector.memset(sums[:, SEQ + SAMP:], 0.0)

                    def prepare(n, u):
                        dve.wait_ge(s_w, n * 32 + (n_tm * 16 + 32))
                        dve.wait_ge(s_wfree, n + (n_tm + 1))
                        split_block((n_tm + u) % 2)
                    prepare(0, 0)
                    dve.wait_ge(s_zero, 1)
                    with dve.Fori(0, NX // 2) as j:
                        for u in range(2):
                            n = j * 2 + u
                            prepare(j * 2 + (u + 1), 1 - u)
                            dve.wait_ge(s_xr, n + 1)
                            dve.wait_ge(s_hist[u], (j + 1) * 16)
                            dve.wait_ge(s_xc, n + START)
                            sample = sums[:, SEQ:SEQ + SAMP].rearrange("p (b t) -> p b t", b=NB)
                            for k in range(CONV):
                                tap = conv_w[:, ds(n, 1), k:k + 1].rearrange("p a k -> p (a k)")
                                for dst, src in ((sums[:, 0:SEQ], xr[:, u, k:k + SEQ]), (sample, xs[:, u, :, k:k + NT])):
                                    if k == 0:
                                        nc.vector.tensor_scalar(dst, src, tap, conv_b[:, ds(n, 1)], ALU.mult, ALU.add)
                                    else:
                                        nc.vector.scalar_tensor_tensor(dst, src, tap, dst, ALU.mult, ALU.add)
                                dve.drain()
                            dve.sem_inc(s_sums, 1)
                            dve.wait_ge(s_stored, n + 1)
                            for f in range(3):
                                p = pt[(u + f) % 2]
                                dve.wait_ge(s_pe, j * 6 + (3 * u + f + 1))
                                if f < 2:
                                    nc.vector.tensor_copy(xt[:, u, 4 * f:4 * f + 4, :], p[:, :, :])
                                else:
                                    nc.vector.tensor_copy(xt[:, u, 8, :], p[:, 0, :])
                                    nc.vector.tensor_copy(tails[:, ds(n * 128, 128)], p[0:TAIL, 1, :])
                                dve.drain()
                                dve.sem_inc(s_ev, 1)
                            dve.sem_inc(s_xt, 1)
                            dve.sem_inc(s_free, 1)
                    prepare(NX + 1, 1)

                @block.scalar
                def _(act):
                    act.sem_inc(s_out, 6)
                    for c in range(chunks):
                        act.wait_ge(s_acc, c + 1)
                        nc.scalar.copy(dt_cm[:, c * NCH:(c + 1) * NCH], acc[c][0:SH, 0:NCH]).then_inc(s_out, 1)
                    act.drain()
                    act.sem_inc(s_dta, 1)
                    act.wait_ge(s_cw, 80)
                    nc.scalar.activation(a_log[:, :], a_log[:, :], ACT.Exp)
                    act.wait_ge(s_dt, 1)
                    nc.scalar.activation(da_cm, da_cm, ACT.Exp)
                    act.drain()
                    nc.scalar.activation(da_cm, da_cm, ACT.Ln, bias=1.0)
                    act.drain()
                    act.sem_inc(s_dta, 1)

                    def take_tm(n, u, j):
                        for m in range(TILES):
                            i = u * TILES + m
                            act.wait_ge(s_acc, j * (2 * TILES) + (TM + i + 1))
                            act.wait_ge(s_st[i % 6], (j * 3 + i // 6) * 16 + START)
                            nc.scalar.copy(o_tm[:, i % 6, :], acc[(TM + i) % 6][:, 0:WCOL]).then_inc(s_out, 1)
                            act.drain()
                            act.dma_start(T["u_tm"][m * 128:(m + 1) * 128, ds(n * WCOL, WCOL)], o_tm[:, i % 6, :]
                                          ).then_inc(s_st[i % 6], 16)
                    tm_blocks(act, take_tm)

                    def gate(block, slot, stored, products, part, cs):
                        if cs[0] == 0:
                            act.wait_ge(s_gst[slot], stored)
                            nc.scalar.copy(bias[:, :], bgc[:, ds(block, 1)])
                            act.drain()
                        for c in cs:
                            act.wait_ge(s_acc, products + (part * chunks + c + 1))
                            nc.scalar.activation(o_gate[:, slot, c * NCH:(c + 1) * NCH], acc[(CM + part * chunks + c) % 6][:, 0:NCH],
                                                 ACT.Sigmoid, bias=bias[:, :]).then_inc(s_out, 1)
                        if cs[-1] == chunks - 1:
                            act.drain()
                            act.dma_start(T["gate_cm"][ds(block * 128, 128), :], o_gate[:, slot, :]).then_inc(s_gst[slot], 16)

                    with act.Fori(0, NX // 2) as j:
                        for u in range(2):
                            n = j * 2 + u
                            before = j * (4 * chunks) + (CM + 2 * chunks * u)
                            act.wait_ge(s_free, n + 1)
                            for c in range(chunks):
                                act.wait_ge(s_acc, j * (4 * chunks) + (CM + 2 * chunks * u + c + 1))
                                src = acc[(CM + c) % 6]
                                m = min(NCH, SEQ - c * NCH)
                                last = nc.scalar.copy(xr[:, u, HIST + c * NCH:HIST + c * NCH + m], src[:, 0:m])
                                if c == chunks - 1:
                                    new = src[:, m:m + SAMP].rearrange("p (b t) -> p b t", b=NB)
                                    nc.scalar.copy(xs[:, u, :, HIST:], new)
                                    nc.scalar.copy(tail[:, u, 0:HIST], src[:, m - HIST:m])
                                    last = nc.scalar.copy(tail[:, u, HIST:].rearrange("p (b t) -> p b t", b=NB), new[:, :, NT - HIST:])
                                last.then_inc(s_out, 1)
                            act.drain()
                            act.sem_inc(s_xr, 1)
                            gate(n, u, j * 16 + START, before, 1, (0, 1))
                            act.wait_ge(s_sums, n + 1)
                            act.wait_ge(s_cst[u], j * 16 + START)
                            nc.scalar.activation(xc[:, u, :], sums[:, :], ACT.Silu)
                            act.drain()
                            act.sem_inc(s_xc, 1)
                            act.dma_start(T["xc_cm"][ds(n * 128, 128), :], xc[:, u, :]).then_inc(s_cst[u], 16)
                            gate(n, u, 0, before, 1, (2,))
                    for i in range(4):
                        gate(NX + i, i % 2, (NX // 2 + i // 2) * 16 + START, CM + (2 * NX + i // 2 * 2) * chunks, i % 2, range(chunks))
                    for i in range(6):
                        act.wait_ge(s_st[i], len(range(i, n_tm * TILES, 6)) * 16 + START)
                    for u in range(2):
                        act.wait_ge(s_gst[u], (NX // 2 + 2) * 16 + START)
                        act.wait_ge(s_cst[u], NX // 2 * 16 + START)

                @block.tensor
                def _(pe):
                    pe.sem_inc(s_wfree, 2)
                    pe.wait_ge(s_dtw, 1)
                    for c in range(chunks):
                        pe.wait_ge(s_out, c + 1)
                        cols = slice(c * NCH, (c + 1) * NCH)
                        product(nc, acc[c][0:SH, 0:NCH], [((dtw_hi[:, k, :], dtw_lo[:, k, :]), (x_hi[:, k, cols], x_lo[:, k, cols]))
                                                          for k in range(KT)]).then_inc(s_acc, 1)

                    def products_tm(n, u, j):
                        hi, lo = tm(w_hi[:, u, :]), tm(w_lo[:, u, :])
                        pe.wait_ge(s_split, n + 1)
                        for m in range(TILES):
                            i = u * TILES + m
                            rows = slice(m * 128, (m + 1) * 128)
                            pe.wait_ge(s_out, j * (2 * TILES) + (TM + i + 1))
                            product(nc, acc[(TM + i) % 6][:, 0:WCOL],
                                    [((x_hi[:, k, rows], x_lo[:, k, rows]), (hi[:, k, :], lo[:, k, :])) for k in range(KT)]
                                    ).then_inc(s_acc, 1)
                        pe.drain()
                        pe.sem_inc(s_wfree, 1)
                    tm_blocks(pe, products_tm)
                    pe.wait_ge(s_dt, 2)
                    for t in range(TILES):
                        for kind, src in ((0, dt_cm[:, :]), (1, da_cm)):
                            off = (kind * TILES + t) * SH
                            last = nc.tensor.transpose(pt[1][:, :, :].rearrange("p a b -> p (a b)")[:, off:off + SH],
                                                       src[:, t * 128:(t + 1) * 128], ident[0:SH, 0:SH])
                    last.then_inc(s_dtp, 1)

                    def block_products(u, before):
                        slot = (n_tm + u) % 2
                        for a in range(2):
                            hi, lo = cm(w_hi[:, slot, :], a), cm(w_lo[:, slot, :], a)
                            for c in range(chunks):
                                cols = slice(c * NCH, (c + 1) * NCH)
                                pe.wait_ge(s_out, before + (a * chunks + c + 1))
                                product(nc, acc[(CM + a * chunks + c) % 6][:, 0:NCH],
                                        [((hi[:, k, :], lo[:, k, :]), (x_hi[:, k, cols], x_lo[:, k, cols])) for k in range(KT)]
                                        ).then_inc(s_acc, 1)
                        pe.drain()
                        pe.sem_inc(s_wfree, 1)
                    with pe.Fori(0, NX // 2) as j:
                        for u in range(2):
                            n = j * 2 + u
                            pe.wait_ge(s_split, n + (n_tm + 1))
                            block_products(u, j * (4 * chunks) + (CM + 2 * chunks * u))
                            pe.wait_ge(s_xc, n + (1 + START))
                            for f in range(3):
                                pe.wait_ge(s_ev, j * 6 + (3 * u + f + 1))
                                p = pt[(u + f) % 2]
                                for t in range(4 * f, min(4 * f + 4, TILES)):
                                    last = nc.tensor.transpose(p[:, t % 4, :], xc[:, u, t * 128:(t + 1) * 128], ident[:, :])
                                if f == 2:
                                    last = nc.tensor.transpose(p[0:TAIL, 1, :], tail[:, u, :], ident[:, :])
                                last.then_inc(s_pe, 1)
                    for u in range(2):
                        pe.wait_ge(s_split, n_tm + NX + u + 1)
                        block_products(u, CM + (2 * NX + 2 * u) * chunks)


def phase_attention_prompt(nc, T, sem):
    with ExitStack() as ctx:
        def sb(name, shape, dt=f32):
            return ctx.enter_context(nc.sbuf_tensor(name, shape, dt))

        def pb(name, shape):
            return ctx.enter_context(nc.psum_tensor(name, shape, f32))

        ident = sb("c_ident", [128, 128])
        rotary = sb("c_rotary", [128, 8, 3, 2 * HD])
        mask_even = sb("mask_even", [128, 4, 256])
        mask_odd = sb("mask_odd", [128, 256])
        mask_half = sb("mask_half", [128, 128])
        qk = sb("c_qk", [128, 2, 3, 2, GW])
        v = sb("c_v", [128, 2, 3, GW])
        rot = sb("c_rot", [128, 2, 3, 2, GW])
        tmp = sb("c_tmp", [128, 3, 2, 2 * HG, HD])
        qT = sb("c_qT", [128, 3, 2, 128])
        kT = sb("c_kT", [128, 3, 2, 2, 128])
        S = sb("c_S", [128, 3, HG, 256])
        P = sb("c_P", [128, 3, HG, 256])
        PT = sb("c_PT", [128, 3, HG, 2, 128])
        mx = sb("c_mx", [128, 3, HG])
        out = sb("c_out", [128, 2, 3, GW + 2 * HG])
        nmx = sb("c_nmx", [128, 3, HG])
        p_qk = pb("c_pqk", [128, 4, 128])
        p_s = [[pb(f"c_ps{s}{i}", [128, 2, 256]) for i in range(2)] for s in range(2)]
        p_t = [pb(f"c_pt{i}", [128, 4, 128]) for i in range(2)]
        p_o = pb("c_po", [128, 512])
        s_const, s_zero = sem("c_const"), sem("c_zero")
        s_in = [[sem(f"c_in{u}{g}") for g in range(3)] for u in range(2)]
        s_v = [[sem(f"c_v{u}{g}") for g in range(3)] for u in range(2)]
        s_free, s_rot, s_qkt, s_qke = sem("c_free"), sem("c_rot"), sem("c_qkt"), sem("c_qke")
        s_sc, s_sce, s_p, s_pt, s_pte, s_o, s_oe = (sem(f"c_{n}") for n in ("sc", "sce", "p", "pt", "pte", "o", "oe"))
        s_nmx, s_masks = sem("c_nmx"), sem("c_masks")
        s_kv = [sem(f"c_kv{u}") for u in range(2)]
        s_st = [sem(f"c_st{u}") for u in range(2)]
        for s in (s_rot, *s_kv, s_qkt, s_p, *s_st, s_pt, s_qke, s_sce, s_oe):
            nc.sync.sem_inc(s, START)
        SC = HD ** -0.5
        def rows(g, j, u):
            if g == 0:
                return [(0, 128, ds((j * 2 + u) * 128, 128))]
            if g == 1:
                return [(0, 128, ds(j + u * 512, 128, step=4))]
            return [(64 * a, 64, ds(j * 4 + (2 * u + a), 64, step=16)) for a in range(2)]

        def tiles(eng, body):
            with eng.Fori(0, 3) as j:
                for u in range(2):
                    body(j * 2 + u, u, j)
            body(6, 0, 3)
            body(7, 1, 3, more=False)

        KV_DMAS = [4, 6]
        with nc.Block() as block:
            @block.sync
            def _(sp):
                for dst, src in ((ident[:, :], T["ident"]), (rotary[:, :, :, :], T["rotary"])):
                    sp.dma_start(dst, src).then_inc(s_const, 16)

                def load_qk(t, u, j):
                    sp.wait_ge(s_rot, t * 3 + START)
                    for g in range(3):
                        for p0, n, r in rows(g, j, u):
                            sp.dma_start(qk[p0:p0 + n, u, g, :, :],
                                         T["u_tm"][r, 0:2 * AW].rearrange("r (a c) -> r a c", a=2)[:, :, g * GW:(g + 1) * GW]
                                         ).then_inc(s_in[u][g], 16)

                def work(t, u, j, more=True):
                    if more:
                        load_qk(t + 1, 1 - u, j + u)
                    sp.wait_ge(s_kv[u], j * (16 * KV_DMAS[u]) + START)
                    sp.wait_ge(s_free, t + 1)
                    for g in range(3):
                        for p0, n, r in rows(g, j, u):
                            c0 = 2 * AW + g * GW
                            sp.dma_start(v[p0:p0 + n, u, g, :], T["u_tm"][r, c0:c0 + GW]).then_inc(s_v[u][g], 16)
                load_qk(0, 0, 0)
                for dst, src in ((mask_even[:, :, :], T["mask_even"]), (mask_odd[:, :], T["mask_odd"]), (mask_half[:, :], T["mask_half"])):
                    sp.dma_start(dst, src).then_inc(s_masks, 16)
                sp.wait_ge(s_zero, 1)
                tiles(sp, work)

            @block.gpsimd
            def _(pool):
                nc.gpsimd.memset(kT[:, :, :, :, :].rearrange("p a b c d -> p (a b c d)"), 0.0)
                nc.gpsimd.memset(v[:, 1, :, :].rearrange("p a b -> p (a b)"), 0.0).then_inc(s_zero, 1)

                def turn(t, u, j, g):
                    pool.wait_ge(s_in[u][g], (j + 1) * (16 if g < 2 else 32))
                    if g == 0:
                        pool.wait_ge(s_qkt, t * 3 + START)
                        pool.wait_ge(s_kv[u], j * (16 * KV_DMAS[u]) + START)
                    x = qk[:, u, g, :, :].rearrange("p a (h c) -> p (a h) c", h=HG)
                    tab = rotary[:, ds(t, 1), g, :].rearrange("p a c -> p (a c)")
                    cos = bc(tab[:, 0:HD].unsqueeze(1), [128, 2 * HG, HD])
                    half = HD // 2
                    for a, b in ((0, half), (half, 0)):
                        sin = bc(tab[:, HD + a:HD + a + half].unsqueeze(1), [128, 2 * HG, half])
                        nc.gpsimd.tensor_tensor(tmp[:, g, 0, :, a:a + half], x[:, :, b:b + half], sin, ALU.mult)
                    nc.gpsimd.tensor_tensor(tmp[:, g, 1, :, :], x, cos, ALU.mult)
                    pool.drain()
                    nc.gpsimd.tensor_tensor(rot[:, u, g, :, :].rearrange("p a (h c) -> p (a h) c", h=HG),
                                            tmp[:, g, 0, :, :], tmp[:, g, 1, :, :], ALU.add).then_inc(s_rot, 1)

                def work(t, u, j, more=True):
                    for g in range(3):
                        turn(t, u, j, g)
                pool.wait_ge(s_const, 32)
                tiles(pool, work)

            @block.vector
            def _(dve):
                dve.wait_ge(s_zero, 1)
                dve.sem_inc(s_sce, 1)
                dve.sem_inc(s_free, 1)
                dve.sem_inc(s_pte, 2)

                def take_qk(t, u, g):
                    dve.wait_ge(s_qkt, t * 3 + (g + 1 + START))
                    nc.vector.tensor_copy(qT[:, g, :, :], p_qk[:, 0:2, :])
                    nc.vector.tensor_copy(kT[:, g, :, u, :], p_qk[:, 2:4, :])
                    dve.drain()
                    dve.sem_inc(s_qke, 1)

                def mask_scores(t, u, j, g):
                    w = 256 if g == 0 or (g == 1 and u == 1) else 128
                    if g == 0 and u == 0:
                        mask = mask_even[:, ds(j, 1), :].rearrange("p a k -> p (a k)")
                    elif g == 2:
                        mask = mask_half[:, :]
                    else:
                        mask = mask_odd[:, :] if u == 1 else mask_even[:, 0, 0:128]
                    if g == 0:
                        dve.wait_ge(s_p, t * 3 + START)
                    dve.wait_ge(s_sc, t * 3 + (g + 1))
                    for h in range(2):
                        nc.vector.tensor_tensor(S[:, g, :, 0:w].rearrange("p (a b) k -> p a b k", b=2)[:, :, h, :],
                                                p_s[(u + g) % 2][h][:, :, 0:w], bc(mask.unsqueeze(1), [128, 2, w]), ALU.add)
                    dve.drain()
                    dve.sem_inc(s_sce, 1)
                    nc.vector.tensor_reduce(mx[:, g, :], S[:, g, :, 0:w], AX.X, ALU.max)
                    dve.drain()
                    nc.vector.tensor_scalar(nmx[:, g, :], mx[:, g, :], -SC, None, ALU.mult).then_inc(s_nmx, 1)

                def take_probs(u, j, g):
                    n = 8 if g == 0 or (g == 1 and u == 1) else 4
                    for i in range(n // 4):
                        k = (0, 2, 3 if u == 0 else 4)[g] + i
                        dve.wait_ge(s_pt, j * 9 + ((0, 4)[u] + k + 1 + START))
                        nc.vector.tensor_copy(PT[:, g, 4 * i // (n // 4):4 * (i + 1) // (n // 4), 0:n // 4, :]
                                              if n == 8 else PT[:, g, :, 0, :],
                                              p_t[((0, 4)[u] + k) % 2][:, :, :].rearrange("p (h w) c -> p h w c", w=2)
                                              if n == 8 else p_t[((0, 4)[u] + k) % 2][:, :, :]
                                              ).then_inc(s_pte, 1)

                def work(t, u, j, more=True):
                    for g in range(3):
                        mask_scores(t, u, j, g)
                    for g in range(3):
                        take_probs(u, j, g)
                        if more:
                            take_qk(t + 1, 1 - u, g)
                for g in range(3):
                    take_qk(0, 0, g)
                dve.wait_ge(s_masks, 48)
                tiles(dve, work)

            @block.scalar
            def _(act):
                with act.Fori(0, 4) as j:
                    for u in range(2):
                        t = j * 2 + u
                        act.wait_ge(s_st[u], j * 64 + START)
                        for g in range(3):
                            w = 256 if g == 0 or (g == 1 and u == 1) else 128
                            act.wait_ge(s_nmx, t * 3 + (g + 1))
                            if g == 0:
                                act.wait_ge(s_pt, j * 9 + (0, 4)[u] + START)
                            for h in range(HG):
                                nc.scalar.activation(P[:, g, h, 0:w], S[:, g, h, 0:w], ACT.Exp, bias=nmx[:, g, h:h + 1],
                                                     scale=SC, accum_out=out[:, u, g, GW + HG + h:GW + HG + h + 1])
                            act.drain()
                            nc.scalar.mul(out[:, u, g, GW:GW + HG], nmx[:, g, :], -1.0).then_inc(s_p, 1)
                        act.wait_ge(s_rot, t * 3 + (3 + START))
                        act.wait_ge(s_v[u][2], (j + 1) * 32)
                        stores = []
                        if u == 1:
                            act.wait_ge(s_v[u][1], (j + 1) * 16)
                            stores.append((T["p_kv"][1], 0, 128, 1, ds(j, 128, step=4)))
                        for p0, n, r in rows(2, j, u):
                            stores.append((T["p_kv"][2], p0, n, 2, r))
                        for dst, p0, n, g, r in stores:
                            view = dst[0, 0].rearrange("r a h c -> r a (h c)")
                            act.dma_start(view[r, 0, :], rot[p0:p0 + n, u, g, 1, :]).then_inc(s_kv[u], 16)
                            act.dma_start(view[r, 1, :], v[p0:p0 + n, u, g, :]).then_inc(s_kv[u], 16)
                        for g in range(3):
                            act.wait_ge(s_o, t * 3 + (g + 1))
                            nc.scalar.copy(out[:, u, g, 0:GW], p_o[:, 0:GW]).then_inc(s_oe, 1)
                            act.drain()
                            for p0, n, r in rows(g, j, u):
                                act.dma_start(T["o_attn"][g, r, :], out[p0:p0 + n, u, g, :]).then_inc(s_st[u], 16)
                view = T["p_kv"][0][0, 0].rearrange("r a h c -> r a (h c)")
                act.dma_start(view[:, 0, :], rot[:, 1, 0, 1, :]).then_inc(s_kv[1], 16)
                act.dma_start(view[:, 1, :], v[:, 1, 0, :]).then_inc(s_kv[1], 16)
                act.wait_ge(s_kv[0], 4 * 16 * KV_DMAS[0] + START)
                act.wait_ge(s_kv[1], 4 * 16 * KV_DMAS[1] + (32 + START))
                act.wait_ge(s_st[0], 4 * 64 + START)
                act.wait_ge(s_st[1], 4 * 64 + START)

            @block.tensor
            def _(pe):
                pe.wait_ge(s_const, 32)
                pe.wait_ge(s_zero, 1)

                def turn_qk(t, u, g):
                    pe.wait_ge(s_rot, t * 3 + (g + 1 + START))
                    pe.wait_ge(s_qke, t * 3 + (g + START))
                    for i in range(4):
                        last = nc.tensor.transpose(p_qk[:, i, :], rot[:, u, g, i // 2, (i % 2) * 128:(i % 2 + 1) * 128], ident[:, :])
                    last.then_inc(s_qkt, 1)

                def scores(t, u, g):
                    wide = g == 0 or (g == 1 and u == 1)
                    pe.wait_ge(s_qke, t * 3 + (g + 1 + START))
                    pe.wait_ge(s_sce, t * 3 + (g + START))
                    for hp in range(2):
                        for h in range(2):
                            q = qT[64 * h:64 * h + 64, g, hp, :]
                            k = (kT[64 * h:64 * h + 64, g, hp, :, :].rearrange("p a b -> p (a b)") if wide
                                 else kT[64 * h:64 * h + 64, g, hp, u, :])
                            last = nc.tensor.matmul(p_s[(u + g) % 2][h][:, hp, 0:256 if wide else 128], q, k, start=True, stop=True)
                    last.then_inc(s_sc, 1)

                def outputs(t, u, j, g, more):
                    wide = g == 0 or (g == 1 and u == 1)
                    n = 8 if wide else 4
                    pe.wait_ge(s_p, t * 3 + (g + 1 + START))
                    for i in range(n // 4):
                        k = (0, 2, 3 if u == 0 else 4)[g] + i
                        first = u == 0 and k == 0
                        pe.wait_ge(s_pte, j * 9 + ((0, 4)[u] + k + 1 + first))
                        for c in range(4):
                            h, w = (2 * i + c // 2, c % 2) if wide else (c, 0)
                            last = nc.tensor.transpose(p_t[((0, 4)[u] + k) % 2][:, c, :],
                                                       P[:, g, h, w * 128:(w + 1) * 128], ident[:, :])
                        last.then_inc(s_pt, 1)
                    if more:
                        turn_qk(t + 1, 1 - u, g)
                    pe.wait_ge(s_pte, j * 9 + ((0, 4)[u] + (0, 2, 3 if u == 0 else 4)[g] + n // 4 + 2))
                    pe.wait_ge(s_oe, t * 3 + (g + START))
                    pe.wait_ge(s_v[u][g], (j + 1) * (16 if g < 2 else 32))
                    slots = (u,) if not wide else ((0, 1))
                    for h in range(HG):
                        for w, slot in enumerate(slots):
                            last = nc.tensor.matmul(p_o[:, h * HD:(h + 1) * HD], PT[:, g, h, w, :],
                                                    v[:, slot, g, h * HD:(h + 1) * HD],
                                                    start=(w == 0), stop=(w == len(slots) - 1))
                    last.then_inc(s_o, 1)

                def work(t, u, j, more=True):
                    for g in range(3):
                        scores(t, u, g)
                    for g in range(3):
                        outputs(t, u, j, g, more)
                    pe.drain()
                    pe.sem_inc(s_free, 1)
                for g in range(3):
                    turn_qk(0, 0, g)
                tiles(pe, work)


def phase_attention_sample(nc, T, sem):
    with ExitStack() as ctx:
        def sb(name, shape, dt=f32):
            return ctx.enter_context(nc.sbuf_tensor(name, shape, dt))

        def pb(name, shape):
            return ctx.enter_context(nc.psum_tensor(name, shape, f32))

        CT = 9
        GT = [(0, 1), (1, 5), (5, 9)]
        ident = sb("d_ident", [128, 128])
        rotary = sb("d_rotary", [128, 2 * HD])
        m_old, m_new = sb("mask_cached", [128, 3, 128]), sb("mask_new", [128, 2, 3, 128])
        new = sb("d_new", [128, 3 * AW])
        rot = sb("d_rot", [128, 2 * AW])
        tmp = sb("d_tmp", [128, 2, 2 * AW // HD, HD])
        kv = sb("d_kv", [128, 3, 2, GW])
        qbd = sb("d_qbd", [128, 3, 2, NB, 2, NT])
        kTn = sb("d_kTn", [128, 3, 2, 128])
        kc = sb("d_kc", [128, 2, CT, GW])
        kT = sb("d_kT", [128, 2, 2 * CT, 128])
        vc = sb("d_vc", [128, NB, CT, GW])
        sT = sb("d_sT", [128, 6, NB * HG * NT])
        S = sb("d_S", [128, 2, 6, 128])
        mx, den = sb("d_mx", [128, 2]), sb("d_den", [128, 2])
        p_st = pb("d_pst", [128, 6, 256])
        p_kt = [pb(f"d_pkt{i}", [128, 3, 128]) for i in range(2)]
        p_r = pb("d_pr", [128, 8, 128])
        p_o = pb("d_po", [128, NB, 2, 2, NT])
        s_const, s_new, s_rot, s_qkt, s_qbd, s_zero = (sem(f"d_{n}") for n in ("const", "new", "rot", "qkt", "qbd", "zero"))
        s_k = [sem(f"d_k{u}") for u in range(2)]
        s_v, s_kfree, s_kt, s_kte, s_st, s_ste = (sem(f"d_{n}") for n in ("v", "kfree", "kt", "kte", "st", "ste"))
        s_r, s_rm, s_p, s_pn, s_pt, s_pte, s_o, s_done, s_kv = (
            sem(f"d_{n}") for n in ("r", "rm", "p", "pn", "pt", "pte", "o", "done", "kv"))
        SC = HD ** -0.5
        G = 6

        def cache_parts(b, a):
            c = [T["cache"][g][0, b, :, a, :, :].rearrange("r h d -> r (h d)") if isinstance(b, int) else
                 T["cache"][g][0, ds(b, 1), :, a, :, :].rearrange("o r h d -> (o r) (h d)") for g in range(3)]
            parts = [((0, 128), (0, 1), c[0].rearrange("(p r) c -> p r c", r=1)),
                     ((0, 128), (1, 5), c[1].rearrange("(p r) c -> p r c", r=4))]
            c2 = c[2].rearrange("(p u a) c -> a p u c", u=8, a=2)
            return parts + [((64 * x, 64 * x + 64), (5, 9), c2[x][:, 0:4, :]) for x in range(2)]

        with nc.Block() as block:
            @block.sync
            def _(sp):
                sp.dma_start(new[:, :], T["u_tm"][SEQ:TOK, 0:3 * AW]).then_inc(s_new, 16)
                for dst, src in ((ident[:, :], T["ident"]), (rotary[:, :], T["rotary_new"]), (m_old[:, :, :], T["mask_cached"]),
                                 (m_new[:, :, :, :], T["mask_new"])):
                    sp.dma_start(dst, src).then_inc(s_const, 16)
                with sp.Fori(0, NB // 2) as j:
                    for u in range(2):
                        b = j * 2 + u
                        sp.wait_ge(s_kfree, j * 2 + (u + 1))
                        for (p0, p1), (c0, c1), src in cache_parts(b, 0):
                            sp.dma_start(kc[p0:p1, u, c0:c1, :], src).then_inc(s_k[u], 16)
                        for (p0, p1), (c0, c1), src in cache_parts(b, 1):
                            sp.dma_start(vc[p0:p1, ds(b, 1), c0:c1, :].rearrange("p o c d -> p (o c) d"), src).then_inc(s_v, 16)

            @block.gpsimd
            def _(pool):
                nc.gpsimd.memset(qbd[:, :, :, :, :, :].rearrange("p a b c d e -> p (a b c d e)"), 0.0)
                nc.gpsimd.memset(T["ya_T"][:, :, SEQ + SAMP:], 0.0).then_inc(s_zero, 1)

            @block.vector
            def _(dve):
                dve.sem_inc(s_kfree, 2)
                dve.wait_ge(s_const, 64)
                dve.wait_ge(s_new, 16)
                x = new[:, 0:2 * AW].rearrange("p (h c) -> p h c", c=HD)
                n, half = 2 * AW // HD, HD // 2
                for a, b in ((0, half), (half, 0)):
                    nc.vector.tensor_tensor(tmp[:, 0, :, a:a + half], x[:, :, b:b + half],
                                            bc(rotary[:, HD + a:HD + a + half].unsqueeze(1), [128, n, half]), ALU.mult)
                nc.vector.tensor_tensor(tmp[:, 1, :, :], x, bc(rotary[:, 0:HD].unsqueeze(1), [128, n, HD]), ALU.mult)
                dve.drain()
                nc.vector.tensor_tensor(rot[:, :].rearrange("p (h c) -> p h c", c=HD), tmp[:, 0, :, :], tmp[:, 1, :, :], ALU.add)
                dve.drain()
                dve.sem_inc(s_rot, 1)
                nc.vector.tensor_copy(kv[:, :, 0, :], rot[:, AW:].rearrange("p (g c) -> p g c", g=3))
                nc.vector.tensor_copy(kv[:, :, 1, :], new[:, 2 * AW:].rearrange("p (g c) -> p g c", g=3))
                dve.drain()
                dve.sem_inc(s_rot, 1)
                dve.wait_ge(s_zero, 1)
                dve.wait_ge(s_qkt, 1)
                pv = p_st[:, :, :].rearrange("p a (b c) -> p (a b) c", c=128)
                for g in range(3):
                    for hh in range(2):
                        r = slice(64 * hh, 64 * hh + 64)
                        for hp in range(2):
                            nc.vector.tensor_copy(qbd[r, g, hp, :, hh, :],
                                                  pv[r, 2 * g + hp, 0:SAMP].rearrange("p (b t) -> p b t", t=NT))
                nc.vector.tensor_copy(kTn[:, :, :, :].rearrange("p a b c -> p (a b) c"), pv[:, 6:12, :])
                dve.drain()
                dve.sem_inc(s_qbd, 1)
                dve.wait_ge(s_st, 1)
                nc.vector.tensor_copy(sT[:, :, :], p_st[:, :, :])
                dve.drain()
                dve.sem_inc(s_ste, 1)
                for half in range(2):
                    dve.wait_ge(s_r, half + 1)
                    nc.vector.tensor_tensor(S[:, half, 0:3, :], p_r[:, 0:3, :], m_old[:, :, :], ALU.add)
                    nc.vector.tensor_tensor(S[:, half, 3:6, :], p_r[:, 3:6, :], m_new[:, half, :, :], ALU.add)
                    dve.drain()
                    dve.sem_inc(s_rm, 1)
                    nc.vector.tensor_reduce(mx[:, half:half + 1], S[:, half, :, :].rearrange("p a k -> p (a k)"), AX.X, ALU.max)
                    dve.drain()
                    nc.vector.tensor_scalar(mx[:, half:half + 1], mx[:, half:half + 1], -SC, None, ALU.mult)
                    dve.drain()
                    dve.sem_inc(s_pn, 1)
                for half in range(2):
                    dve.wait_ge(s_p, half + 1)
                    nc.vector.reciprocal(den[:, half:half + 1], den[:, half:half + 1])
                    dve.drain()
                    nc.vector.tensor_scalar(S[:, half, :, :], S[:, half, :, :], den[:, half:half + 1], None, ALU.mult
                                            ).then_inc(s_pn, 1)
                dve.wait_ge(s_pt, 1)
                nc.vector.tensor_copy(sT[:, :, :], p_st[:, :, :])
                dve.drain()
                dve.sem_inc(s_pte, 1)
                dve.wait_ge(s_o, 1)
                for hh in range(2):
                    r = slice(64 * hh, 64 * hh + 64)
                    for hp in range(2):
                        nc.vector.tensor_copy(T["ya_T"][r, hp, SEQ:SEQ + SAMP].rearrange("p (b t) -> p b t", t=NT),
                                              p_o[r, :, hp, hh, :])
                dve.drain()
                dve.sem_inc(s_done, 1)

            @block.scalar
            def _(act):
                act.wait_ge(s_rot, 2)
                for g, (window, _) in enumerate(GROUPS):
                    end = min(window, PAST + NT)
                    for b in range(NB):
                        act.dma_start(T["s_kv"][g][0, b, end - NT:end, :, :, :].rearrange("r a h d -> r a (h d)"),
                                      kv[b * NT:(b + 1) * NT, g, :, :]).then_inc(s_kv, 16)
                act.sem_inc(s_kte, 2)
                with act.Fori(0, NB // 2) as j:
                    for u in range(2):
                        for q in range(G):
                            n = u * G + q
                            act.wait_ge(s_kt, j * (2 * G) + (n + 1))
                            nc.scalar.copy(kT[:, u, 3 * q:3 * q + 3, :], p_kt[q % 2][:, :, :]).then_inc(s_kte, 1)
                for half in range(2):
                    act.wait_ge(s_pn, half + 1)
                    flat = S[:, half, :, :].rearrange("p a k -> p (a k)")
                    nc.scalar.activation(flat, flat, ACT.Exp, bias=mx[:, half:half + 1], scale=SC,
                                         accum_out=den[:, half:half + 1])
                    act.drain()
                    act.sem_inc(s_p, 1)
                act.wait_ge(s_kv, 16 * 3 * NB)
                act.wait_ge(T["s_cache"], 16 * 3 * NB)
                act.wait_ge(s_done, 1)

            @block.tensor
            def _(pe):
                pe.wait_ge(s_const, 64)
                pe.wait_ge(s_rot, 1)
                pv = p_st[:, :, :].rearrange("p a (b c) -> p (a b) c", c=128)
                for i in range(12):
                    last = nc.tensor.transpose(pv[:, i, :], rot[:, i * 128:(i + 1) * 128], ident[:, :])
                last.then_inc(s_qkt, 1)
                pe.wait_ge(s_qbd, 1)
                for g in range(3):
                    for hp in range(2):
                        out = p_st[:, 3 + g, :].rearrange("p (b h t) -> p b h t", h=HG, t=NT)[:, :, 2 * hp:2 * hp + 2, :]
                        nc.tensor.matmul(out, kTn[:, g, hp, :], qbd[:, g, hp, :, :, :], start=True, stop=True)
                with pe.Fori(0, NB // 2) as j:
                    for u in range(2):
                        b = j * 2 + u
                        pe.wait_ge(s_k[u], (j + 1) * 64)
                        for q in range(G):
                            pe.wait_ge(s_kte, j * (2 * G) + (u * G + q + 1))
                            for i in range(3 * q, 3 * q + 3):
                                last = nc.tensor.transpose(p_kt[q % 2][:, i % 3, :],
                                                           kc[:, u, i // 2, (i % 2) * 128:(i % 2 + 1) * 128], ident[:, :])
                            last.then_inc(s_kt, 1)
                        pe.drain()
                        pe.sem_inc(s_kfree, 1)
                        pe.wait_ge(s_kte, j * (2 * G) + ((u + 1) * G + 2))
                        for g, (c0, c1) in enumerate(GT):
                            for c in range(c0, c1):
                                for hp in range(2):
                                    t = (slice(0, NT), slice(c - c0, NT, 4), slice(2 * (c - c0), 2 * (c - c0) + 2))[g]
                                    out = p_st[:, g, ds(b * (HG * NT) + hp * 2 * NT, 2 * NT)].rearrange(
                                        "p (h t) -> p h t", t=NT)[:, :, t]
                                    q = qbd[:, g, hp, ds(b, 1), :, :].rearrange("p o h t -> p (o h) t")[:, :, t]
                                    last = nc.tensor.matmul(out, kT[:, u, 2 * c + hp, :], q, start=True, stop=True)
                pe.drain()
                pe.sem_inc(s_st, 1)
                pe.wait_ge(s_ste, 1)
                for half in range(2):
                    if half:
                        pe.wait_ge(s_rm, half)
                    for i in range(6):
                        last = nc.tensor.transpose(p_r[:, i, :], sT[:, i, half * 128:(half + 1) * 128], ident[:, :])
                    last.then_inc(s_r, 1)
                pe.wait_ge(s_pn, 4)
                for half in range(2):
                    for i in range(6):
                        last = nc.tensor.transpose(p_st[:, i, half * 128:(half + 1) * 128], S[:, half, i, :], ident[:, :])
                last.then_inc(s_pt, 1)
                pe.wait_ge(s_pte, 1)
                pe.wait_ge(s_v, 16 * 4 * NB)
                for hp in range(2):
                    for g in range(3):
                        c0 = 2 * AW + g * GW + hp * 128
                        probs = sT[:, 3 + g, :].rearrange("p (b h t) -> p b h t", h=HG, t=NT)[:, :, 2 * hp:2 * hp + 2, :]
                        nc.tensor.matmul(p_o[:, :, hp, :, :].rearrange("p b h t -> p b (h t)"), new[:, c0:c0 + 128],
                                         probs.rearrange("p b h t -> p b (h t)"), start=(hp == 0 and g == 0), stop=False,
                                         skip_group_check=True)
                for b in range(NB):
                    for hp in range(2):
                        cols = slice(b * HG * NT + hp * 2 * NT, b * HG * NT + (hp + 1) * 2 * NT)
                        ch = slice(hp * 128, (hp + 1) * 128)
                        work = [(p_o[:, b, hp, :, :], vc[:, b, 0, ch], sT[:, 0, cols])]
                        for g in (1, 2):
                            for c in range(4):
                                t = slice(c, NT, 4) if g == 1 else slice(2 * c, 2 * c + 2)
                                work.append((p_o[:, b, hp, :, t], vc[:, b, GT[g][0] + c, ch],
                                             sT[:, g, cols].rearrange("p (h t) -> p h t", t=NT)[:, :, t]))
                        for i, (out, v, p) in enumerate(work):
                            last = nc.tensor.matmul(out, v, p, start=False, stop=(i == len(work) - 1), skip_group_check=True)
                last.then_inc(s_o, 1)


def phase_ssd(nc, T, sem, sample):
    tag = "f" if sample else "e"
    with ExitStack() as ctx:
        def sb(name, shape, dt=f32):
            return ctx.enter_context(nc.sbuf_tensor(f"{tag}_{name}", shape, dt))

        def pb(name, shape):
            return ctx.enter_context(nc.psum_tensor(f"{tag}_{name}", shape, f32))

        def sm(name):
            return sem(f"{tag}_{name}")

        GH = SH // 2
        pairs = SH // 2
        ident, ident_b = sb("ident", [128, 128]), sb("ident_b", [128, 128], bf16)
        upto, whole = sb("upto", [128, 128]), sb("whole", [128, 128])
        future, future_b = sb("future", [128, 128]), sb("future_b", [128, 128], bf16)
        d_skip = sb("d_skip", [128, SH])
        xb = sb("xb", [128, 2, DI + 2 * SN])
        bct = sb("bct", [128, 2, 4, 128])
        da = sb("da", [128, 2, SH])
        nacs, wexp = sb("nacs", [128, SH]), sb("wexp", [128, SH])
        eacs, wend, cdec = sb("eacs", [128, 2, SH]), sb("wend", [128, SH]), sb("cdec", [128, SH])
        E, M = sb("E", [128, 4, 4, 128]), sb("M", [128, 4, 4, 128])
        xdt, xw, xd = sb("xdt", [128, DI]), sb("xw", [128, DI]), sb("xd", [128, DI])
        y = sb("y", [128, 2, DI])
        p_misc = pb("p_misc", [128, 512])
        p_al = [pb(f"p_al{i}", [128, 4, 128]) for i in range(2)]
        p_yd, p_yo = pb("p_yd", [128, 2, 512]), pb("p_yo", [128, 2, 512])
        p_st = pb("p_st", [128, 512])
        if sample:
            seq_of, seq_cols = sb("seq_of", [128, NB]), sb("seq_cols", [128, NB, 128])
            dax = sb("dax", [128, DI])
            Bm, Cm = sb("Bm", [128, 2, NB, 128]), sb("Cm", [128, 2, NB, 128])
            h0 = T["h0"]
            h0T = sb("h0T", [128, NB, DI])
            dec = sb("dec", [128, pairs, NB])
        else:
            hT = sb("hT", [128, DI])
            hout = sb("hout", [128, pairs, SN])
        consts = [(ident, "ident"), (upto, "upto_seq" if sample else "upto"), (future, "future_seq" if sample else "future"),
                  (d_skip, "d_skip")]
        if sample:
            consts += [(whole, "same_seq"), (seq_of, "seq_of"), (seq_cols, "seq_cols")]
        s_const, s_prep = sm("const"), sm("prep")
        s_in = [sm(f"in{u}") for u in range(2)]
        s_free, s_da, s_misc, s_nacs, s_e, s_al, s_E, s_M = (sm(n) for n in ("free", "da", "misc", "nacs", "e", "al", "E", "M"))
        s_x, s_xd, s_pe, s_st, s_ste, s_h = (sm(n) for n in ("x", "xd", "pe", "st", "ste", "h"))
        s_y, s_ho, s_hp, s_mc = sm("y"), sm("ho"), sm("hp"), sm("mc")
        s_out = [sm(f"out{u}") for u in range(2)]
        s_h0, s_tr, s_tre = sm("h0"), sm("tr"), sm("tre")
        for s in (s_y, *s_out, s_M, s_ste):
            nc.sync.sem_inc(s, START)
        y3 = lambda ap: ap.rearrange("p (h c) -> p h c", c=HD)

        def heads(ap):
            return bc(ap.unsqueeze(2), [128, SH, HD])

        last_pair = SEQ // 128 // 2 - 1

        def chunks(eng, body):
            if sample:
                body(0, 0, 0, more=False)
            else:
                with eng.Fori(0, last_pair) as j:
                    for u in range(2):
                        body(j * 2 + u, u, j)
                body(2 * last_pair, 0, last_pair)
                body(2 * last_pair + 1, 1, last_pair, more=False)

        def rows(n):
            return slice(SEQ, TOK) if sample else ds(n * 128, 128)

        tile_of = (lambda n: slice(TILES - 1, TILES)) if sample else (lambda n: ds(n, 1))
        NQ = 4

        with nc.Block() as block:
            @block.sync
            def _(sp):
                for dst, name in consts:
                    nd = len(dst.shape)
                    sp.dma_start(dst[:, :] if nd == 2 else dst[:, :, :], T[name]).then_inc(s_const, 16)

                def load(n, u, j, more=True):
                    sp.wait_ge(s_free, n + 1)
                    sp.dma_start(xb[:, u, :], T["xc_tm"][rows(n), 0:DI + 2 * SN]).then_inc(s_in[u], 16)
                    sp.dma_start(bct[:, u, :, :], T["xc_cm"][DI:XBC, rows(n)].rearrange("(a p) t -> p a t", p=128)
                                 ).then_inc(s_in[u], 16)
                chunks(sp, load)

            @block.gpsimd
            def _(pool):
                if not sample:
                    nc.gpsimd.memset(whole[:, :], 1.0)
                    nc.gpsimd.memset(hT[:, :], 0.0)
                pool.wait_ge(s_const, 16 * len(consts))
                nc.gpsimd.tensor_copy(ident_b[:, :], ident[:, :])
                nc.gpsimd.tensor_copy(future_b[:, :], future[:, :]).then_inc(s_prep, 1)

                def copy_da(n, u):
                    nc.gpsimd.tensor_copy(da[:, u, :], T["da_tm"][:, tile_of(n), :].rearrange("p a h -> p (a h)")).then_inc(s_da, 1)

                def skip(n, u, j, more=True):
                    pool.wait_ge(s_in[u], (j + 1) * 32)
                    pool.wait_ge(s_y, n + START)
                    nc.gpsimd.tensor_tensor(y3(xd[:, :]), y3(xb[:, u, 0:DI]), heads(d_skip[:, :]), ALU.mult).then_inc(s_xd, 1)
                    if more:
                        copy_da(n + 1, 1 - u)
                copy_da(0, 0)
                if not sample:
                    for b in range(NB):
                        pool.dma_start(T["h0"][:, :, b, :], T["state_ssm"][0, b].rearrange("(j a) c n -> (a c) j n", a=2)
                                       ).then_inc(s_h0, 16)
                chunks(pool, skip)
                if sample:
                    pool.wait_ge(s_hp, 1)
                    for i in range(2 * pairs):
                        p, bs = i // 2, slice(4 * (i % 2), 4 * (i % 2) + 4)
                        hv = h0[:, p, bs, :]
                        nc.gpsimd.tensor_tensor(hv, hv, bc(dec[:, p, bs].unsqueeze(2), [128, 4, SN]), ALU.mult).then_inc(s_h, 1)
                else:
                    pool.wait_ge(s_h0, 16 * NB)

            @block.vector
            def _(dve):
                dve.sem_inc(s_free, 2)
                dve.wait_ge(s_const, 16 * len(consts))
                dve.wait_ge(s_prep, 1)

                def sums(n):
                    dve.wait_ge(s_misc, n + 1)
                    nc.vector.tensor_scalar(nacs[:, :], p_misc[:, 0:SH], -1.0, None, ALU.mult)
                    dve.drain()
                    nc.vector.tensor_tensor(wexp[:, :], p_misc[:, SH:2 * SH], nacs[:, :], ALU.add)
                    dve.drain()
                    dve.sem_inc(s_nacs, 1)

                def work(n, u, j, more=True):
                    dt = T["dt_tm"][:, tile_of(n), :].rearrange("p a h -> p (a h)")
                    dve.wait_ge(s_in[u], (j + 1) * 32)
                    nc.vector.tensor_tensor(y3(xdt[:, :]), y3(xb[:, u, 0:DI]), heads(dt), ALU.mult)
                    dve.drain()
                    if sample:
                        nc.vector.tensor_copy(y3(dax[:, :]), heads(T["da_tm"][:, TILES - 1, :]))
                        for g in range(2):
                            nc.vector.tensor_tensor(Cm[:, g, :, :], bc(bct[:, u, 2 + g, :].unsqueeze(1), [128, NB, 128]),
                                                    seq_cols[:, :, :], ALU.mult)
                            nc.vector.tensor_tensor(Bm[:, g, :, :],
                                                    bc(xb[:, u, DI + g * SN:DI + (g + 1) * SN].unsqueeze(1), [128, NB, 128]),
                                                    bc(seq_of[:, :].unsqueeze(2), [128, NB, 128]), ALU.mult)
                        dve.drain()
                        dve.sem_inc(s_mc, 1)
                    if sample:
                        sums(n)
                    dve.wait_ge(s_e, n + 1)
                    nc.vector.tensor_tensor(y3(xw[:, :]), y3(xdt[:, :]), heads(wend[:, :]), ALU.mult)
                    dve.drain()
                    dve.sem_inc(s_x, 1)
                    for q in range(NQ):
                        dve.wait_ge(s_E, n * NQ + (q + 1))
                        cb = p_misc[:, 128 * (1 + q // 2):128 * (2 + q // 2)]
                        nc.vector.tensor_tensor(M[:, q, :, :], E[:, q, :, :], bc(cb.unsqueeze(1), [128, 4, 128]), ALU.mult
                                                ).then_inc(s_M, 1)
                    if not sample:
                        dve.wait_ge(s_st, n * 2 + 1)
                        for g in range(2):
                            cols = slice(g * 512, (g + 1) * 512)
                            hv = hT[:, cols].rearrange("p (h c) -> p h c", c=HD)
                            nc.vector.tensor_tensor(hv, hv, bc(cdec[:, g * GH:(g + 1) * GH].unsqueeze(2), [128, GH, HD]), ALU.mult)
                            dve.drain()
                            dve.wait_ge(s_st, n * 2 + (g + 1))
                            nc.vector.tensor_tensor(hT[:, cols], hT[:, cols], p_st[:, :], ALU.add)
                            dve.drain()
                            dve.sem_inc(s_ste, 1)
                    if more:
                        sums(n + 1)
                    dve.wait_ge(s_pe, n + 1)
                    dve.wait_ge(s_out[u], j * 16 + START)
                    yv = y[:, u, :]
                    nc.vector.tensor_tensor(y3(yv), p_yo[:, :, :].rearrange("p a (h c) -> p (a h) c", c=HD), heads(eacs[:, u, :]), ALU.mult)
                    dve.drain()
                    nc.vector.tensor_tensor(yv, yv, p_yd[:, :, :].rearrange("p a c -> p (a c)"), ALU.add)
                    dve.drain()
                    dve.wait_ge(s_xd, n + 1)
                    nc.vector.tensor_tensor(yv, yv, xd[:, :], ALU.add)
                    dve.drain()
                    dve.sem_inc(s_y, 1)
                    dve.sem_inc(s_free, 1)
                if not sample:
                    sums(0)
                chunks(dve, work)
                if sample:
                    dve.wait_ge(s_hp, 1)
                    for i in range(2 * pairs):
                        p, half = i // 2, i % 2
                        bs = slice(4 * half, 4 * half + 4)
                        hv = h0[:, p, bs, :]
                        dve.wait_ge(s_h, i + 1)
                        dve.wait_ge(s_st, i + 1)
                        nc.vector.tensor_tensor(hv, hv, p_al[i % 2][:, :, :], ALU.add)
                        dve.drain()
                        dve.sem_inc(s_ste, 1)
                    dve.sem_inc(s_ho, 1)
                else:
                    dve.wait_ge(s_hp, 1)
                    for i in range(2):
                        nc.vector.tensor_copy(hout[:, 4 * i:4 * i + 4, :], p_al[i][:, :, :])
                    dve.drain()
                    dve.sem_inc(s_ho, 1)

            @block.scalar
            def _(act):
                if sample:
                    for i in range(NB * 2):
                        act.wait_ge(s_tr, i + 1)
                        b, half = i // 2, i % 2
                        nc.scalar.copy(h0T[:, b, half * 512:(half + 1) * 512], p_al[i % 2][:, :, :].rearrange("p a c -> p (a c)")
                                       ).then_inc(s_tre, 1)

                def decays(n, u):
                    act.wait_ge(s_nacs, n + 1)
                    nc.scalar.activation(eacs[:, u, :], p_misc[:, 0:SH], ACT.Exp)
                    nc.scalar.activation(wend[:, :], wexp[:, :], ACT.Exp)
                    nc.scalar.activation(cdec[:, :], p_misc[:, SH:2 * SH], ACT.Exp)
                    act.drain()
                    act.sem_inc(s_e, 1)
                    for q in range(NQ):
                        act.wait_ge(s_al, n * NQ + (q + 1))
                        if q == 0:
                            act.wait_ge(s_M, n * NQ + START)
                        for i in range(4):
                            last = nc.scalar.activation(E[:, q, i, :], p_al[q % 2][:, i, :], ACT.Exp,
                                                        bias=nacs[:, 4 * q + i:4 * q + i + 1])
                        last.then_inc(s_E, 1)

                def work(n, u, j, more=True):
                    if more:
                        decays(n + 1, 1 - u)
                    act.wait_ge(s_y, n + (1 + START))
                    act.dma_start(T["y_ssd"][rows(n), :], y[:, u, :]).then_inc(s_out[u], 16)
                decays(0, 0)
                chunks(act, work)
                if sample:
                    act.wait_ge(s_mc, 2)
                    nc.scalar.activation(dec[:, :, :].rearrange("p a b -> p (a b)"), p_misc[:, 384:384 + pairs * NB], ACT.Exp)
                    act.drain()
                    act.sem_inc(s_hp, 1)
                    act.wait_ge(s_ho, 1)
                    for b in range(NB):
                        act.dma_start(T["s_ssm"][0, b].rearrange("(j a) c n -> (a c) j n", a=2), h0[:, :, b, :]
                                      ).then_inc(s_out[1], 16)
                    act.wait_ge(s_out[0], START + 16)
                    act.wait_ge(s_out[1], 16 * NB + START)
                else:
                    act.wait_ge(s_ho, 1)
                    act.dma_start(T["p_ssm"][0, 0].rearrange("(j a) c n -> (a c) j n", a=2), hout[:, :, :]).then_inc(s_out[0], 16)
                    act.wait_ge(s_out[0], 16 * 5 + START)
                    act.wait_ge(s_out[1], 16 * 4 + START)

            @block.tensor
            def _(pe):
                pe.wait_ge(s_const, 16 * len(consts))
                pe.wait_ge(s_prep, 1)
                if sample:
                    for i in range(NB * 2):
                        b, half = i // 2, i % 2
                        if i >= 2:
                            pe.wait_ge(s_tre, i - 1)
                        for k in range(4):
                            last = nc.tensor.transpose(p_al[i % 2][:, k, :], h0[:, half * 4 + k, b, :], ident[:, :])
                        last.then_inc(s_tr, 1)
                    pe.wait_ge(s_tre, NB * 2)

                def work(n, u, j, more=True):
                    pe.wait_ge(s_in[u], (j + 1) * 32)
                    pe.wait_ge(s_da, n + 1)
                    pe.wait_ge(s_M, n * NQ + START)
                    nc.tensor.matmul(p_misc[:, 0:SH], upto[:, :], da[:, u, :], start=True, stop=True)
                    nc.tensor.matmul(p_misc[:, SH:2 * SH], whole[:, :], da[:, u, :], start=True, stop=True)
                    for g in range(2):
                        last = nc.tensor.matmul(p_misc[:, 128 * (1 + g):128 * (2 + g)], bct[:, u, g, :], bct[:, u, 2 + g, :],
                                                start=True, stop=True)
                    last.then_inc(s_misc, 1)
                    for q in range(NQ):
                        if q >= 2:
                            pe.wait_ge(s_E, n * NQ + (q - 1))
                        for i in range(4):
                            h = 4 * q + i
                            nc.tensor.matmul(p_al[q % 2][:, i, :], ident_b[:, :], future_b[:, :], start=True, stop=False)
                            last = nc.tensor.matmul(p_al[q % 2][:, i, :], bc(da[:, u, h:h + 1], [128, 128]), upto[:, :],
                                                    start=False, stop=True)
                        last.then_inc(s_al, 1)
                    pe.wait_ge(s_y, n + START)
                    if sample:
                        pe.wait_ge(s_mc, 1)
                        for g in range(2):
                            for b in range(NB):
                                nc.tensor.matmul(p_yo[:, g, :], Cm[:, g, b, :], h0T[:, b, g * 512:(g + 1) * 512],
                                                 start=(b == 0), stop=(b == NB - 1))
                    else:
                        pe.wait_ge(s_ste, n * 2 + START)
                        for g in range(2):
                            nc.tensor.matmul(p_yo[:, g, :], bct[:, u, 2 + g, :], hT[:, g * 512:(g + 1) * 512], start=True, stop=True)
                        pe.drain()
                        pe.wait_ge(s_x, n + 1)
                        for g in range(2):
                            pe.wait_ge(s_ste, n * 2 + (g + START))
                            nc.tensor.matmul(p_st[:, :], xb[:, u, DI + g * SN:DI + (g + 1) * SN], xw[:, g * 512:(g + 1) * 512],
                                             start=True, stop=True).then_inc(s_st, 1)
                    for h in range(SH):
                        if h % 4 == 0:
                            pe.wait_ge(s_M, n * NQ + (h // 4 + 1 + START))
                        last = nc.tensor.matmul(p_yd[:, h // GH, (h % GH) * HD:(h % GH + 1) * HD], M[:, h // 4, h % 4, :],
                                                xdt[:, h * HD:(h + 1) * HD], start=True, stop=True)
                    last.then_inc(s_pe, 1)
                chunks(pe, work)
                if sample:
                    pe.wait_ge(s_y, START + 1)
                    for p in range(pairs):
                        last = nc.tensor.matmul(p_misc[:, 384 + p * NB:384 + (p + 1) * NB], dax[:, p * 128:(p + 1) * 128],
                                                seq_of[:, :], start=True, stop=True)
                    last.then_inc(s_mc, 1)
                    pe.wait_ge(s_x, 1)
                    pe.wait_ge(s_E, NQ)
                    for i in range(2 * pairs):
                        p, half = i // 2, i % 2
                        if i >= 2:
                            pe.wait_ge(s_ste, i - 1 + START)
                        nc.tensor.matmul(p_al[i % 2][:, :, :], xw[:, p * 128:(p + 1) * 128], Bm[:, p // 4, 4 * half:4 * half + 4, :],
                                         start=True, stop=True).then_inc(s_st, 1)
                else:
                    pe.wait_ge(s_ste, 2 * (SEQ // 128) + START)
                    pe.wait_ge(s_E, NQ * (SEQ // 128))
                    for i in range(pairs):
                        last = nc.tensor.transpose(p_al[i // 4][:, i % 4, :], hT[:, i * 128:(i + 1) * 128], ident[:, :])
                    last.then_inc(s_hp, 1)


def phase_ssd_prompt(nc, T, sem):
    phase_ssd(nc, T, sem, False)


def phase_ssd_sample(nc, T, sem):
    phase_ssd(nc, T, sem, True)


def rows3(j, u):
    return ds((j * 3 + u) * 128, 128)


def phase_branch_inputs(nc, T, sem):
    with ExitStack() as ctx:
        def sb(name, shape, dt=f32):
            return ctx.enter_context(nc.sbuf_tensor(f"g_{name}", shape, dt))

        def sm(name):
            return sem(f"g_{name}")

        ident, nw, eps = sb("ident", [128, 128]), sb("nw", [128, KT]), sb("eps", [128, 1])
        yin, z, junk = sb("yin", [128, 3, DI]), sb("z", [128, 3, DI]), sb("junk", [128, 512])
        ms = sb("ms", [128, 3, 2])
        NP = TILES - 1
        o = sb("o", [128, NP, 3, GW + 2 * HG])
        wt, top = sb("wt", [128, NP, 3, HG]), sb("top", [128, NP, HG])
        scaled, upper = sb("scaled", [128, KT, 128]), sb("upper", [128, KT, 128])
        p_t = ctx.enter_context(nc.psum_tensor("g_pt", [128, 3, KT, 128], f32))
        p_a = ctx.enter_context(nc.psum_tensor("g_pa", [128, 2, 4, 128], f32))
        s_const, s_eps = sm("const"), sm("eps")
        s_in, s_o = [sm(f"in{u}") for u in range(3)], sm("o")
        s_free, s_silu, s_g, s_rms, s_n, s_t, s_top, s_w, s_ys, s_ta, s_ae = (
            sm(n) for n in ("free", "silu", "gg", "rms", "n", "t", "top", "w", "ys", "ta", "ae"))
        with nc.Block() as block:
            @block.sync
            def _(sp):
                sp.dma_start(ident[:, :], T["ident"]).then_inc(s_const, 16)
                sp.dma_start(nw[:, :], T["ssd_norm_w"].rearrange("p a k -> p (a k)")).then_inc(s_const, 16)
                with sp.Fori(0, 3) as j:
                    for u in range(3):
                        sp.wait_ge(s_free, j * 3 + (u + 1))
                        sp.dma_start(yin[:, u, :], T["y_ssd"][rows3(j, u), :]).then_inc(s_in[u], 16)
                        sp.dma_start(z[:, u, :], T["u_tm"][rows3(j, u), ZOFF:XOFF]).then_inc(s_in[u], 16)

            @block.gpsimd
            def _(pool):
                pool.wait_ge(s_silu, 2)
                for g in range(3):
                    pool.dma_start(o[:, :, g, :], T["o_attn"][g].rearrange("(t p) c -> p t c", p=128)).then_inc(s_o, 16)

            @block.vector
            def _(dve):
                def gated(n):
                    dve.wait_ge(s_silu, n + 1)
                    nc.vector.tensor_tensor(yin[:, n % 3, :], yin[:, n % 3, :], z[:, n % 3, :], ALU.mult).then_inc(s_g, 1)

                def normalised(n):
                    u = n % 3
                    dve.wait_ge(s_rms, n + 1)
                    nc.vector.reciprocal(ms[:, u, :], ms[:, u, :])
                    dve.drain()
                    for g in range(2):
                        cols = slice(512 * g, 512 * g + 512)
                        last = nc.vector.tensor_scalar(z[:, u, cols], yin[:, u, cols], ms[:, u, g:g + 1], None, ALU.mult)
                    last.then_inc(s_n, 1)

                def taken(n):
                    cols = slice(n * 128, (n + 1) * 128)
                    dve.wait_ge(s_t, n + 1)
                    for k0 in (0, 4):
                        nc.vector.tensor_tensor(scaled[:, k0:k0 + 4, :], p_t[:, n % 3, k0:k0 + 4, :],
                                                bc(nw[:, k0:k0 + 4].unsqueeze(2), [128, 4, 128]), ALU.mult)
                    dve.drain()
                    split(nc, dve, scaled[:, :, :], T["ys_hi"][:, :, cols], T["ys_lo"][:, :, cols], upper[:, :, :])

                nc.vector.memset(eps[:, :], EPS).then_inc(s_eps, 1)
                dve.wait_ge(s_const, 32)
                for n in range(TILES + 2):
                    if n < TILES:
                        gated(n)
                    if 0 <= n - 1 < TILES:
                        normalised(n - 1)
                    if n >= 2:
                        taken(n - 2)
                dve.wait_ge(s_o, 48)
                mx, den = o[:, :, :, GW:GW + HG], o[:, :, :, GW + HG:]
                nc.vector.tensor_tensor(top[:, :, :], mx[:, :, 0, :], mx[:, :, 1, :], ALU.max)
                dve.drain()
                nc.vector.tensor_tensor(top[:, :, :], top[:, :, :], mx[:, :, 2, :], ALU.max)
                dve.drain()
                nc.vector.tensor_tensor(wt[:, :, :, :], mx, bc(top[:, :, :].unsqueeze(2), [128, NP, 3, HG]), ALU.subtract
                                        ).then_inc(s_top, 1)
                dve.wait_ge(s_w, 1)
                nc.vector.tensor_tensor(den, den, wt[:, :, :, :], ALU.mult)
                dve.drain()
                nc.vector.tensor_tensor(top[:, :, :], den[:, :, 0, :], den[:, :, 1, :], ALU.add)
                dve.drain()
                nc.vector.tensor_tensor(top[:, :, :], top[:, :, :], den[:, :, 2, :], ALU.add)
                dve.drain()
                nc.vector.reciprocal(top[:, :, :], top[:, :, :])
                dve.drain()
                nc.vector.tensor_tensor(wt[:, :, :, :], wt[:, :, :, :], bc(top[:, :, :].unsqueeze(2), [128, NP, 3, HG]), ALU.mult)
                dve.drain()
                for n in range(NP + 1):
                    if n < NP:
                        heads = o[:, n, :, 0:GW].rearrange("p g (h c) -> p g h c", c=HD)
                        nc.vector.tensor_tensor(heads, heads, bc(wt[:, n, :, :].unsqueeze(3), [128, 3, HG, HD]), ALU.mult)
                        dve.drain()
                        for g in (1, 2):
                            nc.vector.tensor_tensor(o[:, n, 0, 0:GW], o[:, n, 0, 0:GW], o[:, n, g, 0:GW], ALU.add)
                            dve.drain()
                        dve.sem_inc(s_ys, 1)
                    if n > 0:
                        cols = slice((n - 1) * 128, n * 128)
                        dve.wait_ge(s_ta, n)
                        nc.vector.tensor_copy(T["ya_T"][:, :, cols], p_a[:, (n - 1) % 2, 0:2, :])
                        dve.drain()
                        dve.sem_inc(s_ae, 1)
                for c in range(3):
                    cols = slice(c * NCH, (c + 1) * NCH)
                    split(nc, dve, T["ya_T"][:, :, cols], T["ya_hi"][:, :, cols], T["ya_lo"][:, :, cols],
                          upper[:, 0:6, :].rearrange("p a b -> p (a b)").rearrange("p (k t) -> p k t", k=2))

            @block.scalar
            def _(act):
                def silu(n):
                    act.wait_ge(s_in[n % 3], (n // 3 + 1) * 32)
                    nc.scalar.activation(z[:, n % 3, :], z[:, n % 3, :], ACT.Silu).then_inc(s_silu, 1)
                act.wait_ge(s_eps, 1)
                silu(0)
                for n in range(TILES):
                    if n + 1 < TILES:
                        silu(n + 1)
                    u = n % 3
                    act.wait_ge(s_g, n + 1)
                    for g in range(2):
                        nc.scalar.activation(junk[:, :], yin[:, u, 512 * g:512 * g + 512], ACT.Square,
                                             accum_out=ms[:, u, g:g + 1])
                        act.drain()
                    nc.scalar.activation(ms[:, u, :], ms[:, u, :], ACT.Sqrt, bias=eps[:, :], scale=1.0 / 512)
                    act.drain()
                    act.sem_inc(s_rms, 1)
                act.wait_ge(s_top, 1)
                nc.scalar.activation(wt[:, :, :, :], wt[:, :, :, :], ACT.Exp)
                act.drain()
                act.sem_inc(s_w, 1)

            @block.tensor
            def _(pe):
                pe.sem_inc(s_free, 3)
                pe.wait_ge(s_const, 32)
                with pe.Fori(0, 3) as j:
                    for u in range(3):
                        pe.wait_ge(s_n, j * 3 + (u + 1))
                        for k in range(KT):
                            nc.tensor.transpose(p_t[:, u, k, :], z[:, u, k * 128:(k + 1) * 128], ident[:, :])
                        pe.drain()
                        pe.sem_inc(s_t, 1)
                        pe.sem_inc(s_free, 1)
                for n in range(NP):
                    pe.wait_ge(s_ys, n + 1)
                    if n >= 2:
                        pe.wait_ge(s_ae, n - 1)
                    for hp in range(2):
                        last = nc.tensor.transpose(p_a[:, n % 2, hp, :], o[:, n, 0, hp * 128:(hp + 1) * 128], ident[:, :])
                    last.then_inc(s_ta, 1)


def phase_merge(nc, T, sem):
    with ExitStack() as ctx:
        def sb(name, shape, dt=f32):
            return ctx.enter_context(nc.sbuf_tensor(f"h_{name}", shape, dt))

        def sm(name):
            return sem(f"h_{name}")

        KA = GW // 128
        w, upper = sb("w", [128, 2, KA + KT, 128]), sb("upper", [128, KA + KT, 128])
        w_hi, w_lo = sb("w_hi", [128, 2, KA + KT, 128]), sb("w_lo", [128, 2, KA + KT, 128])
        sig = sb("sig", [128, 2, 2, TOK])
        zeros = sb("zeros", [128, 512])
        s_zeros, s_unused = sm("zeros"), sm("unused")
        t1 = sb("t1", [128, 2, 3, NCH])
        p_a = ctx.enter_context(nc.psum_tensor("h_pa", [128, 3, 512], f32))
        p_s = ctx.enter_context(nc.psum_tensor("h_ps", [128, 3, 512], f32))
        s_w, s_sig = [sm(f"w{u}") for u in range(2)], [sm(f"sig{u}") for u in range(2)]
        s_wfree, s_sfree, s_mm, s_ev, s_rfree, s_split = (sm(n) for n in ("wfree", "sfree", "mm", "ev", "rfree", "split"))
        gates = T["gate_cm"].rearrange("(g c) t -> c g t", g=2)
        with nc.Block() as block:
            @block.sync
            def _(sp):
                with sp.Fori(0, KT // 2) as j:
                    for u in range(2):
                        cols = ds((j * 2 + u) * 128, 128)
                        sp.wait_ge(s_rfree, j * 2 + (u + 1))
                        sp.dma_start(w[:, u, 0:KA, :], T["w_attn_br"][0].rearrange("(k p) n -> p k n", p=128)[:, :, cols]
                                     ).then_inc(s_w[u], 16)
                        sp.dma_start(w[:, u, KA:, :], T["w_ssd_br"][0].rearrange("(k p) n -> p k n", p=128)[:, :, cols]
                                     ).then_inc(s_w[u], 16)
                        sp.wait_ge(s_sfree, j * 2 + (u + 1))
                        sp.dma_start(sig[:, u, :, :], gates[cols, :, :]).then_inc(s_sig[u], 16)

            @block.gpsimd
            def _(pool):
                nc.gpsimd.memset(zeros[:, :], 0.0).then_inc(s_zeros, 1)
                pool.wait_ge(s_zeros, 1)
                for a in range(D // 512):
                    pool.dma_start(T["o_moe"][NE * 128:, a * 512:(a + 1) * 512].rearrange("(b p) c -> p b c", p=128),
                                   bc(zeros[:, :].unsqueeze(1), [128, NOVF, 512])).then_inc(s_unused, 16)
                pool.wait_ge(s_unused, 16 * (D // 512))

            @block.vector
            def _(dve):
                dve.sem_inc(s_sfree, 2)
                dve.sem_inc(s_rfree, 2)
                dve.sem_inc(s_ev, 3)

                def prepare(n, u, i):
                    dve.wait_ge(s_w[u], (i + 1) * 32)
                    dve.wait_ge(s_wfree, n + 1)
                    split(nc, dve, w[:, u, :, :], w_hi[:, u, :, :], w_lo[:, u, :, :], upper[:, :, :])
                    dve.sem_inc(s_split, 1)
                    dve.sem_inc(s_rfree, 1)

                def merge(n, u, j, more=True):
                    if more:
                        prepare(n + 1, 1 - u, j + u)
                    dve.wait_ge(s_sig[u], (j + 1) * 16)
                    for c in range(3):
                        cols = slice(c * NCH, (c + 1) * NCH)
                        dve.wait_ge(s_mm, j * 6 + (u * 3 + c + 1))
                        nc.vector.tensor_tensor(t1[:, 0, c, :], p_a[:, c, 0:NCH], sig[:, u, 0, cols], ALU.mult)
                        nc.vector.tensor_tensor(t1[:, 1, c, :], p_s[:, c, 0:NCH], sig[:, u, 1, cols], ALU.mult)
                        dve.drain()
                        dve.sem_inc(s_ev, 1)
                        nc.vector.tensor_tensor(T["m_T"][:, ds(n, 1), cols].rearrange("p a t -> p (a t)"),
                                                t1[:, 0, c, :], t1[:, 1, c, :], ALU.add)
                    dve.drain()
                    dve.sem_inc(s_sfree, 1)
                prepare(0, 0, 0)
                with dve.Fori(0, KT // 2 - 1) as j:
                    for u in range(2):
                        merge(j * 2 + u, u, j)
                merge(KT - 2, 0, KT // 2 - 1)
                merge(KT - 1, 1, KT // 2 - 1, more=False)

            @block.tensor
            def _(pe):
                pe.sem_inc(s_wfree, 2)
                with pe.Fori(0, KT // 2) as j:
                    for u in range(2):
                        pe.wait_ge(s_split, j * 2 + (u + 1))
                        for c in range(3):
                            cols = slice(c * NCH, (c + 1) * NCH)
                            pe.wait_ge(s_ev, j * 6 + (u * 3 + c + 1))
                            product(nc, p_a[:, c, 0:NCH], [((w_hi[:, u, k, :], w_lo[:, u, k, :]),
                                                            (T["ya_hi"][:, k, cols], T["ya_lo"][:, k, cols])) for k in range(KA)])
                            product(nc, p_s[:, c, 0:NCH], [((w_hi[:, u, KA + k, :], w_lo[:, u, KA + k, :]),
                                                            (T["ys_hi"][:, k, cols], T["ys_lo"][:, k, cols])) for k in range(KT)]
                                    ).then_inc(s_mm, 1)
                        pe.drain()
                        pe.sem_inc(s_wfree, 1)


def phase_out_router(nc, T, sem):
    with ExitStack() as ctx:
        def sb(name, shape, dt=f32):
            return ctx.enter_context(nc.sbuf_tensor(f"i_{name}", shape, dt))

        def sm(name):
            return sem(f"i_{name}")

        NR = 36
        ident, eps, w2, br = sb("ident", [128, 128]), sb("eps", [128, 1]), sb("w2", [128, D]), sb("br", [128, NR])
        wo, wr = sb("wo", [128, 2, KT, 256]), sb("wr", [128, KT, NR])
        wo_hi, wo_lo = sb("wo_hi", [128, KT, D]), sb("wo_lo", [128, KT, D])
        m_hi, m_lo, upper = sb("m_hi", [128, KT, 2, 128]), sb("m_lo", [128, KT, 2, 128]), sb("upper", [128, KT, 256])
        x, hn, junk, ms = sb("x", [128, 3, D]), sb("hn", [128, 3, D]), sb("junk", [128, D]), sb("ms", [128, 3, 2])
        hnT = sb("hnT", [128, KT, 128])
        p_h = ctx.enter_context(nc.psum_tensor("i_ph", [128, 3, 2, 512], f32))
        p_t = ctx.enter_context(nc.psum_tensor("i_pt", [128, 4, 128], f32))
        p_l = ctx.enter_context(nc.psum_tensor("i_pl", [128, 512], f32))
        s_const, s_wo, s_eps = sm("const"), [sm(f"wo{k}") for k in range(2)], sm("eps")
        s_wsplit, s_m, s_mfree = sm("wsplit"), sm("m"), sm("mfree")
        s_x = [sm(f"x{u}") for u in range(3)]
        s_st, s_hn_st = [sm(f"st{u}") for u in range(3)], [sm(f"hs{u}") for u in range(3)]
        s_mm, s_h, s_rms, s_n, s_t, s_te, s_l, s_le = (sm(n) for n in ("mm", "h", "rms", "n", "t", "te", "l", "le"))
        s_xfree = sm("xfree")
        for s in (*s_st, *s_hn_st, s_te, s_le):
            nc.sync.sem_inc(s, START)
        with nc.Block() as block:
            @block.sync
            def _(sp):
                def load_wo(q):
                    sp.dma_start(wo[:, q % 2, :, :], T["w_out"][0].rearrange("(k p) n -> p k n", p=128)[:, :, 256 * q:256 * q + 256]
                                 ).then_inc(s_wo[q % 2], 16)
                load_wo(0)
                load_wo(1)
                sp.dma_start(ident[:, :], T["ident"]).then_inc(s_const, 16)
                sp.dma_start(w2[:, :], T["norm2_w"].broadcast_to([128, D])).then_inc(s_const, 16)
                sp.dma_start(br[:, :], T["b_router"].broadcast_to([128, NR])).then_inc(s_const, 16)
                sp.dma_start(wr[:, :, :], T["w_router"][0].rearrange("(k p) n -> p k n", p=128)).then_inc(s_const, 16)
                for q in (2, 3):
                    sp.wait_ge(s_wsplit, q - 1)
                    load_wo(q)
                with sp.Fori(0, 3) as j:
                    for u in range(3):
                        if u == 0:
                            sp.wait_ge(s_st[u], j * 16 + START)
                        sp.wait_ge(s_xfree, j * 3 + (u + 1))
                        if u > 0:
                            sp.wait_ge(s_st[u], j * 16 + START)
                        sp.dma_start(x[:, u, :], T["x_all"][rows3(j, u), :]).then_inc(s_x[u], 16)

            @block.vector
            def _(dve):
                nc.vector.memset(eps[:, :], EPS).then_inc(s_eps, 1)
                dve.sem_inc(s_xfree, 3)

                def split_m(t):
                    if t >= 2:
                        dve.wait_ge(s_mfree, t - 1)
                    split(nc, dve, T["m_T"][:, :, t * 128:(t + 1) * 128], m_hi[:, :, t % 2, :], m_lo[:, :, t % 2, :],
                          upper[:, :, 0:128])
                    dve.sem_inc(s_m, 1)
                split_m(0)
                for q in range(4):
                    cols = slice(256 * q, 256 * q + 256)
                    dve.wait_ge(s_wo[q % 2], (q // 2 + 1) * 16)
                    split(nc, dve, wo[:, q % 2, :, :], wo_hi[:, :, cols], wo_lo[:, :, cols], upper[:, :, :])
                    dve.sem_inc(s_wsplit, 1)
                split_m(1)
                dve.wait_ge(s_const, 64)
                for n in range(TILES):
                    u, j = n % 3, n // 3
                    dve.wait_ge(s_x[u], (j + 1) * 16)
                    dve.wait_ge(s_mm, n + 1)
                    nc.vector.tensor_tensor(x[:, u, :], x[:, u, :], p_h[:, u, :, :].rearrange("p a c -> p (a c)"), ALU.add
                                            ).then_inc(s_h, 1)
                    if n + 2 < TILES:
                        split_m(n + 2)
                    dve.wait_ge(s_rms, n + 1)
                    nc.vector.reciprocal(ms[:, u, 1:2], ms[:, u, 1:2])
                    dve.drain()
                    dve.wait_ge(s_hn_st[u], j * 16 + START)
                    nc.vector.scalar_tensor_tensor(hn[:, u, :], x[:, u, :], ms[:, u, 1:2], w2[:, :], ALU.mult, ALU.mult
                                                   ).then_inc(s_n, 1)
                    dve.drain()
                    dve.sem_inc(s_xfree, 1)
                    dve.wait_ge(s_l, n + 1)
                    nc.vector.tensor_tensor(T["logits"][:, n, 0:NR], p_l[:, 0:NR], br[:, :], ALU.add)
                    dve.drain()
                    dve.sem_inc(s_le, 1)

            @block.scalar
            def _(act):
                act.wait_ge(s_eps, 1)
                with act.Fori(0, 3) as j:
                    for u in range(3):
                        n = j * 3 + u
                        act.wait_ge(s_h, n + 1)
                        act.dma_start(T["h"][rows3(j, u), :], x[:, u, :]).then_inc(s_st[u], 16)
                        nc.scalar.activation(junk[:, :], x[:, u, :], ACT.Square, accum_out=ms[:, u, 0:1])
                        act.drain()
                        nc.scalar.activation(ms[:, u, 1:2], ms[:, u, 0:1], ACT.Sqrt, bias=eps[:, :], scale=1.0 / D)
                        act.drain()
                        act.sem_inc(s_rms, 1)
                        act.wait_ge(s_n, n + 1)
                        act.dma_start(T["hn"][rows3(j, u), :], hn[:, u, :]).then_inc(s_hn_st[u], 16)
                        for half in range(2):
                            act.wait_ge(s_t, j * 6 + (2 * u + half + 1))
                            nc.scalar.copy(hnT[:, 4 * half:4 * half + 4, :], p_t[:, :, :]).then_inc(s_te, 1)
                for u in range(3):
                    act.wait_ge(s_st[u], START + 48)
                    act.wait_ge(s_hn_st[u], START + 48)

            @block.tensor
            def _(pe):
                def route(t):
                    pe.wait_ge(s_n, t + 1)
                    for half in range(2):
                        pe.wait_ge(s_te, 2 * t + half + START)
                        for k in range(4):
                            c = (4 * half + k) * 128
                            last = nc.tensor.transpose(p_t[:, k, :], hn[:, t % 3, c:c + 128], ident[:, :])
                        last.then_inc(s_t, 1)
                    pe.wait_ge(s_te, 2 * t + (2 + START))
                    pe.wait_ge(s_le, t + START)
                    for k in range(KT):
                        last = nc.tensor.matmul(p_l[:, 0:NR], hnT[:, k, :], wr[:, k, :], start=(k == 0), stop=(k == KT - 1))
                    last.then_inc(s_l, 1)

                pe.wait_ge(s_const, 64)
                for t in range(TILES):
                    if t >= 3:
                        pe.wait_ge(s_h, t - 2)
                    pe.wait_ge(s_m, t + 1)
                    for c in range(2):
                        if t == 0:
                            pe.wait_ge(s_wsplit, 2 * c + 2)
                        cols = slice(512 * c, 512 * c + 512)
                        last = product(nc, p_h[:, t % 3, c, :], [((m_hi[:, k, t % 2, :], m_lo[:, k, t % 2, :]),
                                                                  (wo_hi[:, k, cols], wo_lo[:, k, cols])) for k in range(KT)])
                    last.then_inc(s_mm, 1)
                    pe.drain()
                    pe.sem_inc(s_mfree, 1)
                    if t >= 1:
                        route(t - 1)
                route(TILES - 1)


def phase_route(nc, T, sem):
    with ExitStack() as ctx:
        def sb(name, shape, dt=f32):
            return ctx.enter_context(nc.sbuf_tensor(f"j_{name}", shape, dt))

        def sm(name):
            return sem(f"j_{name}")

        before, upto, ones = sb("before", [128, 128]), sb("upto", [128, 128]), sb("ones", [128, 128])
        experts, group_of, first = sb("experts", [128, NE]), sb("group_of", [128, NE]), sb("first", [128, NE])
        beyond, fills, row_id = sb("beyond", [128, NE]), sb("fills", [128, 8]), sb("row_id", [128, 1])
        tokens = sb("tokens", [128, TILES], i32)
        e4, lf = sb("e4", [128, TILES, 4]), sb("lf", [128, TILES, NE])
        t32, O = sb("t32", [128, TILES, NE]), sb("O", [128, 3, TILES, NE])
        C = sb("C", [128, TILES + 1, NE])
        top = sb("top", [128, 8, TILES])
        S, far = sb("S", [128, TILES, NE]), sb("far", [128, NE])
        slotf, ovf = sb("slotf", [128, 2, TILES]), sb("ovf", [128, 2, NE])
        col, coli = sb("col", [128, 4]), sb("coli", [128, 2], i32)
        p_pos = ctx.enter_context(nc.psum_tensor("j_pos", [128, TILES, NE], f32))
        p_s = ctx.enter_context(nc.psum_tensor("j_s", [128, 512], f32))
        consts = [(before, "before"), (upto, "upto"), (experts, "experts"), (group_of, "group_of"), (first, "first_wins"),
                  (beyond, "beyond"), (fills, "fills"), (row_id, "row_id"), (tokens, "tokens")]
        s_const, s_zero, s_v, s_a, s_ones, s_C, s_pos, s_cnt, s_nb, s_ovf, s_slot, s_sc, s_tab = (
            sm(n) for n in ("const", "zero", "v", "a", "ones", "C", "pos", "cnt", "nb", "ovf", "slot", "sc", "tab"))
        s_w = sm("w")
        L = T["logits"]
        lc = L[:, :, 0:4]

        def over(ap, n):
            return bc(ap.unsqueeze(2), [128, TILES, n])

        def rows(ap, n):
            return bc(ap.unsqueeze(1), [128, TILES, n])

        with nc.Block() as block:
            @block.sync
            def _(sp):
                sp.dma_start(T["ids"].rearrange("(p b) a -> p (b a)", p=128), T["zero_ids"]).then_inc(s_zero, 16)
                for dst, name in consts:
                    sp.dma_start(dst[:, :], T[name]).then_inc(s_const, 16)
                W = T["expert_weights"]
                for e in range(2):
                    for slot, src in ((W.gate, "w_expert_gate"), (W.up, "w_expert_up"), (W.down, "w_expert_down")):
                        sp.dma_start(slot[:, e, :, :], T[src][0, e].rearrange("(k p) n -> p k n", p=128)).then_inc(s_w, 16)
                sp.wait_ge(s_ovf, 1)
                sp.dma_start(T["ovf"][:, 0:NOVF].rearrange("a k -> k a"), coli[0:NOVF, 0:1]).then_inc(s_tab, 16)
                sp.dma_start(T["ovf"][:, NOVF:NOVF + 1], coli[0:1, 1:2]).then_inc(s_tab, 16)
                sp.wait_ge(s_tab, 32)
                sp.wait_ge(s_w, 96)

            @block.gpsimd
            def _(pool):
                nc.gpsimd.memset(ones[:, :], 1.0).then_inc(s_ones, 1)
                pool.wait_ge(s_zero, 16)
                pool.wait_ge(s_const, 16 * len(consts))
                pool.wait_ge(s_slot, 1)
                for t in range(TILES):
                    n = 128 if t < TILES - 1 else SAMP
                    for k in range(2):
                        pool.indirect_dma_start(
                            out=T["ids"], out_offset=bass.IndirectOffsetOnAxis(ap=T["slots"][0:n, t, k:k + 1], axis=0),
                            in_=tokens[0:n, t:t + 1], in_offset=None).then_inc(s_sc, 16)
                pool.wait_ge(s_sc, 32 * TILES)

            @block.scalar
            def _(act):
                act.wait_ge(s_v, 1)
                nc.scalar.activation(e4[:, :, :], e4[:, :, :], ACT.Exp).then_inc(s_a, 1)
                act.wait_ge(s_v, 2)
                nc.scalar.activation(top[:, 4, :], top[:, 4, :], ACT.Exp).then_inc(s_a, 1)

            @block.vector
            def _(dve):
                def tt(out, a, b, op):
                    nc.vector.tensor_tensor(out, a, b, op)
                    dve.drain()

                def ts(out, a, s1, op0, s2=None, op1=ALU.bypass):
                    nc.vector.tensor_scalar(out, a, s1, s2, op0, op1)
                    dve.drain()

                def red(out, a, op):
                    nc.vector.tensor_reduce(out, a, AX.X, op)
                    dve.drain()

                def choose(values, width, k):
                    red(top[:, k, :], values, ALU.max)
                    tt(t32[:, :, 0:width], values, over(top[:, k, :], width), ALU.is_equal)
                    tt(t32[:, :, 0:width], t32[:, :, 0:width], rows(first[:, 0:width], width), ALU.mult)
                    red(top[:, 6, :], t32[:, :, 0:width], ALU.max)
                    ts(top[:, 6, :], top[:, 6, :], -1.0, ALU.mult, float(NE), ALU.add)

                dve.wait_ge(s_const, 16 * len(consts))
                choose(lc, 4, 0)
                tt(e4[:, :, :], lc, over(top[:, 0, :], 4), ALU.subtract)
                dve.sem_inc(s_v, 1)
                tt(t32[:, :, :], rows(group_of[:, :], NE), over(top[:, 6, :], NE), ALU.not_equal)
                nc.vector.scalar_tensor_tensor(lf[:, :, :], t32[:, :, :], NEG, L[:, :, 4:4 + NE], ALU.mult, ALU.add)
                dve.drain()
                for k in range(2):
                    choose(lf[:, :, :], NE, 2 + k)
                    tt(O[:, k, :, :], rows(experts[:, :], NE), over(top[:, 6, :], NE), ALU.is_equal)
                    if k == 0:
                        nc.vector.scalar_tensor_tensor(lf[:, :, :], O[:, 0, :, :], NEG, lf[:, :, :], ALU.mult, ALU.add)
                        dve.drain()
                tt(top[:, 4, :], top[:, 3, :], top[:, 2, :], ALU.subtract)
                dve.sem_inc(s_v, 1)
                nc.vector.memset(O[SAMP:128, 0, TILES - 1, :], 0.0)
                nc.vector.memset(O[SAMP:128, 1, TILES - 1, :], 0.0)
                dve.drain()
                tt(O[:, 2, :, :], O[:, 0, :, :], O[:, 1, :, :], ALU.add)
                nc.vector.memset(C[:, 0, :], 0.0)
                dve.drain()
                for t in range(TILES):
                    tt(C[:, t + 1, :], C[:, t, :], O[:, 2, t, :], ALU.add)
                dve.sem_inc(s_C, 1)
                dve.wait_ge(s_a, 2)
                red(top[:, 1, :], e4[:, :, :], ALU.add)
                nc.vector.reciprocal(top[:, 1, :], top[:, 1, :])
                ts(top[:, 5, :], top[:, 4, :], 1.0, ALU.add)
                nc.vector.reciprocal(top[:, 5, :], top[:, 5, :])
                dve.drain()
                tt(top[:, 5, :], top[:, 5, :], top[:, 1, :], ALU.mult)
                tt(top[:, 4, :], top[:, 4, :], top[:, 5, :], ALU.mult)
                nc.vector.tensor_copy(T["gates"][:, :, 0], top[:, 5, :])
                nc.vector.tensor_copy(T["gates"][:, :, 1], top[:, 4, :])
                dve.wait_ge(s_cnt, 1)
                nc.vector.tensor_copy(col[0:NE, 0:1], p_s[0:NE, 0:1])
                dve.drain()
                ts(t32[0:NE, 0, 0:8], fills[0:NE, :], col[0:NE, 0:1], ALU.is_lt)
                red(col[0:NE, 1:2], t32[0:NE, 0, 0:8], ALU.add)
                dve.sem_inc(s_nb, 1)
                dve.wait_ge(s_nb, 2)
                nc.vector.tensor_copy(ovf[:, :, :], p_s[:, 64:128].rearrange("p (a e) -> p a e", a=2))
                dve.drain()
                ts(t32[:, 0, :], ovf[:, 1, :], row_id[:, :], ALU.is_le)
                red(col[:, 2:3], t32[:, 0, :], ALU.add)
                ts(col[:, 2:3], col[:, 2:3], float(NE - 1), ALU.min)
                nc.vector.tensor_copy(coli[:, 0:1], col[:, 2:3])
                nc.vector.tensor_copy(coli[:, 1:2], ovf[:, 1, NE - 1:NE])
                dve.drain()
                dve.sem_inc(s_ovf, 1)
                tt(far[:, :], ovf[:, 0, :], beyond[:, :], ALU.add)
                ts(far[:, :], far[:, :], 128.0, ALU.mult)
                dve.wait_ge(s_pos, 1)
                ts(S[:, :, :], p_pos[:, :, :], 128.0, ALU.is_ge)
                tt(S[:, :, :], S[:, :, :], rows(far[:, :], NE), ALU.mult)
                tt(S[:, :, :], S[:, :, :], p_pos[:, :, :], ALU.add)
                nc.vector.scalar_tensor_tensor(S[:, :, :], rows(experts[:, :], NE), 128.0, S[:, :, :], ALU.mult, ALU.add)
                dve.drain()
                for k in range(2):
                    tt(t32[:, :, :], O[:, k, :, :], S[:, :, :], ALU.mult)
                    red(slotf[:, k, :], t32[:, :, :], ALU.add)
                    nc.vector.tensor_copy(T["slots"][:, :, k], slotf[:, k, :])
                dve.drain()
                dve.sem_inc(s_slot, 1)

            @block.tensor
            def _(pe):
                pe.wait_ge(s_const, 16 * len(consts))
                pe.wait_ge(s_ones, 1)
                pe.wait_ge(s_C, 1)
                nc.tensor.matmul(p_s[0:NE, 0:1], C[:, TILES, :], ones[:, 0:1], start=True, stop=True).then_inc(s_cnt, 1)
                for t in range(TILES):
                    nc.tensor.matmul(p_pos[:, t, :], ones[:, :], C[:, t, :], start=True, stop=False)
                    last = nc.tensor.matmul(p_pos[:, t, :], before[:, :], O[:, 2, t, :], start=False, stop=True)
                last.then_inc(s_pos, 1)
                pe.wait_ge(s_nb, 1)
                nb = bc(col[0:NE, 1:2], [NE, 128])
                nc.tensor.matmul(p_s[:, 64:96], nb, before[0:NE, 0:NE], start=True, stop=True)
                nc.tensor.matmul(p_s[:, 96:128], nb, upto[0:NE, 0:NE], start=True, stop=True).then_inc(s_nb, 1)


class ExpertWeights:

    def __init__(self, nc, ctx, tag, n):
        self.gate = ctx.enter_context(nc.sbuf_tensor(f"{tag}_wg", [128, n, KT, FF], f32))
        self.up = ctx.enter_context(nc.sbuf_tensor(f"{tag}_wu", [128, n, KT, FF], f32))
        self.down = ctx.enter_context(nc.sbuf_tensor(f"{tag}_wd", [128, n, FF // 128, D], f32))


class ExpertBuffers:

    def __init__(self, nc, ctx, tag, n, weights):
        def sb(name, shape, dt=f32):
            return ctx.enter_context(nc.sbuf_tensor(f"{tag}_{name}", shape, dt))

        def pb(name, shape):
            return ctx.enter_context(nc.psum_tensor(f"{tag}_{name}", shape, f32))
        self.ident = sb("ident", [128, 128])
        self.ids = sb("ids", [128, n], i32)
        self.rows = sb("rows", [128, n, D])
        self.wg, self.wu, self.wd = weights.gate, weights.up, weights.down
        self.xT = sb("xT", [128, KT, 128])
        self.act, self.hid = sb("act", [128, FF]), sb("hid", [128, FF])
        self.hT = sb("hT", [128, FF // 128, 128])
        self.out = sb("out", [128, n, D])
        self.p_x = pb("px", [128, KT, 128])
        self.p_g, self.p_u = pb("pg", [128, FF]), pb("pu", [128, FF])
        self.p_h = pb("ph", [128, FF // 128, 128])
        self.p_o = pb("po", [128, 2, 512])


def phase_experts(nc, T, sem):
    with ExitStack() as ctx:
        B = ExpertBuffers(nc, ctx, "k", 2, T["expert_weights"])
        N = NE // 2

        def sm(name):
            return sem(f"k_{name}")

        s_seen = sm("seen")
        s_const = sm("const")
        s_id, s_row, s_wg, s_wd, s_out = ([sm(f"{n}{u}") for u in range(2)] for n in ("id", "row", "wgu", "wd", "out"))
        s_wgf, s_wdf, s_xt, s_xe, s_gu, s_silu, s_hid, s_ht, s_hte, s_down, s_oe = (
            sm(n) for n in ("wgf", "wdf", "xt", "xe", "gu", "silu", "hid", "ht", "hte", "down", "oe"))
        for s in (s_hid, *s_out, s_hte, s_oe):
            nc.sync.sem_inc(s, START)
        wg_v = T["w_expert_gate"][0].rearrange("e (k p) f -> p e k f", p=128)
        wu_v = T["w_expert_up"][0].rearrange("e (k p) f -> p e k f", p=128)
        wd_v = T["w_expert_down"][0].rearrange("e (k p) n -> p e k n", p=128)

        def one(ap):
            return ap.rearrange("p e k f -> p (e k) f")

        def pairs(eng, body, count):
            with eng.Fori(0, count) as j:
                for u in range(2):
                    body(j * 2 + u, u, j)

        def rows(n):
            return slice(n * 128, n * 128 + 128) if isinstance(n, int) else ds(n * 128, 128)

        with nc.Block() as block:
            @block.sync
            def _(sp):
                sp.dma_start(B.ident[:, :], T["ident"]).then_inc(s_const, 16)
                for u in range(2):
                    sp.sem_inc(s_wg[u], 32)
                    sp.sem_inc(s_wd[u], 16)
                with sp.Fori(0, N - 1) as j:
                    for u in range(2):
                        e = ds(j * 2 + (u + 2), 1)
                        sp.wait_ge(s_wgf, j * 2 + (u + 1))
                        sp.dma_start(B.wg[:, u, :, :], one(wg_v[:, e, :, :])).then_inc(s_wg[u], 16)
                        sp.dma_start(B.wu[:, u, :, :], one(wu_v[:, e, :, :])).then_inc(s_wg[u], 16)
                        sp.wait_ge(s_wdf, j * 2 + (u + 1))
                        sp.dma_start(B.wd[:, u, :, :], one(wd_v[:, e, :, :])).then_inc(s_wd[u], 16)

            @block.gpsimd
            def _(pool):
                def fetch(n, u, i):
                    pool.wait_ge(s_xt, n + 1)
                    pool.dma_start(B.ids[:, u:u + 1], T["ids"][rows(n), :]).then_inc(s_id[u], 16)
                    pool.wait_ge(s_id[u], (i + 1) * 16)
                    pool.sem_inc(s_seen, 1)
                    pool.indirect_dma_start(out=B.rows[:, u, :], out_offset=None, in_=T["hn"],
                                            in_offset=bass.IndirectOffsetOnAxis(ap=B.ids[:, u:u + 1], axis=0)
                                            ).then_inc(s_row[u], 16)
                with pool.Fori(0, N) as j:
                    for u in range(2):
                        fetch(j * 2 + u, u, j)
                fetch(NE, 0, N)

            @block.vector
            def _(dve):
                def work(n, u, j):
                    dve.wait_ge(s_silu, n + 1)
                    nc.vector.tensor_tensor(B.hid[:, :], B.act[:, :], B.p_u[:, :], ALU.mult).then_inc(s_hid, 1)
                    dve.wait_ge(s_xt, n + 4)
                    nc.vector.tensor_copy(B.xT[:, 0:KT, :], B.p_x[:, :, :]).then_inc(s_xe, 1)
                    dve.wait_ge(s_ht, n + 1)
                    nc.vector.tensor_copy(B.hT[:, :, :], B.p_h[:, :, :]).then_inc(s_hte, 1)
                dve.wait_ge(s_xt, 3)
                nc.vector.tensor_copy(B.xT[:, :, :], B.p_x[:, :, :]).then_inc(s_xe, 1)
                pairs(dve, work, N)

            @block.scalar
            def _(act):
                def work(n, u, j):
                    act.wait_ge(s_down, n + 1)
                    act.wait_ge(s_out[u], j * 16 + START)
                    nc.scalar.copy(B.out[:, u, :], B.p_o[:, :, :].rearrange("p a c -> p (a c)")).then_inc(s_oe, 1)
                    act.drain()
                    act.dma_start(T["o_moe"][rows(n), :], B.out[:, u, :]).then_inc(s_out[u], 16)

                def gate(n):
                    act.wait_ge(s_gu, n + 1)
                    act.wait_ge(s_hid, n + START)
                    nc.scalar.activation(B.act[:, :], B.p_g[:, :], ACT.Silu).then_inc(s_silu, 1)

                def both(n, u, j):
                    gate(n + 1)
                    work(n, u, j)
                gate(0)
                pairs(act, both, N - 1)
                both(NE - 2, 0, N - 1)
                work(NE - 1, 1, N - 1)
                for u in range(2):
                    act.wait_ge(s_out[u], N * 16 + START)

            @block.tensor
            def _(pe):
                pe.sem_inc(s_xt, 2)
                pe.wait_ge(s_const, 16)

                def turn(n, u, i):
                    pe.wait_ge(s_row[u], (i + 1) * 16)
                    for k in range(KT):
                        last = nc.tensor.transpose(B.p_x[:, k, :], B.rows[:, u, k * 128:(k + 1) * 128], B.ident[:, :])
                    last.then_inc(s_xt, 1)

                def gate_up(n, u, i):
                    pe.wait_ge(s_wg[u], (i + 1) * 32)
                    pe.wait_ge(s_xe, n + 1)
                    for p, w in ((B.p_g, B.wg), (B.p_u, B.wu)):
                        for k in range(KT):
                            last = nc.tensor.matmul(p[:, :], B.xT[:, k, :], w[:, u, k, :], start=(k == 0), stop=(k == KT - 1))
                    last.then_inc(s_gu, 1)
                    pe.drain()
                    pe.sem_inc(s_wgf, 1)

                def down(n, u, i):
                    pe.wait_ge(s_hte, n + (1 + START))
                    pe.wait_ge(s_wd[u], (i + 1) * 16)
                    pe.wait_ge(s_oe, n + START)
                    for c in range(2):
                        for k in range(FF // 128):
                            last = nc.tensor.matmul(B.p_o[:, c, :], B.hT[:, k, :], B.wd[:, u, k, 512 * c:512 * c + 512],
                                                    start=(k == 0), stop=(k == FF // 128 - 1))
                    last.then_inc(s_down, 1)
                    pe.drain()
                    pe.sem_inc(s_wdf, 1)

                def work(n, u, j, more=True):
                    turn(n + 1, 1 - u, j + u)
                    pe.wait_ge(s_hid, n + (1 + START))
                    pe.wait_ge(s_hte, n + START)
                    for k in range(FF // 128):
                        last = nc.tensor.transpose(B.p_h[:, k, :], B.hid[:, k * 128:(k + 1) * 128], B.ident[:, :])
                    last.then_inc(s_ht, 1)
                    if more:
                        gate_up(n + 1, 1 - u, j + u)
                    down(n, u, j)
                turn(0, 0, 0)
                gate_up(0, 0, 0)
                pairs(pe, work, N - 1)
                work(NE - 2, 0, N - 1)
                work(NE - 1, 1, N - 1, more=False)


def phase_overflow(nc, T, sem):
    with ExitStack() as ctx:
        B = ExpertBuffers(nc, ctx, "l", 1, ExpertWeights(nc, ctx, "l", 1))
        table = ctx.enter_context(nc.sbuf_tensor("l_table", [1, NOVF + 1], i32))

        def sm(name):
            return sem(f"l_{name}")

        s_seen = sm("seen")
        s_h = sm("h")
        s_tab, s_id, s_row, s_w, s_xt, s_xe, s_gu, s_silu, s_hid, s_ht, s_hte, s_down, s_out, s_done = (
            sm(n) for n in ("tab", "id", "row", "w", "xt", "xe", "gu", "silu", "hid", "ht", "hte", "down", "out", "done"))
        for s in (s_done,):
            nc.sync.sem_inc(s, START)
        wg_v = T["w_expert_gate"][0].rearrange("e (k p) f -> p e k f", p=128)
        wu_v = T["w_expert_up"][0].rearrange("e (k p) f -> p e k f", p=128)
        wd_v = T["w_expert_down"][0].rearrange("e (k p) n -> p e k n", p=128)

        def one(ap):
            return ap.rearrange("p e k f -> p (e k) f")

        def blocks(eng, body):
            eng.wait_ge(s_tab, 32)
            count = eng.value_load(table[0:1, NOVF:NOVF + 1], min_val=0, max_val=NOVF)
            with eng.If(0 < count):
                with eng.Fori(0, NOVF) as k:
                    with eng.If(k < count):
                        body(k)

        with nc.Block() as block:
            @block.sync
            def _(sp):
                sp.dma_start(table[:, :], T["ovf"][:, 0:NOVF + 1]).then_inc(s_tab, 16)
                sp.dma_start(B.ident[:, :], T["ident"]).then_inc(s_tab, 16)

                def body(k):
                    e = ds(sp.value_load(table[0:1, ds(k, 1)], min_val=0, max_val=NE - 1), 1)
                    sp.wait_ge(s_done, k + START)
                    sp.dma_start(B.wg[:, 0, :, :], one(wg_v[:, e, :, :])).then_inc(s_w, 16)
                    sp.dma_start(B.wu[:, 0, :, :], one(wu_v[:, e, :, :])).then_inc(s_w, 16)
                    sp.dma_start(B.wd[:, 0, :, :], one(wd_v[:, e, :, :])).then_inc(s_w, 16)
                for half in range(2):
                    sp.dma_start(T["h_rows"][:, :, half * D // 2:(half + 1) * D // 2],
                                 T["h"].rearrange("(t p) c -> p t c", p=128)[:, :, half * D // 2:(half + 1) * D // 2]
                                 ).then_inc(s_h, 16)
                blocks(sp, body)
                sp.wait_ge(s_h, 32)

            @block.gpsimd
            def _(pool):
                def body(k):
                    pool.wait_ge(s_done, k + START)
                    pool.dma_start(B.ids[:, 0:1], T["ids"][ds(k * 128 + NE * 128, 128), :]).then_inc(s_id, 16)
                    pool.wait_ge(s_id, (k + 1) * 16)
                    pool.sem_inc(s_seen, 1)
                    pool.indirect_dma_start(out=B.rows[:, 0, :], out_offset=None, in_=T["hn"],
                                            in_offset=bass.IndirectOffsetOnAxis(ap=B.ids[:, 0:1], axis=0)).then_inc(s_row, 16)
                blocks(pool, body)

            @block.vector
            def _(dve):
                def body(k):
                    dve.wait_ge(s_xt, k + 1)
                    nc.vector.tensor_copy(B.xT[:, :, :], B.p_x[:, :, :]).then_inc(s_xe, 1)
                    dve.wait_ge(s_silu, k + 1)
                    nc.vector.tensor_tensor(B.hid[:, :], B.act[:, :], B.p_u[:, :], ALU.mult).then_inc(s_hid, 1)
                    dve.wait_ge(s_ht, k + 1)
                    nc.vector.tensor_copy(B.hT[:, :, :], B.p_h[:, :, :]).then_inc(s_hte, 1)
                blocks(dve, body)

            @block.scalar
            def _(act):
                def body(k):
                    act.wait_ge(s_gu, k + 1)
                    nc.scalar.activation(B.act[:, :], B.p_g[:, :], ACT.Silu).then_inc(s_silu, 1)
                    act.wait_ge(s_down, k + 1)
                    nc.scalar.copy(B.out[:, 0, :], B.p_o[:, :, :].rearrange("p a c -> p (a c)"))
                    act.drain()
                    act.dma_start(T["o_moe"][ds(k * 128 + NE * 128, 128), :], B.out[:, 0, :]).then_inc(s_out, 16)
                    act.wait_ge(s_out, (k + 1) * 16)
                    act.sem_inc(s_done, 1)
                blocks(act, body)

            @block.tensor
            def _(pe):
                def body(k):
                    pe.wait_ge(s_row, (k + 1) * 16)
                    for c in range(KT):
                        last = nc.tensor.transpose(B.p_x[:, c, :], B.rows[:, 0, c * 128:(c + 1) * 128], B.ident[:, :])
                    last.then_inc(s_xt, 1)
                    pe.wait_ge(s_xe, k + 1)
                    pe.wait_ge(s_w, (k + 1) * 48)
                    for p, w in ((B.p_g, B.wg), (B.p_u, B.wu)):
                        for c in range(KT):
                            last = nc.tensor.matmul(p[:, :], B.xT[:, c, :], w[:, 0, c, :], start=(c == 0), stop=(c == KT - 1))
                    last.then_inc(s_gu, 1)
                    pe.wait_ge(s_hid, k + 1)
                    for c in range(FF // 128):
                        last = nc.tensor.transpose(B.p_h[:, c, :], B.hid[:, c * 128:(c + 1) * 128], B.ident[:, :])
                    last.then_inc(s_ht, 1)
                    pe.wait_ge(s_hte, k + 1)
                    for h in range(2):
                        for c in range(FF // 128):
                            last = nc.tensor.matmul(B.p_o[:, h, :], B.hT[:, c, :], B.wd[:, 0, c, 512 * h:512 * h + 512],
                                                    start=(c == 0), stop=(c == FF // 128 - 1))
                    last.then_inc(s_down, 1)
                blocks(pe, body)


def phase_combine(nc, T, sem):
    with ExitStack() as ctx:
        def sb(name, shape, dt=f32):
            return ctx.enter_context(nc.sbuf_tensor(f"m_{name}", shape, dt))

        def sm(name):
            return sem(f"m_{name}")

        w, eps, junk, ms = sb("w", [128, D]), sb("eps", [128, 1]), sb("junk", [128, D]), sb("ms", [128, 3, 2])
        h = T["h_rows"]
        o, y = sb("o", [128, 3, 2, D]), sb("y", [128, 3, D])
        idx = sb("idx", [128, 3, 2], i32)
        s_seen = sm("seen")
        s_w, s_eps, s_idx = sm("w"), sm("eps"), sm("idx")
        s_o, s_st = ([sm(f"{n}{u}") for u in range(3)] for n in ("o", "st"))
        s_free, s_sum, s_rms, s_y = sm("free"), sm("sum"), sm("rms"), sm("y")

        with nc.Block() as block:
            @block.sync
            def _(sp):
                sp.dma_start(w[:, :], T["final_norm_w"].broadcast_to([128, D])).then_inc(s_w, 16)

            @block.gpsimd
            def _(pool):
                with pool.Fori(0, 3) as j:
                    for u in range(3):
                        pool.wait_ge(s_free, j * 3 + (u + 1))
                        nc.gpsimd.tensor_copy(idx[:, u, :], T["slots"][:, ds(j * 3 + u, 1), :].rearrange("p a k -> p (a k)")
                                              ).then_inc(s_idx, 1)
                        pool.wait_ge(s_idx, j * 3 + (u + 1))
                        pool.sem_inc(s_seen, 1)
                        for k in range(2):
                            pool.indirect_dma_start(out=o[:, u, k, :], out_offset=None, in_=T["o_moe"],
                                                    in_offset=bass.IndirectOffsetOnAxis(ap=idx[:, u, k:k + 1], axis=0)
                                                    ).then_inc(s_o[u], 16)

            @block.vector
            def _(dve):
                nc.vector.memset(eps[:, :], EPS).then_inc(s_eps, 1)
                dve.sem_inc(s_free, 3)
                dve.wait_ge(s_w, 16)

                def summed(n):
                    u = n % 3
                    dve.wait_ge(s_o[u], (n // 3 + 1) * 32)
                    for k in range(2):
                        nc.vector.scalar_tensor_tensor(h[:, n, :], o[:, u, k, :], T["gates"][:, n, k:k + 1], h[:, n, :],
                                                       ALU.mult, ALU.add)
                        dve.drain()
                    dve.sem_inc(s_sum, 1)
                    dve.sem_inc(s_free, 1)

                def normalised(n):
                    u = n % 3
                    dve.wait_ge(s_rms, n + 1)
                    nc.vector.reciprocal(ms[:, u, 1:2], ms[:, u, 1:2])
                    dve.drain()
                    if n >= 3:
                        dve.wait_ge(s_st[u], n // 3 * 16)
                    nc.vector.scalar_tensor_tensor(y[:, u, :], h[:, n, :], ms[:, u, 1:2], w[:, :], ALU.mult, ALU.mult)
                    dve.drain()
                    dve.sem_inc(s_y, 1)
                for n in range(TILES + 1):
                    if n < TILES:
                        summed(n)
                    if n > 0:
                        normalised(n - 1)

            @block.scalar
            def _(act):
                act.wait_ge(s_eps, 1)

                def squares(n):
                    u = n % 3
                    act.wait_ge(s_sum, n + 1)
                    nc.scalar.activation(junk[:, :], h[:, n, :], ACT.Square, accum_out=ms[:, u, 0:1])
                    act.drain()
                    nc.scalar.activation(ms[:, u, 1:2], ms[:, u, 0:1], ACT.Sqrt, bias=eps[:, :], scale=1.0 / D)
                    act.drain()
                    act.sem_inc(s_rms, 1)
                squares(0)
                for n in range(TILES):
                    if n + 1 < TILES:
                        squares(n + 1)
                    act.wait_ge(s_y, n + 1)
                    act.dma_start(T["y"][n * 128:(n + 1) * 128, :], y[:, n % 3, :]).then_inc(s_st[n % 3], 16)
                for u in range(3):
                    act.wait_ge(s_st[u], 48)




def output_shapes():
    keeps = [min(w, SEQ) for w, _ in GROUPS]
    news = [min(w, PAST + NT) for w, _ in GROUPS]
    return ([("y", (TOK, D))]
            + [(f"p_kv{g}", (1, 1, k, 2, HG, HD)) for g, k in enumerate(keeps)]
            + [("p_conv", (1, 1, CONV - 1, XBC)), ("p_ssm", (1, 1, SH, HD, SN))]
            + [(f"s_kv{g}", (1, NB, k, 2, HG, HD)) for g, k in enumerate(news)]
            + [("s_conv", (1, NB, CONV - 1, XBC)), ("s_ssm", (1, NB, SH, HD, SN))])


def build_program(nc, T):
    with ExitStack() as ctx:
        used = []

        def sem(name):
            used.append(nc.alloc_semaphore(name=name))
            return used[-1]

        def scratch(name, shape, dt=f32):
            T[name] = nc.dram_tensor(f"scratch_{name}", shape, dt, kind="Internal").ap()

        scratch("u_tm", (TOK, XOFF))
        scratch("gate_cm", (2 * D, TOK))
        scratch("xc_tm", (TOK, XBC))
        scratch("xc_cm", (XBC, TOK))
        scratch("o_attn", (3, SEQ, GW + 8))
        scratch("y_ssd", (TOK, D))
        scratch("h", (TOK, D))
        scratch("hn", (TOK, D))
        scratch("ids", (NBLK * 128, 1), i32)
        scratch("o_moe", (NBLK * 128, D))
        scratch("ovf", (1, 32), i32)
        T["p_kv"] = [T[f"p_kv{g}"] for g in range(3)]
        T["s_kv"] = [T[f"s_kv{g}"] for g in range(3)]
        T["cache"] = [T["cache_kv_w128"], T["cache_kv_w512"], T["cache_kv_w2048"]]
        T["s_cache"] = ctx.enter_context(nc.semaphore("cache_moved"))

        def keep(name, shape, dt=f32):
            T[name] = ctx.enter_context(nc.sbuf_tensor(name, shape, dt))

        keep("logits", [128, TILES, 40])
        keep("slots", [128, TILES, 2], i32)
        keep("gates", [128, TILES, 2])
        keep("dt_tm", [128, TILES, SH])
        keep("da_tm", [128, TILES, SH])

        @contextmanager
        def living(*tensors):
            with ExitStack() as own:
                for name, shape in tensors:
                    T[name] = own.enter_context(nc.sbuf_tensor(name, shape, f32))
                yield

        def run(*steps):
            for phase in steps:
                phase(nc, T, sem)
                nc.clear_and_free_semaphores(used)
                used.clear()
                nc.all_engine_barrier()

        run(phase_norm_project)
        with living(("ya_T", [128, 2, TOK])):
            run(phase_attention_prompt, phase_attention_sample)
            with living(("h0", [128, SH // 2, NB, SN])):
                run(phase_ssd_prompt, phase_ssd_sample)
            with living(("m_T", [128, KT, TOK])):
                with living(*((f"{n}_{part}", [128, k, TOK]) for n, k in (("ys", KT), ("ya", 2)) for part in ("hi", "lo"))):
                    run(phase_branch_inputs, phase_merge)
                run(phase_out_router)
        with ExitStack() as own:
            T["expert_weights"] = ExpertWeights(nc, own, "k", 2)
            run(phase_route, phase_experts)
        with living(("h_rows", [128, TILES, D])):
            run(phase_overflow, phase_combine)




_DATA = ["norm1_w", "w_in", "w_attn_br", "w_ssd_br", "b_gate", "w_out", "conv_w", "conv_b", "dt_bias", "A_log", "D_skip",
         "ssd_norm_w", "norm2_w", "b_router_coarse", "b_router_fine", "w_expert_gate", "w_expert_up", "w_expert_down",
         "final_norm_w", "cache_kv_w128", "cache_kv_w512", "cache_kv_w2048", "state_conv", "state_ssm",
         "w_router_coarse", "w_router_fine"]


def shape_constants():
    f = np.float32
    i, j = np.arange(128)[:, None], np.arange(128)[None, :]
    c = {"ident": np.eye(128, dtype=f)}
    c["upto"] = (i <= j).astype(f)
    c["before"] = (i < j).astype(f)
    same = i // NT == j // NT
    c["upto_seq"] = ((i <= j) & same).astype(f)
    c["future"] = np.where(i <= j, 0.0, NEG).astype(f)
    c["future_seq"] = np.where((i <= j) & same, 0.0, NEG).astype(f)
    c["seq_of"] = (i // NT == np.arange(NB)[None, :]).astype(f)
    c["same_seq"] = same.astype(f)
    c["seq_cols"] = np.broadcast_to(np.arange(NB)[:, None] == np.arange(128)[None, :] // NT, (128, NB, 128)).astype(f)
    prev = np.where(j >= i, 0.0, NEG).astype(f)
    cur = np.where(j <= i, 0.0, NEG).astype(f)
    none = np.full((128, 128), NEG, f)
    first = np.stack([np.concatenate([cur, prev if n else none], 1) for n in range(4)], 1)
    c["mask_even"] = np.ascontiguousarray(first)
    c["mask_odd"] = np.concatenate([prev, cur], 1)
    c["mask_half"] = np.where((j <= i) & (i // 64 == j // 64), 0.0, NEG).astype(f)
    inv = (np.float32(10000.0) ** (-np.arange(HD // 2, dtype=f) * f(2.0 / HD))).astype(f)

    def rotary(pos):
        ang = (pos.astype(f)[..., None] * inv).astype(f)
        cs, sn = np.cos(ang), np.sin(ang)
        return np.concatenate([cs, cs, -sn, sn], -1).astype(f)
    p = np.arange(128)
    order = np.zeros((3, 8, 128), np.int64)
    for t in range(8):
        order[0, t] = t * 128 + p
        order[1, t] = t // 2 + 4 * ((t % 2) * 128 + p)
        order[2, t] = 2 * t + p // 64 + 16 * (p % 64)
    c["rotary"] = np.ascontiguousarray(rotary(order).transpose(2, 1, 0, 3))
    c["rotary_new"] = rotary(PAST + p % NT)
    t = (np.arange(128) % NT)[:, None]
    old = np.zeros((128, 3, 128), f)
    old[:, 0] = np.where(j >= t, 0.0, NEG)
    old[:, 1] = np.where(4 * j + t % 4 >= t, 0.0, NEG)
    old[:, 2] = np.where(j // 64 == t % 2, 0.0, NEG)
    c["mask_cached"] = old
    new = np.full((128, 2, 3, 128), NEG, f)
    row, key = np.arange(128)[:, None], np.arange(128)[None, :]
    for half in range(2):
        seq, tt = half * 4 + row // 32, row % NT
        ks, kt = key // NT, key % NT
        for g, ok in enumerate((kt <= tt, (kt == tt) | (kt == tt - 4), kt == tt)):
            new[:, half, g] = np.where((seq == ks) & ok & (key < SAMP), 0.0, NEG)
    c["mask_new"] = new
    c["experts"] = np.broadcast_to(np.arange(NE, dtype=f), (128, NE)).copy()
    c["group_of"] = np.broadcast_to(np.arange(NE, dtype=f) // 8, (128, NE)).copy()
    c["tokens"] = (np.arange(TILES)[None, :] * 128 + np.arange(128)[:, None]).astype(np.int32)
    c["first_wins"] = np.broadcast_to(NE - np.arange(NE, dtype=f), (128, NE)).copy()
    c["beyond"] = np.broadcast_to((NE - 1 - np.arange(NE, dtype=f)), (128, NE)).copy()
    c["fills"] = np.broadcast_to(128.0 * np.arange(1, 9, dtype=f), (128, 8)).copy()
    c["row_id"] = np.arange(128, dtype=f)[:, None].copy()
    c["zero_ids"] = np.zeros((128, NBLK), np.int32)
    return c


def kernel(**inputs):
    import numpy as _np
    import concourse.bacc as _bacc
    from concourse import mybir as _mybir
    from concourse.bass_utils import run_bass_kernel_spmd as _run

    nc = _bacc.Bacc("TRN2", target_bir_lowering=False, num_devices=1)
    x_p, x_s = _np.asarray(inputs["x_prompt"]), _np.asarray(inputs["x_sample"])
    arrays = {"x_all": _np.concatenate([x_p.reshape(SEQ, D), x_s.reshape(SAMP, D),
                                        _np.zeros((TOK - SEQ - SAMP, D), x_p.dtype)])}
    for name in _DATA:
        arrays[name] = _np.asarray(inputs[name])
    arrays["state_conv"] = _np.ascontiguousarray(arrays["state_conv"][0].transpose(2, 0, 1))
    for name in ("norm1_w", "b_gate", "ssd_norm_w", "conv_w", "conv_b"):
        a = arrays[name].reshape(-1, arrays[name].shape[-1] // 128, 128)
        arrays[name] = a.transpose(2, 1, 0) if name == "conv_w" else a.transpose(2, 0, 1)
    arrays["dt_bias"], arrays["A_log"] = arrays["dt_bias"].reshape(SH, 1), arrays["A_log"].reshape(SH, 1)
    arrays["d_skip"] = _np.broadcast_to(arrays.pop("D_skip").reshape(1, SH), (128, SH))
    arrays["b_router"] = _np.concatenate([arrays.pop("b_router_coarse"), arrays.pop("b_router_fine")], -1)
    arrays["w_router"] = _np.concatenate([arrays.pop("w_router_coarse"), arrays.pop("w_router_fine")], -1)
    arrays["final_norm_w"] = arrays["final_norm_w"].reshape(1, D)
    arrays = {f"in_{n}": _np.ascontiguousarray(a) for n, a in arrays.items()}
    arrays.update({f"const_{n}": a for n, a in shape_constants().items()})
    T = {}
    for name, a in arrays.items():
        kind = "ExternalInput"
        T[name.split("_", 1)[1]] = nc.dram_tensor(name, a.shape, _mybir.dt.from_np(a.dtype), kind=kind).ap()
    outs = output_shapes()
    for name, shape in outs:
        T[name] = nc.dram_tensor(f"out_{name}", shape, _mybir.dt.float32, kind="ExternalOutput").ap()
    build_program(nc, T)
    r = _run(nc, [arrays], core_ids=[0])
    got = [_np.asarray(r.results[0][f"out_{name}"]) for name, _ in outs]
    y = got[0]
    return (y[:SEQ].reshape(1, SEQ, D), y[SEQ:SEQ + SAMP].reshape(NB, NT, D), *got[1:])
```
